# Optimizing a Trainium2 kernel written in Bass

```python
import math
import jax, jax.numpy as jnp
from jax import lax
import numpy as np

D_MODEL = 1024
BATCH = 1
SEQ = 512
DEPTH = 2

CHUNK = 64
N_EVEN = (DEPTH + 1) // 2
N_ODD = DEPTH // 2
EPS = 1e-6

POOL_WIDTH = D_MODEL // 2
POOL_WINDOWS = (2, 4, 8, 16)
POOL_N_GROUPS = len(POOL_WINDOWS)
POOL_GROUP = POOL_WIDTH // POOL_N_GROUPS
ATT_HEAD_DIM = 64
ATT_HEADS = (D_MODEL // 2) // ATT_HEAD_DIM
ATT_WIDTH = ATT_HEADS * ATT_HEAD_DIM
ATT_PREV_CHUNKS = 8
REL_CLIP = 256
MIX_IN = POOL_WIDTH + 3 * ATT_WIDTH
MIX_OUT = POOL_WIDTH + ATT_WIDTH

SSM_EXPAND = 2
SSM_D_INNER = SSM_EXPAND * D_MODEL
SSM_HEAD_DIM = 64
SSM_HEADS = SSM_D_INNER // SSM_HEAD_DIM
SSM_GROUPS = 8
SSM_HEADS_PER_GROUP = SSM_HEADS // SSM_GROUPS
SSM_D_STATE = 128
SSM_D_CONV = 4
SSM_CONV_DIM = SSM_D_INNER + 2 * SSM_GROUPS * SSM_D_STATE
SSM_IN = SSM_D_INNER + SSM_CONV_DIM + SSM_HEADS
DT_MIN = 0.001
DT_MAX = 0.1

MOE_GROUPS = 4
MOE_EXPERTS_PER_GROUP = 8
MOE_EXPERTS = MOE_GROUPS * MOE_EXPERTS_PER_GROUP
MOE_TOP_K = 2
MOE_D_FF = D_MODEL // 8


def rmsnorm(x, w):
    xf = x.astype(jnp.float32)
    y = xf * lax.rsqrt(jnp.mean(xf * xf, axis=-1, keepdims=True) + EPS)
    return (y * w.astype(jnp.float32)).astype(x.dtype)

def modulate(h, shift, scale):
    return h * (1 + scale[:, None, :]) + shift[:, None, :]

def pool_mixer(u, pool_w, pool_scale):
    b, s, _ = u.shape
    uf = u.astype(jnp.float32)
    cs = jnp.pad(jnp.cumsum(uf, axis=1), ((0, 0), (1, 0), (0, 0)))
    pos = jnp.arange(1, s + 1, dtype=jnp.float32)
    outs = []
    for g, w in enumerate(POOL_WINDOWS):
        lo, hi = g * POOL_GROUP, (g + 1) * POOL_GROUP
        upper = cs[:, 1:, lo:hi]
        lower = jnp.pad(cs[:, :s + 1 - w, lo:hi], ((0, 0), (w - 1, 0), (0, 0)))
        count = jnp.minimum(pos, w)[None, :, None]
        outs.append((upper - lower) / count - uf[:, :, lo:hi])
    pooled = jnp.stack(outs, axis=2).astype(u.dtype)
    y = jnp.einsum('bsgc,gcd->bsgd', pooled, pool_w).reshape(b, s, POOL_WIDTH)
    return y * pool_scale

def chunk_attention(q, k, v, rel_bias):
    b, s, _ = q.shape
    nc = s // CHUNK
    band = (ATT_PREV_CHUNKS + 1) * CHUNK
    q = q.reshape(b, nc, CHUNK, ATT_HEADS, ATT_HEAD_DIM)
    k = k.reshape(b, nc, CHUNK, ATT_HEADS, ATT_HEAD_DIM)
    v = v.reshape(b, nc, CHUNK, ATT_HEADS, ATT_HEAD_DIM)
    pad = ((0, 0), (ATT_PREV_CHUNKS, 0), (0, 0), (0, 0), (0, 0))
    kp = jnp.pad(k, pad)
    vp = jnp.pad(v, pad)
    k_band = jnp.concatenate([kp[:, j:j + nc] for j in range(ATT_PREV_CHUNKS + 1)], axis=2)
    v_band = jnp.concatenate([vp[:, j:j + nc] for j in range(ATT_PREV_CHUNKS + 1)], axis=2)
    q_off = jnp.arange(CHUNK)[:, None] + ATT_PREV_CHUNKS * CHUNK
    k_off = jnp.arange(band)[None, :]
    rel_idx = jnp.clip(q_off - k_off, -REL_CLIP, REL_CLIP) + REL_CLIP
    bias = rel_bias[:, rel_idx].astype(jnp.float32)
    key_chunk = jnp.arange(nc)[:, None] - ATT_PREV_CHUNKS + jnp.arange(band)[None, :] // CHUNK
    valid = key_chunk >= 0
    scores = jnp.einsum('bclhd,bcshd->bchls', q, k_band).astype(jnp.float32) * (ATT_HEAD_DIM ** -0.5)
    scores = scores + bias[None, None]
    scores = jnp.where(valid[None, :, None, None, :], scores, -1e30)
    p = jax.nn.softmax(scores, axis=-1).astype(v.dtype)
    o = jnp.einsum('bchls,bcshd->bclhd', p, v_band)
    return o.reshape(b, s, ATT_WIDTH)

def mamba2_mixer(h, w_in, conv_w, conv_b, dt_bias, A_log, D_skip, norm_w, w_out):
    b, s, _ = h.shape
    nc = s // CHUNK
    G, R, P, N = SSM_GROUPS, SSM_HEADS_PER_GROUP, SSM_HEAD_DIM, SSM_D_STATE
    f32 = jnp.float32
    zxbcdt = h @ w_in
    z, xbc, dt = jnp.split(zxbcdt, [SSM_D_INNER, SSM_D_INNER + SSM_CONV_DIM], axis=-1)
    xp = jnp.pad(xbc, ((0, 0), (SSM_D_CONV - 1, 0), (0, 0)))
    conv = xp[:, 0:s] * conv_w[0]
    for tap in range(1, SSM_D_CONV):
        conv = conv + xp[:, tap:tap + s] * conv_w[tap]
    xbc = jax.nn.silu(conv + conv_b)
    xs, Bm, Cm = jnp.split(xbc, [SSM_D_INNER, SSM_D_INNER + G * N], axis=-1)
    dt = jax.nn.softplus(dt.astype(f32) + dt_bias.astype(f32))
    A = -jnp.exp(A_log.astype(f32))
    a = (dt * A).reshape(b, nc, CHUNK, G, R)
    xs = xs.astype(f32).reshape(b, nc, CHUNK, G, R, P)
    x_dt = xs * dt.reshape(b, nc, CHUNK, G, R)[..., None]
    Bm = Bm.astype(f32).reshape(b, nc, CHUNK, G, N)
    Cm = Cm.astype(f32).reshape(b, nc, CHUNK, G, N)
    a_cs = jnp.moveaxis(jnp.cumsum(a, axis=2), 2, -1)
    tril = jnp.tril(jnp.ones((CHUNK, CHUNK), dtype=bool))
    seg = jnp.exp(jnp.where(tril, a_cs[..., :, None] - a_cs[..., None, :], -jnp.inf))
    cb = jnp.einsum('bclgn,bcsgn->bcgls', Cm, Bm)
    y_diag = jnp.einsum('bcgls,bcgrls,bcsgrp->bclgrp', cb, seg, x_dt)
    decay_states = jnp.exp(a_cs[..., -1:] - a_cs)
    states = jnp.einsum('bclgn,bcgrl,bclgrp->bcgrpn', Bm, decay_states, x_dt)
    chunk_decay = jnp.exp(a_cs[..., -1])

    def step(carry, inp):
        st, dec = inp
        return carry * dec[..., None, None] + st, carry

    init = jnp.zeros((b, G, R, P, N), f32)
    _, prev = lax.scan(step, init, (jnp.moveaxis(states, 1, 0), jnp.moveaxis(chunk_decay, 1, 0)))
    prev = jnp.moveaxis(prev, 0, 1)
    y_off = jnp.einsum('bclgn,bcgrpn,bcgrl->bclgrp', Cm, prev, jnp.exp(a_cs))
    y = y_diag + y_off + xs * D_skip.astype(f32).reshape(G, R)[:, :, None]
    y = y.reshape(b, s, SSM_D_INNER)
    g = (y * jax.nn.silu(z.astype(f32))).reshape(b, s, G, SSM_D_INNER // G)
    g = g * lax.rsqrt(jnp.mean(g * g, axis=-1, keepdims=True) + EPS)
    g = g.reshape(b, s, SSM_D_INNER) * norm_w.astype(f32)
    return g.astype(h.dtype) @ w_out

def hier_moe(h, w_group, b_group, w_expert, b_expert, w1, w3, w2):
    b, s, d = h.shape
    t = h.reshape(b * s, d)
    tf = t.astype(jnp.float32)
    g_prob = jax.nn.softmax(tf @ w_group.astype(jnp.float32) + b_group.astype(jnp.float32), axis=-1)
    g_val, g_idx = lax.top_k(g_prob, 1)
    e_logits = jnp.einsum('td,dge->tge', tf, w_expert.astype(jnp.float32)) + b_expert.astype(jnp.float32)
    e_logits = e_logits[jnp.arange(b * s), g_idx[:, 0]]
    e_val, e_idx = lax.top_k(jax.nn.softmax(e_logits, axis=-1), MOE_TOP_K)
    e_val = e_val / jnp.sum(e_val, axis=-1, keepdims=True)
    weights = g_val * e_val
    expert_id = g_idx * MOE_EXPERTS_PER_GROUP + e_idx
    combine = jnp.sum(jax.nn.one_hot(expert_id, MOE_EXPERTS, dtype=jnp.float32) * weights[..., None], axis=1)
    hid = jax.nn.silu(jnp.einsum('td,edf->tef', t, w1)) * jnp.einsum('td,edf->tef', t, w3)
    hid = hid * combine.astype(hid.dtype)[:, :, None]
    y = jnp.einsum('tef,efd->td', hid, w2)
    return y.reshape(b, s, d)

def _normal(key, shape, scale):
    return jax.random.normal(key, shape, jnp.float32) * scale

def first_inputs(seed: int = 0) -> dict:
    key = jax.random.key(seed)
    ks = jax.random.split(key, 28)
    D = D_MODEL
    f32 = jnp.float32
    dt0 = jnp.exp(jax.random.uniform(ks[14], (N_ODD, SSM_HEADS), f32) * (math.log(DT_MAX) - math.log(DT_MIN)) + math.log(DT_MIN))
    dt0 = jnp.maximum(dt0, 1e-4)
    return {
        'x': _normal(ks[0], (BATCH, SEQ, D), 1.0),
        'c': _normal(ks[1], (BATCH, D), 1.0),
        'ada_w': _normal(ks[2], (DEPTH, D, 6 * D), 0.5 * D ** -0.5),
        'ada_b': _normal(ks[3], (DEPTH, 6 * D), 0.02),
        'norm1_w': 1.0 + _normal(ks[4], (DEPTH, D), 0.05),
        'norm2_w': 1.0 + _normal(ks[5], (DEPTH, D), 0.05),
        'mix_w_in': _normal(ks[6], (N_EVEN, D, MIX_IN), D ** -0.5),
        'pool_w': _normal(ks[7], (N_EVEN, POOL_N_GROUPS, POOL_GROUP, POOL_GROUP), POOL_GROUP ** -0.5),
        'pool_scale': 1.0 + _normal(ks[8], (N_EVEN, POOL_WIDTH), 0.05),
        'rel_bias': _normal(ks[9], (N_EVEN, ATT_HEADS, 2 * REL_CLIP + 1), 0.2),
        'mix_w_out': _normal(ks[10], (N_EVEN, MIX_OUT, D), MIX_OUT ** -0.5),
        'ssm_w_in': _normal(ks[11], (N_ODD, D, SSM_IN), D ** -0.5),
        'ssm_conv_w': _normal(ks[12], (N_ODD, SSM_D_CONV, SSM_CONV_DIM), SSM_D_CONV ** -0.5),
        'ssm_conv_b': _normal(ks[13], (N_ODD, SSM_CONV_DIM), 0.02),
        'ssm_dt_bias': dt0 + jnp.log(-jnp.expm1(-dt0)),
        'ssm_A_log': jnp.log(jax.random.uniform(ks[15], (N_ODD, SSM_HEADS), f32, 1.0, 16.0)),
        'ssm_D': 1.0 + _normal(ks[16], (N_ODD, SSM_HEADS), 0.1),
        'ssm_norm_w': 1.0 + _normal(ks[17], (N_ODD, SSM_D_INNER), 0.05),
        'ssm_w_out': _normal(ks[18], (N_ODD, SSM_D_INNER, D), SSM_D_INNER ** -0.5),
        'moe_w_group': _normal(ks[19], (DEPTH, D, MOE_GROUPS), D ** -0.5),
        'moe_b_group': _normal(ks[20], (DEPTH, MOE_GROUPS), 0.01),
        'moe_w_expert': _normal(ks[21], (DEPTH, D, MOE_GROUPS, MOE_EXPERTS_PER_GROUP), D ** -0.5),
        'moe_b_expert': _normal(ks[22], (DEPTH, MOE_GROUPS, MOE_EXPERTS_PER_GROUP), 0.01),
        'moe_w1': _normal(ks[23], (DEPTH, MOE_EXPERTS, D, MOE_D_FF), D ** -0.5),
        'moe_w3': _normal(ks[24], (DEPTH, MOE_EXPERTS, D, MOE_D_FF), D ** -0.5),
        'moe_w2': _normal(ks[25], (DEPTH, MOE_EXPERTS, MOE_D_FF, D), MOE_D_FF ** -0.5),
        'final_norm_w': 1.0 + _normal(ks[26], (D,), 0.05),
    }

def first_block(x, c, ada_w, ada_b, norm1_w, norm2_w, mix_w_in, pool_w, pool_scale, rel_bias, mix_w_out,
              ssm_w_in, ssm_conv_w, ssm_conv_b, ssm_dt_bias, ssm_A_log, ssm_D, ssm_norm_w, ssm_w_out,
              moe_w_group, moe_b_group, moe_w_expert, moe_b_expert, moe_w1, moe_w3, moe_w2, final_norm_w):
    c_act = jax.nn.silu(c)
    for layer in range(DEPTH):
        mod = c_act @ ada_w[layer] + ada_b[layer]
        shift1, scale1, gate1, shift2, scale2, gate2 = jnp.split(mod, 6, axis=-1)
        h = modulate(rmsnorm(x, norm1_w[layer]), shift1, scale1)
        i = layer // 2
        if layer % 2 == 0:
            proj = h @ mix_w_in[i]
            u, q, k, v = jnp.split(proj, [POOL_WIDTH, POOL_WIDTH + ATT_WIDTH, POOL_WIDTH + 2 * ATT_WIDTH], axis=-1)
            a_out = pool_mixer(u, pool_w[i], pool_scale[i])
            b_out = chunk_attention(q, k, v, rel_bias[i])
            mix = jnp.concatenate([a_out, b_out], axis=-1) @ mix_w_out[i]
        else:
            mix = mamba2_mixer(h, ssm_w_in[i], ssm_conv_w[i], ssm_conv_b[i], ssm_dt_bias[i], ssm_A_log[i],
                               ssm_D[i], ssm_norm_w[i], ssm_w_out[i])
        x = x + gate1[:, None, :] * mix
        h2 = modulate(rmsnorm(x, norm2_w[layer]), shift2, scale2)
        ffn = hier_moe(h2, moe_w_group[layer], moe_b_group[layer], moe_w_expert[layer], moe_b_expert[layer],
                       moe_w1[layer], moe_w3[layer], moe_w2[layer])
        x = x + gate2[:, None, :] * ffn
    return rmsnorm(x, final_norm_w)


N_EVEN_2 = (DEPTH + 1) // 2
N_ODD_2 = DEPTH // 2
A_GROUPS = 4
A_CHUNK = 128
A_WIDTH = D_MODEL // 2
A_GROUP_CH = A_WIDTH // A_GROUPS
B_HEADS = 8
B_HEAD_DIM = 64
B_WIDTH = B_HEADS * B_HEAD_DIM
Q_BLOCK = 128
MIX_WIDTH = A_WIDTH + B_WIDTH
IN_COLS = 2 * A_WIDTH + 3 * B_WIDTH + B_HEADS
S5_GROUP_CH = 16
S5_GROUPS = D_MODEL // S5_GROUP_CH
S5_STATE = 64
D_FF = 2816
CONV_W = 3
PLE_DIM = 256
NEG_INF = -1e30


def rms_norm(x, g=None):
    xf = x.astype(jnp.float32)
    y = xf * lax.rsqrt(jnp.mean(xf * xf, axis=-1, keepdims=True) + EPS)
    if g is not None:
        y = y * g.astype(jnp.float32)
    return y.astype(x.dtype)

def gmlp_mixer(u, v, v_gain, w_s, b_s):
    bsz, seq = u.shape[0], u.shape[1]
    u = jax.nn.gelu(u)
    v = jax.nn.gelu(v).reshape(bsz, seq, A_GROUPS, A_GROUP_CH)
    v = rms_norm(v, v_gain.reshape(A_GROUPS, A_GROUP_CH))
    v = v.reshape(bsz, seq // A_CHUNK, A_CHUNK, A_GROUPS, A_GROUP_CH)
    tri = jnp.tril(jnp.ones((A_CHUNK, A_CHUNK), dtype=bool))
    w = jnp.where(tri[None], w_s, jnp.zeros_like(w_s))
    sv = jnp.einsum('gts,bnsgc->bntgc', w, v) + b_s.T[None, None, :, :, None]
    return u * sv.reshape(bsz, seq, A_WIDTH)

def fox_attention(q, k, v, f_logit, q_gain, k_gain):
    bsz, seq = q.shape[0], q.shape[1]
    q = rms_norm(q, q_gain)
    k = rms_norm(k, k_gain)
    c = jnp.cumsum(jax.nn.log_sigmoid(f_logit.astype(jnp.float32)), axis=1)
    nb = seq // Q_BLOCK
    qb = q.reshape(bsz, nb, Q_BLOCK, B_HEADS, B_HEAD_DIM).transpose(1, 0, 2, 3, 4)
    cb = c.reshape(bsz, nb, Q_BLOCK, B_HEADS).transpose(1, 0, 2, 3)
    pos_b = jnp.arange(seq, dtype=jnp.int32).reshape(nb, Q_BLOCK)
    kpos = jnp.arange(seq, dtype=jnp.int32)
    ck = c.transpose(0, 2, 1)
    scale = B_HEAD_DIM ** -0.5

    def block(args):
        qi, ci, pi = args
        s = jnp.einsum('bqhd,bkhd->bhqk', qi, k).astype(jnp.float32) * scale
        s = s + ci.transpose(0, 2, 1)[..., None] - ck[:, :, None, :]
        s = jnp.where(kpos[None, :] <= pi[:, None], s, NEG_INF)
        pr = jax.nn.softmax(s, axis=-1)
        return jnp.einsum('bhqk,bkhd->bqhd', pr.astype(v.dtype), v)

    o = lax.map(block, (qb, cb, pos_b))
    return o.transpose(1, 0, 2, 3, 4).reshape(bsz, seq, B_WIDTH)

def _complex_affine_combine(e1, e2):
    a1r, a1i, b1r, b1i = e1
    a2r, a2i, b2r, b2i = e2
    ar = a2r * a1r - a2i * a1i
    ai = a2r * a1i + a2i * a1r
    br = a2r * b1r - a2i * b1i + b2r
    bi = a2r * b1i + a2i * b1r + b2i
    return (ar, ai, br, bi)

def s5_mixer(u, a_re, a_im, log_dt, b_re, b_im, c_re, c_im, d):
    bsz, seq, _ = u.shape
    f32 = jnp.float32
    uf = u.astype(f32).reshape(bsz, seq, S5_GROUPS, S5_GROUP_CH)
    dt = jnp.exp(log_dt.astype(f32))[:, None]
    lr, li = a_re.astype(f32), a_im.astype(f32)
    mag = jnp.exp(lr * dt)
    ab_re, ab_im = mag * jnp.cos(li * dt), mag * jnp.sin(li * dt)
    den = lr * lr + li * li
    nr, ni = ab_re - 1.0, ab_im
    cr = (nr * lr + ni * li) / den
    ci = (ni * lr - nr * li) / den
    br, bi = b_re.astype(f32), b_im.astype(f32)
    bb_re = cr[..., None] * br - ci[..., None] * bi
    bb_im = cr[..., None] * bi + ci[..., None] * br
    bu_re = jnp.einsum('gpc,bsgc->bsgp', bb_re, uf)
    bu_im = jnp.einsum('gpc,bsgc->bsgp', bb_im, uf)
    a_r = jnp.broadcast_to(ab_re, bu_re.shape)
    a_i = jnp.broadcast_to(ab_im, bu_im.shape)
    _, _, xr, xi = lax.associative_scan(_complex_affine_combine, (a_r, a_i, bu_re, bu_im), axis=1)
    y = (jnp.einsum('gcp,bsgp->bsgc', c_re.astype(f32), xr)
         - jnp.einsum('gcp,bsgp->bsgc', c_im.astype(f32), xi)
         + d.astype(f32).reshape(S5_GROUPS, S5_GROUP_CH) * uf)
    return y.reshape(bsz, seq, D_MODEL).astype(u.dtype)

def conv_ffn(x, w_up, conv_w, conv_b, w_down):
    seq = x.shape[1]
    h = x @ w_up
    hp = jnp.pad(h, ((0, 0), (CONV_W - 1, 0), (0, 0)))
    hc = conv_b + conv_w[0] * hp[:, 0:seq]
    for j in range(1, CONV_W):
        hc = hc + conv_w[j] * hp[:, j:j + seq]
    g, up = jnp.split(hc, 2, axis=-1)
    return (jax.nn.silu(g) * up) @ w_down

def second_inputs(seed: int = 0) -> dict:
    key = jax.random.key(seed)
    ks = jax.random.split(key, 32)
    f32 = jnp.float32

    def nrm(k, shape, scale):
        return scale * jax.random.normal(k, shape, f32)

    a_im_base = jnp.broadcast_to(math.pi * jnp.arange(S5_STATE, dtype=f32), (N_ODD_2, S5_GROUPS, S5_STATE))
    return {
        "x": nrm(ks[0], (BATCH, SEQ, D_MODEL), 1.0),
        "p": nrm(ks[1], (DEPTH, BATCH, SEQ, PLE_DIM), 1.0),
        "norm_mix": 1.0 + nrm(ks[2], (DEPTH, D_MODEL), 0.05),
        "norm_ffn": 1.0 + nrm(ks[3], (DEPTH, D_MODEL), 0.05),
        "ev_w_in": nrm(ks[4], (N_EVEN_2, D_MODEL, IN_COLS), D_MODEL ** -0.5),
        "ev_b_fgate": 4.0 + nrm(ks[5], (N_EVEN_2, B_HEADS), 0.5),
        "ev_q_norm": 1.0 + nrm(ks[6], (N_EVEN_2, B_HEAD_DIM), 0.05),
        "ev_k_norm": 1.0 + nrm(ks[7], (N_EVEN_2, B_HEAD_DIM), 0.05),
        "ev_v_norm": 1.0 + nrm(ks[8], (N_EVEN_2, A_WIDTH), 0.05),
        "ev_w_spatial": nrm(ks[9], (N_EVEN_2, A_GROUPS, A_CHUNK, A_CHUNK), A_CHUNK ** -0.5),
        "ev_b_spatial": 1.0 + nrm(ks[10], (N_EVEN_2, A_GROUPS, A_CHUNK), 0.1),
        "ev_w_out": nrm(ks[11], (N_EVEN_2, MIX_WIDTH, D_MODEL), MIX_WIDTH ** -0.5),
        "od_a_re": -0.5 + nrm(ks[12], (N_ODD_2, S5_GROUPS, S5_STATE), 0.01),
        "od_a_im": a_im_base + nrm(ks[13], (N_ODD_2, S5_GROUPS, S5_STATE), 0.01),
        "od_log_dt": jax.random.uniform(ks[14], (N_ODD_2, S5_GROUPS), f32, math.log(1e-3), math.log(1e-1)),
        "od_b_re": nrm(ks[15], (N_ODD_2, S5_GROUPS, S5_STATE, S5_GROUP_CH), (2 * S5_GROUP_CH) ** -0.5),
        "od_b_im": nrm(ks[16], (N_ODD_2, S5_GROUPS, S5_STATE, S5_GROUP_CH), (2 * S5_GROUP_CH) ** -0.5),
        "od_c_re": nrm(ks[17], (N_ODD_2, S5_GROUPS, S5_GROUP_CH, S5_STATE), S5_STATE ** -0.5),
        "od_c_im": nrm(ks[18], (N_ODD_2, S5_GROUPS, S5_GROUP_CH, S5_STATE), S5_STATE ** -0.5),
        "od_d": nrm(ks[19], (N_ODD_2, D_MODEL), 1.0),
        "od_w_glu": nrm(ks[20], (N_ODD_2, D_MODEL, 2 * D_MODEL), D_MODEL ** -0.5),
        "ffn_w_up": nrm(ks[21], (DEPTH, D_MODEL, 2 * D_FF), D_MODEL ** -0.5),
        "ffn_conv_w": nrm(ks[22], (DEPTH, CONV_W, 2 * D_FF), CONV_W ** -0.5),
        "ffn_conv_b": nrm(ks[23], (DEPTH, 2 * D_FF), 0.02),
        "ffn_w_down": nrm(ks[24], (DEPTH, D_FF, D_MODEL), D_FF ** -0.5),
        "ple_w_proj": nrm(ks[25], (DEPTH, PLE_DIM, D_MODEL), PLE_DIM ** -0.5),
        "ple_w_gate": nrm(ks[26], (DEPTH, D_MODEL, D_MODEL), D_MODEL ** -0.5),
    }

def second_block(x, p, norm_mix, norm_ffn, ev_w_in, ev_b_fgate, ev_q_norm, ev_k_norm, ev_v_norm,
              ev_w_spatial, ev_b_spatial, ev_w_out, od_a_re, od_a_im, od_log_dt, od_b_re, od_b_im,
              od_c_re, od_c_im, od_d, od_w_glu, ffn_w_up, ffn_conv_w, ffn_conv_b, ffn_w_down,
              ple_w_proj, ple_w_gate):
    bsz, seq = x.shape[0], x.shape[1]
    splits = [A_WIDTH, 2 * A_WIDTH, 2 * A_WIDTH + B_WIDTH, 2 * A_WIDTH + 2 * B_WIDTH,
              2 * A_WIDTH + 3 * B_WIDTH]
    for i in range(DEPTH):
        h = rms_norm(x, norm_mix[i])
        if i % 2 == 0:
            e = i // 2
            z = h @ ev_w_in[e]
            u_a, v_a, q, k, v_b, f = jnp.split(z, splits, axis=-1)
            y_a = gmlp_mixer(u_a, v_a, ev_v_norm[e], ev_w_spatial[e], ev_b_spatial[e])
            shp = (bsz, seq, B_HEADS, B_HEAD_DIM)
            y_b = fox_attention(q.reshape(shp), k.reshape(shp), v_b.reshape(shp),
                                f + ev_b_fgate[e], ev_q_norm[e], ev_k_norm[e])
            x = x + jnp.concatenate([y_a, y_b], axis=-1) @ ev_w_out[e]
        else:
            o = i // 2
            y = s5_mixer(h, od_a_re[o], od_a_im[o], od_log_dt[o], od_b_re[o], od_b_im[o],
                         od_c_re[o], od_c_im[o], od_d[o])
            g_a, g_b = jnp.split(jax.nn.gelu(y) @ od_w_glu[o], 2, axis=-1)
            x = x + g_a * jax.nn.sigmoid(g_b)
        x = x + conv_ffn(rms_norm(x, norm_ffn[i]), ffn_w_up[i], ffn_conv_w[i], ffn_conv_b[i], ffn_w_down[i])
        gate = jax.nn.sigmoid(rms_norm(x) @ ple_w_gate[i])
        x = x + gate * (p[i] @ ple_w_proj[i])
    return x


def setup_inputs(seed=0):
    out = dict(first_inputs(seed))
    for name, value in second_inputs(seed + 1).items():
        if name != "x":
            out[name + "_2"] = value
    return out


def reference(
    x, c, ada_w, ada_b, norm1_w, norm2_w, mix_w_in, pool_w, pool_scale, rel_bias, mix_w_out,
    ssm_w_in, ssm_conv_w, ssm_conv_b, ssm_dt_bias, ssm_A_log, ssm_D, ssm_norm_w, ssm_w_out,
    moe_w_group, moe_b_group, moe_w_expert, moe_b_expert, moe_w1, moe_w3, moe_w2, final_norm_w,
    p_2, norm_mix_2, norm_ffn_2, ev_w_in_2, ev_b_fgate_2, ev_q_norm_2, ev_k_norm_2, ev_v_norm_2,
    ev_w_spatial_2, ev_b_spatial_2, ev_w_out_2, od_a_re_2, od_a_im_2, od_log_dt_2, od_b_re_2,
    od_b_im_2, od_c_re_2, od_c_im_2, od_d_2, od_w_glu_2, ffn_w_up_2, ffn_conv_w_2, ffn_conv_b_2,
    ffn_w_down_2, ple_w_proj_2, ple_w_gate_2,
):
    x = first_block(
        x, c, ada_w, ada_b, norm1_w, norm2_w, mix_w_in, pool_w, pool_scale, rel_bias, mix_w_out,
        ssm_w_in, ssm_conv_w, ssm_conv_b, ssm_dt_bias, ssm_A_log, ssm_D, ssm_norm_w, ssm_w_out,
        moe_w_group, moe_b_group, moe_w_expert, moe_b_expert, moe_w1, moe_w3, moe_w2,
        final_norm_w,
    )
    return second_block(
        x, p_2, norm_mix_2, norm_ffn_2, ev_w_in_2, ev_b_fgate_2, ev_q_norm_2, ev_k_norm_2,
        ev_v_norm_2, ev_w_spatial_2, ev_b_spatial_2, ev_w_out_2, od_a_re_2, od_a_im_2,
        od_log_dt_2, od_b_re_2, od_b_im_2, od_c_re_2, od_c_im_2, od_d_2, od_w_glu_2, ffn_w_up_2,
        ffn_conv_w_2, ffn_conv_b_2, ffn_w_down_2, ple_w_proj_2, ple_w_gate_2,
    )


_drawn_inputs = setup_inputs


def setup_inputs(seed=0):
    import zlib

    import numpy as np

    out = dict(_drawn_inputs(seed))
    spreads = {}
    factors = {'pool_scale': 3.438,
     'rel_bias': 4.537,
     'ssm_conv_b': 5.634,
     'ssm_norm_w': 2.728,
     'moe_b_group': 6.864,
     'moe_b_expert': 6.677,
     'ev_q_norm_2': 8.0,
     'ev_k_norm_2': 8.0,
     'ev_v_norm_2': 3.865,
     'od_a_re_2': 64.0,
     'od_log_dt_2': 18.171,
     'od_b_re_2': 29.136,
     'od_b_im_2': 28.168,
     'od_c_re_2': 29.672,
     'od_c_im_2': 29.168,
     'ffn_conv_b_2': 3.437,
     'od_a_im_2': 6.325}
    for name, (base, spread) in spreads.items():
        noise = np.random.default_rng([zlib.crc32(name.encode()), seed]).standard_normal(out[name].shape)
        drawn = base * np.exp(spread * noise) if base else spread * noise
        out[name] = __import__('jax').numpy.asarray(drawn.astype(out[name].dtype))
    for name, factor in factors.items():
        out[name] = (out[name] * factor).astype(out[name].dtype)
    return out
```

```python
from contextlib import ExitStack

import concourse.bass as bass
from concourse import mybir

F32 = mybir.dt.float32
F32R = mybir.dt.float32r
I32 = mybir.dt.int32
ACT = mybir.ActivationFunctionType
ALU = mybir.AluOpType
AX = mybir.AxisListType

P = 128
SEQ = 512
D = 1024
KD = D // P
NT = SEQ // P
EPS = 1e-6
NEG = -1e30
UNIT = 2048
HALF = D // 2
HEADS = 8
HD = 64
REL_CLIP = 256
SSM_G = 8
SSM_H = 32
SSM_INNER = 2048
EXPERTS = 32
GROUPS = 4
EPG = 8
FF = 2816
FB = FF // P
S5_P = 64
S5_C = 16
S5_TILES = 32
S5_L = 4
S5_N = SEQ // S5_L
S5_LOW, S5_HIGH = 16, 8
S5_IDX = S5_LOW + S5_HIGH
TRI = sum(SEQ - P * i for i in range(NT))
TRI_AT = [0, 512, 896, 1152]
TWO_PI = 6.283185307179586
ROUND = 12582912.0
TWO_PI_PARTS = (6.28125, 0.00193500518798828125, 3.0199159819e-07)
EXP_SERIES = [1 / f for f in (362880, 40320, 5040, 720, 120, 24, 6, 2, 1)]


class Plan:

    def __init__(self):
        self.unit, self.pair, self.bank = 0, 0, 0
        self.u, self.p, self.b = {}, {}, {}

    def step(self, name, units=0, pairs=0, banks=0):
        self.u[name], self.p[name], self.b[name] = self.unit, self.pair, self.bank
        self.unit += units
        self.pair += pairs
        self.bank += banks


def make_plan():
    plan = Plan()
    plan.step("columns", banks=6)
    plan.step("load", banks=8)
    plan.step("ada", pairs=12)

    def norm(n):
        plan.step(f"norm{n}", banks=1)

    def moe(layer):
        plan.step(f"moe{layer}", units=48, pairs=40, banks=2)

    def ffn(layer):
        plan.step(f"ffn{layer}", units=34, pairs=26)

    def ple(layer):
        plan.step(f"ple{layer}", units=6, pairs=8, banks=2)

    norm(0)
    plan.step("mixin", units=8, pairs=8)
    plan.step("pool", banks=4)
    plan.step("att0", pairs=4, banks=6 * HEADS)
    plan.step("mixout", units=4, pairs=4)
    norm(1)
    moe(0)
    norm(2)
    plan.step("dt", banks=3)
    plan.step("ssm", units=24, pairs=24, banks=8 * SSM_G)
    plan.step("ssmout", units=8, pairs=8)
    norm(3)
    moe(1)
    norm(4)
    norm(5)
    plan.step("evin", units=10, pairs=10)
    plan.step("gate", banks=2)
    plan.step("gmlp", banks=5)
    plan.step("qknorm", banks=8)
    plan.step("att1", pairs=4, banks=6 * HEADS)
    plan.step("s5a", banks=1)
    plan.step("evout", units=4, pairs=4)
    norm(6)
    ffn(0)
    norm(7)
    ple(0)
    norm(8)
    plan.step("s5c", banks=4)
    plan.step("s5", pairs=8, banks=6 * KD)
    plan.step("glu", units=8, pairs=8)
    norm(9)
    ffn(1)
    norm(10)
    ple(1)
    plan.step("store", banks=8)
    return plan


class Engine:

    def __init__(self, eng, chain):
        self.e, self.chain = eng, chain
        self.count = {}

    def _entry(self, sem):
        return self.count.setdefault(sem.name, [0, 0, sem])

    def wait(self, sem, events=1):
        entry = self._entry(sem)
        entry[0] += events
        self.e.wait_ge(sem, entry[1] + entry[0])

    def passed(self, sem, events):
        self._entry(sem)[0] += events

    def link(self, ins):
        ins.then_inc(self.chain, 1)
        self.wait(self.chain)

    def loop(self, times, per):
        return Loop(self, times, per)


class Loop:

    def __init__(self, engine, times, per):
        self.engine, self.times, self.per = engine, times, per

    def __enter__(self):
        self.fori = self.engine.e.Fori(0, self.times)
        i = self.fori.__enter__()
        self.saved = {}
        for sem, n in self.per.items():
            entry = self.engine._entry(sem)
            self.saved[sem.name] = (entry[0], entry[1])
            entry[1] = i * n + (entry[1] + entry[0])
            entry[0] = 0
        return i

    def __exit__(self, *exc):
        if exc[0] is None:
            for sem, n in self.per.items():
                entry = self.engine._entry(sem)
                assert entry[0] == n, (sem.name, entry[0], n)
                done, before = self.saved[sem.name]
                entry[0], entry[1] = done + self.times * n, before
        return self.fori.__exit__(*exc)


def column_vectors(t):
    rows = [
        ("c", t["c"].rearrange("b (k p) -> (b k) p", p=P)),
        ("ada_b", t["ada_b"].rearrange("l (k p) -> (l k) p", p=P)),
        ("norm1", t["norm1_w"].rearrange("l (k p) -> (l k) p", p=P)),
        ("norm2", t["norm2_w"].rearrange("l (k p) -> (l k) p", p=P)),
        ("pool_scale", t["pool_scale"].rearrange("l (k p) -> (l k) p", p=P)),
        ("conv_w", t["ssm_conv_w"].rearrange("l j (k p) -> (l j k) p", p=P)),
        ("conv_b", t["ssm_conv_b"].rearrange("l (k p) -> (l k) p", p=P)),
        ("ssm_norm", t["ssm_norm_w"].rearrange("l (k p) -> (l k) p", p=P)),
        ("final", t["final_norm_w"].rearrange("(k p) -> k p", p=P)),
        ("norm_mix", t["norm_mix_2"].rearrange("l (k p) -> (l k) p", p=P)),
        ("norm_ffn", t["norm_ffn_2"].rearrange("l (k p) -> (l k) p", p=P)),
        ("od_d", t["od_d_2"].rearrange("l (k p) -> (l k) p", p=P)),
        ("fconv_w", t["ffn_conv_w_2"].rearrange("l j (k p) -> (l j k) p", p=P)),
        ("fconv_b", t["ffn_conv_b_2"].rearrange("l (k p) -> (l k) p", p=P)),
    ]
    at, n = {}, 0
    for name, ap in rows:
        at[name] = n
        n += ap.shape[0]
    return rows, at, n


def bcast(ap, dim, n):
    shape = list(ap.shape)
    return ap.unsqueeze(dim).broadcast_to(shape[:dim] + [n] + shape[dim:])


def build(nc, t, out):
    plan = make_plan()
    ctx = ExitStack()

    def sem(name):
        return ctx.enter_context(nc.semaphore(name))

    def sb(name, shape, dt=F32, where=None):
        return (where or ctx).enter_context(nc.sbuf_tensor(name, shape, dt))

    X = sb("X", [P, KD, SEQ])
    HH = sb("HH", [P, KD, SEQ], F32R)
    r = ExitStack()
    HL = sb("HL", [P, KD, SEQ], F32R, r)
    r.close()
    HF = sb("HF", [P, KD, SEQ])
    RAW = sb("RAW", [P, 2, UNIT])
    WH = sb("WH", [P, 2, UNIT], F32R)
    WL = sb("WL", [P, 2, UNIT], F32R)
    rows, col_at, n_cols = column_vectors(t)
    n_row_tiles = -(-n_cols // P)
    COLS = sb("COLS", [P, n_row_tiles * P])
    IDENT = sb("IDENT", [P, P])
    ONES = sb("ONES", [P, P])
    HEAD_ONES = sb("HEAD_ONES", [P, P])
    r = ExitStack()
    LATER = sb("LATER", [P, SEQ], F32, r)
    CAUSAL = sb("CAUSAL", [P, SEQ], F32, r)
    r.close()
    FUP = sb("FUP", [P, 2, SEQ])
    MOD = sb("MOD", [P, 2 * 6 * KD])
    GAIN = sb("GAIN", [P, 4, KD])
    SQ = sb("SQ", [P, 2, SEQ])
    RSTD = sb("RSTD", [P, SEQ])
    TMP = sb("TMP", [P, 2, SEQ])
    r = ExitStack()
    ROUTER_W = sb("ROUTER_W", [P, 2, KD, GROUPS + EXPERTS], F32, r)
    ROUTER_B = sb("ROUTER_B", [P, 2, GROUPS + EXPERTS], F32, r)
    DT_W = sb("DT_W", [P, KD, SSM_H], F32, r)
    DT_ROW = sb("DT_ROW", [P, 2, SSM_H], F32, r)
    D_ROW = sb("D_ROW", [P, SSM_H], F32, r)
    D_COL = sb("D_COL", [P, 2 * SSM_G], F32, r)
    r.close()
    S5K = sb("S5K", [P, 5, S5_TILES])
    A_POW = sb("A_POW", [P, 2, S5_L + 1, S5_TILES])
    A_REV = sb("A_REV", [P, 2, S5_L, S5_TILES])
    SPARE = sb("SPARE", [P, (4064 - 23 * 4 * S5_TILES) // 4])
    FG_W = sb("FG_W", [P, KD, HEADS])
    FG_B = sb("FG_B", [P, HEADS])
    QK_GAIN = sb("QK_GAIN", [P, 2])
    INV_COUNT = sb("INV_COUNT", [P, 16])
    FALLING = sb("FALLING", [P, EPG])
    C_ACT = sb("C_ACT", [P, KD])
    MX = sb("MX", [P, 2, 2, NT])
    TURN = sb("TURN", [P, 2])
    SUMS = sb("SUMS", [P, 2, NT])

    def region():
        return ExitStack()

    r = region()
    STRIP = sb("STRIP", [P, HEADS, SEQ], F32, r)
    XTOK = sb("XTOK", [P, NT, D], F32, r)
    ROWS = sb("ROWS", [P, n_row_tiles, P], F32, r)
    ADA = sb("ADA", [P, 2, 4, D], F32, r)
    ADA_ACC = sb("ADA_ACC", [P, 2, D], F32, r)
    REL = sb("REL", [P, 640], F32, r)
    r.close()
    r = region()
    STRIP_ = sb("STRIP_", [P, HEADS, SEQ], F32, r)
    Q0 = sb("Q0", [P, 4, SEQ], F32, r)
    K0 = sb("K0", [P, 4, SEQ], F32, r)
    V0 = sb("V0", [P, NT, HALF], F32, r)
    S0 = sb("S0", [P, 2, TRI], F32, r)
    PT0 = sb("PT0", [P, 2, TRI], F32, r)
    U = sb("U", [P, 4, SEQ], F32, r)
    POOLED = sb("POOLED", [P, 4, SEQ], F32, r)
    PSCR = sb("PSCR", [P, 2, SEQ], F32, r)
    POOL_W = sb("POOL_W", [P, 4, P], F32, r)
    r.close()
    r = region()
    MHH = sb("MHH", [P, 16, SEQ], F32R, r)
    MHL = sb("MHL", [P, 16, SEQ], F32R, r)
    COMB_ROW = sb("COMB_ROW", [P, 2, SEQ], F32, r)
    LOGIT = sb("LOGIT", [P, NT, GROUPS + EXPERTS], F32, r)
    GATE = sb("GATE", [P, 12, NT, EPG], F32, r)
    ESEL = sb("ESEL", [P, NT, GROUPS, EPG], F32, r)
    COMB = sb("COMB", [P, NT, GROUPS, EPG], F32, r)
    COMB_T = sb("COMB_T", [EXPERTS, SEQ], F32, r)
    r.close()
    r = region()
    G = sb("G", [P, 2 * SSM_G, SEQ], F32, r)
    ZS = sb("ZS", [P, 2, 2, SEQ], F32, r)
    CONV = sb("CONV", [P, 2, 4, SEQ], F32, r)
    XDT = sb("XDT", [P, NT, 256], F32, r)
    CBM = sb("CBM", [P, TRI], F32, r)
    DECAY = sb("DECAY", [P, 2, TRI], F32, r)
    ACS_ROW = sb("ACS_ROW", [P, 2, SEQ], F32, r)
    DT = sb("DT", [P, NT, SSM_H], F32, r)
    DTS = sb("DTS", [P, 6, NT, SSM_H], F32, r)
    ACS = sb("ACS", [SSM_H, 2, SEQ], F32, r)
    ACS_COL = sb("ACS_COL", [P, NT, SSM_H], F32, r)
    r.close()
    r = region()
    UA = sb("UA", [P, 4, SEQ], F32, r)
    VA = sb("VA", [P, NT, HALF], F32, r)
    VSQ = sb("VSQ", [P, NT, HALF], F32, r)
    Q1 = sb("Q1", [P, 4, SEQ], F32, r)
    K1 = sb("K1", [P, 4, SEQ], F32, r)
    V1 = sb("V1", [P, NT, HALF], F32, r)
    S1 = sb("S1", [P, 2, TRI], F32, r)
    PT1 = sb("PT1", [P, 2, TRI], F32, r)
    SPAT = sb("SPAT", [P, 4, P], F32, r)
    SPAT_T = sb("SPAT_T", [P, 4, P], F32, r)
    SPAT_B = sb("SPAT_B", [P, 4, P], F32, r)
    V_GAIN = sb("V_GAIN", [P, HALF], F32, r)
    FGL = sb("FGL", [P, 6, NT, HEADS], F32, r)
    FCUM = sb("FCUM", [HEADS, 2, SEQ], F32, r)
    MINUS_HEAD = sb("MINUS_HEAD", [HEADS, HEADS, P], F32, r)
    VR = sb("VR", [P, 16], F32, r)
    AROW = sb("AROW", [S5_TILES, 2, P], F32, r)
    LDT_ROW = sb("LDT_ROW", [P, 2 * S5_TILES], F32, r)
    r.close()
    r = region()
    FHH = sb("FHH", [P, FB, SEQ], F32R, r)
    FHL = sb("FHL", [P, FB, SEQ], F32R, r)
    r.close()
    r = region()
    PTOK = sb("PTOK", [P, NT, 256], F32, r)
    PH = sb("PH", [P, 2, SEQ], F32R, r)
    PL = sb("PL", [P, 2, SEQ], F32R, r)
    PROJ = sb("PROJ", [P, 4, SEQ], F32, r)
    OTOK = sb("OTOK", [P, NT, D], F32, r)
    r.close()
    r = region()
    BB = sb("BB", [P, 2, S5_TILES, S5_C], F32, r)
    CK = sb("CK", [P, 2, S5_TILES, S5_C], F32, r)
    TAB = sb("TAB", [P, 2, S5_TILES, S5_IDX], F32, r)
    W1X = sb("W1X", [P, 2, 2, 4, S5_L, 2, S5_C], F32, r)
    r2 = region()
    CRAW = sb("CRAW", [P, 2, KD, 2, S5_P], F32, r2)
    BRAW = sb("BRAW", [P, 2, S5_TILES, S5_C], F32, r2)
    ANGLE = sb("ANGLE", [P, 2, S5_TILES, S5_IDX], F32, r2)
    r2.close()
    TURNING = sb("TURNING", [P, 2, 3, 4, S5_N], F32, r)
    PRP = sb("PRP", [P, 2, 4, S5_N], F32, r)
    PAD = sb("PAD", [P, S5_N * 4], F32, r)
    CAX = sb("CAX", [P, 2, 2, 4, S5_L + 1, 2, S5_C], F32, r)
    W1_T = sb("W1_T", [P, 2, 2, 4, P], F32, r)
    W3 = sb("W3", [P, 2, 4, P], F32, r)
    U4 = sb("U4", [P, 2, 4, S5_N], F32, r)
    XS = sb("XS", [P, 2, 4, S5_N], F32, r)
    PR = sb("PR", [P, 4, 4, S5_N], F32, r)
    S5_AT = sb("S5_AT", [P, S5_IDX], F32, r)
    FIRST = sb("FIRST", [P, S5_N], F32, r)
    Y4 = sb("Y4", [P, 4, S5_N], F32, r)
    r.close()

    PAIR = [ctx.enter_context(nc.psum_tensor(f"PAIR{i}", [P, 2, SEQ], F32)) for i in range(2)]
    BANK = [ctx.enter_context(nc.psum_tensor(f"BANK{i}", [P, SEQ], F32)) for i in range(4)]

    strip_dram = nc.dram_tensor("strip_scratch", (P, HEADS, 640), F32, kind="Internal").ap()
    rel_dram = nc.dram_tensor("rel_scratch", (HEADS, 640), F32, kind="Internal").ap()
    comb_dram = nc.dram_tensor("comb_scratch", (2, EXPERTS, SEQ), F32, kind="Internal").ap()
    acs_dram = nc.dram_tensor("acs_scratch", (SSM_H, SEQ), F32, kind="Internal").ap()

    landed = [sem("unit_landed0"), sem("unit_landed1")]
    split_hi = sem("split_hi")
    split_ready = sem("split_ready")
    unit_done = sem("unit_done")
    evac = [sem("pair_evacuated0"), sem("pair_evacuated1")]
    bank_ready = sem("bank_ready")
    bank_free = [sem(f"bank_free{i}") for i in range(4)]
    pair_ready = sem("small_pair_ready")
    consts_ready = sem("consts_ready")
    dve_chain, act_chain, pool_chain = sem("dve_chain"), sem("act_chain"), sem("pool_chain")
    x_landed, rows_landed, small_landed = sem("x_landed"), sem("rows_landed"), sem("small_landed")
    ada_landed = [sem("ada_landed0"), sem("ada_landed1")]
    ada_used, ada_summed = sem("ada_used"), sem("ada_summed")
    c_ready, x_ready = sem("c_ready"), sem("x_ready")
    sq_ready, sq_used, var_ready, root_ready = sem("sq_ready"), sem("sq_used"), sem("var_ready"), sem("root_ready")
    pre_ready, hi_ready, h_ready = sem("pre_ready"), sem("hi_ready"), sem("h_ready")

    def take_bank(pe, b, turns=0):
        if b // 4 + (0 if isinstance(turns, int) else 1) > 0:
            pe.e.wait_ge(bank_free[b % 4], turns + b // 4)
        return BANK[b % 4]

    def full_bank(eng, b, turns=0):
        eng.e.wait_ge(bank_ready, turns * 4 + (b + 1))
        return BANK[b % 4]

    def take_pair(pe, p, turns=0):
        if p // 2 + (0 if isinstance(turns, int) else 1) > 0:
            pe.e.wait_ge(evac[p % 2], turns + p // 2)
        return PAIR[p % 2]

    def mm3(o, wh, wl, xh, xl, start, stop):
        nc.tensor.matmul(o, wh, xh, start=start, stop=False)
        nc.tensor.matmul(o, wh, xl, start=False, stop=False)
        return nc.tensor.matmul(o, wl, xh, start=False, stop=stop)

    def unit_channels(pe, u, pair, xh, xl, tiles, first=True, last=True, off=0, blocks=2, at=0):
        s = u % 2
        pe.e.wait_ge(split_ready, off + (u + 1))
        for m in range(blocks):
            for k in range(tiles):
                c = (k * blocks + m) * P
                ins = mm3(pair[:, at + m, :], WH[:, s, c:c + P], WL[:, s, c:c + P], xh(k), xl(k),
                          first and k == 0, last and k == tiles - 1)
        ins.then_inc(unit_done, 1)

    def unit_tokens(pe, u, pair):
        s = u % 2
        pe.e.wait_ge(split_ready, u + 1)
        for tt in range(NT):
            o = pair[:, tt // 2, (tt % 2) * 256:(tt % 2) * 256 + 256]
            for k in range(KD):
                c, a = slice(k * 256, k * 256 + 256), slice(tt * P, tt * P + P)
                ins = mm3(o, HH[:, k, a], HL[:, k, a], WH[:, s, c], WL[:, s, c], k == 0, k == KD - 1)
        ins.then_inc(unit_done, 1)

    def full_pair(eng, u, p, off=0):
        eng.e.wait_ge(unit_done, off + (u + 1))
        return PAIR[p % 2]

    hh = lambda k: HH[:, k, :]
    hl = lambda k: HL[:, k, :]

    def mod(layer, c, k):
        at = (layer * 6 + c) * KD + k
        return MOD[:, at:at + 1]

    def col(name, i):
        at = col_at[name] + i
        return COLS[:, at:at + 1]

    dram = lambda name, offset, ap: bass.AP(t[name].tensor, t[name].offset + offset, ap)

    sp_unit = [0]

    def load_unit(sp, first, second, off=0, u=None):
        if u is None:
            u = sp_unit[0]
            sp_unit[0] += 1
        s = u % 2
        if u >= 2 or not isinstance(off, int):
            sp.wait_ge(split_ready, off + (u - 1))
        for src, dst in (first, second):
            sp.dma_start(dst(RAW[:, s, :]), src).then_inc(landed[s], 16)

    def block_unit(w, c0, rows=KD, row0=0):
        h = rows // 2
        view = w.rearrange("(k p) n -> p k n", p=P)
        part = lambda a, b: (view[:, row0 + a:row0 + b, bass.ds(c0, 256)] if not isinstance(c0, int)
                             else view[:, row0 + a:row0 + b, c0:c0 + 256],
                             lambda raw: raw[:, a * 256:b * 256].rearrange("p (k n) -> p k n", n=256))
        return part(0, h), part(h, rows)

    def paired_unit(w1, c1, w2, c2):
        def part(w, c, m):
            cols = slice(c, c + P) if isinstance(c, int) else bass.ds(c, P)
            return (w.rearrange("(k p) n -> p k n", p=P)[:, :, cols],
                    lambda raw: raw.rearrange("p (k m n) -> p k m n", m=2, n=P)[:, :, m, :])
        return part(w1, c1, 0), part(w2, c2, 1)

    def sp_load_all(engine):
        sp = engine.e
        mix_in, mix_out = t["mix_w_in"][0], t["mix_w_out"][0]
        with engine.loop(2, {ada_used: 12}) as layer:
            with engine.loop(3, {ada_used: 4}) as i:
                for b in range(2):
                    for h in range(2):
                        engine.wait(ada_used)
                        src = t["ada_w"][bass.ds(layer, 1)].rearrange("l (k p) n -> p (l k) n", p=P)
                        sp.dma_start(ADA[:, h], src[:, 4 * h:4 * h + 4, bass.ds(i * 2 * D + b * D, D)])\
                          .then_inc(ada_landed[h], 16)

        def plain(w, n):
            for i in range(n):
                load_unit(sp, *block_unit(w, i * 256))

        def moe(layer):
            u0 = plan.u[f"moe{layer}"]
            with sp.Fori(0, 2) as half:
                with sp.Fori(0, 8) as i:
                    for b in range(2):
                        w = [t[n][layer][bass.ds(half * 16 + i * 2 + b, 1)].rearrange("e d f -> (e d) f")
                             for n in ("moe_w1", "moe_w3")]
                        load_unit(sp, *paired_unit(w[0], 0, w[1], 0), off=half * 24 + i * 2, u=u0 + b)
                with sp.Fori(0, 4) as c:
                    for kh in range(2):
                        w = t["moe_w2"][layer][bass.ds(half * 16 + kh * 8, 8)].rearrange("e f n -> (e f) n")
                        load_unit(sp, *block_unit(w, c * 256), off=half * 24 + c * 2, u=u0 + 16 + kh)
            sp_unit[0] += 48

        def ffn(layer):
            u0 = plan.u[f"ffn{layer}"]
            w = t["ffn_w_up_2"][layer]
            with sp.Fori(0, FB // 2) as i:
                for b in range(2):
                    load_unit(sp, *paired_unit(w, i * 256 + b * P, w, i * 256 + (b * P + FF)), off=i * 2, u=u0 + b)
            w = t["ffn_w_down_2"][layer]
            with sp.Fori(0, 2) as i:
                for c in range(2):
                    for j, (k0, n) in enumerate(((0, 8), (8, 8), (16, 6))):
                        load_unit(sp, *block_unit(w, i * 512 + c * 256, n, k0), off=i * 6, u=u0 + FB + 3 * c + j)
            sp_unit[0] += 34

        def ple(layer):
            wp, wg = t["ple_w_proj_2"][layer], t["ple_w_gate_2"][layer]
            for half in range(2):
                view = wp.rearrange("(k p) n -> p k n", p=P)
                part = lambda k: (view[:, k, half * 512:half * 512 + 512], lambda raw: raw[:, k * 512:k * 512 + 512])
                load_unit(sp, part(0), part(1))
                for i in range(2):
                    load_unit(sp, *block_unit(wg, half * 512 + i * 256))

        plain(mix_in, 8)
        plain(mix_out, 4)
        moe(0)
        w = t["ssm_w_in"][0]
        with sp.Fori(0, SSM_G // 2) as i:
            for b in range(2):
                u = plan.u["ssm"] + 3 * b
                load_unit(sp, *block_unit(w, i * 512 + b * 256), off=i * 6, u=u)
                load_unit(sp, *block_unit(w, i * 512 + (SSM_INNER + b * 256)), off=i * 6, u=u + 1)
                c = i * 256 + (2 * SSM_INNER + b * P)
                load_unit(sp, *paired_unit(w, c, w, c + SSM_G * P), off=i * 6, u=u + 2)
        sp_unit[0] += 24
        for half in range(2):
            for i in range(4):
                load_unit(sp, *block_unit(t["ssm_w_out"][0], i * 256, KD, half * KD))
        moe(1)
        plain(t["ev_w_in_2"][0], 10)
        plain(t["ev_w_out_2"][0], 4)
        ffn(0)
        ple(0)
        w = t["od_w_glu_2"][0]
        for i in range(KD):
            load_unit(sp, *paired_unit(w, i * P, w, D + i * P))
        ffn(1)
        ple(1)
        assert sp_unit[0] == plan.unit

    def pool_constants(engine):
        pool, link = engine.e, engine.link
        pool.memset(IDENT[:], 0.0)
        pool.memset(ONES[:], 1.0)
        pool.memset(HEAD_ONES[:], 0.0)
        pool.memset(LATER[:], 1.0)
        for n in range(16):
            pool.memset(INV_COUNT[:, n:n + 1], 1.0 / (n + 1))
        for n in range(EPG):
            pool.memset(FALLING[:, n:n + 1], float(EPG - n))
        link(pool.memset(CAUSAL[:], 0.0))
        for h in range(2):
            link(pool.memset(HEAD_ONES[h * HD:h * HD + HD, h * HD:h * HD + HD], 1.0))
        pool.affine_select(out=IDENT[:], in_=IDENT[:], compare_op=ALU.not_equal, fill=1.0, base=0,
                           pattern=[[-1, P]], channel_multiplier=1)
        pool.affine_select(out=LATER[:], in_=LATER[:], compare_op=ALU.is_ge, fill=0.0, base=0,
                           pattern=[[1, SEQ]], channel_multiplier=-1)
        pool.affine_select(out=CAUSAL[:], in_=CAUSAL[:], compare_op=ALU.is_ge, fill=NEG, base=SEQ - P,
                           pattern=[[-1, SEQ]], channel_multiplier=1).then_inc(consts_ready, 1)

    def split_unit(pool, u, off=0):
        s = u % 2
        pool.wait_ge(landed[s], off * 16 + 32 * (u // 2 + 1))
        if u >= 2 or not isinstance(off, int):
            pool.wait_ge(unit_done, off + (u - 1))
        pool.tensor_tensor(TURN[:, s:s + 1], ONES[:, 0:1], ONES[:, 0:1], ALU.mult)
        pool.tensor_scalar(WH[:, s], RAW[:, s], 1.0, 1.0, ALU.mult, ALU.mult).then_inc(split_hi, 1)
        pool.wait_ge(split_hi, off + (u + 1))
        pool.tensor_tensor(WL[:, s], RAW[:, s], WH[:, s].bitcast(F32), ALU.subtract).then_inc(split_ready, 1)

    def split_units(pool, first, last):
        if last - first >= 4:
            with pool.Fori(0, (last - first) // 2) as i:
                for b in range(2):
                    split_unit(pool, first + b, off=i * 2)
        else:
            for u in range(first, last):
                split_unit(pool, u)

    def act_loads(act):
        def load(dst, src, s):
            act.dma_start(dst, src).then_inc(s, 16)
            n_small[0] += s is small_landed

        n = 0
        for name, ap in rows:
            at, left, done = col_at[name], ap.shape[0], 0
            while left:
                k = min(left, P - at % P)
                load(ROWS[at % P:at % P + k, at // P, :], ap[done:done + k], rows_landed)
                at, left, done, n = at + k, left - k, done + k, n + 1
        row_dmas.append(n)
        load(XTOK[:], t["x"][0].rearrange("(t p) d -> p t d", p=P), x_landed)
        for layer in range(2):
            load(ROUTER_W[:, layer, :, 0:GROUPS], t["moe_w_group"][layer].rearrange("(k p) g -> p k g", p=P), small_landed)
            load(ROUTER_W[:, layer, :, GROUPS:], t["moe_w_expert"][layer].rearrange("(k p) g e -> p k (g e)", p=P), small_landed)
            load(ROUTER_B[:, layer, 0:GROUPS], t["moe_b_group"][layer].partition_broadcast(P), small_landed)
            load(ROUTER_B[:, layer, GROUPS:], t["moe_b_expert"][layer].rearrange("g e -> (g e)").partition_broadcast(P), small_landed)
        load(DT_W[:], t["ssm_w_in"][0][:, 3 * SSM_INNER:].rearrange("(k p) n -> p k n", p=P), small_landed)
        load(DT_ROW[:, 0, :], t["ssm_dt_bias"][0].partition_broadcast(P), small_landed)
        load(DT_ROW[:, 1, :], t["ssm_A_log"][0].partition_broadcast(P), small_landed)
        load(D_ROW[:], t["ssm_D"][0].partition_broadcast(P), small_landed)
        load(FG_W[:], t["ev_w_in_2"][0][:, 5 * HALF:].rearrange("(k p) n -> p k n", p=P), small_landed)
        load(FG_B[:], t["ev_b_fgate_2"][0].partition_broadcast(P), small_landed)
        for i, name in enumerate(("ev_q_norm_2", "ev_k_norm_2")):
            for h in range(2):
                load(QK_GAIN[h * HD:h * HD + HD, i:i + 1], dram(name, 0, [[1, HD], [1, 1]]), small_landed)
        clipped = SEQ - 1 - REL_CLIP
        load(REL[0:HEADS, clipped:640], t["rel_flip"][0, :, 0:640 - clipped], rel_step)
        act.wait_ge(rel_step, 16)
        act.activation(REL[0:HEADS, 0:clipped], REL[0:HEADS, clipped:clipped + 1].broadcast_to([HEADS, clipped]), ACT.Copy)\
           .then_inc(rel_step, 1)
        act.wait_ge(rel_step, 17)
        load(rel_dram, REL[0:HEADS, :], rel_step)
        act.wait_ge(rel_step, 33)
        load(strip_dram, rel_dram.partition_broadcast(P), rel_step)
        act.wait_ge(rel_step, 49)
        load(STRIP[:], bass.AP(strip_dram.tensor, P - 1, [[HEADS * 640 - 1, P], [640, HEADS], [1, SEQ]]), strip_landed)
        b = plan.b["columns"]
        act.wait_ge(bank_free[b % 4], b // 4 + 1)
        act.activation(C_ACT[:], COLS[:, col_at["c"]:col_at["c"] + KD], ACT.Silu).then_inc(c_ready, 1)

    row_dmas, n_small = [], [0]
    rel_step, strip_landed, strip_ready = sem("rel_step"), sem("strip_landed"), sem("strip_ready")
    mod_ready = sem("mod_ready")

    def pe_start(pe):
        b = plan.b["columns"]
        pe.e.wait_ge(consts_ready, 1)
        pe.e.wait_ge(rows_landed, 16 * row_dmas[0])
        for r in range(n_row_tiles):
            n = min(P, n_cols - r * P)
            bank = take_bank(pe, b + r)
            nc.tensor.transpose(bank[:, 0:n], ROWS[0:n, r, :], IDENT[0:n, 0:n]).then_inc(bank_ready, 1)
        b = plan.b["load"]
        pe.e.wait_ge(x_landed, 16)
        for k in range(KD):
            bank = take_bank(pe, b + k)
            for tt in range(NT):
                ins = nc.tensor.transpose(bank[:, tt * P:tt * P + P], XTOK[:, tt, k * P:k * P + P], IDENT[:])
            ins.then_inc(bank_ready, 1)
        for q in range(12):
            pe.e.wait_ge(ada_used, 2 + 2 * (q + 1))
            pair = take_pair(pe, plan.p["ada"] + q)
            for m in range(KD):
                ins = nc.tensor.matmul(pair[:, 0, m:m + 1], ADA_ACC[:, q % 2, m * P:m * P + P], ONES[:, 0:1],
                                       start=True, stop=True)
            ins.then_inc(pair_ready, 1)

    def dve_start(dve):
        for h in range(2):
            dve.e.memset(ADA_ACC[:, h, :], 0.0).then_inc(ada_used, 1)
        b = plan.b["columns"]
        for r in range(n_row_tiles):
            n = min(P, n_cols - r * P)
            dve.e.tensor_copy(COLS[:, r * P:r * P + n], full_bank(dve, b + r)[:, 0:n]).then_inc(bank_free[(b + r) % 4], 1)
        b = plan.b["load"]
        for k in range(KD):
            dve.e.tensor_copy(X[:, k, :], full_bank(dve, b + k)[:]).then_inc(bank_free[(b + k) % 4], 1)
        dve.e.wait_ge(bank_free[(b + k) % 4], (b + k) // 4 + 1)
        dve.wait(c_ready)
        dve.wait(ada_used, 2)
        for q in range(12):
            for h in range(2):
                dve.wait(ada_landed[h], 16)
                for k in range(4):
                    src, c = ADA[:, h, k, :], C_ACT[:, 4 * h + k:4 * h + k + 1]
                    acc = ADA_ACC[:, q % 2, :]
                    if h == 0 and k == 0:
                        if q >= 2:
                            dve.e.wait_ge(pair_ready, q - 1)
                        ins = dve.e.tensor_scalar(acc, src, c, None, ALU.mult)
                    else:
                        ins = dve.e.scalar_tensor_tensor(acc, src, c, acc, ALU.mult, ALU.add)
                    if k < 3:
                        dve.link(ins)
                ins.then_inc(ada_used, 1)
                dve.wait(ada_used)
            dve.e.wait_ge(pair_ready, q + 1)
            at = col_at["ada_b"] + q * KD
            dve.e.tensor_tensor(MOD[:, q * KD:q * KD + KD], PAIR[q % 2][:, 0, 0:KD], COLS[:, at:at + KD], ALU.add)\
                 .then_inc(evac[q % 2], 1)
        dve.e.wait_ge(evac[0], 6)
        dve.e.wait_ge(evac[1], 6)
        for n in range(4):
            layer, which = n // 2, n % 2
            at, w = (layer * 6 + 1 + 3 * which) * KD, col_at[("norm1", "norm2")[which]] + layer * KD
            dve.e.scalar_tensor_tensor(GAIN[:, n, :], MOD[:, at:at + KD], 1.0, COLS[:, w:w + KD], ALU.add, ALU.mult)\
                 .then_inc(mod_ready, 1)
        dve.wait(strip_landed, 16)
        dve.e.memset(STRIP[0:HD, :, SEQ - HD:SEQ], NEG).then_inc(strip_ready, 1)
        dve.wait(mod_ready, 4)

    norm_gain = {0: lambda k: GAIN[:, 0, k:k + 1], 1: lambda k: GAIN[:, 1, k:k + 1], 2: lambda k: GAIN[:, 2, k:k + 1],
                 3: lambda k: GAIN[:, 3, k:k + 1], 4: lambda k: col("final", k), 5: lambda k: col("norm_mix", k),
                 6: lambda k: col("norm_ffn", k), 7: lambda k: 1.0, 8: lambda k: col("norm_mix", KD + k),
                 9: lambda k: col("norm_ffn", KD + k), 10: lambda k: 1.0}
    norm_shift = {0: (0, 0), 1: (0, 3), 2: (1, 0), 3: (1, 3)}
    FINAL, PLAIN = 4, 8

    def pe_norm(pe, n):
        bank = take_bank(pe, plan.b[f"norm{n}"])
        for k in range(KD):
            pe.wait(sq_ready)
            ins = nc.tensor.matmul(bank[:], ONES[:], SQ[:, k % 2, :], start=k == 0, stop=k == KD - 1)
            if k < KD - 1:
                ins.then_inc(sq_used, 1)
        ins.then_inc(bank_ready, 1)

    def act_root(act, tile, ready):
        act.wait(ready)
        act.e.activation(tile, tile, ACT.Sqrt).then_inc(root_ready, 1)

    def act_norm(act, n):
        pairs = plan.p[f"norm{n}"]
        if n == 0:
            b = plan.b["load"] + KD - 1
            act.e.wait_ge(bank_free[b % 4], b // 4 + 1)
        if n == FINAL + 1:
            act.wait(x_ready)
        for s in range(2):
            act.e.wait_ge(evac[s], pairs // 2)
        for k in range(KD):
            if k >= 2:
                act.wait(sq_used)
            act.e.activation(SQ[:, k % 2, :], X[:, k, :], ACT.Square).then_inc(sq_ready, 1)
        act.wait(sq_used, KD - 1 - (KD - 2))
        act_root(act, RSTD[:], var_ready)
        if n in (FINAL, PLAIN):
            return
        for k in range(KD):
            act.wait(pre_ready)
            if n in norm_shift:
                ins = act.e.activation(HH[:, k, :], TMP[:, k % 2, :], ACT.Identity, bias=mod(*norm_shift[n], k))
            else:
                ins = act.e.activation(HH[:, k, :], TMP[:, k % 2, :], ACT.Copy)
            ins.then_inc(hi_ready, 1)

    def dve_rstd(dve, total, tile, count):
        ins = dve.e.tensor_scalar(tile, total, 1.0 / count, EPS, ALU.mult, ALU.add)
        ins.then_inc(var_ready, 1)
        dve.wait(root_ready)
        dve.link(dve.e.reciprocal(tile, tile))

    def dve_norm(dve, n):
        b = plan.b[f"norm{n}"]
        bank = full_bank(dve, b)
        dve.e.tensor_scalar(RSTD[:], bank[:], 1.0 / D, EPS, ALU.mult, ALU.add).then_inc(var_ready, 1)
        dve.wait(root_ready)
        dve.e.reciprocal(RSTD[:], RSTD[:]).then_inc(bank_free[b % 4], 1)
        dve.e.wait_ge(bank_free[b % 4], b // 4 + 1)
        gain = norm_gain[n]
        if n in (FINAL, PLAIN):
            to = X if n == FINAL else HF
            for k in range(KD):
                ins = dve.e.scalar_tensor_tensor(to[:, k, :], X[:, k, :], gain(k), RSTD[:], ALU.mult, ALU.mult)
            ins.then_inc(x_ready if n == FINAL else h_ready, 1)
            dve.passed(x_ready if n == FINAL else h_ready, 1)
            return

        def pre(k):
            dve.e.scalar_tensor_tensor(TMP[:, k % 2, :], X[:, k, :], gain(k), RSTD[:], ALU.mult, ALU.mult)\
                 .then_inc(pre_ready, 1)

        pre(0)
        for k in range(KD):
            if k + 1 < KD:
                if k:
                    dve.wait(h_ready)
                pre(k + 1)
            dve.wait(pre_ready)
            dve.wait(hi_ready)
            hi = HH[:, k, :].bitcast(F32)
            if n in norm_shift:
                ins = dve.e.scalar_tensor_tensor(HL[:, k, :], TMP[:, k % 2, :], mod(*norm_shift[n], k), hi,
                                                 ALU.add, ALU.subtract)
            else:
                ins = dve.e.tensor_tensor(HL[:, k, :], TMP[:, k % 2, :], hi, ALU.subtract)
            ins.then_inc(h_ready, 1)
        dve.passed(h_ready, 2)

    def dve_residual(dve, name, n, units_per_pair, gate):
        for i in range(n):
            p = plan.p[name] + i
            pair = full_pair(dve, plan.u[name] + (i + 1) * units_per_pair - 1, p)
            c = 2 * (i % 4)
            if gate is None:
                dve.e.tensor_tensor(X[:, c:c + 2, :], pair[:], X[:, c:c + 2, :], ALU.add).then_inc(evac[p % 2], 1)
            else:
                for m in range(2):
                    ins = dve.e.scalar_tensor_tensor(X[:, c + m, :], pair[:, m, :], mod(*gate, c + m), X[:, c + m, :],
                                                     ALU.mult, ALU.add)
                ins.then_inc(evac[p % 2], 1)

    def pe_matrix(pe, name, n, xh=hh, xl=hl):
        for i in range(n):
            pair = take_pair(pe, plan.p[name] + i)
            unit_channels(pe, plan.u[name] + i, pair, xh, xl, KD)

    def pe_mixin(pe):
        pe.wait(h_ready, KD)
        pe_matrix(pe, "mixin", 6)
        for i in range(6, 8):
            unit_tokens(pe, plan.u["mixin"] + i, take_pair(pe, plan.p["mixin"] + i))

    def act_copy_pairs(act, name, first, n, to, tokens, func=ACT.Copy):
        for i in range(n):
            u, p = plan.u[name] + first + i, plan.p[name] + first + i
            pair = full_pair(act, u, p)
            if tokens:
                ins = act.e.activation(to[:, :, i * 256:i * 256 + 256],
                                       pair[:].rearrange("p b (j n) -> p (b j) n", n=256), func)
            else:
                ins = act.e.activation(to[:, 2 * i:2 * i + 2, :], pair[:], func)
            ins.then_inc(evac[p % 2], 1)

    def act_mixin(act):
        act.e.dma_start(POOL_W[:], t["pool_w"][0].rearrange("g c d -> c g d")).then_inc(pool_w_landed, 16)
        act_copy_pairs(act, "mixin", 0, 2, U, False)
        act_copy_pairs(act, "mixin", 2, 2, Q0, False)
        act_copy_pairs(act, "mixin", 4, 2, K0, False)
        act_copy_pairs(act, "mixin", 6, 2, V0, True)

    pool_w_landed = sem("pool_w_landed")
    pooled_ready = sem("pooled_ready")

    def dve_pool_window(dve, g):
        u, w = U[:, g, :], 2 << g
        if g % 2 == 0:
            p = plan.p["mixin"] + g // 2
            dve.e.wait_ge(evac[p % 2], p // 2 + 1)
        cur = u
        for level in range(g + 1):
            sh, new = 1 << level, PSCR[:, level % 2, :]
            dve.e.tensor_tensor(new[:, sh:], cur[:, sh:], cur[:, :SEQ - sh], ALU.add)
            dve.link(dve.e.tensor_copy(new[:, :sh], cur[:, :sh]))
            cur = new
        dve.e.scalar_tensor_tensor(POOLED[:, g, w:], cur[:, w:], 1.0 / w, u[:, w:], ALU.mult, ALU.subtract)
        dve.link(dve.e.tensor_tensor(POOLED[:, g, :w], cur[:, :w], INV_COUNT[:, :w], ALU.mult))
        dve.e.tensor_tensor(POOLED[:, g, :w], POOLED[:, g, :w], u[:, :w], ALU.subtract).then_inc(pooled_ready, 1)

    def pe_pool(pe):
        pe.e.wait_ge(pool_w_landed, 16)
        for g in range(4):
            pe.wait(pooled_ready)
            bank = take_bank(pe, plan.b["pool"] + g)
            nc.tensor.matmul(bank[:], POOL_W[:, g, :], POOLED[:, g, :], start=True, stop=True).then_inc(bank_ready, 1)

    def dve_pool(dve):
        for g in range(4):
            dve_pool_window(dve, g)
        dve.e.wait_ge(unit_done, plan.u["mixin"] + 8)
        for g in range(4):
            b = plan.b["pool"] + g
            if g >= 2:
                dve.e.wait_ge(bank_free[(b - 2) % 4], (b - 2) // 4 + 1)
            dve.e.tensor_scalar(TMP[:, g % 2, :], full_bank(dve, b)[:], col("pool_scale", g), None, ALU.mult)\
                 .then_inc(pre_ready, 1)
            dve.wait(pre_ready)
            dve.wait(hi_ready)
            dve.e.tensor_tensor(HL[:, g, :], TMP[:, g % 2, :], HH[:, g, :].bitcast(F32), ALU.subtract)\
                 .then_inc(bank_free[b % 4], 1)

    def act_pool(act):
        for g in range(4):
            act.wait(pre_ready)
            act.e.activation(HH[:, g, :], TMP[:, g % 2, :], ACT.Copy).then_inc(hi_ready, 1)

    SEG = [0, P, 3 * P, 6 * P]
    HOME = {3: (0, 0), 2: (1, 0), 0: (1, 3 * P), 1: (2, 0)}
    PT_HOME = {0: (0, 0), 1: (1, 0), 3: (1, 3 * P), 2: (2, 0)}
    att_sems = [{s: sem(f"att{n}_{s}") for s in ("scaled", "exp", "probs", "out")} for n in range(2)]

    def att_bank(n, h, turned, i):
        if turned:
            at = 3 + 6 * h + 3 if h + 1 < HEADS else 3 + 6 * h
        else:
            at = 6 * h - 3 if h else 0
        return plan.b[f"att{n}"] + at + i

    def pe_attention(pe, n, q, k, v, s, pt, fox):
        w = att_sems[n]

        def scores(h):
            a, tile = (h % 2) * HD, h // 2
            for i in range(3):
                b = att_bank(n, h, False, i)
                bank = take_bank(pe, b)
                mine = [j for j in HOME if HOME[j][0] == i]
                for j in mine:
                    at, wide = HOME[j][1], P * (j + 1)
                    ins = nc.tensor.matmul(bank[:, at:at + wide], q[a:a + HD, tile, j * P:j * P + P],
                                           k[a:a + HD, tile, 0:wide], start=True, stop=not fox)
                    if fox:
                        ins = nc.tensor.matmul(bank[:, at:at + wide], MINUS_HEAD[:, h, :], FCUM[:, 1, 0:wide],
                                               start=False, stop=True)
                ins.then_inc(bank_ready, 1)

        scores(0)
        for h in range(HEADS):
            if h + 1 < HEADS:
                scores(h + 1)
            pe.wait(w["probs"])
            for i in range(3):
                bank = take_bank(pe, att_bank(n, h, True, i))
                for kt in [x for x in PT_HOME if PT_HOME[x][0] == i]:
                    for j in range(kt, NT):
                        at = PT_HOME[kt][1] + (j - kt) * P
                        ins = nc.tensor.transpose(bank[:, at:at + P], s[:, h % 2, SEG[j] + kt * P:SEG[j] + kt * P + P],
                                                  IDENT[:])
                ins.then_inc(bank_ready, 1)
            p = plan.p[f"att{n}"] + h // 2
            if h % 2 == 0:
                pair = take_pair(pe, p)
            b = att_bank(n, h, True, 2)
            pe.e.wait_ge(bank_free[b % 4], b // 4 + 1)
            a = (h % 2) * HD
            for kt in range(NT):
                ins = nc.tensor.matmul(pair[a:a + HD, 0, kt * P:SEQ], v[:, kt, h * HD:h * HD + HD],
                                       pt[:, h % 2, TRI_AT[kt]:TRI_AT[kt] + SEQ - kt * P],
                                       start=kt == 0, stop=kt == NT - 1)
            ins.then_inc(w["out"], 1)

    def dve_attention(dve, n, s, bias):
        w = att_sems[n]

        def scale(h):
            for i in range(3):
                b = att_bank(n, h, False, i)
                bank = full_bank(dve, b)
                for j in [x for x in HOME if HOME[x][0] == i]:
                    at, wide = HOME[j][1], P * (j + 1)
                    ins = dve.e.scalar_tensor_tensor(s[:, h % 2, SEG[j]:SEG[j] + wide], bank[:, at:at + wide],
                                                     HD ** -0.5, bias(h)[:, SEQ - wide:SEQ], ALU.mult, ALU.add)
                ins.then_inc(bank_free[b % 4], 1)
            dve.e.wait_ge(bank_free[b % 4], b // 4 + 1)
            for j in range(NT):
                ins = dve.e.tensor_reduce(MX[:, h % 2, 0, j:j + 1], s[:, h % 2, SEG[j]:SEG[j] + P * (j + 1)], AX.X, ALU.max)
            dve.link(ins)
            dve.e.tensor_scalar(MX[:, h % 2, 1, :], MX[:, h % 2, 0, :], -1.0, None, ALU.mult).then_inc(w["scaled"], 1)

        def normalise(h):
            dve.wait(w["exp"])
            dve.link(dve.e.reciprocal(SUMS[:, h % 2, :], SUMS[:, h % 2, :]))
            for j in range(NT):
                seg = s[:, h % 2, SEG[j]:SEG[j] + P * (j + 1)]
                ins = dve.e.tensor_scalar(seg, seg, SUMS[:, h % 2, j:j + 1], None, ALU.mult)
            ins.then_inc(w["probs"], 1)

        def rest(i):
            p = plan.p[f"att{n}"] + i
            dve.wait(hi_ready)
            dve.e.tensor_tensor(HL[:, 4 + i, :], PAIR[p % 2][:, 0, :], HH[:, 4 + i, :].bitcast(F32),
                                ALU.subtract).then_inc(evac[p % 2], 1)

        scale(0)
        for h in range(HEADS):
            if h + 1 < HEADS:
                scale(h + 1)
            normalise(h)
            if h % 2 == 0 and h:
                rest(h // 2 - 1)
        rest(HEADS // 2 - 1)

    def act_attention(act, n, s, pt):
        w = att_sems[n]

        def exponential(h):
            act.wait(w["scaled"])
            for j in range(NT):
                seg = s[:, h % 2, SEG[j]:SEG[j] + P * (j + 1)]
                ins = act.e.activation(seg, seg, ACT.Exp, bias=MX[:, h % 2, 1, j:j + 1], accum_out=SUMS[:, h % 2, j:j + 1])
            ins.then_inc(w["exp"], 1)

        def high(i):
            p = plan.p[f"att{n}"] + i
            act.wait(w["out"], 2)
            act.e.activation(HH[:, 4 + i, :], PAIR[p % 2][:, 0, :], ACT.Copy).then_inc(hi_ready, 1)

        exponential(0)
        for h in range(HEADS):
            if h + 1 < HEADS:
                exponential(h + 1)
            if h % 2 == 0 and h:
                high(h // 2 - 1)
            for i in range(3):
                b = att_bank(n, h, True, i)
                bank = full_bank(act, b)
                tiles = [x for x in PT_HOME if PT_HOME[x][0] == i]
                for kt in tiles:
                    at, wide = PT_HOME[kt][1], SEQ - kt * P
                    ins = act.e.activation(pt[:, h % 2, TRI_AT[kt]:TRI_AT[kt] + wide], bank[:, at:at + wide], ACT.Copy)
                ins.then_inc(bank_free[b % 4], 1)
        high(HEADS // 2 - 1)

    def pe_after_h(pe, pairs):
        for s in range(2):
            pe.e.wait_ge(evac[s], pairs // 2)

    moe_sems = {s: sem(f"moe_{s}") for s in ("logit", "comb", "comb_saved", "exp_in", "exp_out", "up", "hidden",
                                             "hidden_hi", "hidden_ready")}
    comb_landed = [sem("comb_landed0"), sem("comb_landed1")]

    def pe_small_logits(pe, bank, w, n):
        for tt in range(NT):
            for k in range(KD):
                for part, first in ((HH, True), (HL, False)):
                    ins = nc.tensor.matmul(bank[:, tt * n:tt * n + n], part[:, k, tt * P:tt * P + P].bitcast(F32), w[:, k, :],
                                           start=first and k == 0, stop=not first and k == KD - 1)
        ins.then_inc(bank_ready, 1)

    def dve_first_max(dve, values, best, mark, scratch, n):
        dve.link(dve.e.tensor_reduce(best, values, AX.X, ALU.max))
        dve.link(dve.e.tensor_tensor(scratch, values, bcast(best, 2, n), ALU.is_equal))
        dve.link(dve.e.tensor_tensor(scratch, scratch, bcast(FALLING[:, EPG - n:EPG], 1, NT), ALU.mult))
        first = GATE[:, 11, :, 0]
        dve.link(dve.e.tensor_reduce(first, scratch, AX.X, ALU.max))
        dve.link(dve.e.tensor_tensor(mark, scratch, bcast(first, 2, n), ALU.is_equal))

    def dve_router(dve, layer):
        w = moe_sems
        b = plan.b[f"moe{layer}"]
        if layer == 0:
            dve.e.wait_ge(small_landed, 16 * n_small[0])
        bank = full_bank(dve, b)
        nl = GROUPS + EXPERTS
        dve.e.tensor_tensor(LOGIT[:], bank[:, 0:NT * nl].rearrange("p (t n) -> p t n", n=nl),
                            bcast(ROUTER_B[:, layer, :], 1, NT), ALU.add).then_inc(bank_free[b % 4], 1)
        dve.e.wait_ge(bank_free[b % 4], b // 4 + 1)
        gl = LOGIT[:, :, 0:GROUPS]
        group, e1, e2, scratch = GATE[:, 0, :, 0:GROUPS], GATE[:, 1], GATE[:, 2], GATE[:, 3]
        gmax, top1, top2 = GATE[:, 4, :, 0], GATE[:, 4, :, 1], GATE[:, 4, :, 2]
        gprob, share1, share2 = GATE[:, 4, :, 3], GATE[:, 4, :, 4], GATE[:, 4, :, 5]
        es, es2 = GATE[:, 5], GATE[:, 6]
        expo = GATE[:, 7]
        dve_first_max(dve, gl, gmax, group, scratch[:, :, 0:GROUPS], GROUPS)
        dve.e.tensor_tensor(expo[:, :, 0:GROUPS], gl, bcast(gmax, 2, GROUPS), ALU.subtract)
        dve.link(dve.e.tensor_tensor(ESEL[:], LOGIT[:, :, GROUPS:].rearrange("p t (g e) -> p t g e", e=EPG),
                                     bcast(group, 3, EPG), ALU.mult))
        dve.link(dve.e.tensor_reduce(es, ESEL[:].rearrange("p t g e -> p t e g"), AX.X, ALU.add))
        dve_first_max(dve, es, top1, e1, scratch, EPG)
        dve.link(dve.e.scalar_tensor_tensor(es2, e1, 2 * NEG, es, ALU.mult, ALU.add))
        dve_first_max(dve, es2, top2, e2, scratch, EPG)
        dve.e.tensor_tensor(expo[:, :, GROUPS], top2, top1, ALU.subtract).then_inc(w["exp_in"], 1)
        dve.wait(w["exp_out"])
        dve.e.tensor_reduce(gprob, expo[:, :, 0:GROUPS], AX.X, ALU.add)
        dve.link(dve.e.tensor_scalar(share1, expo[:, :, GROUPS], 1.0, None, ALU.add))
        dve.link(dve.e.tensor_tensor(share1, share1, gprob, ALU.mult))
        dve.link(dve.e.reciprocal(share1, share1))
        dve.link(dve.e.tensor_tensor(share2, share1, expo[:, :, GROUPS], ALU.mult))
        dve.e.tensor_tensor(e1, e1, bcast(share1, 2, EPG), ALU.mult)
        dve.link(dve.e.tensor_tensor(e2, e2, bcast(share2, 2, EPG), ALU.mult))
        dve.link(dve.e.tensor_tensor(e1, e1, e2, ALU.add))
        dve.e.tensor_tensor(COMB[:], bcast(e1, 2, GROUPS), bcast(group, 3, EPG), ALU.mult).then_inc(w["comb"], 1)
        b += 1
        dve.e.tensor_copy(COMB_T[:], full_bank(dve, b)[0:EXPERTS, :]).then_inc(bank_free[b % 4], 1)

    def pe_router(pe, layer):
        b = plan.b[f"moe{layer}"]
        if layer == 0:
            pe.e.wait_ge(small_landed, 16 * n_small[0])
        pe.wait(h_ready, KD)
        pe_small_logits(pe, take_bank(pe, b), ROUTER_W[:, layer], GROUPS + EXPERTS)

    def pe_router_turn(pe, layer):
        b = plan.b[f"moe{layer}"]
        pe.wait(moe_sems["comb"])
        bank = take_bank(pe, b + 1)
        for tt in range(NT):
            ins = nc.tensor.transpose(bank[0:EXPERTS, tt * P:tt * P + P], COMB[:, tt].rearrange("p g e -> p (g e)"), IDENT[:])
        ins.then_inc(bank_ready, 1)

    def act_router(act, layer):
        w = moe_sems
        act.wait(w["exp_in"])
        expo = GATE[:, 7, :, 0:GROUPS + 1]
        act.e.activation(expo, expo, ACT.Exp).then_inc(w["exp_out"], 1)
        b = plan.b[f"moe{layer}"] + 1
        act.e.wait_ge(bank_free[b % 4], b // 4 + 1)
        act.e.dma_start(comb_dram[layer], COMB_T[:]).then_inc(w["comb_saved"], 16)
        act.wait(w["comb_saved"], 16)

    def pe_moe(pe, layer):
        w = moe_sems
        u0, p0 = plan.u[f"moe{layer}"], plan.p[f"moe{layer}"]
        with pe.e.Fori(0, 2) as half:
            with pe.e.Fori(0, 8) as i:
                for b in range(2):
                    pair = take_pair(pe, p0 + b, half * 10 + i)
                    unit_channels(pe, u0 + b, pair, hh, hl, KD, off=half * 24 + i * 2)
            with pe.e.Fori(0, 2) as i:
                for c in range(2):
                    pair = take_pair(pe, p0 + 16 + c, half * 10 + i)
                    if c == 0:
                        pe.e.wait_ge(w["hidden_ready"], half * 16 + (layer * 32 + 16))
                    for kh in range(2):
                        unit_channels(pe, u0 + 16 + 2 * c + kh, pair, lambda k: MHH[:, 8 * kh + k, :],
                                      lambda k: MHL[:, 8 * kh + k, :], KD, first=kh == 0, last=kh == 1, off=half * 24 + i * 4)

    def act_moe(act, layer):
        w = moe_sems
        u0, p0 = plan.u[f"moe{layer}"], plan.p[f"moe{layer}"]
        with act.loop(2, {w["hidden"]: 16}) as half:
            with act.loop(8, {w["hidden"]: 2}) as i:
                for b in range(2):
                    row = comb_dram[layer][bass.ds(half * 16 + i * 2 + b, 1), :]
                    act.e.dma_start(COMB_ROW[:, b, :], row.rearrange("a n -> (a n)").partition_broadcast(P))\
                         .then_inc(comb_landed[b], 16)
                    pair = full_pair(act, u0 + b, p0 + b, half * 24 + i * 2)
                    act.e.activation(SQ[:, b, :], pair[:, 0, :], ACT.Silu).then_inc(w["up"], 1)
                    act.wait(w["hidden"])
                    act.e.wait_ge(consts_ready, 1)
                    act.e.activation(MHH[:, bass.ds(i * 2 + b, 1), :], TMP[:, b:b + 1, :], ACT.Copy).then_inc(w["hidden_hi"], 1)

    def dve_moe(dve, layer):
        w = moe_sems
        u0, p0 = plan.u[f"moe{layer}"], plan.p[f"moe{layer}"]
        per = {w["up"]: 2, w["hidden"]: 2, w["hidden_hi"]: 2, comb_landed[0]: 16, comb_landed[1]: 16}
        with dve.loop(2, {s: 8 * n for s, n in per.items()}) as half:
            with dve.loop(8, per) as i:
                for b in range(2):
                    pair = PAIR[b]
                    dve.wait(w["up"])
                    dve.e.tensor_tensor(SQ[:, b, :], SQ[:, b, :], pair[:, 1, :], ALU.mult).then_inc(evac[b], 1)
                    dve.e.wait_ge(evac[b], half * 10 + i + ((p0 + b) // 2 + 1))
                    dve.wait(comb_landed[b], 16)
                    dve.e.tensor_tensor(TMP[:, b, :], SQ[:, b, :], COMB_ROW[:, b, :], ALU.mult).then_inc(w["hidden"], 1)
                    dve.wait(w["hidden"])
                    dve.wait(w["hidden_hi"])
                    dve.e.tensor_tensor(MHL[:, bass.ds(i * 2 + b, 1), :], TMP[:, b:b + 1, :],
                                        MHH[:, bass.ds(i * 2 + b, 1), :].bitcast(F32), ALU.subtract).then_inc(w["hidden_ready"], 1)
            with dve.e.Fori(0, 2) as i:
                for c in range(2):
                    pair = full_pair(dve, u0 + 16 + 2 * c + 1, p0 + 16 + c, half * 24 + i * 4)
                    for m in range(2):
                        x = X[:, bass.ds(i * 4 + 2 * c + m, 1), :]
                        g = MOD[:, bass.ds(i * 4 + (layer * 6 + 5) * KD + 2 * c + m, 1)]
                        ins = dve.e.scalar_tensor_tensor(x, pair[:, m:m + 1, :], g, x, ALU.mult, ALU.add)
                    ins.then_inc(evac[c], 1)

    ssm_sems = {s: sem(f"ssm_{s}") for s in ("exp_in", "exp_out", "log_ready", "cum_ready", "cum_saved", "conv_in", "conv_ready",
                                             "decay_in", "decay_out", "masked", "first_head", "gated")}
    row_landed = [sem("decay_row_landed0"), sem("decay_row_landed1")]
    SERIES = [1 / 13, 1 / 11, 1 / 9, 1 / 7, 1 / 5, 1 / 3]

    def at(expr, n, size=1):
        return slice(n, n + size) if isinstance(expr, int) else bass.ds(expr + n, size)

    def settle(act):
        act.e.wait_ge(consts_ready, 1)

    def dve_softplus(dve, x, o, s, exp_in, exp_out, sign):
        dve.link(dve.e.tensor_scalar(s[0], x, -1.0, None, ALU.mult))
        dve.e.tensor_tensor(s[0], s[0], x, ALU.max).then_inc(exp_in, 1)
        dve.wait(exp_out)
        dve.link(dve.e.tensor_scalar(s[1], s[0], 2.0, None, ALU.add))
        dve.link(dve.e.reciprocal(s[1], s[1]))
        dve.link(dve.e.tensor_tensor(s[1], s[0], s[1], ALU.mult))
        dve.link(dve.e.tensor_tensor(s[2], s[1], s[1], ALU.mult))
        dve.link(dve.e.tensor_scalar(s[3], s[2], SERIES[0], None, ALU.mult))
        for c in SERIES[1:]:
            dve.link(dve.e.scalar_tensor_tensor(s[3], s[3], c, s[2], ALU.add, ALU.mult))
        dve.link(dve.e.scalar_tensor_tensor(s[3], s[3], 1.0, s[1], ALU.add, ALU.mult))
        dve.link(dve.e.tensor_scalar(s[0], x, 0.0, None, ALU.max if sign > 0 else ALU.min))
        dve.link(dve.e.scalar_tensor_tensor(o, s[3], 2.0 * sign, s[0], ALU.mult, ALU.add))

    def act_softplus(act, y, exp_in, exp_out):
        act.wait(exp_in)
        act.e.activation(y, y, ACT.Exp, scale=-1.0).then_inc(exp_out, 1)

    def pe_dt(pe):
        b = plan.b["dt"]
        pe.wait(h_ready, KD)
        pe_small_logits(pe, take_bank(pe, b), DT_W, SSM_H)
        pe.wait(ssm_sems["log_ready"])
        bank = take_bank(pe, b + 1)
        for tt in range(NT):
            ins = nc.tensor.transpose(bank[0:SSM_H, tt * P:tt * P + P], DTS[:, 4, tt, :], IDENT[:])
        ins.then_inc(bank_ready, 1)
        pe.wait(ssm_sems["cum_ready"])
        bank = take_bank(pe, b + 2)
        for tt in range(NT):
            ins = nc.tensor.transpose(bank[:, tt * SSM_H:tt * SSM_H + SSM_H], ACS[:, 1, tt * P:tt * P + P],
                                      IDENT[0:SSM_H, 0:SSM_H])
        ins.then_inc(bank_ready, 1)

    def act_dt(act):
        w = ssm_sems
        act.wait(w["exp_in"])
        act.e.activation(DTS[:, 0], DTS[:, 0], ACT.Exp, scale=-1.0)
        act.e.activation(DT_ROW[:, 1, :], DT_ROW[:, 1, :], ACT.Exp).then_inc(w["exp_out"], 1)
        act.wait(w["cum_ready"])
        act.e.dma_start(acs_dram, ACS[:, 1, :]).then_inc(w["cum_saved"], 16)
        act.wait(w["cum_saved"], 16)
        for hh in range(2):
            act_decay_row(act, 0, hh)

    def act_decay_row(act, e, head):
        act.e.dma_start(ACS_ROW[:, head % 2, :], acs_dram[at(e, head), :].rearrange("a n -> (a n)").partition_broadcast(P))\
             .then_inc(row_landed[head % 2], 16)

    def dve_dt(dve):
        w, b = ssm_sems, plan.b["dt"]
        for h in range(2):
            dve.e.tensor_copy(D_COL[h * HD:h * HD + HD, :], D_ROW[h * HD:h * HD + HD, :].rearrange("p (m h) -> p h m", h=2)[:, h, :])
        dve.e.tensor_tensor(DTS[:, 5], full_bank(dve, b)[:, 0:NT * SSM_H].rearrange("p (t h) -> p t h", h=SSM_H),
                            bcast(DT_ROW[:, 0, :], 1, NT), ALU.add).then_inc(bank_free[b % 4], 1)
        dve.e.wait_ge(bank_free[b % 4], b // 4 + 1)
        dve_softplus(dve, DTS[:, 5], DT[:], [DTS[:, i] for i in range(4)], w["exp_in"], w["exp_out"], 1)
        dve.e.scalar_tensor_tensor(DTS[:, 4], DT[:], -1.0, bcast(DT_ROW[:, 1, :], 1, NT), ALU.mult, ALU.mult)\
             .then_inc(w["log_ready"], 1)
        b += 1
        dve.e.tensor_copy(ACS[:, 0, :], full_bank(dve, b)[0:SSM_H, :]).then_inc(bank_free[b % 4], 1)
        dve.e.wait_ge(bank_free[b % 4], b // 4 + 1)
        dve.e.tensor_tensor_scan(ACS[:, 1, :], ONES[0:SSM_H, 0:1].broadcast_to([SSM_H, SEQ]), ACS[:, 0, :], 0.0,
                                 ALU.mult, ALU.add).then_inc(w["cum_ready"], 1)
        b += 1
        dve.link(dve.e.tensor_copy(ACS_COL[:].rearrange("p t h -> p (t h)"), full_bank(dve, b)[:, 0:NT * SSM_H]))
        dve.e.tensor_copy(RSTD[0:1, 0:1], ONES[0:1, 0:1]).then_inc(bank_free[b % 4], 1)

    def pe_ssm_units(pe, e, c):
        for j in range(3):
            p = plan.p["ssm"] + 3 * c + j
            pair = take_pair(pe, p, turns(e, 3))
            unit_channels(pe, plan.u["ssm"] + 3 * c + j, pair, hh, hl, KD, off=times(e, 6))

    def turns(e, n):
        return 0 if e is None else e * n

    times = turns

    def act_ssm_units(act, e, c):
        w, par = ssm_sems, c % 2
        u, p = plan.u["ssm"] + 3 * c, plan.p["ssm"] + 3 * c
        pair = full_pair(act, u, p, times(e, 6))
        act.e.activation(ZS[:, par], pair[:], ACT.Silu).then_inc(evac[p % 2], 1)
        for j, tiles in ((1, (2 * c, 2 * c + 1)), (2, (16 + c, 24 + c))):
            pair = full_pair(act, u + j, p + j, times(e, 6))
            settle(act)
            for m, ct in enumerate(tiles):
                step = 4 if j == 1 else 2
                wc = COLS[:, at(times(e, step), col_at["conv_w"] + 3 * 32 + ct)]
                bc = COLS[:, at(times(e, step), col_at["conv_b"] + ct)]
                act.e.activation(CONV[:, par, 2 * (j - 1) + m, :], pair[:, m, :], ACT.Identity, bias=bc, scale=wc)\
                     .then_inc(w["conv_in"], 1)
            act.e.wait_ge(evac[(p + j) % 2], turns(e, 3) + ((p + j) // 2 + 1))
            both = CONV[:, par, 2 * (j - 1):2 * j, :]
            act.e.activation(both, both, ACT.Silu).then_inc(w["conv_ready"], 1)

    def dve_ssm_units(dve, e, c):
        w, par = ssm_sems, c % 2
        for j, tiles in ((1, (2 * c, 2 * c + 1)), (2, (16 + c, 24 + c))):
            p = plan.p["ssm"] + 3 * c + j
            pair = PAIR[p % 2]
            for m, ct in enumerate(tiles):
                acc = CONV[:, par, 2 * (j - 1) + m, :]
                dve.wait(w["conv_in"])
                for sh in range(1, 4):
                    step = 4 if j == 1 else 2
                    wc = COLS[:, at(times(e, step), col_at["conv_w"] + (3 - sh) * 32 + ct)]
                    ins = dve.e.scalar_tensor_tensor(acc[:, sh:], pair[:, m, :SEQ - sh], wc, acc[:, sh:], ALU.mult, ALU.add)
                    if m == 0 or sh < 3:
                        dve.link(ins)
            ins.then_inc(evac[p % 2], 1)

    def ssm_bank(c, j):
        return plan.b["ssm"] + 8 * c + j

    CB_HOME = {0: (2, 0), 1: (3, 0), 3: (3, 384), 2: (4, 0)}

    def pe_ssm_scores(pe, e, c):
        par = c % 2
        pe.wait(ssm_sems["conv_ready"], 2)
        for m in range(2):
            bank = take_bank(pe, ssm_bank(c, m), turns(e, 4))
            for tt in range(NT):
                ins = nc.tensor.transpose(bank[:, tt * P:tt * P + P], CONV[:, par, m, tt * P:tt * P + P], IDENT[:])
            ins.then_inc(bank_ready, 1)
        for j in (2, 3, 4):
            bank = take_bank(pe, ssm_bank(c, j), turns(e, 4))
            for i in [x for x in CB_HOME if CB_HOME[x][0] == j]:
                a, wide = CB_HOME[i][1], SEQ - i * P
                ins = nc.tensor.matmul(bank[:, a:a + wide], CONV[:, par, 2, i * P:i * P + P], CONV[:, par, 3, i * P:SEQ],
                                       start=True, stop=True)
            ins.then_inc(bank_ready, 1)

    def pe_ssm_heads(pe, e, c):
        w = ssm_sems
        for hd in range(4):
            m, a = hd // 2, (hd % 2) * HD
            if hd % 2 == 0:
                bank = take_bank(pe, ssm_bank(c, 5 + m), turns(e, 4))
            pe.wait(w["masked"])
            for i in range(NT):
                ins = nc.tensor.matmul(bank[a:a + HD, i * P:SEQ], XDT[:, i, hd * HD:hd * HD + HD],
                                       DECAY[:, hd % 2, TRI_AT[i]:TRI_AT[i] + SEQ - i * P], start=i == 0, stop=i == NT - 1)
            if hd == 0:
                ins.then_inc(w["first_head"], 1)
            elif hd % 2:
                ins.then_inc(bank_ready, 1)
        pe.wait(sq_ready)
        bank = take_bank(pe, ssm_bank(c, 7), turns(e, 4))
        for m in range(2):
            ins = nc.tensor.matmul(bank[:], ONES[:], SQ[:, m, :], start=m == 0, stop=m == 1)
        ins.then_inc(bank_ready, 1)

    def act_ssm_decay(act, e, c, heads, more):
        w = ssm_sems
        for hd in heads:
            act.wait(w["decay_in"])
            act.e.activation(DECAY[:, hd % 2, :], DECAY[:, hd % 2, :], ACT.Exp).then_inc(w["decay_out"], 1)
            if more or hd < 2:
                act_decay_row(act, 0 if e is None else e * 8, 4 * c + hd + 2)

    def act_ssm_norm(act, e, c):
        w = ssm_sems
        act.wait(w["gated"])
        settle(act)
        act.e.activation(SQ[:], G[:, at(times(e, 4), 2 * c, 2), :], ACT.Square).then_inc(sq_ready, 1)
        act_root(act, RSTD[:], var_ready)

    def dve_ssm_scores(dve, e, c):
        for m in range(2):
            b = ssm_bank(c, m)
            bank = full_bank(dve, b, turns(e, 4))
            dt = DT[:, :, at(times(e, 8), 4 * c + 2 * m, 2)]
            dve.e.tensor_tensor(XDT[:, :, m * P:m * P + P].rearrange("p t (h q) -> p t h q", q=HD),
                                bank[:].rearrange("p (t h q) -> p t h q", t=NT, q=HD), bcast(dt, 3, HD), ALU.mult)\
                 .then_inc(bank_free[b % 4], 1)
        for j in (2, 3, 4):
            b = ssm_bank(c, j)
            bank = full_bank(dve, b, turns(e, 4))
            for i in [x for x in CB_HOME if CB_HOME[x][0] == j]:
                a, wide = CB_HOME[i][1], SEQ - i * P
                ins = dve.e.tensor_tensor(CBM[:, TRI_AT[i]:TRI_AT[i] + wide], bank[:, a:a + wide], LATER[:, 0:wide], ALU.mult)
            ins.then_inc(bank_free[b % 4], 1)

    def dve_ssm_decay(dve, e, c, heads):
        w = ssm_sems
        for hd in heads:
            if hd == 2:
                dve.wait(w["first_head"])
            if hd == 3:
                full_bank(dve, ssm_bank(c, 5), turns(e, 4))
            dve.wait(row_landed[hd % 2], 16)
            for i in range(NT):
                cum = ACS_COL[:, i, at(times(e, 8), 4 * c + hd)]
                ins = dve.e.tensor_scalar(DECAY[:, hd % 2, TRI_AT[i]:TRI_AT[i] + SEQ - i * P], ACS_ROW[:, hd % 2, i * P:SEQ],
                                          cum, 0.0, ALU.subtract, ALU.min)
            ins.then_inc(w["decay_in"], 1)
        for hd in heads:
            dve.wait(w["decay_out"])
            dve.e.tensor_tensor(DECAY[:, hd % 2, :], DECAY[:, hd % 2, :], CBM[:], ALU.mult).then_inc(w["masked"], 1)

    def dve_ssm_output(dve, e, c):
        w, par = ssm_sems, c % 2
        for m in range(2):
            b = ssm_bank(c, 5 + m)
            bank = full_bank(dve, b, turns(e, 4))
            dve.e.scalar_tensor_tensor(TMP[:, m, :], CONV[:, par, m, :], D_COL[:, at(times(e, 4), 2 * c + m)], bank[:],
                                       ALU.mult, ALU.add).then_inc(bank_free[b % 4], 1)
        dve.e.wait_ge(bank_free[b % 4], turns(e, 4) + (b // 4 + 1))
        dve.e.tensor_tensor(G[:, at(times(e, 4), 2 * c, 2), :], TMP[:], ZS[:, par], ALU.mult).then_inc(w["gated"], 1)
        b = ssm_bank(c, 7)
        bank = full_bank(dve, b, turns(e, 4))
        dve.e.tensor_scalar(RSTD[:], bank[:], 1.0 / 256, EPS, ALU.mult, ALU.add).then_inc(var_ready, 1)
        dve.wait(root_ready)
        dve.e.reciprocal(RSTD[:], RSTD[:]).then_inc(bank_free[b % 4], 1)
        dve.e.wait_ge(bank_free[b % 4], turns(e, 4) + (b // 4 + 1))
        for m in range(2):
            gm = G[:, at(times(e, 4), 2 * c + m), :]
            ins = dve.e.scalar_tensor_tensor(gm, gm, COLS[:, at(times(e, 4), col_at["ssm_norm"] + 2 * c + m)],
                                             bcast(RSTD[:], 1, 1), ALU.mult, ALU.mult)
        dve.link(ins)

    def ssm_program(eng, units, first, second, per):
        units(None, 0)
        with eng.loop(SSM_G // 2 - 1, per) as i:
            for c in range(2):
                first(i, c)
                units(i, c + 1)
                second(i, c, True)
        first(None, SSM_G - 2)
        units(None, SSM_G - 1)
        second(None, SSM_G - 2, True)
        first(None, SSM_G - 1)
        second(None, SSM_G - 1, False)

    def pe_ssm(pe):
        w = ssm_sems
        ssm_program(pe, lambda e, c: pe_ssm_units(pe, e, c), lambda e, c: pe_ssm_scores(pe, e, c),
                    lambda e, c, more: pe_ssm_heads(pe, e, c), {w["conv_ready"]: 4, w["masked"]: 8, sq_ready: 2})

    def act_ssm(act):
        w = ssm_sems

        def second(e, c, more):
            act_ssm_decay(act, e, c, (2, 3), more)
            act_ssm_norm(act, e, c)

        ssm_program(act, lambda e, c: act_ssm_units(act, e, c), lambda e, c: act_ssm_decay(act, e, c, (0, 1), True), second,
                    {w["decay_in"]: 8, w["gated"]: 2, var_ready: 2})

    def dve_ssm(dve):
        w = ssm_sems

        def first(e, c):
            dve_ssm_scores(dve, e, c)
            dve_ssm_decay(dve, e, c, (0, 1))

        def second(e, c, more):
            dve_ssm_decay(dve, e, c, (2, 3))
            dve_ssm_output(dve, e, c)

        ssm_program(dve, lambda e, c: dve_ssm_units(dve, e, c), first, second,
                    {w["conv_in"]: 8, w["first_head"]: 2, w["decay_out"]: 8, row_landed[0]: 64, row_landed[1]: 64,
                     root_ready: 2, dve.chain: 22})

    def act_ssm_out(act):
        for half in range(2):
            act.e.wait_ge(unit_done, plan.u["ssmout"] + 4 * half)
            if half == 0:
                act.wait(g_ready)
            for k in range(KD):
                act.e.activation(HH[:, k, :], G[:, half * KD + k, :], ACT.Copy).then_inc(hi_ready, 1)

    g_ready = sem("g_ready")

    def dve_ssm_out(dve):
        dve.e.tensor_copy(RSTD[:, 0:1], ONES[:, 0:1]).then_inc(g_ready, 1)
        for half in range(2):
            for k in range(KD):
                dve.wait(hi_ready)
                dve.e.tensor_tensor(HL[:, k, :], G[:, half * KD + k, :], HH[:, k, :].bitcast(F32), ALU.subtract)\
                     .then_inc(h_ready, 1)
            dve.passed(h_ready, KD)
            for i in range(4):
                p = plan.p["ssmout"] + 4 * half + i
                pair = full_pair(dve, plan.u["ssmout"] + 4 * half + i, p)
                for m in range(2):
                    c = 2 * i + m
                    ins = dve.e.scalar_tensor_tensor(X[:, c, :], pair[:, m, :], mod(1, 2, c), X[:, c, :], ALU.mult, ALU.add)
                ins.then_inc(evac[p % 2], 1)

    def pe_ssm_out(pe):
        for half in range(2):
            pe.wait(h_ready, KD)
            for i in range(4):
                pair = take_pair(pe, plan.p["ssmout"] + 4 * half + i)
                unit_channels(pe, plan.u["ssmout"] + 4 * half + i, pair, hh, hl, KD)

    gate_sems = {s: sem(f"gate_{s}") for s in ("exp_in", "exp_out", "log_ready", "cum_ready")}
    gmlp_landed, half_ready, qk_ready, spatial_ready = (sem(s) for s in ("gmlp_landed", "half_ready", "qk_ready", "spatial_ready"))

    def pe_evin(pe):
        pe.wait(h_ready, KD)
        for i in range(10):
            u, pair = plan.u["evin"] + i, take_pair(pe, plan.p["evin"] + i)
            if i in (2, 3, 8, 9):
                unit_tokens(pe, u, pair)
            else:
                unit_channels(pe, u, pair, hh, hl, KD)
        b = plan.b["gate"]
        pe_small_logits(pe, take_bank(pe, b), FG_W, HEADS)
        pe.wait(gate_sems["log_ready"])
        bank = take_bank(pe, b + 1)
        for tt in range(NT):
            ins = nc.tensor.transpose(bank[0:HEADS, tt * P:tt * P + P], FGL[:, 5, tt, :], IDENT[:])
        ins.then_inc(bank_ready, 1)

    def act_evin(act):
        act.e.dma_start(SPAT[:], t["ev_w_spatial_2"][0].rearrange("g t s -> t g s")).then_inc(gmlp_landed, 16)
        act.e.dma_start(SPAT_B[:], t["ev_b_spatial_2"][0].partition_broadcast(P)).then_inc(gmlp_landed, 16)
        act.e.dma_start(V_GAIN[:], t["ev_v_norm_2"][0].partition_broadcast(P)).then_inc(gmlp_landed, 16)
        act_copy_pairs(act, "evin", 0, 2, UA, False, ACT.Gelu_apprx_tanh)
        act_copy_pairs(act, "evin", 2, 2, VA, True, ACT.Gelu_apprx_tanh)
        act_copy_pairs(act, "evin", 4, 2, Q1, False)
        act_copy_pairs(act, "evin", 6, 2, K1, False)
        act_copy_pairs(act, "evin", 8, 2, V1, True)
        act_softplus(act, FGL[:, 0], gate_sems["exp_in"], gate_sems["exp_out"])

    def dve_evin(dve):
        w, b = gate_sems, plan.b["gate"]
        dve.e.tensor_scalar(MINUS_HEAD[:], bcast(IDENT[0:HEADS, 0:HEADS], 2, P), -HD ** 0.5, None, ALU.mult)
        bank = full_bank(dve, b)
        dve.e.tensor_tensor(FGL[:, 5], bank[:, 0:NT * HEADS].rearrange("p (t h) -> p t h", h=HEADS),
                            bcast(FG_B[:], 1, NT), ALU.add).then_inc(bank_free[b % 4], 1)
        dve.e.wait_ge(bank_free[b % 4], b // 4 + 1)
        dve_softplus(dve, FGL[:, 5], FGL[:, 4], [FGL[:, i] for i in range(4)], w["exp_in"], w["exp_out"], -1)
        dve.e.tensor_copy(FGL[:, 5], FGL[:, 4]).then_inc(w["log_ready"], 1)
        b += 1
        dve.e.tensor_copy(FCUM[:, 0, :], full_bank(dve, b)[0:HEADS, :]).then_inc(bank_free[b % 4], 1)
        dve.e.wait_ge(bank_free[b % 4], b // 4 + 1)
        dve.e.tensor_tensor_scan(FCUM[:, 1, :], ONES[0:HEADS, 0:1].broadcast_to([HEADS, SEQ]), FCUM[:, 0, :], 0.0,
                                 ALU.mult, ALU.add).then_inc(w["cum_ready"], 1)

    def pe_gmlp(pe):
        b = plan.b["gmlp"]
        pe.e.wait_ge(gmlp_landed, 48)
        bank = take_bank(pe, b)
        for g in range(4):
            ins = nc.tensor.transpose(bank[:, g * P:g * P + P], SPAT[:, g, :], IDENT[:])
        ins.then_inc(bank_ready, 1)
        pe.wait(spatial_ready)
        for g in range(4):
            bank = take_bank(pe, b + 1 + g)
            for n in range(NT):
                ins = nc.tensor.matmul(bank[:, n * P:n * P + P], VA[:, n, g * P:g * P + P], SPAT_T[:, g, :], start=True, stop=True)
            ins.then_inc(bank_ready, 1)

    def act_gmlp(act):
        act_root(act, VR[:], var_ready)
        for g in range(4):
            act.wait(pre_ready)
            act.e.activation(HH[:, g, :], TMP[:, g % 2, :], ACT.Copy).then_inc(hi_ready, 1)

    def dve_gmlp(dve):
        b = plan.b["gmlp"]
        for s in range(2):
            dve.e.wait_ge(evac[s], plan.p["gate"] // 2)
        dve.e.wait_ge(gmlp_landed, 48)
        bank = full_bank(dve, b)
        dve.e.tensor_tensor(SPAT_T[:], bank[:].rearrange("p (g t) -> p g t", t=P), bcast(LATER[:, 0:P], 1, 4), ALU.mult)\
             .then_inc(bank_free[b % 4], 1)
        groups = VA[:].rearrange("p n (g c) -> p (n g) c", c=P)
        dve.link(dve.e.tensor_tensor(VSQ[:], VA[:], VA[:], ALU.mult))
        dve.link(dve.e.tensor_reduce(VR[:], VSQ[:].rearrange("p n (g c) -> p (n g) c", c=P), AX.X, ALU.add))
        dve_rstd(dve, VR[:], VR[:], P)
        dve.link(dve.e.tensor_tensor(groups, groups, bcast(VR[:], 2, P), ALU.mult))
        dve.e.tensor_tensor(VA[:], VA[:], bcast(V_GAIN[:], 1, NT), ALU.mult).then_inc(spatial_ready, 1)
        for g in range(4):
            bank = full_bank(dve, b + 1 + g)
            tmp = TMP[:, g % 2, :]
            if g >= 2:
                dve.wait(half_ready)
            dve.e.tensor_tensor(tmp.rearrange("p (n t) -> p n t", t=P), bank[:].rearrange("p (n t) -> p n t", t=P),
                                bcast(SPAT_B[:, g, :], 1, NT), ALU.add).then_inc(bank_free[(b + 1 + g) % 4], 1)
            dve.e.wait_ge(bank_free[(b + 1 + g) % 4], (b + 1 + g) // 4 + 1)
            dve.e.tensor_tensor(tmp, tmp, UA[:, g, :], ALU.mult).then_inc(pre_ready, 1)
            dve.wait(pre_ready)
            dve.wait(hi_ready)
            dve.e.tensor_tensor(HL[:, g, :], tmp, HH[:, g, :].bitcast(F32), ALU.subtract).then_inc(half_ready, 1)

    def pe_qknorm(pe):
        b = plan.b["qknorm"]
        for n in range(8):
            pe.wait(sq_ready)
            bank = take_bank(pe, b + n)
            nc.tensor.matmul(bank[:], HEAD_ONES[:], SQ[:, n % 2, :], start=True, stop=True).then_inc(bank_ready, 1)
        pe.wait(qk_ready, 2)
        pe.wait(gate_sems["cum_ready"])

    def act_qknorm(act):
        b = plan.b["qknorm"]
        for s in range(2):
            act.e.wait_ge(evac[s], plan.p["gate"] // 2)
        for i, arr in enumerate((Q1, K1)):
            for m in range(4):
                n = 4 * i + m
                if n >= 2:
                    act.e.wait_ge(bank_ready, b + n - 1)
                act.e.activation(SQ[:, n % 2, :], arr[:, m, :], ACT.Square).then_inc(sq_ready, 1)
            last = b + 4 * i + 3
            act.e.wait_ge(bank_free[last % 4], last // 4 + 1)
            act.e.activation(VSQ[:], VSQ[:], ACT.Sqrt).then_inc(root_ready, 1)

    def dve_qknorm(dve):
        b = plan.b["qknorm"]
        for i, arr in enumerate((Q1, K1)):
            if i:
                dve.wait(qk_ready)
            for m in range(4):
                n = b + 4 * i + m
                dve.e.tensor_scalar(VSQ[:, m, :], full_bank(dve, n)[:], 1.0 / HD, EPS, ALU.mult, ALU.add)\
                     .then_inc(bank_free[n % 4], 1)
            dve.wait(root_ready)
            dve.link(dve.e.reciprocal(VSQ[:], VSQ[:]))
            for m in range(4):
                ins = dve.e.scalar_tensor_tensor(arr[:, m, :], arr[:, m, :], QK_GAIN[:, i:i + 1], VSQ[:, m, :], ALU.mult, ALU.mult)
            ins.then_inc(qk_ready, 1)

    ffn_sems = {s: sem(f"ffn_{s}") for s in ("conv_in", "gate", "hidden", "hidden_hi", "hidden_ready")}
    FFN_PARTS = ((0, 8), (8, 8), (16, 6))

    def pe_ffn(pe, layer):
        w, u0, p0 = ffn_sems, plan.u[f"ffn{layer}"], plan.p[f"ffn{layer}"]
        pe.wait(h_ready, KD)
        with pe.e.Fori(0, FB // 2) as i:
            for b in range(2):
                unit_channels(pe, u0 + b, take_pair(pe, p0 + b, i), hh, hl, KD, off=i * 2)
        with pe.e.Fori(0, 2) as i:
            for c in range(2):
                pair = take_pair(pe, p0 + FB + c, i)
                if c == 0:
                    pe.e.wait_ge(w["hidden_ready"], FB * (layer + 1))
                for j, (k0, n) in enumerate(FFN_PARTS):
                    unit_channels(pe, u0 + FB + 3 * c + j, pair, lambda k: FHH[:, k0 + k, :], lambda k: FHL[:, k0 + k, :], n,
                                  first=j == 0, last=j == 2, off=i * 6)

    def act_ffn(act, layer):
        w, u0, p0 = ffn_sems, plan.u[f"ffn{layer}"], plan.p[f"ffn{layer}"]
        with act.loop(FB // 2, {w["hidden"]: 2}) as i:
            for b in range(2):
                pair = full_pair(act, u0 + b, p0 + b, i * 2)
                settle(act)
                for m in range(2):
                    wc = COLS[:, bass.ds(i * 2 + (col_at["fconv_w"] + layer * 6 * FB + 4 * FB + m * FB + b), 1)]
                    bc = COLS[:, bass.ds(i * 2 + (col_at["fconv_b"] + layer * 2 * FB + m * FB + b), 1)]
                    act.e.activation((SQ, FUP)[m][:, b, :], pair[:, m, :], ACT.Identity, bias=bc, scale=wc).then_inc(w["conv_in"], 1)
                act.e.wait_ge(evac[b], i + ((p0 + b) // 2 + 1))
                act.e.activation(SQ[:, b, :], SQ[:, b, :], ACT.Silu).then_inc(w["gate"], 1)
                act.wait(w["hidden"])
                settle(act)
                act.e.activation(FHH[:, bass.ds(i * 2 + b, 1), :], TMP[:, b:b + 1, :], ACT.Copy).then_inc(w["hidden_hi"], 1)

    def dve_ffn(dve, layer):
        w, u0, p0 = ffn_sems, plan.u[f"ffn{layer}"], plan.p[f"ffn{layer}"]
        with dve.loop(FB // 2, {w["conv_in"]: 4, w["gate"]: 2, w["hidden"]: 2, w["hidden_hi"]: 2, dve.chain: 2}) as i:
            for b in range(2):
                pair = PAIR[b]
                dve.wait(w["conv_in"], 2)
                for sh in (1, 2):
                    for m in range(2):
                        wc = COLS[:, bass.ds(i * 2 + (col_at["fconv_w"] + layer * 6 * FB + (2 - sh) * 2 * FB + m * FB + b), 1)]
                        acc = (SQ, FUP)[m][:, b, sh:]
                        ins = dve.e.scalar_tensor_tensor(acc, pair[:, m, :SEQ - sh], wc, acc, ALU.mult, ALU.add)
                    if sh == 1:
                        dve.link(ins)
                ins.then_inc(evac[b], 1)
                dve.wait(w["gate"])
                dve.e.tensor_tensor(TMP[:, b, :], SQ[:, b, :], FUP[:, b, :], ALU.mult).then_inc(w["hidden"], 1)
                dve.wait(w["hidden"])
                dve.wait(w["hidden_hi"])
                f = bass.ds(i * 2 + b, 1)
                dve.e.tensor_tensor(FHL[:, f, :], TMP[:, b:b + 1, :], FHH[:, f, :].bitcast(F32), ALU.subtract)\
                     .then_inc(w["hidden_ready"], 1)
        with dve.e.Fori(0, 2) as i:
            for c in range(2):
                pair = full_pair(dve, u0 + FB + 3 * c + 2, p0 + FB + c, i * 6)
                x = X[:, bass.ds(i * 4 + 2 * c, 2), :]
                dve.e.tensor_tensor(x, pair[:], x, ALU.add).then_inc(evac[c], 1)

    ple_landed, ple_hi, ple_gate = sem("ple_landed"), sem("ple_hi"), sem("ple_gate")

    def act_ple_load(act, layer):
        for s in range(2):
            act.e.wait_ge(evac[s], plan.p[f"ple{layer}"] // 2)
        act.e.dma_start(PTOK[:], t["p_2"][layer, 0].rearrange("(t p) d -> p t d", p=P)).then_inc(ple_landed, 16)

    def pe_ple(pe, layer):
        b, u0, p0 = plan.b[f"ple{layer}"], plan.u[f"ple{layer}"], plan.p[f"ple{layer}"]
        pe.wait(ple_landed, 16)
        for k in range(2):
            bank = take_bank(pe, b + k)
            for tt in range(NT):
                ins = nc.tensor.transpose(bank[:, tt * P:tt * P + P], PTOK[:, tt, k * P:k * P + P], IDENT[:])
            ins.then_inc(bank_ready, 1)
        for k in range(2):
            pe.e.wait_ge(bank_free[(b + k) % 4], (b + k) // 4 + 1)
        for half in range(2):
            u, p = u0 + 3 * half, p0 + 4 * half
            pe.e.wait_ge(split_ready, u + 1)
            for q in range(2):
                pair = take_pair(pe, p + q)
                for m in range(2):
                    for k in range(2):
                        c = (k * 4 + 2 * q + m) * P
                        ins = mm3(pair[:, m, :], WH[:, u % 2, c:c + P], WL[:, u % 2, c:c + P], PH[:, k, :], PL[:, k, :], k == 0, k == 1)
            ins.then_inc(unit_done, 1)
            if half == 0:
                pe.wait(h_ready, KD)
            for i in range(2):
                unit_channels(pe, u + 1 + i, take_pair(pe, p + 2 + i), hh, hl, KD)

    def act_ple(act, layer):
        b, u0, p0 = plan.b[f"ple{layer}"], plan.u[f"ple{layer}"], plan.p[f"ple{layer}"]
        for k in range(2):
            act.e.activation(PH[:, k, :], full_bank(act, b + k)[:], ACT.Copy).then_inc(ple_hi, 1)
        for half in range(2):
            u, p = u0 + 3 * half, p0 + 4 * half
            for i in range(4):
                pair = full_pair(act, u + max(i - 1, 0), p + i)
                if half and i == 0 or i == 3:
                    act.e.wait_ge(evac[(p + i - 1) % 2], (p + i - 1) // 2 + 1)
                if i < 2:
                    act.e.activation(PROJ[:, 2 * i:2 * i + 2, :], pair[:], ACT.Copy).then_inc(evac[(p + i) % 2], 1)
                else:
                    act.e.activation(SQ[:], pair[:], ACT.Sigmoid).then_inc(ple_gate, 1)

    def dve_ple(dve, layer):
        b, p0 = plan.b[f"ple{layer}"], plan.p[f"ple{layer}"]
        for k in range(2):
            dve.wait(ple_hi)
            dve.e.tensor_tensor(PL[:, k, :], full_bank(dve, b + k)[:], PH[:, k, :].bitcast(F32), ALU.subtract)\
                 .then_inc(bank_free[(b + k) % 4], 1)

    def dve_ple_gates(dve, layer):
        p0 = plan.p[f"ple{layer}"]
        for half in range(2):
            for i in range(2):
                p, c = p0 + 4 * half + 2 + i, 4 * half + 2 * i
                dve.wait(ple_gate)
                dve.link(dve.e.tensor_tensor(TMP[:], SQ[:], PROJ[:, 2 * i:2 * i + 2, :], ALU.mult))
                dve.e.tensor_tensor(X[:, c:c + 2, :], TMP[:], X[:, c:c + 2, :], ALU.add).then_inc(evac[p % 2], 1)

    glu_gate = sem("glu_gate")

    def pe_glu(pe):
        pe.wait(h_ready, KD)
        pe_matrix(pe, "glu", KD)

    def act_glu(act):
        for i in range(KD):
            pair = full_pair(act, plan.u["glu"] + i, plan.p["glu"] + i)
            act.e.activation(SQ[:, i % 2, :], pair[:, 1, :], ACT.Sigmoid).then_inc(glu_gate, 1)

    def dve_glu(dve):
        for i in range(KD):
            p = plan.p["glu"] + i
            dve.wait(glu_gate)
            dve.link(dve.e.tensor_tensor(TMP[:, i % 2, :], PAIR[p % 2][:, 0, :], SQ[:, i % 2, :], ALU.mult))
            dve.e.tensor_tensor(X[:, i, :], TMP[:, i % 2, :], X[:, i, :], ALU.add).then_inc(evac[p % 2], 1)

    s5_sems = {s: sem(f"s5_{s}") for s in ("a_landed", "landed", "vec_in", "vec_out", "consts", "bb", "angles", "tab", "w1x",
                                           "ca", "turning", "bu", "state", "gelu")}
    CR, CI, STEP_HI, STEP_LO, MAG4 = range(5)
    BELOW_TWO_PI = 6.283185
    GRID = 16384.0

    def act_s5_rows(act):
        for i, name in enumerate(("od_a_re_2", "od_a_im_2")):
            act.e.dma_start(AROW[:, i, :], t[name][0].rearrange("(t h) p -> t (h p)", h=2)).then_inc(s5_sems["a_landed"], 16)
        act.e.dma_start(LDT_ROW[:], t["od_log_dt_2"][0].partition_broadcast(P)).then_inc(s5_sems["a_landed"], 16)

    def pe_s5_vectors(pe):
        b = plan.b["s5a"]
        pe.e.wait_ge(s5_sems["a_landed"], 48)
        bank = take_bank(pe, b)
        for i in range(2):
            ins = nc.tensor.transpose(bank[:, i * S5_TILES:i * S5_TILES + S5_TILES], AROW[:, i, :], IDENT[0:S5_TILES, 0:S5_TILES])
        ins.then_inc(bank_ready, 1)

    S5_NAMES = ("lr", "li", "ldt", "dt", "e", "th", "n", "turn", "red", "cos", "sin", "half", "big", "ec", "poly", "small",
                "em1", "mag", "nr", "den", "p", "q", "turn4")
    vec = {name: S1[:, 0, i * S5_TILES:(i + 1) * S5_TILES] for i, name in enumerate(S5_NAMES)}

    def act_s5_vectors(act):
        w = s5_sems
        act.wait(w["vec_in"])
        act.e.activation(vec["dt"], vec["ldt"], ACT.Exp).then_inc(w["vec_out"], 1)
        act.wait(w["vec_in"])
        act.e.activation(vec["big"], vec["e"], ACT.Exp)
        act.e.activation(vec["sin"], vec["red"], ACT.Sin)
        act.e.activation(vec["half"], vec["red"], ACT.Sin, scale=0.5)
        act.e.activation(vec["cos"], vec["q"], ACT.Sin, scale=BELOW_TWO_PI).then_inc(w["vec_out"], 1)

    def dve_s5_vectors(dve):
        w, v = s5_sems, vec

        def tt(o, a, b, op):
            dve.link(dve.e.tensor_tensor(o, a, b, op))

        def ts(o, a, s1, s2, *ops):
            dve.link(dve.e.tensor_scalar(o, a, s1, s2, *ops))

        def stt(o, a, s, b, op1, op2):
            dve.link(dve.e.scalar_tensor_tensor(o, a, s, b, op1, op2))

        def nearest(o, a):
            ts(o, a, ROUND, ROUND, ALU.add, ALU.subtract)

        b = plan.b["s5a"]
        bank = full_bank(dve, b)
        dve.e.tensor_copy(v["lr"], bank[:, 0:S5_TILES])
        dve.e.tensor_copy(v["li"], bank[:, S5_TILES:2 * S5_TILES]).then_inc(bank_free[b % 4], 1)
        dve.e.wait_ge(s5_sems["a_landed"], 48)
        for h in range(2):
            ins = dve.e.tensor_copy(v["ldt"][h * HD:h * HD + HD, :], LDT_ROW[h * HD:h * HD + HD, :].rearrange("p (t h) -> p h t", h=2)[:, h, :])
        ins.then_inc(w["vec_in"], 1)
        dve.wait(w["vec_out"])
        tt(v["e"], v["lr"], v["dt"], ALU.mult)
        tt(v["th"], v["li"], v["dt"], ALU.mult)
        ts(v["n"], v["th"], 1 / TWO_PI, None, ALU.mult)
        nearest(v["n"], v["n"])
        stt(v["red"], v["n"], -TWO_PI_PARTS[0], v["th"], ALU.mult, ALU.add)
        stt(v["red"], v["n"], -TWO_PI_PARTS[1], v["red"], ALU.mult, ALU.add)
        stt(v["red"], v["n"], -TWO_PI_PARTS[2], v["red"], ALU.mult, ALU.add)
        ts(v["turn"], v["red"], 1 / TWO_PI, 0.5, ALU.mult, ALU.min)
        ts(v["turn"], v["turn"], -0.5, None, ALU.max)
        ts(v["red"], v["red"], BELOW_TWO_PI / 2, -BELOW_TWO_PI / 2, ALU.min, ALU.max)
        ts(v["q"], v["turn"], 0.25, None, ALU.add)
        nearest(v["p"], v["q"])
        dve.e.tensor_tensor(v["q"], v["q"], v["p"], ALU.subtract).then_inc(w["vec_in"], 1)
        ts(v["ec"], v["e"], 0.5, -0.5, ALU.min, ALU.max)
        ts(v["poly"], v["ec"], EXP_SERIES[0], None, ALU.mult)
        for c in EXP_SERIES[1:]:
            stt(v["poly"], v["poly"], c, v["ec"], ALU.add, ALU.mult)
        tt(v["p"], v["e"], v["e"], ALU.mult)
        ts(v["small"], v["p"], 0.25, None, ALU.is_lt)
        dve.wait(w["vec_out"])
        ts(v["big"], v["big"], 1.0, None, ALU.subtract)
        tt(v["poly"], v["poly"], v["big"], ALU.subtract)
        tt(v["poly"], v["poly"], v["small"], ALU.mult)
        tt(v["em1"], v["poly"], v["big"], ALU.add)
        ts(v["mag"], v["em1"], 1.0, None, ALU.add)
        tt(v["half"], v["half"], v["half"], ALU.mult)
        tt(v["nr"], v["em1"], v["cos"], ALU.mult)
        stt(v["nr"], v["half"], -2.0, v["nr"], ALU.mult, ALU.add)
        power = lambda part, n: A_POW[:, part, n, :]
        tt(power(0, 1), v["mag"], v["cos"], ALU.mult)
        tt(power(1, 1), v["mag"], v["sin"], ALU.mult)
        tt(v["den"], v["lr"], v["lr"], ALU.mult)
        tt(v["p"], v["li"], v["li"], ALU.mult)
        tt(v["den"], v["den"], v["p"], ALU.add)
        dve.link(dve.e.reciprocal(v["den"], v["den"]))
        for o, a, b, op in ((CR, ("nr", "lr"), "li", ALU.add), (CI, ("nr", "li"), "lr", ALU.subtract)):
            tt(v["p"], v[a[0]], v[a[1]], ALU.mult)
            tt(v["q"], power(1, 1), v[b], ALU.mult)
            tt(v["q"], v["q"], v["p"], op)
            tt(S5K[:, o, :], v["q"], v["den"], ALU.mult)
        dve.e.memset(power(0, 0), 1.0)
        dve.link(dve.e.memset(power(1, 0), 0.0))
        for n in range(2, S5_L + 1):
            tt(v["p"], power(0, n - 1), power(0, 1), ALU.mult)
            tt(v["q"], power(1, n - 1), power(1, 1), ALU.mult)
            tt(power(0, n), v["p"], v["q"], ALU.subtract)
            tt(v["p"], power(0, n - 1), power(1, 1), ALU.mult)
            tt(v["q"], power(1, n - 1), power(0, 1), ALU.mult)
            tt(power(1, n), v["p"], v["q"], ALU.add)
        for n in range(S5_L):
            ins = dve.e.tensor_copy(A_REV[:, :, n, :], A_POW[:, :, S5_L - 1 - n, :])
        tt(v["p"], v["mag"], v["mag"], ALU.mult)
        tt(S5K[:, MAG4, :], v["p"], v["p"], ALU.mult)
        ts(v["turn4"], v["turn"], float(S5_L), None, ALU.mult)
        nearest(v["p"], v["turn4"])
        tt(v["turn4"], v["turn4"], v["p"], ALU.subtract)
        ts(v["p"], v["turn4"], GRID, None, ALU.mult)
        nearest(v["p"], v["p"])
        ts(S5K[:, STEP_HI, :], v["p"], 1 / GRID, None, ALU.mult)
        tt(S5K[:, STEP_LO, :], v["turn4"], S5K[:, STEP_HI, :], ALU.subtract)

    def act_s5_load(act):
        w = s5_sems
        for i, (bn, cn) in enumerate((("od_b_re_2", "od_c_re_2"), ("od_b_im_2", "od_c_im_2"))):
            act.e.dma_start(BRAW[:, i], t[bn][0].rearrange("(t h) p c -> (h p) t c", h=2)).then_inc(w["landed"], 16)
            for twice in range(2):
                act.e.dma_start(CRAW[:, i, :, twice, :], t[cn][0].rearrange("(k g) c p -> (g c) k p", g=8)).then_inc(w["landed"], 16)

    def at4(e, k, size=4):
        return slice(4 * k, 4 * k + 4) if e is None else bass.ds(e * 8 + 4 * k, 4)

    def step_at(e, k):
        return slice(k, k + 1) if e is None else bass.ds(e * 2 + k, 1)

    def s5_a(k, i):
        return plan.b["s5"] + (4 + 6 * (k - 1) + i if k else i)

    def s5_y(k):
        return plan.b["s5"] + (4 + 6 * k + 4 if k < KD - 1 else 6 * KD - 2)

    def s5_out(k):
        return s5_y(k) + 1

    def s5_loop(eng, first, step, last, per):
        first()
        step(None, 0)
        with eng.loop((KD - 2) // 2, per) as e:
            for k in (1, 2):
                step(e, k)
        step(None, KD - 1)
        last()

    def t2(e, n):
        return 0 if e is None else e * n

    def pool_s5_consts(pool):
        w = s5_sems
        pool.e.wait_ge(s5_sems["landed"], 96)
        for s in range(2):
            pool.e.wait_ge(evac[s], plan.p["s5"] // 2)
        for n in range(S5_LOW):
            pool.e.memset(S5_AT[:, n:n + 1], float(n))
        for n in range(S5_HIGH):
            pool.e.memset(S5_AT[:, S5_LOW + n:S5_LOW + n + 1], float(n * S5_LOW))
        pool.link(pool.e.memset(FIRST[:], 1.0))
        pool.e.memset(FIRST[:, 0:1], 0.0)
        pool.e.memset(W3[:], 0.0)
        pool.e.memset(W1X[:], 0.0)
        pool.e.memset(CAX[:], 0.0).then_inc(w["consts"], 1)
        pool.wait(w["consts"])
        pool.wait(w["bb"])
        pool.wait(w["tab"])
        pool.e.wait_ge(bank_ready, plan.b["s5c"] + 4)

    def pool_tt(pool, o, a, b, op):
        pool.link(pool.e.tensor_tensor(o, a, b, op))

    def pool_s5_step(pool, k):
        w, par, tiles = s5_sems, k % 2, slice(4 * k, 4 * k + 4)
        if k >= 2:
            pool.e.wait_ge(bank_ready, s5_a(k - 2, 2) + 1)
        q = PRP[:].rearrange("p a t n -> p (a t n)").rearrange("p (q t j c) -> p q t j c", q=4, t=4, j=S5_L)
        shape = lambda a: bcast(a, 2, S5_L)
        br, bi = (shape(BB[:, i, tiles, :]) for i in range(2))
        ar, ai = (bcast(A_REV[:, i, :, tiles].rearrange("p j t -> p t j"), 3, S5_C) for i in range(2))
        for i, (a, b) in enumerate(((br, ar), (bi, ai), (br, ai), (bi, ar))):
            pool_tt(pool, q[:, i], a, b, ALU.mult)
        for part, op in ((0, ALU.subtract), (1, ALU.add)):
            for h in range(2):
                rows = slice(h * HD, h * HD + HD)
                ins = pool.e.tensor_tensor(W1X[rows, par, part, :, :, h, :], q[rows, 2 * part], q[rows, 2 * part + 1], op)
                if part + h < 2:
                    pool.link(ins)
        ins.then_inc(w["w1x"], 1)
        pool.wait(w["w1x"])
        if k >= 2:
            pool.e.wait_ge(w["state"], k - 1)
        low = lambda i: bcast(TAB[:, i, tiles, 0:S5_LOW], 2, S5_HIGH)
        high = lambda i: bcast(TAB[:, i, tiles, S5_LOW:], 3, S5_LOW)
        table = lambda i: TURNING[:, par, i].rearrange("p t (h l) -> p t h l", l=S5_LOW)
        tmp = [PRP[:, i].rearrange("p t (h l) -> p t h l", l=S5_LOW) for i in range(2)]
        for i, (a, b, c, d, op) in enumerate(((1, 1, 0, 0, ALU.subtract), (0, 1, 1, 0, ALU.add))):
            pool_tt(pool, tmp[0], high(a), low(b), ALU.mult)
            pool_tt(pool, tmp[1], high(c), low(d), ALU.mult)
            pool_tt(pool, table(i), tmp[0], tmp[1], op)
        pool.e.tensor_tensor(TURNING[:, par, 2], bcast(FIRST[:], 1, 4), bcast(S5K[:, MAG4, tiles], 2, S5_N), ALU.mult)\
            .then_inc(w["turning"], 1)
        pool.wait(w["turning"])

    def pool_s5(pool):
        pool_s5_consts(pool)
        for k in range(KD):
            pool_s5_step(pool, k)

    def pe_s5_prepare(pe, e, k):
        w, par = s5_sems, k % 2
        pe.wait(w["w1x"])
        for part in range(2):
            bank = take_bank(pe, s5_a(k, part), t2(e, 3))
            for i in range(4):
                ins = nc.tensor.transpose(bank[:, i * P:i * P + P], W1X[:, par, part, i].rearrange("p j h c -> p (j h c)"), IDENT[:])
            ins.then_inc(bank_ready, 1)
        pe.wait(w["ca"])
        bank = take_bank(pe, s5_a(k, 2), t2(e, 3))
        for i in range(4):
            for part in range(2):
                ins = nc.tensor.matmul(bank[0:32, i * P:i * P + P], W1X[:, par, part, i, S5_L - 1].rearrange("p h c -> p (h c)"),
                                       CAX[:, par, part, i, 0:S5_L].rearrange("p j h c -> p (j h c)"), start=part == 0, stop=part == 1)
        ins.then_inc(bank_ready, 1)
        bank = take_bank(pe, s5_a(k, 3), t2(e, 3))
        for i in range(4):
            for j in range(S5_L):
                src = HF[:, step_at(e, k), :].rearrange("p k (n l) -> p (k n) l", l=S5_L)[:, :, j]
                ins = nc.tensor.matmul(bank[32 * j:32 * j + 32, i * P:i * P + P], IDENT[:, 32 * i:32 * i + 32], src, start=True, stop=True)
        ins.then_inc(bank_ready, 1)
        pair = take_pair(pe, plan.p["s5"] + k, t2(e, 1))
        b = s5_a(k, 3)
        pe.e.wait_ge(bank_free[b % 4], t2(e, 3) + (b // 4 + 1))
        for part in range(2):
            for i in range(4):
                ins = nc.tensor.matmul(pair[:, part, i * P:i * P + P], W1_T[:, par, part, i, :], U4[:, par, i, :], start=True, stop=True)
        ins.then_inc(w["bu"], 1)

    def pe_s5_output(pe, e, k):
        w, par = s5_sems, k % 2
        pe.wait(w["state"])
        bank = take_bank(pe, s5_y(k), t2(e, 3))
        for i in range(4):
            nc.tensor.matmul(bank[:, i * P:i * P + P], W3[:, par, i, :], U4[:, par, i, :], start=True, stop=False)
            for part in range(2):
                ins = nc.tensor.matmul(bank[:, i * P + 1:i * P + P], CAX[:, par, part, i, 1:].rearrange("p j h c -> p (j h c)"),
                                       XS[:, part, i, 0:S5_N - 1], start=False, stop=part == 1)
        ins.then_inc(bank_ready, 1)
        bank = take_bank(pe, s5_out(k), t2(e, 3))
        b = s5_y(k)
        pe.e.wait_ge(bank_free[b % 4], t2(e, 3) + (b // 4 + 1))
        for i in range(4):
            for j in range(S5_L):
                ins = nc.tensor.matmul(bank[32 * i:32 * i + 32, :].rearrange("p (n l) -> p n l", l=S5_L)[:, :, j],
                                       IDENT[:, 32 * j:32 * j + 32], Y4[:, i, :], start=True, stop=True)
        ins.then_inc(bank_ready, 1)

    def pe_s5(pe):
        w = s5_sems
        b = plan.b["s5c"]
        pe.e.wait_ge(w["landed"], 96)
        for m in range(4):
            bank = take_bank(pe, b + m)
            for n in range(4):
                part, k = m // 2, 4 * (m % 2) + n
                ins = nc.tensor.transpose(bank[:, n * P:n * P + P], CRAW[:, part, k].rearrange("p d q -> p (d q)"), IDENT[:])
            ins.then_inc(bank_ready, 1)
        pe.wait(h_ready)

        def step(e, k):
            if e is not None or k < KD - 1:
                pe_s5_prepare(pe, e, k + 1)
            pe_s5_output(pe, e, k)

        pe_s5_prepare(pe, None, 0)
        for k in range(KD):
            step(None, k)

    def act_s5_prepare(act, e, k):
        par = k % 2
        if k >= 2:
            act.e.wait_ge(bank_ready, t2(e, 12) + (s5_y(k - 2) + 1))
        for part in range(2):
            b = s5_a(k, part)
            bank = full_bank(act, b, t2(e, 3))
            act.e.activation(W1_T[:, par, part].rearrange("p t n -> p (t n)"), bank[:], ACT.Copy).then_inc(bank_free[b % 4], 1)
        b = s5_a(k, 2)
        kernel = full_bank(act, b, t2(e, 3))[0:32, :].rearrange("p (t n) -> p t n", n=P)
        for j in range(S5_L):
            ins = act.e.activation(W3[32 * j:32 * j + 32, par, :, 32 * j:], kernel[:, :, 0:P - 32 * j], ACT.Copy)
        ins.then_inc(bank_free[b % 4], 1)
        b = s5_a(k, 3)
        act.e.activation(U4[:, par].rearrange("p t n -> p (t n)"), full_bank(act, b, t2(e, 3))[:], ACT.Copy).then_inc(bank_free[b % 4], 1)

    def act_s5_output(act, e, k):
        b = s5_y(k)
        if e is not None or k:
            act.e.wait_ge(bank_ready, t2(e, 12) + (s5_out(k - 1) + 1))
        act.e.activation(Y4[:].rearrange("p t n -> p (t n)"), full_bank(act, b, t2(e, 3))[:], ACT.Copy).then_inc(bank_free[b % 4], 1)

    def act_s5_gelu(act, e, k):
        w, par, b = s5_sems, k % 2, s5_out(k)
        act.e.wait_ge(bank_free[b % 4], t2(e, 3) + (b // 4 + 1))
        act.e.activation(SQ[:, par, :], TMP[:, par, :], ACT.Gelu_apprx_tanh).then_inc(w["gelu"], 1)
        act.wait(w["gelu"])
        settle(act)
        act.e.activation(HH[:, step_at(e, k), :], SQ[:, par:par + 1, :], ACT.Copy).then_inc(hi_ready, 1)

    def act_s5(act):
        w, b = s5_sems, plan.b["s5c"]
        for m in range(4):
            bank = full_bank(act, b + m)[:].rearrange("p (t h c) -> p t h c", h=2, c=S5_C)
            for h in range(2):
                rows = slice(h * HD, h * HD + HD)
                ins = act.e.activation(CK[rows, m // 2, 16 * (m % 2):16 * (m % 2) + 16, :], bank[rows, :, h, :], ACT.Copy)
            ins.then_inc(bank_free[(b + m) % 4], 1)
        act.wait(w["angles"])
        act.e.activation(TAB[:], TAB[:], ACT.Sin, scale=BELOW_TWO_PI).then_inc(w["tab"], 1)
        act.wait(w["consts"])

        def step(e, k):
            if e is not None or k < KD - 1:
                act_s5_prepare(act, e, k + 1)
            act_s5_output(act, e, k)
            if e is not None or k:
                act_s5_gelu(act, e, k - 1)

        s5_loop(act, lambda: act_s5_prepare(act, None, 0), step, lambda: act_s5_gelu(act, None, KD - 1), {w["gelu"]: 2})

    def dve_s5_start(dve):
        w = s5_sems
        dve.e.wait_ge(w["landed"], 96)
        dve.wait(w["consts"])
        q = [PR[:, i].rearrange("p t n -> p (t n)").rearrange("p (t c) -> p t c", c=S5_C) for i in range(4)]
        cr, ci = (bcast(S5K[:, i, :], 2, S5_C) for i in (CR, CI))
        for i, (a, b) in enumerate(((0, cr), (1, ci), (1, cr), (0, ci))):
            ins = dve.e.tensor_tensor(q[i], BRAW[:, a], b, ALU.mult)
        dve.link(ins)
        dve.e.tensor_tensor(BB[:, 0], q[0], q[1], ALU.subtract)
        dve.e.tensor_tensor(BB[:, 1], q[2], q[3], ALU.add).then_inc(w["bb"], 1)
        x, n = ANGLE[:, 0], ANGLE[:, 1]
        index = bcast(S5_AT[:], 1, S5_TILES)
        nearest = lambda: dve.link(dve.e.tensor_scalar(n, x, ROUND, ROUND, ALU.add, ALU.subtract))
        dve.link(dve.e.tensor_tensor(x, bcast(S5K[:, STEP_HI, :], 2, S5_IDX), index, ALU.mult))
        nearest()
        dve.link(dve.e.tensor_tensor(x, x, n, ALU.subtract))
        dve.link(dve.e.tensor_tensor(n, bcast(S5K[:, STEP_LO, :], 2, S5_IDX), index, ALU.mult))
        dve.link(dve.e.tensor_tensor(x, x, n, ALU.add))
        nearest()
        dve.link(dve.e.tensor_tensor(TAB[:, 0], x, n, ALU.subtract))
        dve.link(dve.e.tensor_scalar(x, x, 0.25, None, ALU.add))
        nearest()
        dve.e.tensor_tensor(TAB[:, 1], x, n, ALU.subtract).then_inc(w["angles"], 1)
        b = plan.b["s5c"] + 3
        dve.e.wait_ge(bank_free[b % 4], b // 4 + 1)

    def dve_s5_prepare(dve, e, k):
        w, par, tiles = s5_sems, k % 2, at4(e, k)
        if k >= 2:
            dve.e.wait_ge(bank_ready, t2(e, 12) + (s5_y(k - 2) + 1))
        n = 4 * (S5_L + 1) * S5_C
        q = [PR[:, i].rearrange("p t n -> p (t n)")[:, 0:n].rearrange("p (t j c) -> p t j c", t=4, c=S5_C) for i in range(4)]
        cr, ci = (bcast(CK[:, i, tiles, :], 2, S5_L + 1) for i in range(2))
        ar, ai = (bcast(A_POW[:, i, :, tiles].rearrange("p j t -> p t j"), 3, S5_C) for i in range(2))
        for i, (a, b) in enumerate(((cr, ar), (ci, ai), (cr, ai), (ci, ar))):
            ins = dve.e.tensor_tensor(q[i], a, b, ALU.mult)
        dve.link(ins)
        for h in range(2):
            rows = slice(h * HD, h * HD + HD)
            dve.e.tensor_tensor(CAX[rows, par, 0, :, :, h, :], q[0][rows], q[1][rows], ALU.subtract)
            ins = dve.e.scalar_tensor_tensor(CAX[rows, par, 1, :, :, h, :], q[2][rows], -1.0, q[3][rows], ALU.mult, ALU.subtract)
        ins.then_inc(w["ca"], 1)
        dve.wait(w["ca"])

    def dve_s5_states(dve, e, k):
        w, par, p = s5_sems, k % 2, plan.p["s5"] + k
        pair = PAIR[p % 2]
        dve.wait(w["bu"])
        dve.wait(w["turning"])
        flat = lambda a: a.rearrange("p t n -> p (t n)")
        cos, sin, decay = (flat(TURNING[:, par, i]) for i in range(3))
        q = [flat(PR[:, i]) for i in range(4)]
        for i, (part, tab) in enumerate(((0, cos), (1, sin), (1, cos), (0, sin))):
            ins = dve.e.tensor_tensor(q[i], pair[:, part, :], tab, ALU.mult)
        ins.then_inc(evac[p % 2], 1)
        dve.e.wait_ge(evac[p % 2], t2(e, 1) + (p // 2 + 1))
        dve.e.tensor_tensor(q[0], q[0], q[1], ALU.add)
        dve.link(dve.e.tensor_tensor(q[2], q[2], q[3], ALU.subtract))
        for i in (0, 2):
            ins = dve.e.tensor_tensor_scan(q[i + 1], decay, q[i], 0.0, ALU.mult, ALU.add)
        dve.link(ins)
        if e is not None or k:
            dve.e.wait_ge(bank_ready, t2(e, 12) + (s5_y(k - 1) + 1))
        for part, (a, b, op) in enumerate(((cos, sin, ALU.subtract), (sin, cos, ALU.add))):
            dve.e.tensor_tensor(q[0], q[1], a, ALU.mult)
            dve.link(dve.e.tensor_tensor(q[2], q[3], b, ALU.mult))
            ins = dve.e.tensor_tensor(flat(XS[:, part]), q[0], q[2], op)
            if part == 0:
                dve.link(ins)
        ins.then_inc(w["state"], 1)
        dve.wait(w["state"])

    def dve_s5_skip(dve, e, k):
        par, b = k % 2, s5_out(k)
        d = COLS[:, col_at["od_d"] + k:col_at["od_d"] + k + 1] if e is None else COLS[:, bass.ds(e * 2 + (col_at["od_d"] + k), 1)]
        bank = full_bank(dve, b, t2(e, 3))
        dve.e.scalar_tensor_tensor(TMP[:, par:par + 1, :], HF[:, step_at(e, k), :], d, bank[:].rearrange("p (a n) -> p a n", a=1),
                                   ALU.mult, ALU.add).then_inc(bank_free[b % 4], 1)
        dve.wait(hi_ready)
        dve.e.tensor_tensor(HL[:, step_at(e, k), :], SQ[:, par:par + 1, :], HH[:, step_at(e, k), :].bitcast(F32), ALU.subtract)\
             .then_inc(h_ready, 1)
        dve.passed(h_ready, 1)

    def dve_s5(dve):
        w = s5_sems
        dve_s5_start(dve)

        def step(e, k):
            if e is not None or k < KD - 1:
                dve_s5_prepare(dve, e, k + 1)
            dve_s5_states(dve, e, k)
            if e is not None or k:
                dve_s5_skip(dve, e, k - 1)

        s5_loop(dve, lambda: dve_s5_prepare(dve, None, 0), step, lambda: dve_s5_skip(dve, None, KD - 1),
                {w["bu"]: 2, w["turning"]: 2, w["state"]: 2, w["ca"]: 2, hi_ready: 2, h_ready: 2, dve.chain: 12})

    out_saved = sem("out_saved")

    def sp_store(sp):
        for b in range(plan.b["store"] + KD - 4, plan.b["store"] + KD):
            sp.wait_ge(bank_free[b % 4], b // 4 + 1)
        sp.dma_start(out[0].rearrange("(t p) d -> p t d", p=P), OTOK[:]).then_inc(out_saved, 16)
        sp.wait_ge(out_saved, 16)

    def pe_store(pe):
        b = plan.b["store"]
        pe_after_h(pe, plan.p["store"])
        for k in range(KD):
            bank = take_bank(pe, b + k)
            for tt in range(NT):
                ins = nc.tensor.transpose(bank[:, tt * P:tt * P + P], X[:, k, tt * P:tt * P + P], IDENT[:])
            ins.then_inc(bank_ready, 1)

    def act_store(act):
        b = plan.b["store"]
        for k in range(KD):
            bank = full_bank(act, b + k)
            act.e.activation(OTOK[:, :, k * P:k * P + P], bank[:].rearrange("p (t c) -> p t c", c=P), ACT.Copy)\
                 .then_inc(bank_free[(b + k) % 4], 1)

    def act_program(act):
        act_loads(act.e)
        act_norm(act, 0)
        act_mixin(act)
        act_pool(act)
        act_attention(act, 0, S0, PT0)
        act_norm(act, 1)
        act_router(act, 0)
        act_moe(act, 0)
        act_norm(act, 2)
        act_dt(act)
        act_ssm(act)
        act_ssm_out(act)
        act_norm(act, 3)
        act_router(act, 1)
        act_moe(act, 1)
        act_norm(act, FINAL)
        act_norm(act, 5)
        act_s5_rows(act)
        act_evin(act)
        act_gmlp(act)
        act_qknorm(act)
        act_attention(act, 1, S1, PT1)
        act_s5_vectors(act)
        act_norm(act, 6)
        act_ffn(act, 0)
        act_ple_load(act, 0)
        act_s5_load(act)
        act_norm(act, 7)
        act_ple(act, 0)
        act_norm(act, PLAIN)
        act_s5(act)
        act_glu(act)
        act_norm(act, 9)
        act_ffn(act, 1)
        act_ple_load(act, 1)
        act_norm(act, 10)
        act_ple(act, 1)

    def pe_program(pe):
        pe_start(pe)
        pe_norm(pe, 0)
        pe_mixin(pe)
        pe_pool(pe)
        pe_attention(pe, 0, Q0, K0, V0, S0, PT0, False)
        pe_banks_read(pe, plan.b["att0"])
        pe_after_h(pe, plan.p["mixout"])
        pe_matrix(pe, "mixout", 4)
        pe_norm(pe, 1)
        pe_router(pe, 0)
        pe_router_turn(pe, 0)
        pe_moe(pe, 0)
        pe_norm(pe, 2)
        pe_dt(pe)
        pe_ssm(pe)
        pe_ssm_out(pe)
        pe_norm(pe, 3)
        pe_router(pe, 1)
        pe_router_turn(pe, 1)
        pe_moe(pe, 1)
        pe_norm(pe, FINAL)
        pe_norm(pe, 5)
        pe_evin(pe)
        pe_gmlp(pe)
        pe_qknorm(pe)
        pe_attention(pe, 1, Q1, K1, V1, S1, PT1, True)
        pe_s5_vectors(pe)
        pe.wait(half_ready, 4)
        pe_after_h(pe, plan.p["evout"])
        pe_matrix(pe, "evout", 4)
        pe_norm(pe, 6)
        pe_ffn(pe, 0)
        pe_norm(pe, 7)
        pe_ple(pe, 0)
        pe_norm(pe, PLAIN)
        pe_s5(pe)
        pe_glu(pe)
        pe_norm(pe, 9)
        pe_ffn(pe, 1)
        pe_norm(pe, 10)
        pe_ple(pe, 1)

    def dve_program(dve):
        dve_start(dve)
        dve_norm(dve, 0)
        dve_pool(dve)
        dve.wait(strip_ready)
        dve_attention(dve, 0, S0, lambda h: STRIP[:, h, :])
        dve_residual(dve, "mixout", 4, 1, (0, 2))
        dve_norm(dve, 1)
        dve_router(dve, 0)
        dve_moe(dve, 0)
        dve_norm(dve, 2)
        dve_dt(dve)
        dve_ssm(dve)
        dve_ssm_out(dve)
        dve_norm(dve, 3)
        dve_router(dve, 1)
        dve_moe(dve, 1)
        dve_norm(dve, FINAL)
        dve_norm(dve, 5)
        dve_evin(dve)
        dve_gmlp(dve)
        dve_qknorm(dve)
        dve_attention(dve, 1, S1, lambda h: CAUSAL[:])
        dve_s5_vectors(dve)
        dve_residual(dve, "evout", 4, 1, None)
        dve_norm(dve, 6)
        dve_ffn(dve, 0)
        dve_norm(dve, 7)
        dve_ple(dve, 0)
        dve_ple_gates(dve, 0)
        dve_norm(dve, PLAIN)
        dve_s5(dve)
        dve_glu(dve)
        dve_norm(dve, 9)
        dve_ffn(dve, 1)
        dve_norm(dve, 10)
        dve_ple(dve, 1)
        dve_ple_gates(dve, 1)

    def pe_banks_read(pe, b):
        for k in range(b - 4, b):
            pe.e.wait_ge(bank_free[k % 4], k // 4 + 1)

    sp_chain, pe_chain = sem("sp_chain"), sem("pe_chain")

    with ctx:
        block = ctx.enter_context(nc.Block())

        @block.scalar
        def _(eng):
            act = Engine(eng, act_chain)
            act_program(act)
            act_store(act)

        @block.sync
        def _(eng):
            sp = Engine(eng, sp_chain)
            sp_load_all(sp)
            sp_store(eng)

        @block.gpsimd
        def _(eng):
            pool = Engine(eng, pool_chain)
            pool_constants(pool)
            before = min(plan.u["glu"] + 2, plan.unit)
            split_units(eng, 0, 2)
            split_units(eng, 2, before)
            if plan.unit > plan.u["glu"]:
                pool_s5(pool)
                split_units(eng, before, plan.unit)

        @block.tensor
        def _(eng):
            pe = Engine(eng, pe_chain)
            pe_program(pe)
            pe_store(pe)

        @block.vector
        def _(eng):
            dve_program(Engine(eng, dve_chain))


def kernel(**inputs):
    import numpy as np
    import concourse.bacc as bacc
    from concourse.bass_utils import run_bass_kernel_spmd

    nc = bacc.Bacc("TRN2", target_bir_lowering=False, num_devices=1)
    arrays = {f"in_{name}": np.ascontiguousarray(value) for name, value in inputs.items()}
    arrays["in_rel_flip"] = np.ascontiguousarray(np.asarray(inputs["rel_bias"])[..., ::-1])
    t = {name[3:]: nc.dram_tensor(name, a.shape, F32, kind="ExternalInput").ap() for name, a in arrays.items()}
    out = nc.dram_tensor("out_0_dram", (1, SEQ, D), F32, kind="ExternalOutput").ap()
    build(nc, t, out)
    return run_bass_kernel_spmd(nc, [arrays], core_ids=[0]).results[0]["out_0_dram"]
```

```python
from contextlib import ExitStack

import concourse.bass as bass
from concourse import mybir

F32 = mybir.dt.float32
F32R = mybir.dt.float32r
I32 = mybir.dt.int32
ACT = mybir.ActivationFunctionType
ALU = mybir.AluOpType
AX = mybir.AxisListType

P = 128
SEQ = 512
D = 1024
KD = D // P
NT = SEQ // P
EPS = 1e-6
NEG = -1e30
UNIT = 2048
HALF = D // 2
HEADS = 8
HD = 64
REL_CLIP = 256
SSM_G = 8
SSM_H = 32
SSM_INNER = 2048
EXPERTS = 32
GROUPS = 4
EPG = 8
SLOTS = -(-(EXPERTS + (2 * SEQ - EXPERTS) // P) // 4) * 4
FF = 2816
FB = FF // P
S5_P = 64
S5_C = 16
S5_TILES = 32
S5_L = 4
S5_N = SEQ // S5_L
S5_LOW, S5_HIGH = 16, 8
S5_IDX = S5_LOW + S5_HIGH
TRI = sum(SEQ - P * i for i in range(NT))
TRI_AT = [0, 512, 896, 1152]
TWO_PI = 6.283185307179586
ROUND = 12582912.0
TWO_PI_PARTS = (6.28125, 0.00193500518798828125, 3.0199159819e-07)
EXP_SERIES = [1 / f for f in (362880, 40320, 5040, 720, 120, 24, 6, 2, 1)]


class Plan:

    def __init__(self):
        self.unit, self.pair, self.bank = 0, 0, 0
        self.u, self.p, self.b = {}, {}, {}

    def step(self, name, units=0, pairs=0, banks=0):
        self.u[name], self.p[name], self.b[name] = self.unit, self.pair, self.bank
        self.unit += units
        self.pair += pairs
        self.bank += banks


def make_plan():
    plan = Plan()
    plan.step("columns", banks=6)
    plan.step("load", banks=8)
    plan.step("ada", pairs=12)

    def norm(n):
        plan.step(f"norm{n}", banks=1)

    def moe(layer):
        plan.step(f"moe{layer}", units=SLOTS, pairs=NT + 2 * SLOTS + 4, banks=4 + 2 * SLOTS)

    def ffn(layer):
        plan.step(f"ffn{layer}", units=34, pairs=26)

    def ple(layer):
        plan.step(f"ple{layer}", units=6, pairs=8, banks=2)

    norm(0)
    plan.step("mixin", units=8, pairs=8)
    plan.step("pool", banks=4)
    plan.step("att0", pairs=4, banks=6 * HEADS)
    plan.step("mixout", units=4, pairs=4)
    norm(1)
    moe(0)
    norm(2)
    plan.step("dt", banks=4)
    plan.step("ssm", units=24, pairs=24, banks=8 * SSM_G)
    plan.step("ssmout", units=8, pairs=8)
    norm(3)
    moe(1)
    norm(4)
    norm(5)
    plan.step("evin", units=10, pairs=10)
    plan.step("gate", banks=3)
    plan.step("gmlp", banks=5)
    plan.step("qknorm", banks=8)
    plan.step("att1", pairs=4, banks=6 * HEADS)
    plan.step("s5a", banks=1)
    plan.step("evout", units=4, pairs=4)
    norm(6)
    ffn(0)
    norm(7)
    ple(0)
    norm(8)
    plan.step("s5c", banks=4)
    plan.step("s5", pairs=8, banks=6 * KD)
    plan.step("glu", units=8, pairs=8)
    norm(9)
    ffn(1)
    norm(10)
    ple(1)
    plan.step("store", banks=8)
    return plan


class Engine:

    def __init__(self, eng, chain):
        self.e, self.chain = eng, chain
        self.count = {}

    def _entry(self, sem):
        return self.count.setdefault(sem.name, [0, 0, sem])

    def wait(self, sem, events=1):
        entry = self._entry(sem)
        entry[0] += events
        self.e.wait_ge(sem, entry[1] + entry[0])

    def seen(self, sem):
        entry = self._entry(sem)
        return entry[1] + entry[0]

    def passed(self, sem, events):
        self._entry(sem)[0] += events

    def link(self, ins):
        ins.then_inc(self.chain, 1)
        self.wait(self.chain)

    def loop(self, times, per):
        return Loop(self, times, per)


class Loop:

    def __init__(self, engine, times, per):
        self.engine, self.times, self.per = engine, times, per

    def __enter__(self):
        self.fori = self.engine.e.Fori(0, self.times)
        i = self.fori.__enter__()
        self.saved = {}
        for sem, n in self.per.items():
            entry = self.engine._entry(sem)
            self.saved[sem.name] = (entry[0], entry[1])
            entry[1] = i * n + (entry[1] + entry[0])
            entry[0] = 0
        return i

    def __exit__(self, *exc):
        if exc[0] is None:
            for sem, n in self.per.items():
                entry = self.engine._entry(sem)
                assert entry[0] == n, (sem.name, entry[0], n)
                done, before = self.saved[sem.name]
                entry[0], entry[1] = done + self.times * n, before
        return self.fori.__exit__(*exc)


def column_vectors(t):
    rows = [
        ("c", t["c"].rearrange("b (k p) -> (b k) p", p=P)),
        ("ada_b", t["ada_b"].rearrange("l (k p) -> (l k) p", p=P)),
        ("norm1", t["norm1_w"].rearrange("l (k p) -> (l k) p", p=P)),
        ("norm2", t["norm2_w"].rearrange("l (k p) -> (l k) p", p=P)),
        ("pool_scale", t["pool_scale"].rearrange("l (k p) -> (l k) p", p=P)),
        ("conv_w", t["ssm_conv_w"].rearrange("l j (k p) -> (l j k) p", p=P)),
        ("conv_b", t["ssm_conv_b"].rearrange("l (k p) -> (l k) p", p=P)),
        ("ssm_norm", t["ssm_norm_w"].rearrange("l (k p) -> (l k) p", p=P)),
        ("final", t["final_norm_w"].rearrange("(k p) -> k p", p=P)),
        ("norm_mix", t["norm_mix_2"].rearrange("l (k p) -> (l k) p", p=P)),
        ("norm_ffn", t["norm_ffn_2"].rearrange("l (k p) -> (l k) p", p=P)),
        ("od_d", t["od_d_2"].rearrange("l (k p) -> (l k) p", p=P)),
        ("fconv_w", t["ffn_conv_w_2"].rearrange("l j (k p) -> (l j k) p", p=P)),
        ("fconv_b", t["ffn_conv_b_2"].rearrange("l (k p) -> (l k) p", p=P)),
    ]
    at, n = {}, 0
    for name, ap in rows:
        at[name] = n
        n += ap.shape[0]
    return rows, at, n


def bcast(ap, dim, n):
    shape = list(ap.shape)
    return ap.unsqueeze(dim).broadcast_to(shape[:dim] + [n] + shape[dim:])


def build(nc, t, out):
    plan = make_plan()
    ctx = ExitStack()

    def sem(name):
        return ctx.enter_context(nc.semaphore(name))

    def sb(name, shape, dt=F32, where=None):
        return (where or ctx).enter_context(nc.sbuf_tensor(name, shape, dt))

    X = sb("X", [P, KD, SEQ])
    HH = sb("HH", [P, KD, SEQ], F32R)
    r = ExitStack()
    HL = sb("HL", [P, KD, SEQ], F32R, r)
    r.close()
    HF = sb("HF", [P, KD, SEQ])
    RAW = sb("RAW", [P, 2, UNIT])
    WH = sb("WH", [P, 2, UNIT], F32R)
    WL = sb("WL", [P, 2, UNIT], F32R)
    rows, col_at, n_cols = column_vectors(t)
    n_row_tiles = -(-n_cols // P)
    COLS = sb("COLS", [P, n_row_tiles * P])
    IDENT = sb("IDENT", [P, P])
    ONES = sb("ONES", [P, P])
    HEAD_ONES = sb("HEAD_ONES", [P, P])
    r = ExitStack()
    LATER = sb("LATER", [P, SEQ], F32, r)
    CAUSAL = sb("CAUSAL", [P, SEQ], F32, r)
    r.close()
    FUP = sb("FUP", [P, 2, SEQ])
    MOD = sb("MOD", [P, 2 * 6 * KD])
    GAIN = sb("GAIN", [P, 4, KD])
    SQ = sb("SQ", [P, 2, SEQ])
    RSTD = sb("RSTD", [P, SEQ])
    TMP = sb("TMP", [P, 2, SEQ])
    r = ExitStack()
    ROUTER_W = sb("ROUTER_W", [P, 2, KD, GROUPS + EXPERTS], F32, r)
    ROUTER_B = sb("ROUTER_B", [P, 2, GROUPS + EXPERTS], F32, r)
    DT_W = sb("DT_W", [P, KD, SSM_H], F32, r)
    DT_ROW = sb("DT_ROW", [P, 2, SSM_H], F32, r)
    D_ROW = sb("D_ROW", [P, SSM_H], F32, r)
    D_COL = sb("D_COL", [P, 2 * SSM_G], F32, r)
    r.close()
    S5K = sb("S5K", [P, 5, S5_TILES])
    A_POW = sb("A_POW", [P, 2, S5_L + 1, S5_TILES])
    A_REV = sb("A_REV", [P, 2, S5_L, S5_TILES])
    SPARE = sb("SPARE", [P, (4064 - 23 * 4 * S5_TILES) // 4])
    FG_W = sb("FG_W", [P, KD, HEADS])
    FG_B = sb("FG_B", [P, HEADS])
    QK_GAIN = sb("QK_GAIN", [P, 2])
    INV_COUNT = sb("INV_COUNT", [P, 16])
    FALLING = sb("FALLING", [P, EPG])
    C_ACT = sb("C_ACT", [P, KD])
    MX = sb("MX", [P, 2, 2, NT])
    TURN = sb("TURN", [P, 2])
    SUMS = sb("SUMS", [P, 2, NT])

    def region():
        return ExitStack()

    r = region()
    STRIP = sb("STRIP", [P, HEADS, SEQ], F32, r)
    XTOK = sb("XTOK", [P, NT, D], F32, r)
    ROWS = sb("ROWS", [P, n_row_tiles, P], F32, r)
    ADA = sb("ADA", [P, 2, 4, D], F32, r)
    ADA_ACC = sb("ADA_ACC", [P, 2, D], F32, r)
    REL = sb("REL", [P, 640], F32, r)
    UNUSED = sb("UNUSED", [SLOTS, P], F32, r)
    r.close()
    r = region()
    STRIP_ = sb("STRIP_", [P, HEADS, SEQ], F32, r)
    Q0 = sb("Q0", [P, 4, SEQ], F32, r)
    K0 = sb("K0", [P, 4, SEQ], F32, r)
    V0 = sb("V0", [P, NT, HALF], F32, r)
    S0 = sb("S0", [P, 2, TRI], F32, r)
    PT0 = sb("PT0", [P, 2, TRI], F32, r)
    U = sb("U", [P, 4, SEQ], F32, r)
    POOLED = sb("POOLED", [P, 4, SEQ], F32, r)
    PSCR = sb("PSCR", [P, 2, SEQ], F32, r)
    POOL_W = sb("POOL_W", [P, 4, P], F32, r)
    r.close()
    r = region()
    r2 = region()
    HTOK = sb("HTOK", [P, NT, D], F32, r2)
    r2.close()
    W2H = sb("W2H", [P, 2, D], F32R, r)
    W2L = sb("W2L", [P, 2, D], F32R, r)
    W2RAW = sb("W2RAW", [P, 2, D], F32, r)
    XG = sb("XG", [P, 2, D], F32, r)
    OG = sb("OG", [P, 2, D], F32, r)
    GH = sb("GH", [P, 2, KD, P], F32R, r)
    GL = sb("GL", [P, 2, KD, P], F32R, r)
    HS = sb("HS", [P, 2, P], F32, r)
    HID = sb("HID", [P, 2, P], F32, r)
    HTH = sb("HTH", [P, 2, P], F32R, r)
    HTL = sb("HTL", [P, 2, P], F32R, r)
    IDENT_R = sb("IDENT_R", [P, P], F32R, r)
    STRICT = sb("STRICT", [P, P], F32, r)
    ROUTER_WH = sb("ROUTER_WH", [P, KD, GROUPS + EXPERTS], F32R, r)
    ROUTER_WL = sb("ROUTER_WL", [P, KD, GROUPS + EXPERTS], F32R, r)
    LOGIT = sb("LOGIT", [P, NT, GROUPS + EXPERTS], F32, r)
    GATE = sb("GATE", [P, 12, NT, EPG], F32, r)
    ESEL = sb("ESEL", [P, NT, GROUPS, EPG], F32, r)
    MASK = sb("MASK", [P, 2, NT, EXPERTS], F32, r)
    BOTH = sb("BOTH", [P, NT, EXPERTS], F32, r)
    SHARE = sb("SHARE", [P, 2, NT], F32, r)
    PLACE = sb("PLACE", [P, 3, EXPERTS], F32, r)
    POS = sb("POS", [P, 2, NT], F32, r)
    POS_I = sb("POS_I", [P, 2, NT], I32, r)
    ROW_AT = sb("ROW_AT", [P, 2, NT], F32, r)
    SLOT_AT = sb("SLOT_AT", [P, SLOTS], F32, r)
    SLOT_E = sb("SLOT_E", [P, SLOTS], F32, r)
    SLOT_I = sb("SLOT_I", [P, SLOTS], I32, r)
    GATHER_I = sb("GATHER_I", [P, SLOTS], I32, r)
    SCATTER_I = sb("SCATTER_I", [P, SLOTS], I32, r)
    OWNER = sb("OWNER", [P, SLOTS, EXPERTS], F32, r)
    LIST = sb("LIST", [SLOTS, P], F32, r)
    r.close()
    r = region()
    G = sb("G", [P, 2 * SSM_G, SEQ], F32, r)
    ZS = sb("ZS", [P, 2, 2, SEQ], F32, r)
    CONV = sb("CONV", [P, 2, 4, SEQ], F32, r)
    r2 = region()
    DT_WH = sb("DT_WH", [P, KD, SSM_H], F32R, r2)
    DT_WL = sb("DT_WL", [P, KD, SSM_H], F32R, r2)
    r2.close()
    XDT = sb("XDT", [P, NT, 256], F32, r)
    CBM = sb("CBM", [P, TRI], F32, r)
    DECAY = sb("DECAY", [P, 2, TRI], F32, r)
    ACS_ROW = sb("ACS_ROW", [P, 2, SEQ], F32, r)
    DT = sb("DT", [P, NT, SSM_H], F32, r)
    DTS = sb("DTS", [P, 6, NT, SSM_H], F32, r)
    ACS = sb("ACS", [SSM_H, 2, SEQ], F32, r)
    ACS_COL = sb("ACS_COL", [P, NT, SSM_H], F32, r)
    r.close()
    r = region()
    UA = sb("UA", [P, 4, SEQ], F32, r)
    VA = sb("VA", [P, NT, HALF], F32, r)
    VSQ = sb("VSQ", [P, NT, HALF], F32, r)
    Q1 = sb("Q1", [P, 4, SEQ], F32, r)
    K1 = sb("K1", [P, 4, SEQ], F32, r)
    V1 = sb("V1", [P, NT, HALF], F32, r)
    S1 = sb("S1", [P, 2, TRI], F32, r)
    PT1 = sb("PT1", [P, 2, TRI], F32, r)
    SPAT = sb("SPAT", [P, 4, P], F32, r)
    SPAT_T = sb("SPAT_T", [P, 4, P], F32, r)
    SPAT_B = sb("SPAT_B", [P, 4, P], F32, r)
    V_GAIN = sb("V_GAIN", [P, HALF], F32, r)
    FG_WH = sb("FG_WH", [P, KD, HEADS], F32R, r)
    FG_WL = sb("FG_WL", [P, KD, HEADS], F32R, r)
    FGL = sb("FGL", [P, 6, NT, HEADS], F32, r)
    FCUM = sb("FCUM", [HEADS, 2, SEQ], F32, r)
    MINUS_HEAD = sb("MINUS_HEAD", [HEADS, HEADS, P], F32, r)
    VR = sb("VR", [P, 16], F32, r)
    AROW = sb("AROW", [S5_TILES, 2, P], F32, r)
    LDT_ROW = sb("LDT_ROW", [P, 2 * S5_TILES], F32, r)
    r.close()
    r = region()
    FHH = sb("FHH", [P, FB, SEQ], F32R, r)
    FHL = sb("FHL", [P, FB, SEQ], F32R, r)
    r.close()
    r = region()
    PTOK = sb("PTOK", [P, NT, 256], F32, r)
    PH = sb("PH", [P, 2, SEQ], F32R, r)
    PL = sb("PL", [P, 2, SEQ], F32R, r)
    PROJ = sb("PROJ", [P, 4, SEQ], F32, r)
    OTOK = sb("OTOK", [P, NT, D], F32, r)
    r.close()
    r = region()
    BB = sb("BB", [P, 2, S5_TILES, S5_C], F32, r)
    CK = sb("CK", [P, 2, S5_TILES, S5_C], F32, r)
    TAB = sb("TAB", [P, 2, S5_TILES, S5_IDX], F32, r)
    W1X = sb("W1X", [P, 2, 2, 4, S5_L, 2, S5_C], F32, r)
    r2 = region()
    CRAW = sb("CRAW", [P, 2, KD, 2, S5_P], F32, r2)
    BRAW = sb("BRAW", [P, 2, S5_TILES, S5_C], F32, r2)
    ANGLE = sb("ANGLE", [P, 2, S5_TILES, S5_IDX], F32, r2)
    r2.close()
    TURNING = sb("TURNING", [P, 2, 3, 4, S5_N], F32, r)
    PRP = sb("PRP", [P, 2, 4, S5_N], F32, r)
    PAD = sb("PAD", [P, S5_N * 4], F32, r)
    CAX = sb("CAX", [P, 2, 2, 4, S5_L + 1, 2, S5_C], F32, r)
    W1_T = sb("W1_T", [P, 2, 2, 4, P], F32, r)
    W3 = sb("W3", [P, 2, 4, P], F32, r)
    U4 = sb("U4", [P, 2, 4, S5_N], F32, r)
    XS = sb("XS", [P, 2, 4, S5_N], F32, r)
    PR = sb("PR", [P, 4, 4, S5_N], F32, r)
    S5_AT = sb("S5_AT", [P, S5_IDX], F32, r)
    FIRST = sb("FIRST", [P, S5_N], F32, r)
    Y4 = sb("Y4", [P, 4, S5_N], F32, r)
    r.close()

    PAIR = [ctx.enter_context(nc.psum_tensor(f"PAIR{i}", [P, 2, SEQ], F32)) for i in range(2)]
    BANK = [ctx.enter_context(nc.psum_tensor(f"BANK{i}", [P, SEQ], F32)) for i in range(4)]

    strip_dram = nc.dram_tensor("strip_scratch", (P, HEADS, 640), F32, kind="Internal").ap()
    rel_dram = nc.dram_tensor("rel_scratch", (HEADS, 640), F32, kind="Internal").ap()
    list_dram = [nc.dram_tensor(f"list_scratch{i}", (SLOTS * P, 1), F32, kind="Internal").ap() for i in range(2)]
    htok_dram = nc.dram_tensor("htok_scratch", (SEQ, D), F32, kind="Internal").ap()
    y_dram = nc.dram_tensor("y_scratch", (2 * SEQ, D), F32, kind="Internal").ap()
    acs_dram = nc.dram_tensor("acs_scratch", (SSM_H, SEQ), F32, kind="Internal").ap()

    landed = [sem("unit_landed0"), sem("unit_landed1")]
    split_hi = sem("split_hi")
    split_ready = sem("split_ready")
    unit_done = sem("unit_done")
    evac = [sem("pair_evacuated0"), sem("pair_evacuated1")]
    bank_ready = sem("bank_ready")
    bank_free = [sem(f"bank_free{i}") for i in range(4)]
    pair_ready = sem("small_pair_ready")
    consts_ready = sem("consts_ready")
    dve_chain, act_chain, pool_chain = sem("dve_chain"), sem("act_chain"), sem("pool_chain")
    x_landed, rows_landed, small_landed = sem("x_landed"), sem("rows_landed"), sem("small_landed")
    ada_landed = [sem("ada_landed0"), sem("ada_landed1")]
    ada_used, ada_summed = sem("ada_used"), sem("ada_summed")
    c_ready, x_ready = sem("c_ready"), sem("x_ready")
    sq_ready, sq_used, var_ready, root_ready = sem("sq_ready"), sem("sq_used"), sem("var_ready"), sem("root_ready")
    pre_ready, hi_ready, h_ready = sem("pre_ready"), sem("hi_ready"), sem("h_ready")
    norm_pre, norm_hi = sem("norm_pre"), sem("norm_hi")

    def take_bank(pe, b, turns=0):
        if b // 4 + (0 if isinstance(turns, int) else 1) > 0:
            pe.e.wait_ge(bank_free[b % 4], turns + b // 4)
        return BANK[b % 4]

    def full_bank(eng, b, turns=0):
        eng.e.wait_ge(bank_ready, turns * 4 + (b + 1))
        return BANK[b % 4]

    def take_pair(pe, p, turns=0):
        if p // 2 + (0 if isinstance(turns, int) else 1) > 0:
            pe.e.wait_ge(evac[p % 2], turns + p // 2)
        return PAIR[p % 2]

    def mm3(o, wh, wl, xh, xl, start, stop):
        nc.tensor.matmul(o, wh, xh, start=start, stop=False)
        nc.tensor.matmul(o, wh, xl, start=False, stop=False)
        return nc.tensor.matmul(o, wl, xh, start=False, stop=stop)

    def unit_channels(pe, u, pair, xh, xl, tiles, first=True, last=True, off=0):
        s = u % 2
        pe.e.wait_ge(split_ready, off + (u + 1))
        for m in range(2):
            for k in range(tiles):
                c = (k * 2 + m) * P
                ins = mm3(pair[:, m, :], WH[:, s, c:c + P], WL[:, s, c:c + P], xh(k), xl(k),
                          first and k == 0, last and k == tiles - 1)
        ins.then_inc(unit_done, 1)

    def first_unit(pe, u, pair, h, off=0):
        s = u % 2
        pe.e.wait_ge(split_ready, off + (u + 1))
        for k in range(KD):
            pe.e.wait_ge(h_ready, h + k + 1)
            for m in range(2):
                c = (k * 2 + m) * P
                ins = mm3(pair[:, m, :], WH[:, s, c:c + P], WL[:, s, c:c + P], HH[:, k, :], HL[:, k, :], k == 0, k == KD - 1)
        ins.then_inc(unit_done, 1)

    def unit_tokens(pe, u, pair):
        s = u % 2
        pe.e.wait_ge(split_ready, u + 1)
        for tt in range(NT):
            o = pair[:, tt // 2, (tt % 2) * 256:(tt % 2) * 256 + 256]
            for k in range(KD):
                c, a = slice(k * 256, k * 256 + 256), slice(tt * P, tt * P + P)
                ins = mm3(o, HH[:, k, a], HL[:, k, a], WH[:, s, c], WL[:, s, c], k == 0, k == KD - 1)
        ins.then_inc(unit_done, 1)

    def full_pair(eng, u, p, off=0):
        eng.e.wait_ge(unit_done, off + (u + 1))
        return PAIR[p % 2]

    hh = lambda k: HH[:, k, :]
    hl = lambda k: HL[:, k, :]

    def mod(layer, c, k):
        at = (layer * 6 + c) * KD + k
        return MOD[:, at:at + 1]

    def col(name, i):
        at = col_at[name] + i
        return COLS[:, at:at + 1]

    dram = lambda name, offset, ap: bass.AP(t[name].tensor, t[name].offset + offset, ap)

    sp_unit = [0]

    def load_unit(sp, first, second, off=0, u=None):
        if u is None:
            u = sp_unit[0]
            sp_unit[0] += 1
        s = u % 2
        if u >= 2 or not isinstance(off, int):
            sp.wait_ge(split_ready, off + (u - 1))
        for src, dst in (first, second):
            sp.dma_start(dst(RAW[:, s, :]), src).then_inc(landed[s], 16)

    def block_unit(w, c0, rows=KD, row0=0):
        h = rows // 2
        view = w.rearrange("(k p) n -> p k n", p=P)
        part = lambda a, b: (view[:, row0 + a:row0 + b, bass.ds(c0, 256)] if not isinstance(c0, int)
                             else view[:, row0 + a:row0 + b, c0:c0 + 256],
                             lambda raw: raw[:, a * 256:b * 256].rearrange("p (k n) -> p k n", n=256))
        return part(0, h), part(h, rows)

    def paired_unit(w1, c1, w2, c2):
        def part(w, c, m):
            cols = slice(c, c + P) if isinstance(c, int) else bass.ds(c, P)
            return (w.rearrange("(k p) n -> p k n", p=P)[:, :, cols],
                    lambda raw: raw.rearrange("p (k m n) -> p k m n", m=2, n=P)[:, :, m, :])
        return part(w1, c1, 0), part(w2, c2, 1)

    def sp_load_all(engine):
        sp = engine.e
        mix_in, mix_out = t["mix_w_in"][0], t["mix_w_out"][0]
        with engine.loop(2, {ada_used: 12}) as layer:
            with engine.loop(3, {ada_used: 4}) as i:
                for b in range(2):
                    for h in range(2):
                        engine.wait(ada_used)
                        src = t["ada_w"][bass.ds(layer, 1)].rearrange("l (k p) n -> p (l k) n", p=P)
                        sp.dma_start(ADA[:, h], src[:, 4 * h:4 * h + 4, bass.ds(i * 2 * D + b * D, D)])\
                          .then_inc(ada_landed[h], 16)

        def plain(w, n):
            for i in range(n):
                load_unit(sp, *block_unit(w, i * 256))

        def ffn(layer):
            u0 = plan.u[f"ffn{layer}"]
            w = t["ffn_w_up_2"][layer]
            with sp.Fori(0, FB // 2) as i:
                for b in range(2):
                    load_unit(sp, *paired_unit(w, i * 256 + b * P, w, i * 256 + (b * P + FF)), off=i * 2, u=u0 + b)
            w = t["ffn_w_down_2"][layer]
            with sp.Fori(0, 2) as i:
                for c in range(2):
                    for j, (k0, n) in enumerate(((0, 8), (8, 8), (16, 6))):
                        load_unit(sp, *block_unit(w, i * 512 + c * 256, n, k0), off=i * 6, u=u0 + FB + 3 * c + j)
            sp_unit[0] += 34

        def ple(layer):
            wp, wg = t["ple_w_proj_2"][layer], t["ple_w_gate_2"][layer]
            for half in range(2):
                view = wp.rearrange("(k p) n -> p k n", p=P)
                part = lambda k: (view[:, k, half * 512:half * 512 + 512], lambda raw: raw[:, k * 512:k * 512 + 512])
                load_unit(sp, part(0), part(1))
                for i in range(2):
                    load_unit(sp, *block_unit(wg, half * 512 + i * 256))

        plain(mix_in, 8)
        plain(mix_out, 4)
        sp_moe(engine, 0)
        w = t["ssm_w_in"][0]
        with sp.Fori(0, SSM_G // 2) as i:
            for b in range(2):
                u = plan.u["ssm"] + 3 * b
                load_unit(sp, *block_unit(w, i * 512 + b * 256), off=i * 6, u=u)
                load_unit(sp, *block_unit(w, i * 512 + (SSM_INNER + b * 256)), off=i * 6, u=u + 1)
                c = i * 256 + (2 * SSM_INNER + b * P)
                load_unit(sp, *paired_unit(w, c, w, c + SSM_G * P), off=i * 6, u=u + 2)
        sp_unit[0] += 24
        for half in range(2):
            for i in range(4):
                load_unit(sp, *block_unit(t["ssm_w_out"][0], i * 256, KD, half * KD))
        sp_moe(engine, 1)
        plain(t["ev_w_in_2"][0], 10)
        plain(t["ev_w_out_2"][0], 4)
        ffn(0)
        ple(0)
        w = t["od_w_glu_2"][0]
        for i in range(KD):
            load_unit(sp, *paired_unit(w, i * P, w, D + i * P))
        ffn(1)
        ple(1)
        assert sp_unit[0] == plan.unit

    def pool_constants(engine):
        pool, link = engine.e, engine.link
        pool.memset(IDENT[:], 0.0)
        pool.memset(ONES[:], 1.0)
        pool.memset(HEAD_ONES[:], 0.0)
        pool.memset(LATER[:], 1.0)
        for n in range(16):
            pool.memset(INV_COUNT[:, n:n + 1], 1.0 / (n + 1))
        for n in range(EPG):
            pool.memset(FALLING[:, n:n + 1], float(EPG - n))
        link(pool.memset(CAUSAL[:], 0.0))
        for h in range(2):
            link(pool.memset(HEAD_ONES[h * HD:h * HD + HD, h * HD:h * HD + HD], 1.0))
        pool.memset(UNUSED[:], float(4 * 2 * SEQ))
        pool.affine_select(out=IDENT[:], in_=IDENT[:], compare_op=ALU.not_equal, fill=1.0, base=0,
                           pattern=[[-1, P]], channel_multiplier=1)
        pool.affine_select(out=LATER[:], in_=LATER[:], compare_op=ALU.is_ge, fill=0.0, base=0,
                           pattern=[[1, SEQ]], channel_multiplier=-1)
        pool.affine_select(out=CAUSAL[:], in_=CAUSAL[:], compare_op=ALU.is_ge, fill=NEG, base=SEQ - P,
                           pattern=[[-1, SEQ]], channel_multiplier=1).then_inc(consts_ready, 1)

    def split_unit(pool, u, off=0):
        s = u % 2
        pool.wait_ge(landed[s], off * 16 + 32 * (u // 2 + 1))
        if u >= 2 or not isinstance(off, int):
            pool.wait_ge(unit_done, off + (u - 1))
        pool.tensor_tensor(TURN[:, s:s + 1], ONES[:, 0:1], ONES[:, 0:1], ALU.mult)
        pool.tensor_scalar(WH[:, s], RAW[:, s], 1.0, 1.0, ALU.mult, ALU.mult).then_inc(split_hi, 1)
        pool.wait_ge(split_hi, off + (u + 1))
        pool.tensor_tensor(WL[:, s], RAW[:, s], WH[:, s].bitcast(F32), ALU.subtract).then_inc(split_ready, 1)

    def split_units(pool, first, last):
        last = min(last, plan.unit)
        if last - first >= 4:
            with pool.Fori(0, (last - first) // 2) as i:
                for b in range(2):
                    split_unit(pool, first + b, off=i * 2)
        else:
            for u in range(first, last):
                split_unit(pool, u)

    def act_loads(act):
        def load(dst, src, s):
            act.dma_start(dst, src).then_inc(s, 16)
            n_small[0] += s is small_landed

        n = 0
        for name, ap in rows:
            at, left, done = col_at[name], ap.shape[0], 0
            while left:
                k = min(left, P - at % P)
                load(ROWS[at % P:at % P + k, at // P, :], ap[done:done + k], rows_landed)
                at, left, done, n = at + k, left - k, done + k, n + 1
        row_dmas.append(n)
        load(XTOK[:], t["x"][0].rearrange("(t p) d -> p t d", p=P), x_landed)
        for layer in range(2):
            load(ROUTER_W[:, layer, :, 0:GROUPS], t["moe_w_group"][layer].rearrange("(k p) g -> p k g", p=P), small_landed)
            load(ROUTER_W[:, layer, :, GROUPS:], t["moe_w_expert"][layer].rearrange("(k p) g e -> p k (g e)", p=P), small_landed)
            load(ROUTER_B[:, layer, 0:GROUPS], t["moe_b_group"][layer].partition_broadcast(P), small_landed)
            load(ROUTER_B[:, layer, GROUPS:], t["moe_b_expert"][layer].rearrange("g e -> (g e)").partition_broadcast(P), small_landed)
        load(DT_W[:], t["ssm_w_in"][0][:, 3 * SSM_INNER:].rearrange("(k p) n -> p k n", p=P), small_landed)
        load(DT_ROW[:, 0, :], t["ssm_dt_bias"][0].partition_broadcast(P), small_landed)
        load(DT_ROW[:, 1, :], t["ssm_A_log"][0].partition_broadcast(P), small_landed)
        load(D_ROW[:], t["ssm_D"][0].partition_broadcast(P), small_landed)
        load(FG_W[:], t["ev_w_in_2"][0][:, 5 * HALF:].rearrange("(k p) n -> p k n", p=P), small_landed)
        load(FG_B[:], t["ev_b_fgate_2"][0].partition_broadcast(P), small_landed)
        for i, name in enumerate(("ev_q_norm_2", "ev_k_norm_2")):
            for h in range(2):
                load(QK_GAIN[h * HD:h * HD + HD, i:i + 1], dram(name, 0, [[1, HD], [1, 1]]), small_landed)
        clipped = SEQ - 1 - REL_CLIP
        load(REL[0:HEADS, clipped:640], t["rel_flip"][0, :, 0:640 - clipped], rel_step)
        act.wait_ge(consts_ready, 1)
        for layer in range(2):
            load(list_dram[layer].rearrange("(s p) a -> s (p a)", p=P), UNUSED[:], list_filled)
        act.wait_ge(rel_step, 16)
        act.activation(REL[0:HEADS, 0:clipped], REL[0:HEADS, clipped:clipped + 1].broadcast_to([HEADS, clipped]), ACT.Copy)\
           .then_inc(rel_step, 1)
        act.wait_ge(rel_step, 17)
        load(rel_dram, REL[0:HEADS, :], rel_step)
        act.wait_ge(rel_step, 33)
        load(strip_dram, rel_dram.partition_broadcast(P), rel_step)
        act.wait_ge(rel_step, 49)
        load(STRIP[:], bass.AP(strip_dram.tensor, P - 1, [[HEADS * 640 - 1, P], [640, HEADS], [1, SEQ]]), strip_landed)
        b = plan.b["columns"]
        act.wait_ge(bank_free[b % 4], b // 4 + 1)
        act.activation(C_ACT[:], COLS[:, col_at["c"]:col_at["c"] + KD], ACT.Silu).then_inc(c_ready, 1)

    row_dmas, n_small = [], [0]
    list_filled = sem("list_filled")
    rel_step, strip_landed, strip_ready = sem("rel_step"), sem("strip_landed"), sem("strip_ready")
    mod_ready = sem("mod_ready")

    def pe_start(pe):
        b = plan.b["columns"]
        pe.e.wait_ge(consts_ready, 1)
        pe.e.wait_ge(rows_landed, 16 * row_dmas[0])
        for r in range(n_row_tiles):
            n = min(P, n_cols - r * P)
            bank = take_bank(pe, b + r)
            nc.tensor.transpose(bank[:, 0:n], ROWS[0:n, r, :], IDENT[0:n, 0:n]).then_inc(bank_ready, 1)
        b = plan.b["load"]
        pe.e.wait_ge(x_landed, 16)
        for k in range(KD):
            bank = take_bank(pe, b + k)
            for tt in range(NT):
                ins = nc.tensor.transpose(bank[:, tt * P:tt * P + P], XTOK[:, tt, k * P:k * P + P], IDENT[:])
            ins.then_inc(bank_ready, 1)
        for q in range(12):
            pe.e.wait_ge(ada_used, 2 + 2 * (q + 1))
            pair = take_pair(pe, plan.p["ada"] + q)
            for m in range(KD):
                ins = nc.tensor.matmul(pair[:, 0, m:m + 1], ADA_ACC[:, q % 2, m * P:m * P + P], ONES[:, 0:1],
                                       start=True, stop=True)
            ins.then_inc(pair_ready, 1)

    def dve_start(dve):
        for h in range(2):
            dve.e.memset(ADA_ACC[:, h, :], 0.0).then_inc(ada_used, 1)
        b = plan.b["columns"]
        for r in range(n_row_tiles):
            n = min(P, n_cols - r * P)
            dve.e.tensor_copy(COLS[:, r * P:r * P + n], full_bank(dve, b + r)[:, 0:n]).then_inc(bank_free[(b + r) % 4], 1)
        b = plan.b["load"]
        for k in range(KD):
            dve.e.tensor_copy(X[:, k, :], full_bank(dve, b + k)[:]).then_inc(bank_free[(b + k) % 4], 1)
        dve.e.wait_ge(bank_free[(b + k) % 4], (b + k) // 4 + 1)
        dve.wait(c_ready)
        dve.wait(ada_used, 2)
        for q in range(12):
            for h in range(2):
                dve.wait(ada_landed[h], 16)
                for k in range(4):
                    src, c = ADA[:, h, k, :], C_ACT[:, 4 * h + k:4 * h + k + 1]
                    acc = ADA_ACC[:, q % 2, :]
                    if h == 0 and k == 0:
                        if q >= 2:
                            dve.e.wait_ge(pair_ready, q - 1)
                        ins = dve.e.tensor_scalar(acc, src, c, None, ALU.mult)
                    else:
                        ins = dve.e.scalar_tensor_tensor(acc, src, c, acc, ALU.mult, ALU.add)
                    if k < 3:
                        dve.link(ins)
                ins.then_inc(ada_used, 1)
                dve.wait(ada_used)
            dve.e.wait_ge(pair_ready, q + 1)
            at = col_at["ada_b"] + q * KD
            dve.e.tensor_tensor(MOD[:, q * KD:q * KD + KD], PAIR[q % 2][:, 0, 0:KD], COLS[:, at:at + KD], ALU.add)\
                 .then_inc(evac[q % 2], 1)
        dve.e.wait_ge(evac[0], 6)
        dve.e.wait_ge(evac[1], 6)
        for n in range(4):
            layer, which = n // 2, n % 2
            at, w = (layer * 6 + 1 + 3 * which) * KD, col_at[("norm1", "norm2")[which]] + layer * KD
            dve.e.scalar_tensor_tensor(GAIN[:, n, :], MOD[:, at:at + KD], 1.0, COLS[:, w:w + KD], ALU.add, ALU.mult)\
                 .then_inc(mod_ready, 1)
        dve.wait(strip_landed, 16)
        dve.e.memset(STRIP[0:HD, :, SEQ - HD:SEQ], NEG).then_inc(strip_ready, 1)
        dve.wait(mod_ready, 4)

    norm_gain = {0: lambda k: GAIN[:, 0, k:k + 1], 1: lambda k: GAIN[:, 1, k:k + 1], 2: lambda k: GAIN[:, 2, k:k + 1],
                 3: lambda k: GAIN[:, 3, k:k + 1], 4: lambda k: col("final", k), 5: lambda k: col("norm_mix", k),
                 6: lambda k: col("norm_ffn", k), 7: lambda k: 1.0, 8: lambda k: col("norm_mix", KD + k),
                 9: lambda k: col("norm_ffn", KD + k), 10: lambda k: 1.0}
    norm_shift = {0: (0, 0), 1: (0, 3), 2: (1, 0), 3: (1, 3)}
    FINAL, PLAIN = 4, 8

    def pe_norm(pe, n):
        bank = take_bank(pe, plan.b[f"norm{n}"])
        for k in range(KD):
            pe.wait(sq_ready)
            ins = nc.tensor.matmul(bank[:], ONES[:], SQ[:, k % 2, :], start=k == 0, stop=k == KD - 1)
            if k < KD - 1:
                ins.then_inc(sq_used, 1)
        ins.then_inc(bank_ready, 1)

    def act_root(act, tile, ready):
        act.wait(ready)
        act.e.activation(tile, tile, ACT.Sqrt).then_inc(root_ready, 1)

    def residual_pairs(n):
        last = plan.p[f"norm{n}"]
        if n in (1, 2, 3, 4, 6, 7, 10):
            return [last - 4 + k // 2 for k in range(KD)]
        return [last - 1] * KD

    def norm_buffer(k):
        return (TMP, SQ)[k // 2 % 2][:, k % 2, :]

    def act_norm(act, n):
        pairs = residual_pairs(n)
        if n == 0:
            b = plan.b["load"] + KD - 1
            act.e.wait_ge(bank_free[b % 4], b // 4 + 1)
        if n == FINAL + 1:
            act.wait(x_ready)
        for k in range(KD):
            if k == 0 or pairs[k] != pairs[k - 1]:
                for p in (pairs[k] - 1, pairs[k]):
                    act.e.wait_ge(evac[p % 2], p // 2 + 1)
            if k >= 2:
                act.wait(sq_used)
            act.e.activation(SQ[:, k % 2, :], X[:, k, :], ACT.Square).then_inc(sq_ready, 1)
        act.wait(sq_used)
        act_root(act, RSTD[:], var_ready)
        if n in (FINAL, PLAIN):
            return
        for k in range(KD):
            act.wait(norm_pre)
            act.e.activation(HH[:, k, :], norm_buffer(k), ACT.Copy).then_inc(norm_hi, 1)

    def pool_norm(pool):
        for k in range(KD):
            pool.wait(norm_hi)
            pool.e.tensor_tensor(HL[:, k, :], norm_buffer(k), HH[:, k, :].bitcast(F32), ALU.subtract).then_inc(h_ready, 1)

    def dve_rstd(dve, total, tile, count):
        ins = dve.e.tensor_scalar(tile, total, 1.0 / count, EPS, ALU.mult, ALU.add)
        ins.then_inc(var_ready, 1)
        dve.wait(root_ready)
        dve.link(dve.e.reciprocal(tile, tile))

    def dve_norm(dve, n):
        b = plan.b[f"norm{n}"]
        bank = full_bank(dve, b)
        dve.e.tensor_scalar(RSTD[:], bank[:], 1.0 / D, EPS, ALU.mult, ALU.add).then_inc(var_ready, 1)
        dve.wait(root_ready)
        dve.e.reciprocal(RSTD[:], RSTD[:]).then_inc(bank_free[b % 4], 1)
        dve.e.wait_ge(bank_free[b % 4], b // 4 + 1)
        gain = norm_gain[n]
        if n in (FINAL, PLAIN):
            to = X if n == FINAL else HF
            for k in range(KD):
                ins = dve.e.scalar_tensor_tensor(to[:, k, :], X[:, k, :], gain(k), RSTD[:], ALU.mult, ALU.mult)
            ins.then_inc(x_ready if n == FINAL else h_ready, 1)
            dve.passed(x_ready if n == FINAL else h_ready, 1)
            return

        def scale(k):
            if k >= 4:
                dve.wait(h_ready)
            if n in norm_shift:
                dve.e.tensor_tensor(norm_buffer(k), X[:, k, :], RSTD[:], ALU.mult).then_inc(dve.chain, 1)
            else:
                dve.e.scalar_tensor_tensor(norm_buffer(k), X[:, k, :], gain(k), RSTD[:], ALU.mult, ALU.mult).then_inc(norm_pre, 1)

        scale(0)
        for k in range(KD):
            if k + 1 < KD:
                scale(k + 1)
            if n in norm_shift:
                dve.wait(dve.chain)
                dve.e.tensor_scalar(norm_buffer(k), norm_buffer(k), gain(k), mod(*norm_shift[n], k), ALU.mult, ALU.add)\
                     .then_inc(norm_pre, 1)
        dve.passed(h_ready, 4)

    def dve_residual(dve, name, n, units_per_pair, gate):
        for i in range(n):
            p = plan.p[name] + i
            pair = full_pair(dve, plan.u[name] + (i + 1) * units_per_pair - 1, p)
            c = 2 * (i % 4)
            if gate is None:
                dve.e.tensor_tensor(X[:, c:c + 2, :], pair[:], X[:, c:c + 2, :], ALU.add).then_inc(evac[p % 2], 1)
            else:
                for m in range(2):
                    ins = dve.e.scalar_tensor_tensor(X[:, c + m, :], pair[:, m, :], mod(*gate, c + m), X[:, c + m, :],
                                                     ALU.mult, ALU.add)
                ins.then_inc(evac[p % 2], 1)

    def pe_matrix(pe, name, n, first=0):
        for i in range(first, n):
            unit_channels(pe, plan.u[name] + i, take_pair(pe, plan.p[name] + i), hh, hl, KD)

    def pe_mixin(pe):
        first_unit(pe, plan.u["mixin"], take_pair(pe, plan.p["mixin"]), pe.seen(h_ready))
        pe.passed(h_ready, KD)
        pe_matrix(pe, "mixin", 6, 1)
        for i in range(6, 8):
            unit_tokens(pe, plan.u["mixin"] + i, take_pair(pe, plan.p["mixin"] + i))

    def act_copy_pairs(act, name, first, n, to, tokens, func=ACT.Copy):
        for i in range(n):
            u, p = plan.u[name] + first + i, plan.p[name] + first + i
            pair = full_pair(act, u, p)
            if tokens:
                ins = act.e.activation(to[:, :, i * 256:i * 256 + 256],
                                       pair[:].rearrange("p b (j n) -> p (b j) n", n=256), func)
            else:
                ins = act.e.activation(to[:, 2 * i:2 * i + 2, :], pair[:], func)
            ins.then_inc(evac[p % 2], 1)

    def act_mixin(act):
        act.e.dma_start(POOL_W[:], t["pool_w"][0].rearrange("g c d -> c g d")).then_inc(pool_w_landed, 16)
        act_copy_pairs(act, "mixin", 0, 2, U, False)
        act_copy_pairs(act, "mixin", 2, 2, Q0, False)
        act_copy_pairs(act, "mixin", 4, 2, K0, False)
        act_copy_pairs(act, "mixin", 6, 2, V0, True)

    pool_w_landed = sem("pool_w_landed")
    pooled_ready = sem("pooled_ready")

    def dve_pool_window(dve, g):
        u, w = U[:, g, :], 2 << g
        if g % 2 == 0:
            p = plan.p["mixin"] + g // 2
            dve.e.wait_ge(evac[p % 2], p // 2 + 1)
        cur = u
        for level in range(g + 1):
            sh, new = 1 << level, PSCR[:, level % 2, :]
            dve.e.tensor_tensor(new[:, sh:], cur[:, sh:], cur[:, :SEQ - sh], ALU.add)
            dve.link(dve.e.tensor_copy(new[:, :sh], cur[:, :sh]))
            cur = new
        dve.e.scalar_tensor_tensor(POOLED[:, g, w:], cur[:, w:], 1.0 / w, u[:, w:], ALU.mult, ALU.subtract)
        dve.link(dve.e.tensor_tensor(POOLED[:, g, :w], cur[:, :w], INV_COUNT[:, :w], ALU.mult))
        dve.e.tensor_tensor(POOLED[:, g, :w], POOLED[:, g, :w], u[:, :w], ALU.subtract).then_inc(pooled_ready, 1)

    def pe_pool(pe):
        pe.e.wait_ge(pool_w_landed, 16)
        for g in range(4):
            pe.wait(pooled_ready)
            bank = take_bank(pe, plan.b["pool"] + g)
            nc.tensor.matmul(bank[:], POOL_W[:, g, :], POOLED[:, g, :], start=True, stop=True).then_inc(bank_ready, 1)

    def dve_pool(dve):
        for g in range(4):
            dve_pool_window(dve, g)
        dve.e.wait_ge(unit_done, plan.u["mixin"] + 8)
        for g in range(4):
            b = plan.b["pool"] + g
            if g >= 2:
                dve.e.wait_ge(bank_free[(b - 2) % 4], (b - 2) // 4 + 1)
            dve.e.tensor_scalar(TMP[:, g % 2, :], full_bank(dve, b)[:], col("pool_scale", g), None, ALU.mult)\
                 .then_inc(pre_ready, 1)
            dve.wait(pre_ready)
            dve.wait(hi_ready)
            dve.e.tensor_tensor(HL[:, g, :], TMP[:, g % 2, :], HH[:, g, :].bitcast(F32), ALU.subtract)\
                 .then_inc(bank_free[b % 4], 1)

    def act_pool(act):
        for g in range(4):
            act.wait(pre_ready)
            act.e.activation(HH[:, g, :], TMP[:, g % 2, :], ACT.Copy).then_inc(hi_ready, 1)

    SEG = [0, P, 3 * P, 6 * P]
    HOME = {3: (0, 0), 2: (1, 0), 0: (1, 3 * P), 1: (2, 0)}
    PT_HOME = {0: (0, 0), 1: (1, 0), 3: (1, 3 * P), 2: (2, 0)}
    att_sems = [{s: sem(f"att{n}_{s}") for s in ("scaled", "exp", "probs", "out")} for n in range(2)]

    def att_bank(n, h, turned, i):
        if turned:
            at = 3 + 6 * h + 3 if h + 1 < HEADS else 3 + 6 * h
        else:
            at = 6 * h - 3 if h else 0
        return plan.b[f"att{n}"] + at + i

    def pe_attention(pe, n, q, k, v, s, pt, fox):
        w = att_sems[n]

        def scores(h):
            a, tile = (h % 2) * HD, h // 2
            for i in range(3):
                b = att_bank(n, h, False, i)
                bank = take_bank(pe, b)
                mine = [j for j in HOME if HOME[j][0] == i]
                for j in mine:
                    at, wide = HOME[j][1], P * (j + 1)
                    ins = nc.tensor.matmul(bank[:, at:at + wide], q[a:a + HD, tile, j * P:j * P + P],
                                           k[a:a + HD, tile, 0:wide], start=True, stop=not fox)
                    if fox:
                        ins = nc.tensor.matmul(bank[:, at:at + wide], MINUS_HEAD[:, h, :], FCUM[:, 1, 0:wide],
                                               start=False, stop=True)
                ins.then_inc(bank_ready, 1)

        scores(0)
        for h in range(HEADS):
            if h + 1 < HEADS:
                scores(h + 1)
            pe.wait(w["probs"])
            for i in range(3):
                bank = take_bank(pe, att_bank(n, h, True, i))
                for kt in [x for x in PT_HOME if PT_HOME[x][0] == i]:
                    for j in range(kt, NT):
                        at = PT_HOME[kt][1] + (j - kt) * P
                        ins = nc.tensor.transpose(bank[:, at:at + P], s[:, h % 2, SEG[j] + kt * P:SEG[j] + kt * P + P],
                                                  IDENT[:])
                ins.then_inc(bank_ready, 1)
            p = plan.p[f"att{n}"] + h // 2
            if h % 2 == 0:
                pair = take_pair(pe, p)
            b = att_bank(n, h, True, 2)
            pe.e.wait_ge(bank_free[b % 4], b // 4 + 1)
            a = (h % 2) * HD
            for kt in range(NT):
                ins = nc.tensor.matmul(pair[a:a + HD, 0, kt * P:SEQ], v[:, kt, h * HD:h * HD + HD],
                                       pt[:, h % 2, TRI_AT[kt]:TRI_AT[kt] + SEQ - kt * P],
                                       start=kt == 0, stop=kt == NT - 1)
            ins.then_inc(w["out"], 1)

    def dve_attention(dve, n, s, bias):
        w = att_sems[n]

        def scale(h):
            for i in range(3):
                b = att_bank(n, h, False, i)
                bank = full_bank(dve, b)
                for j in [x for x in HOME if HOME[x][0] == i]:
                    at, wide = HOME[j][1], P * (j + 1)
                    ins = dve.e.scalar_tensor_tensor(s[:, h % 2, SEG[j]:SEG[j] + wide], bank[:, at:at + wide],
                                                     HD ** -0.5, bias(h)[:, SEQ - wide:SEQ], ALU.mult, ALU.add)
                ins.then_inc(bank_free[b % 4], 1)
            dve.e.wait_ge(bank_free[b % 4], b // 4 + 1)
            for j in range(NT):
                ins = dve.e.tensor_reduce(MX[:, h % 2, 0, j:j + 1], s[:, h % 2, SEG[j]:SEG[j] + P * (j + 1)], AX.X, ALU.max)
            dve.link(ins)
            dve.e.tensor_scalar(MX[:, h % 2, 1, :], MX[:, h % 2, 0, :], -1.0, None, ALU.mult).then_inc(w["scaled"], 1)

        def normalise(h):
            dve.wait(w["exp"])
            dve.link(dve.e.reciprocal(SUMS[:, h % 2, :], SUMS[:, h % 2, :]))
            for j in range(NT):
                seg = s[:, h % 2, SEG[j]:SEG[j] + P * (j + 1)]
                ins = dve.e.tensor_scalar(seg, seg, SUMS[:, h % 2, j:j + 1], None, ALU.mult)
            ins.then_inc(w["probs"], 1)

        def rest(i):
            p = plan.p[f"att{n}"] + i
            dve.wait(hi_ready)
            dve.e.tensor_tensor(HL[:, 4 + i, :], PAIR[p % 2][:, 0, :], HH[:, 4 + i, :].bitcast(F32),
                                ALU.subtract).then_inc(evac[p % 2], 1)

        scale(0)
        for h in range(HEADS):
            if h + 1 < HEADS:
                scale(h + 1)
            normalise(h)
            if h % 2 == 0 and h:
                rest(h // 2 - 1)
        rest(HEADS // 2 - 1)

    def act_attention(act, n, s, pt):
        w = att_sems[n]

        def exponential(h):
            act.wait(w["scaled"])
            for j in range(NT):
                seg = s[:, h % 2, SEG[j]:SEG[j] + P * (j + 1)]
                ins = act.e.activation(seg, seg, ACT.Exp, bias=MX[:, h % 2, 1, j:j + 1], accum_out=SUMS[:, h % 2, j:j + 1])
            ins.then_inc(w["exp"], 1)

        def high(i):
            p = plan.p[f"att{n}"] + i
            act.wait(w["out"], 2)
            act.e.activation(HH[:, 4 + i, :], PAIR[p % 2][:, 0, :], ACT.Copy).then_inc(hi_ready, 1)

        exponential(0)
        for h in range(HEADS):
            if h + 1 < HEADS:
                exponential(h + 1)
            if h % 2 == 0 and h:
                high(h // 2 - 1)
            for i in range(3):
                b = att_bank(n, h, True, i)
                bank = full_bank(act, b)
                tiles = [x for x in PT_HOME if PT_HOME[x][0] == i]
                for kt in tiles:
                    at, wide = PT_HOME[kt][1], SEQ - kt * P
                    ins = act.e.activation(pt[:, h % 2, TRI_AT[kt]:TRI_AT[kt] + wide], bank[:, at:at + wide], ACT.Copy)
                ins.then_inc(bank_free[b % 4], 1)
        high(HEADS // 2 - 1)

    def pe_after_h(pe, pairs):
        for s in range(2):
            pe.e.wait_ge(evac[s], pairs // 2)

    moe_sems = {s: sem(f"moe_{s}") for s in ("exp_in", "exp_out", "consts", "mask", "shares", "position", "experts", "listed",
                                             "list_landed", "index", "saved", "rows_hi", "silu", "hidden_hi", "w2_hi",
                                             "w2_ready", "summed", "rows", "down", "combined",
                                             "y_turned")}
    gathered = [sem("gathered0"), sem("gathered1")]
    scattered = [sem("scattered0"), sem("scattered1")]
    y_landed = [sem("y_landed0"), sem("y_landed1")]
    w2_landed = [sem("w2_landed0"), sem("w2_landed1")]

    narrow_ready = sem("narrow_ready")

    def dve_cut_narrow(dve, wh, wl, w):
        dve.link(dve.e.tensor_copy(wh, w))
        dve.e.tensor_tensor(wl, w, wh.bitcast(F32), ALU.subtract).then_inc(narrow_ready, 1)

    def pe_logits(pe, b, wh, wl, n, fresh):
        pe.wait(narrow_ready)
        bank = take_bank(pe, b)
        for k in range(KD):
            if fresh:
                pe.wait(h_ready)
            ins = mm3(bank[0:n, :], wh[:, k, :], wl[:, k, :], HH[:, k, :], HL[:, k, :], k == 0, k == KD - 1)
        ins.then_inc(bank_ready, 1)
        pe.e.wait_ge(bank_free[b % 4], b // 4 + 1)
        bank = take_bank(pe, b + 1)
        for tt in range(NT):
            ins = nc.tensor.transpose(bank[:, tt * n:tt * n + n], RSTD[0:n, tt * P:tt * P + P], IDENT[0:n, 0:n])
        ins.then_inc(bank_ready, 1)

    def dve_logits(dve, b, n):
        bank = full_bank(dve, b)
        dve.e.tensor_copy(RSTD[0:n, :], bank[0:n, :]).then_inc(bank_free[b % 4], 1)
        return full_bank(dve, b + 1)[:, 0:NT * n].rearrange("p (t n) -> p t n", n=n)

    def dve_first_max(dve, values, best, mark, scratch, n):
        dve.link(dve.e.tensor_reduce(best, values, AX.X, ALU.max))
        dve.link(dve.e.tensor_tensor(scratch, values, bcast(best, 2, n), ALU.is_equal))
        dve.link(dve.e.tensor_tensor(scratch, scratch, bcast(FALLING[:, EPG - n:EPG], 1, NT), ALU.mult))
        first = GATE[:, 11, :, 0]
        dve.link(dve.e.tensor_reduce(first, scratch, AX.X, ALU.max))
        dve.link(dve.e.tensor_tensor(mark, scratch, bcast(first, 2, n), ALU.is_equal))

    def dve_router(dve, layer):
        w = moe_sems
        b = plan.b[f"moe{layer}"]
        logits = dve_logits(dve, b, GROUPS + EXPERTS)
        b += 1
        dve.e.tensor_tensor(LOGIT[:], logits, bcast(ROUTER_B[:, layer, :], 1, NT), ALU.add).then_inc(bank_free[b % 4], 1)
        dve.e.wait_ge(bank_free[b % 4], b // 4 + 1)
        gl = LOGIT[:, :, 0:GROUPS]
        group, e1, e2, scratch = GATE[:, 0, :, 0:GROUPS], GATE[:, 1], GATE[:, 2], GATE[:, 3]
        gmax, top1, top2 = GATE[:, 4, :, 0], GATE[:, 4, :, 1], GATE[:, 4, :, 2]
        gprob = GATE[:, 4, :, 3]
        es, es2 = GATE[:, 5], GATE[:, 6]
        expo = GATE[:, 7]
        dve_first_max(dve, gl, gmax, group, scratch[:, :, 0:GROUPS], GROUPS)
        dve.e.tensor_tensor(expo[:, :, 0:GROUPS], gl, bcast(gmax, 2, GROUPS), ALU.subtract)
        dve.link(dve.e.tensor_tensor(ESEL[:], LOGIT[:, :, GROUPS:].rearrange("p t (g e) -> p t g e", e=EPG),
                                     bcast(group, 3, EPG), ALU.mult))
        dve.link(dve.e.tensor_reduce(es, ESEL[:].rearrange("p t g e -> p t e g"), AX.X, ALU.add))
        dve_first_max(dve, es, top1, e1, scratch, EPG)
        dve.link(dve.e.scalar_tensor_tensor(es2, e1, 2 * NEG, es, ALU.mult, ALU.add))
        dve_first_max(dve, es2, top2, e2, scratch, EPG)
        dve.e.tensor_tensor(expo[:, :, GROUPS], top2, top1, ALU.subtract).then_inc(w["exp_in"], 1)
        for r, e in enumerate((e1, e2)):
            ins = dve.e.tensor_tensor(MASK[:, r].rearrange("p t (g e) -> p t g e", e=EPG), bcast(e, 2, GROUPS),
                                      bcast(group, 3, EPG), ALU.mult)
        dve.link(ins)
        dve.e.tensor_tensor(BOTH[:], MASK[:, 0], MASK[:, 1], ALU.add).then_inc(w["mask"], 1)
        dve.wait(w["exp_out"])
        dve.e.tensor_reduce(gprob, expo[:, :, 0:GROUPS], AX.X, ALU.add)
        dve.link(dve.e.tensor_scalar(SHARE[:, 0, :], expo[:, :, GROUPS], 1.0, None, ALU.add))
        dve.link(dve.e.tensor_tensor(SHARE[:, 0, :], SHARE[:, 0, :], gprob, ALU.mult))
        dve.link(dve.e.reciprocal(SHARE[:, 0, :], SHARE[:, 0, :]))
        dve.link(dve.e.tensor_tensor(SHARE[:, 1, :], SHARE[:, 0, :], expo[:, :, GROUPS], ALU.mult))
        b += 1
        bank = full_bank(dve, b)
        total = bank[:, NT * EXPERTS:(NT + 1) * EXPERTS]
        n, end, base = PLACE[:, 0, :], PLACE[:, 1, :], PLACE[:, 2, :]
        dve.link(dve.e.tensor_scalar(n, total, 0.5, None, ALU.is_gt))
        for i in range(1, NT):
            dve.link(dve.e.scalar_tensor_tensor(n, total, i * P + 0.5, n, ALU.is_gt, ALU.add))
        dve.link(dve.e.tensor_tensor_scan(end, ONES[:, 0:1].broadcast_to([P, EXPERTS]), n, 0.0, ALU.mult, ALU.add))
        dve.link(dve.e.tensor_tensor(base, end, n, ALU.subtract))
        dve.link(dve.e.tensor_scalar(base, base, float(P), None, ALU.mult))
        place = bank[:, 0:NT * EXPERTS].rearrange("p (t e) -> p t e", e=EXPERTS)
        dve.e.tensor_tensor(BOTH[:], place, bcast(base, 1, NT), ALU.add).then_inc(bank_free[b % 4], 1)
        dve.e.wait_ge(bank_free[b % 4], b // 4 + 1)
        dve.link(dve.e.tensor_tensor(MASK[:], MASK[:], bcast(BOTH[:], 1, 2), ALU.mult))
        dve.link(dve.e.tensor_reduce(POS[:], MASK[:], AX.X, ALU.add))
        dve.e.tensor_copy(POS_I[:], POS[:]).then_inc(w["position"], 1)
        dve.wait(w["consts"])
        dve.link(dve.e.tensor_tensor(OWNER[:], bcast(end, 1, SLOTS), bcast(SLOT_AT[:], 2, EXPERTS), ALU.is_le))
        dve.link(dve.e.tensor_reduce(SLOT_E[:], OWNER[:], AX.X, ALU.add))
        dve.e.tensor_scalar(SLOT_I[:], SLOT_E[:], float(EXPERTS - 1), None, ALU.min).then_inc(w["experts"], 1)
        b += 1
        v = full_bank(dve, b)[:, 0:SLOTS]
        dve.wait(w["experts"])
        dve.link(dve.e.tensor_scalar(SLOT_E[:], v, SEQ - 0.5, float(SEQ), ALU.is_gt, ALU.mult))
        dve.link(dve.e.tensor_tensor(GATHER_I[:], v, SLOT_E[:], ALU.subtract))
        dve.e.tensor_copy(SCATTER_I[:], v).then_inc(bank_free[b % 4], 1)

    def pe_router(pe, layer):
        w, b, p0 = moe_sems, plan.b[f"moe{layer}"], plan.p[f"moe{layer}"]
        pe_logits(pe, b, ROUTER_WH, ROUTER_WL, GROUPS + EXPERTS, True)
        for tt in range(NT):
            pair = take_pair(pe, p0 + tt)
            for k in range(KD):
                o = pair[:, k // 4, (k % 4) * P:(k % 4) * P + P]
                nc.tensor.matmul(o, HH[:, k, tt * P:tt * P + P], IDENT_R[:], start=True, stop=False)
                ins = nc.tensor.matmul(o, HL[:, k, tt * P:tt * P + P], IDENT_R[:], start=False, stop=True)
            ins.then_inc(w["summed"], 1)
        pe.wait(w["mask"])
        bank = take_bank(pe, b + 2)
        for tt in range(NT + 1):
            o = bank[:, tt * EXPERTS:(tt + 1) * EXPERTS]
            before = range(min(tt, NT))
            for t0 in before:
                ins = nc.tensor.matmul(o, ONES[:], BOTH[:, t0, :], start=t0 == 0, stop=tt == NT and t0 == NT - 1)
            if tt < NT:
                ins = nc.tensor.matmul(o, STRICT[:], BOTH[:, tt, :], start=tt == 0, stop=True)
        ins.then_inc(bank_ready, 1)
        pe.wait(w["list_landed"], 16)
        bank = take_bank(pe, b + 3)
        nc.tensor.transpose(bank[:, 0:SLOTS], LIST[:], IDENT[0:SLOTS, 0:SLOTS]).then_inc(bank_ready, 1)

    def dve_router_weights(dve, layer):
        if layer == 0:
            dve.e.wait_ge(small_landed, 16 * n_small[0])
        dve.e.tensor_copy(IDENT_R[:], IDENT[:])
        dve.e.tensor_tensor(STRICT[:], LATER[:, 0:P], IDENT[:], ALU.subtract)
        dve_cut_narrow(dve, ROUTER_WH[:], ROUTER_WL[:], ROUTER_W[:, layer])

    def act_router(act, layer):
        w, p0 = moe_sems, plan.p[f"moe{layer}"]
        act.wait(w["exp_in"])
        expo = GATE[:, 7, :, 0:GROUPS + 1]
        act.e.activation(expo, expo, ACT.Exp).then_inc(w["exp_out"], 1)
        for tt in range(NT):
            act.wait(w["summed"])
            p = p0 + tt
            act.e.activation(HTOK[:, tt, :].rearrange("p (b n) -> p b n", b=2), PAIR[p % 2][:], ACT.Copy).then_inc(evac[p % 2], 1)
            act.e.wait_ge(evac[p % 2], p // 2 + 1)
            act.e.dma_start(htok_dram[tt * P:tt * P + P, :], HTOK[:, tt, :]).then_inc(w["saved"], 16)
        act.wait(w["listed"], 8 * 16)
        act.e.dma_start(LIST[:], list_dram[layer].rearrange("(s p) a -> s (p a)", p=P)).then_inc(w["list_landed"], 16)

    def rows_pair(layer, s):
        return plan.p[f"moe{layer}"] + NT + 2 * s

    def slot_bank(layer, s, turned):
        return plan.b[f"moe{layer}"] + 4 + 2 * s + turned

    def slot_loop(eng, first, step, per):
        first()
        step(None, 0)
        with eng.loop(SLOTS // 2 - 1, per) as e:
            for s in (1, 2):
                step(e, s)
        step(None, SLOTS - 1)
        step(None, SLOTS)

    def stage(e, s, behind=0):
        return e is not None or 0 <= s - behind < SLOTS

    def pe_moe(pe, layer):
        w, u0 = moe_sems, plan.u[f"moe{layer}"]

        rows_of = lambda s: XG[:, s % 2, :].rearrange("p (c k) -> p c k", k=KD)

        def rows(e, s):
            pe.wait(gathered[s % 2], 16)
            pair = take_pair(pe, rows_pair(layer, s), turns(e, 2))
            for k in range(KD):
                ins = nc.tensor.transpose(pair[:, k // 4, (k % 4) * P:(k % 4) * P + P], rows_of(s)[:, :, k], IDENT[:])
            ins.then_inc(w["rows"], 1)

        def up(e, s):
            p, u, bank = rows_pair(layer, s), u0 + s, take_bank(pe, slot_bank(layer, s, 0), turns(e, 1))
            pe.e.wait_ge(evac[p % 2], turns(e, 2) + (p // 2 + 1))
            pe.e.wait_ge(split_ready, turns(e, 2) + (u + 1))
            for k in range(KD):
                wh, wl = (a[:, u % 2].rearrange("p (m k n) -> p k m n", m=2, k=KD)[:, k] for a in (WH, WL))
                ins = mm3(bank[:, 0:256].rearrange("p (m n) -> p m n", m=2), GH[:, s % 2, k, :], GL[:, s % 2, k, :], wh, wl,
                          k == 0, k == KD - 1)
            ins.then_inc(unit_done, 1)

        def turn(e, s):
            b = slot_bank(layer, s, 0)
            pe.e.wait_ge(bank_free[b % 4], turns(e, 1) + (b // 4 + 1))
            bank = take_bank(pe, b + 1, turns(e, 1))
            nc.tensor.transpose(bank[:, 0:P], HID[:, s % 2, :], IDENT[:]).then_inc(bank_ready, 2)

        def down(e, s):
            b, p = slot_bank(layer, s, 1), rows_pair(layer, s) + 1
            pair = take_pair(pe, p, turns(e, 2))
            pe.e.wait_ge(bank_free[b % 4], turns(e, 1) + (b // 4 + 1))
            pe.wait(w["w2_ready"])
            for m in range(2):
                c = slice(m * SEQ, m * SEQ + SEQ)
                ins = mm3(pair[:, m, :], HTH[:, s % 2, :], HTL[:, s % 2, :], W2H[:, s % 2, c], W2L[:, s % 2, c], True, True)
            ins.then_inc(w["down"], 1)

        def step(e, s):
            if stage(e, s, -1):
                rows(e, s + 1)
            if stage(e, s, 1):
                turn(e, s - 1)
            if stage(e, s):
                up(e, s)
            if stage(e, s, 1):
                down(e, s - 1)

        slot_loop(pe, lambda: rows(None, 0), step, {gathered[0]: 16, gathered[1]: 16, w["w2_ready"]: 2})
        for tt in range(NT):
            pe.wait(w["combined"])
        for i in range(4):
            pair = take_pair(pe, rows_pair(layer, SLOTS) + i)
            for m in range(2):
                for tt in range(NT):
                    c = (2 * i + m) * P
                    ins = nc.tensor.transpose(pair[:, m, tt * P:tt * P + P], HTOK[:, tt, c:c + P], IDENT[:])
            ins.then_inc(w["y_turned"], 1)

    def act_moe(act, layer):
        w, u0 = moe_sems, plan.u[f"moe{layer}"]

        def rows(e, s):
            act.wait(w["rows"])
            act.e.activation(GH[:, s % 2].rearrange("p (b k) n -> p b (k n)", b=2), PAIR[rows_pair(layer, s) % 2][:], ACT.Copy)\
                 .then_inc(w["rows_hi"], 1)

        def turned(e, s):
            bank = full_bank(act, slot_bank(layer, s, 1), turns(e, 1))
            act.e.activation(HTH[:, s % 2, :], bank[:, 0:P], ACT.Copy).then_inc(w["hidden_hi"], 1)

        def weights(e, s):
            u = u0 + s
            act.e.wait_ge(landed[u % 2], turns(e, 32) + 32 * (u // 2 + 1))
            act.e.wait_ge(unit_done, turns(e, 2) + (u - 1))
            act.e.activation(WH[:, u % 2], RAW[:, u % 2], ACT.Copy).then_inc(split_hi, 1)

        def hidden(e, s):
            bank = BANK[slot_bank(layer, s, 0) % 4]
            act.e.wait_ge(unit_done, turns(e, 2) + (u0 + s + 1))
            act.e.activation(HS[:, s % 2, :], bank[:, 0:P], ACT.Silu).then_inc(w["silu"], 1)

        def first():
            weights(None, 0)
            rows(None, 0)

        def step(e, s):
            if stage(e, s, -1):
                rows(e, s + 1)
            if stage(e, s, 1):
                turned(e, s - 1)
            if stage(e, s, -1):
                weights(e, s + 1)
            if stage(e, s):
                hidden(e, s)

        slot_loop(act, first, step, {w["rows"]: 2})
        for c in range(2):
            act.e.wait_ge(scattered[c], 16 * (SLOTS // 2) * (layer + 1))
        for tt in range(NT):
            to = (XG, OG)[tt % 2]
            if tt >= 2:
                act.e.wait_ge(w["combined"], 4 * layer + tt - 1)
            for r in range(2):
                row = r * SEQ + tt * P
                act.e.dma_start(to[:, r, :], y_dram[row:row + P, :]).then_inc(y_landed[tt % 2], 16)

    def dve_moe(dve, layer):
        w, u0 = moe_sems, plan.u[f"moe{layer}"]

        def rows(e, s):
            p = rows_pair(layer, s)
            dve.wait(w["rows_hi"])
            dve.e.tensor_tensor(GL[:, s % 2].rearrange("p (b k) n -> p b (k n)", b=2), PAIR[p % 2][:],
                                GH[:, s % 2].rearrange("p (b k) n -> p b (k n)", b=2).bitcast(F32), ALU.subtract).then_inc(evac[p % 2], 1)

        def turned(e, s):
            b = slot_bank(layer, s, 1)
            dve.wait(w["hidden_hi"])
            dve.e.tensor_tensor(HTL[:, s % 2, :], BANK[b % 4][:, 0:P], HTH[:, s % 2, :].bitcast(F32), ALU.subtract)\
                 .then_inc(bank_free[b % 4], 1)

        def weights(e, s):
            u = u0 + s
            dve.e.wait_ge(split_hi, turns(e, 2) + (u + 1))
            dve.e.tensor_tensor(WL[:, u % 2], RAW[:, u % 2], WH[:, u % 2].bitcast(F32), ALU.subtract).then_inc(split_ready, 1)

        def hidden(e, s):
            b = slot_bank(layer, s, 0)
            dve.wait(w["silu"])
            dve.e.tensor_tensor(HID[:, s % 2, :], HS[:, s % 2, :], BANK[b % 4][:, P:2 * P], ALU.mult).then_inc(bank_free[b % 4], 1)

        def output(e, s):
            p = rows_pair(layer, s) + 1
            dve.wait(w["down"])
            if e is not None or s >= 2:
                dve.e.wait_ge(scattered[s % 2], turns(e, 16) + 16 * (SLOTS // 2 * layer + s // 2))
            dve.e.tensor_copy(OG[:, s % 2, :].rearrange("p (b n) -> p b n", b=2), PAIR[p % 2][:]).then_inc(evac[p % 2], 1)

        def first():
            weights(None, 0)
            rows(None, 0)

        def step(e, s):
            if stage(e, s, -1):
                rows(e, s + 1)
            if stage(e, s, 1):
                turned(e, s - 1)
            if stage(e, s, -1):
                weights(e, s + 1)
            if stage(e, s):
                hidden(e, s)
            if stage(e, s, 1):
                output(e, s - 1)

        slot_loop(dve, first, step, {w["rows_hi"]: 2, w["hidden_hi"]: 2, w["silu"]: 2, w["down"]: 2})
        for tt in range(NT):
            src = (XG, OG)[tt % 2]
            dve.wait(y_landed[tt % 2], 32)
            dve.link(dve.e.tensor_scalar(HTOK[:, tt, :], src[:, 0, :], SHARE[:, 0, tt:tt + 1], None, ALU.mult))
            dve.e.scalar_tensor_tensor(HTOK[:, tt, :], src[:, 1, :], SHARE[:, 1, tt:tt + 1], HTOK[:, tt, :], ALU.mult, ALU.add)\
                 .then_inc(w["combined"], 1)
        for i in range(4):
            p = rows_pair(layer, SLOTS) + i
            dve.wait(w["y_turned"])
            for m in range(2):
                c = 2 * i + m
                ins = dve.e.scalar_tensor_tensor(X[:, c, :], PAIR[p % 2][:, m, :], mod(layer, 5, c), X[:, c, :], ALU.mult, ALU.add)
            ins.then_inc(evac[p % 2], 1)

    def pool_moe(pool, layer):
        w = moe_sems
        pool.e.memset(XG[:], 0.0)
        pool.e.iota(SLOT_AT[:], [[1, SLOTS]], base=0, channel_multiplier=0, allow_small_or_imprecise_dtypes=True)
        pool.e.iota(ROW_AT[:], [[SEQ, 2], [P, NT]], base=0, channel_multiplier=1, allow_small_or_imprecise_dtypes=True)\
            .then_inc(w["consts"], 1)
        pool.wait(w["consts"])
        pool.wait(w["position"])
        pool.e.wait_ge(list_filled, 32)
        for r in range(2):
            for tt in range(NT):
                pool.e.indirect_dma_start(list_dram[layer], bass.IndirectOffsetOnAxis(ap=POS_I[:, r, tt:tt + 1], axis=0),
                                          ROW_AT[:, r, tt:tt + 1], None).then_inc(w["listed"], 16)
        b = plan.b[f"moe{layer}"] + 3
        pool.e.wait_ge(bank_free[b % 4], b // 4 + 1)
        pool.wait(w["saved"], 16 * NT)

        def gather(s):
            if s >= 2:
                p = rows_pair(layer, s - 2)
                pool.e.wait_ge(evac[p % 2], p // 2 + 1)
            pool.e.indirect_dma_start(XG[:, s % 2, :], None, htok_dram, bass.IndirectOffsetOnAxis(ap=GATHER_I[:, s:s + 1], axis=0),
                                      bounds_check=SEQ - 1, oob_is_err=False).then_inc(gathered[s % 2], 16)

        def scatter(s):
            p = rows_pair(layer, s) + 1
            pool.e.wait_ge(evac[p % 2], p // 2 + 1)
            pool.e.indirect_dma_start(y_dram, bass.IndirectOffsetOnAxis(ap=SCATTER_I[:, s:s + 1], axis=0), OG[:, s % 2, :], None,
                                      bounds_check=2 * SEQ - 1, oob_is_err=False).then_inc(scattered[s % 2], 16)

        def weights(s):
            if s >= 2:
                p = rows_pair(layer, s - 2) + 1
                pool.e.wait_ge(evac[p % 2], p // 2 + 1)
            pool.e.wait_ge(w2_landed[s % 2], 16 * (SLOTS // 2 * layer + s // 2 + 1))
            pool.e.tensor_scalar(W2H[:, s % 2], W2RAW[:, s % 2], 1.0, 1.0, ALU.mult, ALU.mult).then_inc(w["w2_hi"], 1)
            pool.wait(w["w2_hi"])
            pool.e.tensor_tensor(W2L[:, s % 2], W2RAW[:, s % 2], W2H[:, s % 2].bitcast(F32), ALU.subtract).then_inc(w["w2_ready"], 1)

        gather(0)
        gather(1)
        for s in range(SLOTS):
            if s + 2 < SLOTS:
                gather(s + 2)
            if s >= 2:
                scatter(s - 2)
            weights(s)
        scatter(SLOTS - 2)
        scatter(SLOTS - 1)

    def sp_moe(engine, layer):
        w, sp, u0 = moe_sems, engine.e, plan.u[f"moe{layer}"]
        engine.wait(w["experts"])

        def two_slots(i, first):
            for c in range(2):
                expert = sp.value_load(SLOT_I[0:1, at(i, first + c)], min_val=0, max_val=EXPERTS - 1)
                w1, w3, w2 = (t[n][layer][bass.ds(expert, 1)].rearrange("e d f -> (e d) f") for n in ("moe_w1", "moe_w3", "moe_w2"))
                part = lambda m, wm: (wm.rearrange("(p k) n -> p (k n)", k=KD), lambda raw: raw[:, m * D:m * D + D])
                load_unit(sp, part(0, w1), part(1, w3), off=i, u=u0 + first + c)
                if layer or first:
                    sp.wait_ge(w["w2_ready"], i + (SLOTS * layer + first + c - 1))
                sp.dma_start(W2RAW[:, c, :], w2).then_inc(w2_landed[c], 16)

        two_slots(0, 0)
        with sp.Fori(0, SLOTS // 2 - 1) as i:
            two_slots(i * 2, 2)
        sp_unit[0] += SLOTS


    ssm_sems = {s: sem(f"ssm_{s}") for s in ("exp_in", "exp_out", "log_ready", "cum_ready", "cum_saved", "conv_in", "conv_ready",
                                             "decay_in", "decay_out", "masked", "first_head", "gated")}
    row_landed = [sem("decay_row_landed0"), sem("decay_row_landed1")]
    SERIES = [1 / 13, 1 / 11, 1 / 9, 1 / 7, 1 / 5, 1 / 3]

    def at(expr, n, size=1):
        return slice(n, n + size) if isinstance(expr, int) else bass.ds(expr + n, size)

    def settle(act):
        act.e.wait_ge(consts_ready, 1)

    def dve_softplus(dve, x, o, s, exp_in, exp_out, sign):
        dve.link(dve.e.tensor_scalar(s[0], x, -1.0, None, ALU.mult))
        dve.e.tensor_tensor(s[0], s[0], x, ALU.max).then_inc(exp_in, 1)
        dve.wait(exp_out)
        dve.link(dve.e.tensor_scalar(s[1], s[0], 2.0, None, ALU.add))
        dve.link(dve.e.reciprocal(s[1], s[1]))
        dve.link(dve.e.tensor_tensor(s[1], s[0], s[1], ALU.mult))
        dve.link(dve.e.tensor_tensor(s[2], s[1], s[1], ALU.mult))
        dve.link(dve.e.tensor_scalar(s[3], s[2], SERIES[0], None, ALU.mult))
        for c in SERIES[1:]:
            dve.link(dve.e.scalar_tensor_tensor(s[3], s[3], c, s[2], ALU.add, ALU.mult))
        dve.link(dve.e.scalar_tensor_tensor(s[3], s[3], 1.0, s[1], ALU.add, ALU.mult))
        dve.link(dve.e.tensor_scalar(s[0], x, 0.0, None, ALU.max if sign > 0 else ALU.min))
        dve.link(dve.e.scalar_tensor_tensor(o, s[3], 2.0 * sign, s[0], ALU.mult, ALU.add))

    def act_softplus(act, y, exp_in, exp_out):
        act.wait(exp_in)
        act.e.activation(y, y, ACT.Exp, scale=-1.0).then_inc(exp_out, 1)

    def pe_dt(pe):
        b = plan.b["dt"]
        pe_logits(pe, b, DT_WH, DT_WL, SSM_H, True)
        b += 1
        pe.wait(ssm_sems["log_ready"])
        bank = take_bank(pe, b + 1)
        for tt in range(NT):
            ins = nc.tensor.transpose(bank[0:SSM_H, tt * P:tt * P + P], DTS[:, 4, tt, :], IDENT[:])
        ins.then_inc(bank_ready, 1)
        pe.wait(ssm_sems["cum_ready"])
        bank = take_bank(pe, b + 2)
        for tt in range(NT):
            ins = nc.tensor.transpose(bank[:, tt * SSM_H:tt * SSM_H + SSM_H], ACS[:, 1, tt * P:tt * P + P],
                                      IDENT[0:SSM_H, 0:SSM_H])
        ins.then_inc(bank_ready, 1)

    def act_dt(act):
        w = ssm_sems
        act.wait(w["exp_in"])
        act.e.activation(DTS[:, 0], DTS[:, 0], ACT.Exp, scale=-1.0)
        act.e.activation(DT_ROW[:, 1, :], DT_ROW[:, 1, :], ACT.Exp).then_inc(w["exp_out"], 1)
        act.wait(w["cum_ready"])
        act.e.dma_start(acs_dram, ACS[:, 1, :]).then_inc(w["cum_saved"], 16)
        act.wait(w["cum_saved"], 16)
        for hh in range(2):
            act_decay_row(act, 0, hh)

    def act_decay_row(act, e, head):
        act.e.dma_start(ACS_ROW[:, head % 2, :], acs_dram[at(e, head), :].rearrange("a n -> (a n)").partition_broadcast(P))\
             .then_inc(row_landed[head % 2], 16)

    def dve_dt(dve):
        w, b = ssm_sems, plan.b["dt"]
        for h in range(2):
            dve.e.tensor_copy(D_COL[h * HD:h * HD + HD, :], D_ROW[h * HD:h * HD + HD, :].rearrange("p (m h) -> p h m", h=2)[:, h, :])
        logits = dve_logits(dve, b, SSM_H)
        b += 1
        dve.e.tensor_tensor(DTS[:, 5], logits, bcast(DT_ROW[:, 0, :], 1, NT), ALU.add).then_inc(bank_free[b % 4], 1)
        dve.e.wait_ge(bank_free[b % 4], b // 4 + 1)
        dve_softplus(dve, DTS[:, 5], DT[:], [DTS[:, i] for i in range(4)], w["exp_in"], w["exp_out"], 1)
        dve.e.scalar_tensor_tensor(DTS[:, 4], DT[:], -1.0, bcast(DT_ROW[:, 1, :], 1, NT), ALU.mult, ALU.mult)\
             .then_inc(w["log_ready"], 1)
        b += 1
        dve.e.tensor_copy(ACS[:, 0, :], full_bank(dve, b)[0:SSM_H, :]).then_inc(bank_free[b % 4], 1)
        dve.e.wait_ge(bank_free[b % 4], b // 4 + 1)
        dve.e.tensor_tensor_scan(ACS[:, 1, :], ONES[0:SSM_H, 0:1].broadcast_to([SSM_H, SEQ]), ACS[:, 0, :], 0.0,
                                 ALU.mult, ALU.add).then_inc(w["cum_ready"], 1)
        b += 1
        dve.link(dve.e.tensor_copy(ACS_COL[:].rearrange("p t h -> p (t h)"), full_bank(dve, b)[:, 0:NT * SSM_H]))
        dve.e.tensor_copy(RSTD[0:1, 0:1], ONES[0:1, 0:1]).then_inc(bank_free[b % 4], 1)

    def pe_ssm_units(pe, e, c):
        for j in range(3):
            p = plan.p["ssm"] + 3 * c + j
            pair = take_pair(pe, p, turns(e, 3))
            unit_channels(pe, plan.u["ssm"] + 3 * c + j, pair, hh, hl, KD, off=times(e, 6))

    def turns(e, n):
        return 0 if e is None else e * n

    times = turns

    def act_ssm_units(act, e, c):
        w, par = ssm_sems, c % 2
        u, p = plan.u["ssm"] + 3 * c, plan.p["ssm"] + 3 * c
        pair = full_pair(act, u, p, times(e, 6))
        act.e.activation(ZS[:, par], pair[:], ACT.Silu).then_inc(evac[p % 2], 1)
        for j, tiles in ((1, (2 * c, 2 * c + 1)), (2, (16 + c, 24 + c))):
            pair = full_pair(act, u + j, p + j, times(e, 6))
            settle(act)
            for m, ct in enumerate(tiles):
                step = 4 if j == 1 else 2
                wc = COLS[:, at(times(e, step), col_at["conv_w"] + 3 * 32 + ct)]
                bc = COLS[:, at(times(e, step), col_at["conv_b"] + ct)]
                act.e.activation(CONV[:, par, 2 * (j - 1) + m, :], pair[:, m, :], ACT.Identity, bias=bc, scale=wc)\
                     .then_inc(w["conv_in"], 1)
            act.e.wait_ge(evac[(p + j) % 2], turns(e, 3) + ((p + j) // 2 + 1))
            both = CONV[:, par, 2 * (j - 1):2 * j, :]
            act.e.activation(both, both, ACT.Silu).then_inc(w["conv_ready"], 1)

    def dve_ssm_units(dve, e, c):
        w, par = ssm_sems, c % 2
        for j, tiles in ((1, (2 * c, 2 * c + 1)), (2, (16 + c, 24 + c))):
            p = plan.p["ssm"] + 3 * c + j
            pair = PAIR[p % 2]
            for m, ct in enumerate(tiles):
                acc = CONV[:, par, 2 * (j - 1) + m, :]
                dve.wait(w["conv_in"])
                for sh in range(1, 4):
                    step = 4 if j == 1 else 2
                    wc = COLS[:, at(times(e, step), col_at["conv_w"] + (3 - sh) * 32 + ct)]
                    ins = dve.e.scalar_tensor_tensor(acc[:, sh:], pair[:, m, :SEQ - sh], wc, acc[:, sh:], ALU.mult, ALU.add)
                    if m == 0 or sh < 3:
                        dve.link(ins)
            ins.then_inc(evac[p % 2], 1)

    def ssm_bank(c, j):
        return plan.b["ssm"] + 8 * c + j

    CB_HOME = {0: (2, 0), 1: (3, 0), 3: (3, 384), 2: (4, 0)}

    def pe_ssm_scores(pe, e, c):
        par = c % 2
        pe.wait(ssm_sems["conv_ready"], 2)
        for m in range(2):
            bank = take_bank(pe, ssm_bank(c, m), turns(e, 4))
            for tt in range(NT):
                ins = nc.tensor.transpose(bank[:, tt * P:tt * P + P], CONV[:, par, m, tt * P:tt * P + P], IDENT[:])
            ins.then_inc(bank_ready, 1)
        for j in (2, 3, 4):
            bank = take_bank(pe, ssm_bank(c, j), turns(e, 4))
            for i in [x for x in CB_HOME if CB_HOME[x][0] == j]:
                a, wide = CB_HOME[i][1], SEQ - i * P
                ins = nc.tensor.matmul(bank[:, a:a + wide], CONV[:, par, 2, i * P:i * P + P], CONV[:, par, 3, i * P:SEQ],
                                       start=True, stop=True)
            ins.then_inc(bank_ready, 1)

    def pe_ssm_heads(pe, e, c):
        w = ssm_sems
        for hd in range(4):
            m, a = hd // 2, (hd % 2) * HD
            if hd % 2 == 0:
                bank = take_bank(pe, ssm_bank(c, 5 + m), turns(e, 4))
            pe.wait(w["masked"])
            for i in range(NT):
                ins = nc.tensor.matmul(bank[a:a + HD, i * P:SEQ], XDT[:, i, hd * HD:hd * HD + HD],
                                       DECAY[:, hd % 2, TRI_AT[i]:TRI_AT[i] + SEQ - i * P], start=i == 0, stop=i == NT - 1)
            if hd == 0:
                ins.then_inc(w["first_head"], 1)
            elif hd % 2:
                ins.then_inc(bank_ready, 1)
        pe.wait(sq_ready)
        bank = take_bank(pe, ssm_bank(c, 7), turns(e, 4))
        for m in range(2):
            ins = nc.tensor.matmul(bank[:], ONES[:], SQ[:, m, :], start=m == 0, stop=m == 1)
        ins.then_inc(bank_ready, 1)

    def act_ssm_decay(act, e, c, heads, more):
        w = ssm_sems
        for hd in heads:
            act.wait(w["decay_in"])
            act.e.activation(DECAY[:, hd % 2, :], DECAY[:, hd % 2, :], ACT.Exp).then_inc(w["decay_out"], 1)
            if more or hd < 2:
                act_decay_row(act, 0 if e is None else e * 8, 4 * c + hd + 2)

    def act_ssm_norm(act, e, c):
        w = ssm_sems
        act.wait(w["gated"])
        settle(act)
        act.e.activation(SQ[:], G[:, at(times(e, 4), 2 * c, 2), :], ACT.Square).then_inc(sq_ready, 1)
        act_root(act, RSTD[:], var_ready)

    def dve_ssm_scores(dve, e, c):
        for m in range(2):
            b = ssm_bank(c, m)
            bank = full_bank(dve, b, turns(e, 4))
            dt = DT[:, :, at(times(e, 8), 4 * c + 2 * m, 2)]
            dve.e.tensor_tensor(XDT[:, :, m * P:m * P + P].rearrange("p t (h q) -> p t h q", q=HD),
                                bank[:].rearrange("p (t h q) -> p t h q", t=NT, q=HD), bcast(dt, 3, HD), ALU.mult)\
                 .then_inc(bank_free[b % 4], 1)
        for j in (2, 3, 4):
            b = ssm_bank(c, j)
            bank = full_bank(dve, b, turns(e, 4))
            for i in [x for x in CB_HOME if CB_HOME[x][0] == j]:
                a, wide = CB_HOME[i][1], SEQ - i * P
                ins = dve.e.tensor_tensor(CBM[:, TRI_AT[i]:TRI_AT[i] + wide], bank[:, a:a + wide], LATER[:, 0:wide], ALU.mult)
            ins.then_inc(bank_free[b % 4], 1)

    def dve_ssm_decay(dve, e, c, heads):
        w = ssm_sems
        for hd in heads:
            if hd == 2:
                dve.wait(w["first_head"])
            if hd == 3:
                full_bank(dve, ssm_bank(c, 5), turns(e, 4))
            dve.wait(row_landed[hd % 2], 16)
            for i in range(NT):
                cum = ACS_COL[:, i, at(times(e, 8), 4 * c + hd)]
                ins = dve.e.tensor_scalar(DECAY[:, hd % 2, TRI_AT[i]:TRI_AT[i] + SEQ - i * P], ACS_ROW[:, hd % 2, i * P:SEQ],
                                          cum, 0.0, ALU.subtract, ALU.min)
            ins.then_inc(w["decay_in"], 1)
        for hd in heads:
            dve.wait(w["decay_out"])
            dve.e.tensor_tensor(DECAY[:, hd % 2, :], DECAY[:, hd % 2, :], CBM[:], ALU.mult).then_inc(w["masked"], 1)

    def dve_ssm_output(dve, e, c):
        w, par = ssm_sems, c % 2
        for m in range(2):
            b = ssm_bank(c, 5 + m)
            bank = full_bank(dve, b, turns(e, 4))
            dve.e.scalar_tensor_tensor(TMP[:, m, :], CONV[:, par, m, :], D_COL[:, at(times(e, 4), 2 * c + m)], bank[:],
                                       ALU.mult, ALU.add).then_inc(bank_free[b % 4], 1)
        dve.e.wait_ge(bank_free[b % 4], turns(e, 4) + (b // 4 + 1))
        dve.e.tensor_tensor(G[:, at(times(e, 4), 2 * c, 2), :], TMP[:], ZS[:, par], ALU.mult).then_inc(w["gated"], 1)
        b = ssm_bank(c, 7)
        bank = full_bank(dve, b, turns(e, 4))
        dve.e.tensor_scalar(RSTD[:], bank[:], 1.0 / 256, EPS, ALU.mult, ALU.add).then_inc(var_ready, 1)
        dve.wait(root_ready)
        dve.e.reciprocal(RSTD[:], RSTD[:]).then_inc(bank_free[b % 4], 1)
        dve.e.wait_ge(bank_free[b % 4], turns(e, 4) + (b // 4 + 1))
        for m in range(2):
            gm = G[:, at(times(e, 4), 2 * c + m), :]
            ins = dve.e.scalar_tensor_tensor(gm, gm, COLS[:, at(times(e, 4), col_at["ssm_norm"] + 2 * c + m)],
                                             bcast(RSTD[:], 1, 1), ALU.mult, ALU.mult)
        dve.link(ins)

    def ssm_program(eng, units, first, second, per):
        units(None, 0)
        with eng.loop(SSM_G // 2 - 1, per) as i:
            for c in range(2):
                first(i, c)
                units(i, c + 1)
                second(i, c, True)
        first(None, SSM_G - 2)
        units(None, SSM_G - 1)
        second(None, SSM_G - 2, True)
        first(None, SSM_G - 1)
        second(None, SSM_G - 1, False)

    def pe_ssm(pe):
        w = ssm_sems
        ssm_program(pe, lambda e, c: pe_ssm_units(pe, e, c), lambda e, c: pe_ssm_scores(pe, e, c),
                    lambda e, c, more: pe_ssm_heads(pe, e, c), {w["conv_ready"]: 4, w["masked"]: 8, sq_ready: 2})

    def act_ssm(act):
        w = ssm_sems

        def second(e, c, more):
            act_ssm_decay(act, e, c, (2, 3), more)
            act_ssm_norm(act, e, c)

        ssm_program(act, lambda e, c: act_ssm_units(act, e, c), lambda e, c: act_ssm_decay(act, e, c, (0, 1), True), second,
                    {w["decay_in"]: 8, w["gated"]: 2, var_ready: 2})

    def dve_ssm(dve):
        w = ssm_sems

        def first(e, c):
            dve_ssm_scores(dve, e, c)
            dve_ssm_decay(dve, e, c, (0, 1))

        def second(e, c, more):
            dve_ssm_decay(dve, e, c, (2, 3))
            dve_ssm_output(dve, e, c)

        ssm_program(dve, lambda e, c: dve_ssm_units(dve, e, c), first, second,
                    {w["conv_in"]: 8, w["first_head"]: 2, w["decay_out"]: 8, row_landed[0]: 64, row_landed[1]: 64,
                     root_ready: 2, dve.chain: 22})

    def act_ssm_out(act):
        for half in range(2):
            act.e.wait_ge(unit_done, plan.u["ssmout"] + 4 * half)
            if half == 0:
                act.wait(g_ready)
            for k in range(KD):
                act.e.activation(HH[:, k, :], G[:, half * KD + k, :], ACT.Copy).then_inc(hi_ready, 1)

    g_ready = sem("g_ready")

    def dve_ssm_out(dve):
        dve.e.tensor_copy(RSTD[:, 0:1], ONES[:, 0:1]).then_inc(g_ready, 1)
        for half in range(2):
            for k in range(KD):
                dve.wait(hi_ready)
                dve.e.tensor_tensor(HL[:, k, :], G[:, half * KD + k, :], HH[:, k, :].bitcast(F32), ALU.subtract)\
                     .then_inc(h_ready, 1)
            dve.passed(h_ready, KD)
            for i in range(4):
                p = plan.p["ssmout"] + 4 * half + i
                pair = full_pair(dve, plan.u["ssmout"] + 4 * half + i, p)
                for m in range(2):
                    c = 2 * i + m
                    ins = dve.e.scalar_tensor_tensor(X[:, c, :], pair[:, m, :], mod(1, 2, c), X[:, c, :], ALU.mult, ALU.add)
                ins.then_inc(evac[p % 2], 1)

    def pe_ssm_out(pe):
        for half in range(2):
            pe.wait(h_ready, KD)
            for i in range(4):
                pair = take_pair(pe, plan.p["ssmout"] + 4 * half + i)
                unit_channels(pe, plan.u["ssmout"] + 4 * half + i, pair, hh, hl, KD)

    gate_sems = {s: sem(f"gate_{s}") for s in ("exp_in", "exp_out", "log_ready", "cum_ready")}
    gmlp_landed, half_ready, qk_ready, spatial_ready = (sem(s) for s in ("gmlp_landed", "half_ready", "qk_ready", "spatial_ready"))

    def pe_evin(pe):
        for i in range(10):
            u, pair = plan.u["evin"] + i, take_pair(pe, plan.p["evin"] + i)
            if i == 0:
                first_unit(pe, u, pair, pe.seen(h_ready))
                pe.passed(h_ready, KD)
            elif i in (2, 3, 8, 9):
                unit_tokens(pe, u, pair)
            else:
                unit_channels(pe, u, pair, hh, hl, KD)
        b = plan.b["gate"]
        pe_logits(pe, b, FG_WH, FG_WL, HEADS, False)
        b += 1
        pe.wait(gate_sems["log_ready"])
        bank = take_bank(pe, b + 1)
        for tt in range(NT):
            ins = nc.tensor.transpose(bank[0:HEADS, tt * P:tt * P + P], FGL[:, 5, tt, :], IDENT[:])
        ins.then_inc(bank_ready, 1)

    def act_evin(act):
        act.e.dma_start(SPAT[:], t["ev_w_spatial_2"][0].rearrange("g t s -> t g s")).then_inc(gmlp_landed, 16)
        act.e.dma_start(SPAT_B[:], t["ev_b_spatial_2"][0].partition_broadcast(P)).then_inc(gmlp_landed, 16)
        act.e.dma_start(V_GAIN[:], t["ev_v_norm_2"][0].partition_broadcast(P)).then_inc(gmlp_landed, 16)
        act_copy_pairs(act, "evin", 0, 2, UA, False, ACT.Gelu_apprx_tanh)
        act_copy_pairs(act, "evin", 2, 2, VA, True, ACT.Gelu_apprx_tanh)
        act_copy_pairs(act, "evin", 4, 2, Q1, False)
        act_copy_pairs(act, "evin", 6, 2, K1, False)
        act_copy_pairs(act, "evin", 8, 2, V1, True)
        act_softplus(act, FGL[:, 0], gate_sems["exp_in"], gate_sems["exp_out"])

    def dve_evin(dve):
        w, b = gate_sems, plan.b["gate"]
        dve.e.tensor_scalar(MINUS_HEAD[:], bcast(IDENT[0:HEADS, 0:HEADS], 2, P), -HD ** 0.5, None, ALU.mult)
        dve_cut_narrow(dve, FG_WH[:], FG_WL[:], FG_W[:])
        logits = dve_logits(dve, b, HEADS)
        b += 1
        dve.e.tensor_tensor(FGL[:, 5], logits, bcast(FG_B[:], 1, NT), ALU.add).then_inc(bank_free[b % 4], 1)
        dve.e.wait_ge(bank_free[b % 4], b // 4 + 1)
        dve_softplus(dve, FGL[:, 5], FGL[:, 4], [FGL[:, i] for i in range(4)], w["exp_in"], w["exp_out"], -1)
        dve.e.tensor_copy(FGL[:, 5], FGL[:, 4]).then_inc(w["log_ready"], 1)
        b += 1
        dve.e.tensor_copy(FCUM[:, 0, :], full_bank(dve, b)[0:HEADS, :]).then_inc(bank_free[b % 4], 1)
        dve.e.wait_ge(bank_free[b % 4], b // 4 + 1)
        dve.e.tensor_tensor_scan(FCUM[:, 1, :], ONES[0:HEADS, 0:1].broadcast_to([HEADS, SEQ]), FCUM[:, 0, :], 0.0,
                                 ALU.mult, ALU.add).then_inc(w["cum_ready"], 1)

    def pe_gmlp(pe):
        b = plan.b["gmlp"]
        pe.e.wait_ge(gmlp_landed, 48)
        bank = take_bank(pe, b)
        for g in range(4):
            ins = nc.tensor.transpose(bank[:, g * P:g * P + P], SPAT[:, g, :], IDENT[:])
        ins.then_inc(bank_ready, 1)
        pe.wait(spatial_ready)
        for g in range(4):
            bank = take_bank(pe, b + 1 + g)
            for n in range(NT):
                ins = nc.tensor.matmul(bank[:, n * P:n * P + P], VA[:, n, g * P:g * P + P], SPAT_T[:, g, :], start=True, stop=True)
            ins.then_inc(bank_ready, 1)

    def act_gmlp(act):
        act_root(act, VR[:], var_ready)
        for g in range(4):
            act.wait(pre_ready)
            act.e.activation(HH[:, g, :], TMP[:, g % 2, :], ACT.Copy).then_inc(hi_ready, 1)

    def dve_gmlp(dve):
        b = plan.b["gmlp"]
        for s in range(2):
            dve.e.wait_ge(evac[s], plan.p["gate"] // 2)
        dve.e.wait_ge(gmlp_landed, 48)
        bank = full_bank(dve, b)
        dve.e.tensor_tensor(SPAT_T[:], bank[:].rearrange("p (g t) -> p g t", t=P), bcast(LATER[:, 0:P], 1, 4), ALU.mult)\
             .then_inc(bank_free[b % 4], 1)
        groups = VA[:].rearrange("p n (g c) -> p (n g) c", c=P)
        dve.link(dve.e.tensor_tensor(VSQ[:], VA[:], VA[:], ALU.mult))
        dve.link(dve.e.tensor_reduce(VR[:], VSQ[:].rearrange("p n (g c) -> p (n g) c", c=P), AX.X, ALU.add))
        dve_rstd(dve, VR[:], VR[:], P)
        dve.link(dve.e.tensor_tensor(groups, groups, bcast(VR[:], 2, P), ALU.mult))
        dve.e.tensor_tensor(VA[:], VA[:], bcast(V_GAIN[:], 1, NT), ALU.mult).then_inc(spatial_ready, 1)
        for g in range(4):
            bank = full_bank(dve, b + 1 + g)
            tmp = TMP[:, g % 2, :]
            if g >= 2:
                dve.wait(half_ready)
            dve.e.tensor_tensor(tmp.rearrange("p (n t) -> p n t", t=P), bank[:].rearrange("p (n t) -> p n t", t=P),
                                bcast(SPAT_B[:, g, :], 1, NT), ALU.add).then_inc(bank_free[(b + 1 + g) % 4], 1)
            dve.e.wait_ge(bank_free[(b + 1 + g) % 4], (b + 1 + g) // 4 + 1)
            dve.e.tensor_tensor(tmp, tmp, UA[:, g, :], ALU.mult).then_inc(pre_ready, 1)
            dve.wait(pre_ready)
            dve.wait(hi_ready)
            dve.e.tensor_tensor(HL[:, g, :], tmp, HH[:, g, :].bitcast(F32), ALU.subtract).then_inc(half_ready, 1)

    def pe_qknorm(pe):
        b = plan.b["qknorm"]
        for n in range(8):
            pe.wait(sq_ready)
            bank = take_bank(pe, b + n)
            nc.tensor.matmul(bank[:], HEAD_ONES[:], SQ[:, n % 2, :], start=True, stop=True).then_inc(bank_ready, 1)
        pe.wait(qk_ready, 2)
        pe.wait(gate_sems["cum_ready"])

    def act_qknorm(act):
        b = plan.b["qknorm"]
        for s in range(2):
            act.e.wait_ge(evac[s], plan.p["gate"] // 2)
        for i, arr in enumerate((Q1, K1)):
            for m in range(4):
                n = 4 * i + m
                if n >= 2:
                    act.e.wait_ge(bank_ready, b + n - 1)
                act.e.activation(SQ[:, n % 2, :], arr[:, m, :], ACT.Square).then_inc(sq_ready, 1)
            last = b + 4 * i + 3
            act.e.wait_ge(bank_free[last % 4], last // 4 + 1)
            act.e.activation(VSQ[:], VSQ[:], ACT.Sqrt).then_inc(root_ready, 1)

    def dve_qknorm(dve):
        b = plan.b["qknorm"]
        for i, arr in enumerate((Q1, K1)):
            if i:
                dve.wait(qk_ready)
            for m in range(4):
                n = b + 4 * i + m
                dve.e.tensor_scalar(VSQ[:, m, :], full_bank(dve, n)[:], 1.0 / HD, EPS, ALU.mult, ALU.add)\
                     .then_inc(bank_free[n % 4], 1)
            dve.wait(root_ready)
            dve.link(dve.e.reciprocal(VSQ[:], VSQ[:]))
            for m in range(4):
                ins = dve.e.scalar_tensor_tensor(arr[:, m, :], arr[:, m, :], QK_GAIN[:, i:i + 1], VSQ[:, m, :], ALU.mult, ALU.mult)
            ins.then_inc(qk_ready, 1)

    ffn_sems = {s: sem(f"ffn_{s}") for s in ("conv_in", "gate", "hidden", "hidden_hi", "hidden_ready")}
    FFN_PARTS = ((0, 8), (8, 8), (16, 6))

    def pe_ffn(pe, layer):
        w, u0, p0 = ffn_sems, plan.u[f"ffn{layer}"], plan.p[f"ffn{layer}"]
        with pe.e.Fori(0, FB // 2) as i:
            first_unit(pe, u0, take_pair(pe, p0, i), pe.seen(h_ready), off=i * 2)
            unit_channels(pe, u0 + 1, take_pair(pe, p0 + 1, i), hh, hl, KD, off=i * 2)
        pe.passed(h_ready, KD)
        with pe.e.Fori(0, 2) as i:
            for c in range(2):
                pair = take_pair(pe, p0 + FB + c, i)
                if c == 0:
                    pe.e.wait_ge(w["hidden_ready"], FB * (layer + 1))
                for j, (k0, n) in enumerate(FFN_PARTS):
                    unit_channels(pe, u0 + FB + 3 * c + j, pair, lambda k: FHH[:, k0 + k, :], lambda k: FHL[:, k0 + k, :], n,
                                  first=j == 0, last=j == 2, off=i * 6)

    def act_ffn(act, layer):
        w, u0, p0 = ffn_sems, plan.u[f"ffn{layer}"], plan.p[f"ffn{layer}"]
        with act.loop(FB // 2, {w["hidden"]: 2}) as i:
            for b in range(2):
                pair = full_pair(act, u0 + b, p0 + b, i * 2)
                settle(act)
                for m in range(2):
                    wc = COLS[:, bass.ds(i * 2 + (col_at["fconv_w"] + layer * 6 * FB + 4 * FB + m * FB + b), 1)]
                    bc = COLS[:, bass.ds(i * 2 + (col_at["fconv_b"] + layer * 2 * FB + m * FB + b), 1)]
                    act.e.activation((SQ, FUP)[m][:, b, :], pair[:, m, :], ACT.Identity, bias=bc, scale=wc).then_inc(w["conv_in"], 1)
                act.e.wait_ge(evac[b], i + ((p0 + b) // 2 + 1))
                act.e.activation(SQ[:, b, :], SQ[:, b, :], ACT.Silu).then_inc(w["gate"], 1)
                act.wait(w["hidden"])
                settle(act)
                act.e.activation(FHH[:, bass.ds(i * 2 + b, 1), :], TMP[:, b:b + 1, :], ACT.Copy).then_inc(w["hidden_hi"], 1)

    def dve_ffn(dve, layer):
        w, u0, p0 = ffn_sems, plan.u[f"ffn{layer}"], plan.p[f"ffn{layer}"]
        with dve.loop(FB // 2, {w["conv_in"]: 4, w["gate"]: 2, w["hidden"]: 2, w["hidden_hi"]: 2, dve.chain: 2}) as i:
            for b in range(2):
                pair = PAIR[b]
                dve.wait(w["conv_in"], 2)
                for sh in (1, 2):
                    for m in range(2):
                        wc = COLS[:, bass.ds(i * 2 + (col_at["fconv_w"] + layer * 6 * FB + (2 - sh) * 2 * FB + m * FB + b), 1)]
                        acc = (SQ, FUP)[m][:, b, sh:]
                        ins = dve.e.scalar_tensor_tensor(acc, pair[:, m, :SEQ - sh], wc, acc, ALU.mult, ALU.add)
                    if sh == 1:
                        dve.link(ins)
                ins.then_inc(evac[b], 1)
                dve.wait(w["gate"])
                dve.e.tensor_tensor(TMP[:, b, :], SQ[:, b, :], FUP[:, b, :], ALU.mult).then_inc(w["hidden"], 1)
                dve.wait(w["hidden"])
                dve.wait(w["hidden_hi"])
                f = bass.ds(i * 2 + b, 1)
                dve.e.tensor_tensor(FHL[:, f, :], TMP[:, b:b + 1, :], FHH[:, f, :].bitcast(F32), ALU.subtract)\
                     .then_inc(w["hidden_ready"], 1)
        with dve.e.Fori(0, 2) as i:
            for c in range(2):
                pair = full_pair(dve, u0 + FB + 3 * c + 2, p0 + FB + c, i * 6)
                x = X[:, bass.ds(i * 4 + 2 * c, 2), :]
                dve.e.tensor_tensor(x, pair[:], x, ALU.add).then_inc(evac[c], 1)

    ple_landed, ple_hi, ple_gate = sem("ple_landed"), sem("ple_hi"), sem("ple_gate")

    def act_ple_load(act, layer):
        for s in range(2):
            act.e.wait_ge(evac[s], plan.p[f"ple{layer}"] // 2)
        act.e.dma_start(PTOK[:], t["p_2"][layer, 0].rearrange("(t p) d -> p t d", p=P)).then_inc(ple_landed, 16)

    def pe_ple(pe, layer):
        b, u0, p0 = plan.b[f"ple{layer}"], plan.u[f"ple{layer}"], plan.p[f"ple{layer}"]
        pe.wait(ple_landed, 16)
        for k in range(2):
            bank = take_bank(pe, b + k)
            for tt in range(NT):
                ins = nc.tensor.transpose(bank[:, tt * P:tt * P + P], PTOK[:, tt, k * P:k * P + P], IDENT[:])
            ins.then_inc(bank_ready, 1)
        for k in range(2):
            pe.e.wait_ge(bank_free[(b + k) % 4], (b + k) // 4 + 1)
        for half in range(2):
            u, p = u0 + 3 * half, p0 + 4 * half
            pe.e.wait_ge(split_ready, u + 1)
            for q in range(2):
                pair = take_pair(pe, p + q)
                for m in range(2):
                    for k in range(2):
                        c = (k * 4 + 2 * q + m) * P
                        ins = mm3(pair[:, m, :], WH[:, u % 2, c:c + P], WL[:, u % 2, c:c + P], PH[:, k, :], PL[:, k, :], k == 0, k == 1)
            ins.then_inc(unit_done, 1)
            for i in range(2):
                pair = take_pair(pe, p + 2 + i)
                if half == 0 and i == 0:
                    first_unit(pe, u + 1, pair, pe.seen(h_ready))
                    pe.passed(h_ready, KD)
                else:
                    unit_channels(pe, u + 1 + i, pair, hh, hl, KD)

    def act_ple(act, layer):
        b, u0, p0 = plan.b[f"ple{layer}"], plan.u[f"ple{layer}"], plan.p[f"ple{layer}"]
        for k in range(2):
            act.e.activation(PH[:, k, :], full_bank(act, b + k)[:], ACT.Copy).then_inc(ple_hi, 1)
        for half in range(2):
            u, p = u0 + 3 * half, p0 + 4 * half
            for i in range(4):
                pair = full_pair(act, u + max(i - 1, 0), p + i)
                if half and i == 0 or i == 3:
                    act.e.wait_ge(evac[(p + i - 1) % 2], (p + i - 1) // 2 + 1)
                if i < 2:
                    act.e.activation(PROJ[:, 2 * i:2 * i + 2, :], pair[:], ACT.Copy).then_inc(evac[(p + i) % 2], 1)
                else:
                    act.e.activation(SQ[:], pair[:], ACT.Sigmoid).then_inc(ple_gate, 1)

    def dve_ple(dve, layer):
        b, p0 = plan.b[f"ple{layer}"], plan.p[f"ple{layer}"]
        for k in range(2):
            dve.wait(ple_hi)
            dve.e.tensor_tensor(PL[:, k, :], full_bank(dve, b + k)[:], PH[:, k, :].bitcast(F32), ALU.subtract)\
                 .then_inc(bank_free[(b + k) % 4], 1)

    def dve_ple_gates(dve, layer):
        p0 = plan.p[f"ple{layer}"]
        for half in range(2):
            for i in range(2):
                p, c = p0 + 4 * half + 2 + i, 4 * half + 2 * i
                dve.wait(ple_gate)
                dve.link(dve.e.tensor_tensor(TMP[:], SQ[:], PROJ[:, 2 * i:2 * i + 2, :], ALU.mult))
                dve.e.tensor_tensor(X[:, c:c + 2, :], TMP[:], X[:, c:c + 2, :], ALU.add).then_inc(evac[p % 2], 1)

    glu_gate = sem("glu_gate")

    def pe_glu(pe):
        pe.wait(h_ready, KD)
        pe_matrix(pe, "glu", KD)

    def act_glu(act):
        for i in range(KD):
            pair = full_pair(act, plan.u["glu"] + i, plan.p["glu"] + i)
            act.e.activation(SQ[:, i % 2, :], pair[:, 1, :], ACT.Sigmoid).then_inc(glu_gate, 1)

    def dve_glu(dve):
        for i in range(KD):
            p = plan.p["glu"] + i
            dve.wait(glu_gate)
            dve.link(dve.e.tensor_tensor(TMP[:, i % 2, :], PAIR[p % 2][:, 0, :], SQ[:, i % 2, :], ALU.mult))
            dve.e.tensor_tensor(X[:, i, :], TMP[:, i % 2, :], X[:, i, :], ALU.add).then_inc(evac[p % 2], 1)

    s5_sems = {s: sem(f"s5_{s}") for s in ("a_landed", "landed", "vec_in", "vec_out", "consts", "bb", "angles", "tab", "w1x",
                                           "ca", "turning", "bu", "state", "gelu")}
    CR, CI, STEP_HI, STEP_LO, MAG4 = range(5)
    BELOW_TWO_PI = 6.283185
    GRID = 16384.0

    def act_s5_rows(act):
        for i, name in enumerate(("od_a_re_2", "od_a_im_2")):
            act.e.dma_start(AROW[:, i, :], t[name][0].rearrange("(t h) p -> t (h p)", h=2)).then_inc(s5_sems["a_landed"], 16)
        act.e.dma_start(LDT_ROW[:], t["od_log_dt_2"][0].partition_broadcast(P)).then_inc(s5_sems["a_landed"], 16)

    def pe_s5_vectors(pe):
        b = plan.b["s5a"]
        pe.e.wait_ge(s5_sems["a_landed"], 48)
        bank = take_bank(pe, b)
        for i in range(2):
            ins = nc.tensor.transpose(bank[:, i * S5_TILES:i * S5_TILES + S5_TILES], AROW[:, i, :], IDENT[0:S5_TILES, 0:S5_TILES])
        ins.then_inc(bank_ready, 1)

    S5_NAMES = ("lr", "li", "ldt", "dt", "e", "th", "n", "turn", "red", "cos", "sin", "half", "big", "ec", "poly", "small",
                "em1", "mag", "nr", "den", "p", "q", "turn4")
    vec = {name: S1[:, 0, i * S5_TILES:(i + 1) * S5_TILES] for i, name in enumerate(S5_NAMES)}

    def act_s5_vectors(act):
        w = s5_sems
        act.wait(w["vec_in"])
        act.e.activation(vec["dt"], vec["ldt"], ACT.Exp).then_inc(w["vec_out"], 1)
        act.wait(w["vec_in"])
        act.e.activation(vec["big"], vec["e"], ACT.Exp)
        act.e.activation(vec["sin"], vec["red"], ACT.Sin)
        act.e.activation(vec["half"], vec["red"], ACT.Sin, scale=0.5)
        act.e.activation(vec["cos"], vec["q"], ACT.Sin, scale=BELOW_TWO_PI).then_inc(w["vec_out"], 1)

    def dve_s5_vectors(dve):
        w, v = s5_sems, vec

        def tt(o, a, b, op):
            dve.link(dve.e.tensor_tensor(o, a, b, op))

        def ts(o, a, s1, s2, *ops):
            dve.link(dve.e.tensor_scalar(o, a, s1, s2, *ops))

        def stt(o, a, s, b, op1, op2):
            dve.link(dve.e.scalar_tensor_tensor(o, a, s, b, op1, op2))

        def nearest(o, a):
            ts(o, a, ROUND, ROUND, ALU.add, ALU.subtract)

        b = plan.b["s5a"]
        bank = full_bank(dve, b)
        dve.e.tensor_copy(v["lr"], bank[:, 0:S5_TILES])
        dve.e.tensor_copy(v["li"], bank[:, S5_TILES:2 * S5_TILES]).then_inc(bank_free[b % 4], 1)
        dve.e.wait_ge(s5_sems["a_landed"], 48)
        for h in range(2):
            ins = dve.e.tensor_copy(v["ldt"][h * HD:h * HD + HD, :], LDT_ROW[h * HD:h * HD + HD, :].rearrange("p (t h) -> p h t", h=2)[:, h, :])
        ins.then_inc(w["vec_in"], 1)
        dve.wait(w["vec_out"])
        tt(v["e"], v["lr"], v["dt"], ALU.mult)
        tt(v["th"], v["li"], v["dt"], ALU.mult)
        ts(v["n"], v["th"], 1 / TWO_PI, None, ALU.mult)
        nearest(v["n"], v["n"])
        stt(v["red"], v["n"], -TWO_PI_PARTS[0], v["th"], ALU.mult, ALU.add)
        stt(v["red"], v["n"], -TWO_PI_PARTS[1], v["red"], ALU.mult, ALU.add)
        stt(v["red"], v["n"], -TWO_PI_PARTS[2], v["red"], ALU.mult, ALU.add)
        ts(v["turn"], v["red"], 1 / TWO_PI, 0.5, ALU.mult, ALU.min)
        ts(v["turn"], v["turn"], -0.5, None, ALU.max)
        ts(v["red"], v["red"], BELOW_TWO_PI / 2, -BELOW_TWO_PI / 2, ALU.min, ALU.max)
        ts(v["q"], v["turn"], 0.25, None, ALU.add)
        nearest(v["p"], v["q"])
        dve.e.tensor_tensor(v["q"], v["q"], v["p"], ALU.subtract).then_inc(w["vec_in"], 1)
        ts(v["ec"], v["e"], 0.5, -0.5, ALU.min, ALU.max)
        ts(v["poly"], v["ec"], EXP_SERIES[0], None, ALU.mult)
        for c in EXP_SERIES[1:]:
            stt(v["poly"], v["poly"], c, v["ec"], ALU.add, ALU.mult)
        tt(v["p"], v["e"], v["e"], ALU.mult)
        ts(v["small"], v["p"], 0.25, None, ALU.is_lt)
        dve.wait(w["vec_out"])
        ts(v["big"], v["big"], 1.0, None, ALU.subtract)
        tt(v["poly"], v["poly"], v["big"], ALU.subtract)
        tt(v["poly"], v["poly"], v["small"], ALU.mult)
        tt(v["em1"], v["poly"], v["big"], ALU.add)
        ts(v["mag"], v["em1"], 1.0, None, ALU.add)
        tt(v["half"], v["half"], v["half"], ALU.mult)
        tt(v["nr"], v["em1"], v["cos"], ALU.mult)
        stt(v["nr"], v["half"], -2.0, v["nr"], ALU.mult, ALU.add)
        power = lambda part, n: A_POW[:, part, n, :]
        tt(power(0, 1), v["mag"], v["cos"], ALU.mult)
        tt(power(1, 1), v["mag"], v["sin"], ALU.mult)
        tt(v["den"], v["lr"], v["lr"], ALU.mult)
        tt(v["p"], v["li"], v["li"], ALU.mult)
        tt(v["den"], v["den"], v["p"], ALU.add)
        dve.link(dve.e.reciprocal(v["den"], v["den"]))
        for o, a, b, op in ((CR, ("nr", "lr"), "li", ALU.add), (CI, ("nr", "li"), "lr", ALU.subtract)):
            tt(v["p"], v[a[0]], v[a[1]], ALU.mult)
            tt(v["q"], power(1, 1), v[b], ALU.mult)
            tt(v["q"], v["q"], v["p"], op)
            tt(S5K[:, o, :], v["q"], v["den"], ALU.mult)
        dve.e.memset(power(0, 0), 1.0)
        dve.link(dve.e.memset(power(1, 0), 0.0))
        for n in range(2, S5_L + 1):
            tt(v["p"], power(0, n - 1), power(0, 1), ALU.mult)
            tt(v["q"], power(1, n - 1), power(1, 1), ALU.mult)
            tt(power(0, n), v["p"], v["q"], ALU.subtract)
            tt(v["p"], power(0, n - 1), power(1, 1), ALU.mult)
            tt(v["q"], power(1, n - 1), power(0, 1), ALU.mult)
            tt(power(1, n), v["p"], v["q"], ALU.add)
        for n in range(S5_L):
            ins = dve.e.tensor_copy(A_REV[:, :, n, :], A_POW[:, :, S5_L - 1 - n, :])
        tt(v["p"], v["mag"], v["mag"], ALU.mult)
        tt(S5K[:, MAG4, :], v["p"], v["p"], ALU.mult)
        ts(v["turn4"], v["turn"], float(S5_L), None, ALU.mult)
        nearest(v["p"], v["turn4"])
        tt(v["turn4"], v["turn4"], v["p"], ALU.subtract)
        ts(v["p"], v["turn4"], GRID, None, ALU.mult)
        nearest(v["p"], v["p"])
        ts(S5K[:, STEP_HI, :], v["p"], 1 / GRID, None, ALU.mult)
        tt(S5K[:, STEP_LO, :], v["turn4"], S5K[:, STEP_HI, :], ALU.subtract)

    def act_s5_load(act):
        w = s5_sems
        for i, (bn, cn) in enumerate((("od_b_re_2", "od_c_re_2"), ("od_b_im_2", "od_c_im_2"))):
            act.e.dma_start(BRAW[:, i], t[bn][0].rearrange("(t h) p c -> (h p) t c", h=2)).then_inc(w["landed"], 16)
            for twice in range(2):
                act.e.dma_start(CRAW[:, i, :, twice, :], t[cn][0].rearrange("(k g) c p -> (g c) k p", g=8)).then_inc(w["landed"], 16)

    def at4(e, k, size=4):
        return slice(4 * k, 4 * k + 4) if e is None else bass.ds(e * 8 + 4 * k, 4)

    def step_at(e, k):
        return slice(k, k + 1) if e is None else bass.ds(e * 2 + k, 1)

    def s5_a(k, i):
        return plan.b["s5"] + (4 + 6 * (k - 1) + i if k else i)

    def s5_y(k):
        return plan.b["s5"] + (4 + 6 * k + 4 if k < KD - 1 else 6 * KD - 2)

    def s5_out(k):
        return s5_y(k) + 1

    def s5_loop(eng, first, step, last, per):
        first()
        step(None, 0)
        with eng.loop((KD - 2) // 2, per) as e:
            for k in (1, 2):
                step(e, k)
        step(None, KD - 1)
        last()

    def t2(e, n):
        return 0 if e is None else e * n

    def pool_s5_consts(pool):
        w = s5_sems
        pool.e.wait_ge(s5_sems["landed"], 96)
        for s in range(2):
            pool.e.wait_ge(evac[s], plan.p["s5"] // 2)
        for n in range(S5_LOW):
            pool.e.memset(S5_AT[:, n:n + 1], float(n))
        for n in range(S5_HIGH):
            pool.e.memset(S5_AT[:, S5_LOW + n:S5_LOW + n + 1], float(n * S5_LOW))
        pool.link(pool.e.memset(FIRST[:], 1.0))
        pool.e.memset(FIRST[:, 0:1], 0.0)
        pool.e.memset(W3[:], 0.0)
        pool.e.memset(W1X[:], 0.0)
        pool.e.memset(CAX[:], 0.0).then_inc(w["consts"], 1)
        pool.wait(w["consts"])
        pool.wait(w["bb"])
        pool.wait(w["tab"])
        pool.e.wait_ge(bank_ready, plan.b["s5c"] + 4)

    def pool_tt(pool, o, a, b, op):
        pool.link(pool.e.tensor_tensor(o, a, b, op))

    def pool_s5_step(pool, k):
        w, par, tiles = s5_sems, k % 2, slice(4 * k, 4 * k + 4)
        if k >= 2:
            pool.e.wait_ge(bank_ready, s5_a(k - 2, 2) + 1)
        q = PRP[:].rearrange("p a t n -> p (a t n)").rearrange("p (q t j c) -> p q t j c", q=4, t=4, j=S5_L)
        shape = lambda a: bcast(a, 2, S5_L)
        br, bi = (shape(BB[:, i, tiles, :]) for i in range(2))
        ar, ai = (bcast(A_REV[:, i, :, tiles].rearrange("p j t -> p t j"), 3, S5_C) for i in range(2))
        for i, (a, b) in enumerate(((br, ar), (bi, ai), (br, ai), (bi, ar))):
            pool_tt(pool, q[:, i], a, b, ALU.mult)
        for part, op in ((0, ALU.subtract), (1, ALU.add)):
            for h in range(2):
                rows = slice(h * HD, h * HD + HD)
                ins = pool.e.tensor_tensor(W1X[rows, par, part, :, :, h, :], q[rows, 2 * part], q[rows, 2 * part + 1], op)
                if part + h < 2:
                    pool.link(ins)
        ins.then_inc(w["w1x"], 1)
        pool.wait(w["w1x"])
        if k >= 2:
            pool.e.wait_ge(w["state"], k - 1)
        low = lambda i: bcast(TAB[:, i, tiles, 0:S5_LOW], 2, S5_HIGH)
        high = lambda i: bcast(TAB[:, i, tiles, S5_LOW:], 3, S5_LOW)
        table = lambda i: TURNING[:, par, i].rearrange("p t (h l) -> p t h l", l=S5_LOW)
        tmp = [PRP[:, i].rearrange("p t (h l) -> p t h l", l=S5_LOW) for i in range(2)]
        for i, (a, b, c, d, op) in enumerate(((1, 1, 0, 0, ALU.subtract), (0, 1, 1, 0, ALU.add))):
            pool_tt(pool, tmp[0], high(a), low(b), ALU.mult)
            pool_tt(pool, tmp[1], high(c), low(d), ALU.mult)
            pool_tt(pool, table(i), tmp[0], tmp[1], op)
        pool.e.tensor_tensor(TURNING[:, par, 2], bcast(FIRST[:], 1, 4), bcast(S5K[:, MAG4, tiles], 2, S5_N), ALU.mult)\
            .then_inc(w["turning"], 1)
        pool.wait(w["turning"])

    def pool_s5(pool):
        pool_s5_consts(pool)
        for k in range(KD):
            pool_s5_step(pool, k)

    def pe_s5_prepare(pe, e, k):
        w, par = s5_sems, k % 2
        pe.wait(w["w1x"])
        for part in range(2):
            bank = take_bank(pe, s5_a(k, part), t2(e, 3))
            for i in range(4):
                ins = nc.tensor.transpose(bank[:, i * P:i * P + P], W1X[:, par, part, i].rearrange("p j h c -> p (j h c)"), IDENT[:])
            ins.then_inc(bank_ready, 1)
        pe.wait(w["ca"])
        bank = take_bank(pe, s5_a(k, 2), t2(e, 3))
        for i in range(4):
            for part in range(2):
                ins = nc.tensor.matmul(bank[0:32, i * P:i * P + P], W1X[:, par, part, i, S5_L - 1].rearrange("p h c -> p (h c)"),
                                       CAX[:, par, part, i, 0:S5_L].rearrange("p j h c -> p (j h c)"), start=part == 0, stop=part == 1)
        ins.then_inc(bank_ready, 1)
        bank = take_bank(pe, s5_a(k, 3), t2(e, 3))
        for i in range(4):
            for j in range(S5_L):
                src = HF[:, step_at(e, k), :].rearrange("p k (n l) -> p (k n) l", l=S5_L)[:, :, j]
                ins = nc.tensor.matmul(bank[32 * j:32 * j + 32, i * P:i * P + P], IDENT[:, 32 * i:32 * i + 32], src, start=True, stop=True)
        ins.then_inc(bank_ready, 1)
        pair = take_pair(pe, plan.p["s5"] + k, t2(e, 1))
        b = s5_a(k, 3)
        pe.e.wait_ge(bank_free[b % 4], t2(e, 3) + (b // 4 + 1))
        for part in range(2):
            for i in range(4):
                ins = nc.tensor.matmul(pair[:, part, i * P:i * P + P], W1_T[:, par, part, i, :], U4[:, par, i, :], start=True, stop=True)
        ins.then_inc(w["bu"], 1)

    def pe_s5_output(pe, e, k):
        w, par = s5_sems, k % 2
        pe.wait(w["state"])
        bank = take_bank(pe, s5_y(k), t2(e, 3))
        for i in range(4):
            nc.tensor.matmul(bank[:, i * P:i * P + P], W3[:, par, i, :], U4[:, par, i, :], start=True, stop=False)
            for part in range(2):
                ins = nc.tensor.matmul(bank[:, i * P + 1:i * P + P], CAX[:, par, part, i, 1:].rearrange("p j h c -> p (j h c)"),
                                       XS[:, part, i, 0:S5_N - 1], start=False, stop=part == 1)
        ins.then_inc(bank_ready, 1)
        bank = take_bank(pe, s5_out(k), t2(e, 3))
        b = s5_y(k)
        pe.e.wait_ge(bank_free[b % 4], t2(e, 3) + (b // 4 + 1))
        for i in range(4):
            for j in range(S5_L):
                ins = nc.tensor.matmul(bank[32 * i:32 * i + 32, :].rearrange("p (n l) -> p n l", l=S5_L)[:, :, j],
                                       IDENT[:, 32 * j:32 * j + 32], Y4[:, i, :], start=True, stop=True)
        ins.then_inc(bank_ready, 1)

    def pe_s5(pe):
        w = s5_sems
        b = plan.b["s5c"]
        pe.e.wait_ge(w["landed"], 96)
        for m in range(4):
            bank = take_bank(pe, b + m)
            for n in range(4):
                part, k = m // 2, 4 * (m % 2) + n
                ins = nc.tensor.transpose(bank[:, n * P:n * P + P], CRAW[:, part, k].rearrange("p d q -> p (d q)"), IDENT[:])
            ins.then_inc(bank_ready, 1)
        pe.wait(h_ready)

        def step(e, k):
            if e is not None or k < KD - 1:
                pe_s5_prepare(pe, e, k + 1)
            pe_s5_output(pe, e, k)

        pe_s5_prepare(pe, None, 0)
        for k in range(KD):
            step(None, k)

    def act_s5_prepare(act, e, k):
        par = k % 2
        if k >= 2:
            act.e.wait_ge(bank_ready, t2(e, 12) + (s5_y(k - 2) + 1))
        for part in range(2):
            b = s5_a(k, part)
            bank = full_bank(act, b, t2(e, 3))
            act.e.activation(W1_T[:, par, part].rearrange("p t n -> p (t n)"), bank[:], ACT.Copy).then_inc(bank_free[b % 4], 1)
        b = s5_a(k, 2)
        kernel = full_bank(act, b, t2(e, 3))[0:32, :].rearrange("p (t n) -> p t n", n=P)
        for j in range(S5_L):
            ins = act.e.activation(W3[32 * j:32 * j + 32, par, :, 32 * j:], kernel[:, :, 0:P - 32 * j], ACT.Copy)
        ins.then_inc(bank_free[b % 4], 1)
        b = s5_a(k, 3)
        act.e.activation(U4[:, par].rearrange("p t n -> p (t n)"), full_bank(act, b, t2(e, 3))[:], ACT.Copy).then_inc(bank_free[b % 4], 1)

    def act_s5_output(act, e, k):
        b = s5_y(k)
        if e is not None or k:
            act.e.wait_ge(bank_ready, t2(e, 12) + (s5_out(k - 1) + 1))
        act.e.activation(Y4[:].rearrange("p t n -> p (t n)"), full_bank(act, b, t2(e, 3))[:], ACT.Copy).then_inc(bank_free[b % 4], 1)

    def act_s5_gelu(act, e, k):
        w, par, b = s5_sems, k % 2, s5_out(k)
        act.e.wait_ge(bank_free[b % 4], t2(e, 3) + (b // 4 + 1))
        act.e.activation(SQ[:, par, :], TMP[:, par, :], ACT.Gelu_apprx_tanh).then_inc(w["gelu"], 1)
        act.wait(w["gelu"])
        settle(act)
        act.e.activation(HH[:, step_at(e, k), :], SQ[:, par:par + 1, :], ACT.Copy).then_inc(hi_ready, 1)

    def act_s5(act):
        w, b = s5_sems, plan.b["s5c"]
        for m in range(4):
            bank = full_bank(act, b + m)[:].rearrange("p (t h c) -> p t h c", h=2, c=S5_C)
            for h in range(2):
                rows = slice(h * HD, h * HD + HD)
                ins = act.e.activation(CK[rows, m // 2, 16 * (m % 2):16 * (m % 2) + 16, :], bank[rows, :, h, :], ACT.Copy)
            ins.then_inc(bank_free[(b + m) % 4], 1)
        act.wait(w["angles"])
        act.e.activation(TAB[:], TAB[:], ACT.Sin, scale=BELOW_TWO_PI).then_inc(w["tab"], 1)
        act.wait(w["consts"])

        def step(e, k):
            if e is not None or k < KD - 1:
                act_s5_prepare(act, e, k + 1)
            if e is not None or k:
                act_s5_gelu(act, e, k - 1)
            act_s5_output(act, e, k)

        s5_loop(act, lambda: act_s5_prepare(act, None, 0), step, lambda: act_s5_gelu(act, None, KD - 1), {w["gelu"]: 2})

    def dve_s5_start(dve):
        w = s5_sems
        dve.e.wait_ge(w["landed"], 96)
        dve.wait(w["consts"])
        q = [PR[:, i].rearrange("p t n -> p (t n)").rearrange("p (t c) -> p t c", c=S5_C) for i in range(4)]
        cr, ci = (bcast(S5K[:, i, :], 2, S5_C) for i in (CR, CI))
        for i, (a, b) in enumerate(((0, cr), (1, ci), (1, cr), (0, ci))):
            ins = dve.e.tensor_tensor(q[i], BRAW[:, a], b, ALU.mult)
        dve.link(ins)
        dve.e.tensor_tensor(BB[:, 0], q[0], q[1], ALU.subtract)
        dve.e.tensor_tensor(BB[:, 1], q[2], q[3], ALU.add).then_inc(w["bb"], 1)
        x, n = ANGLE[:, 0], ANGLE[:, 1]
        index = bcast(S5_AT[:], 1, S5_TILES)
        nearest = lambda: dve.link(dve.e.tensor_scalar(n, x, ROUND, ROUND, ALU.add, ALU.subtract))
        dve.link(dve.e.tensor_tensor(x, bcast(S5K[:, STEP_HI, :], 2, S5_IDX), index, ALU.mult))
        nearest()
        dve.link(dve.e.tensor_tensor(x, x, n, ALU.subtract))
        dve.link(dve.e.tensor_tensor(n, bcast(S5K[:, STEP_LO, :], 2, S5_IDX), index, ALU.mult))
        dve.link(dve.e.tensor_tensor(x, x, n, ALU.add))
        nearest()
        dve.link(dve.e.tensor_tensor(TAB[:, 0], x, n, ALU.subtract))
        dve.link(dve.e.tensor_scalar(x, x, 0.25, None, ALU.add))
        nearest()
        dve.e.tensor_tensor(TAB[:, 1], x, n, ALU.subtract).then_inc(w["angles"], 1)
        b = plan.b["s5c"] + 3
        dve.e.wait_ge(bank_free[b % 4], b // 4 + 1)

    def dve_s5_prepare(dve, e, k):
        w, par, tiles = s5_sems, k % 2, at4(e, k)
        if k >= 2:
            dve.e.wait_ge(bank_ready, t2(e, 12) + (s5_y(k - 2) + 1))
        n = 4 * (S5_L + 1) * S5_C
        q = [PR[:, i].rearrange("p t n -> p (t n)")[:, 0:n].rearrange("p (t j c) -> p t j c", t=4, c=S5_C) for i in range(4)]
        cr, ci = (bcast(CK[:, i, tiles, :], 2, S5_L + 1) for i in range(2))
        ar, ai = (bcast(A_POW[:, i, :, tiles].rearrange("p j t -> p t j"), 3, S5_C) for i in range(2))
        for i, (a, b) in enumerate(((cr, ar), (ci, ai), (cr, ai), (ci, ar))):
            ins = dve.e.tensor_tensor(q[i], a, b, ALU.mult)
        dve.link(ins)
        for h in range(2):
            rows = slice(h * HD, h * HD + HD)
            dve.e.tensor_tensor(CAX[rows, par, 0, :, :, h, :], q[0][rows], q[1][rows], ALU.subtract)
            ins = dve.e.scalar_tensor_tensor(CAX[rows, par, 1, :, :, h, :], q[2][rows], -1.0, q[3][rows], ALU.mult, ALU.subtract)
        ins.then_inc(w["ca"], 1)
        dve.wait(w["ca"])

    def dve_s5_states(dve, e, k):
        w, par, p = s5_sems, k % 2, plan.p["s5"] + k
        pair = PAIR[p % 2]
        dve.wait(w["bu"])
        dve.wait(w["turning"])
        flat = lambda a: a.rearrange("p t n -> p (t n)")
        cos, sin, decay = (flat(TURNING[:, par, i]) for i in range(3))
        q = [flat(PR[:, i]) for i in range(4)]
        for i, (part, tab) in enumerate(((0, cos), (1, sin), (1, cos), (0, sin))):
            ins = dve.e.tensor_tensor(q[i], pair[:, part, :], tab, ALU.mult)
        ins.then_inc(evac[p % 2], 1)
        dve.e.wait_ge(evac[p % 2], t2(e, 1) + (p // 2 + 1))
        dve.e.tensor_tensor(q[0], q[0], q[1], ALU.add)
        dve.link(dve.e.tensor_tensor(q[2], q[2], q[3], ALU.subtract))
        for i in (0, 2):
            ins = dve.e.tensor_tensor_scan(q[i + 1], decay, q[i], 0.0, ALU.mult, ALU.add)
        dve.link(ins)
        if e is not None or k:
            dve.e.wait_ge(bank_ready, t2(e, 12) + (s5_y(k - 1) + 1))
        for part, (a, b, op) in enumerate(((cos, sin, ALU.subtract), (sin, cos, ALU.add))):
            dve.e.tensor_tensor(q[0], q[1], a, ALU.mult)
            dve.link(dve.e.tensor_tensor(q[2], q[3], b, ALU.mult))
            ins = dve.e.tensor_tensor(flat(XS[:, part]), q[0], q[2], op)
            if part == 0:
                dve.link(ins)
        ins.then_inc(w["state"], 1)
        dve.wait(w["state"])

    def dve_s5_skip(dve, e, k):
        par, b = k % 2, s5_out(k)
        d = COLS[:, col_at["od_d"] + k:col_at["od_d"] + k + 1] if e is None else COLS[:, bass.ds(e * 2 + (col_at["od_d"] + k), 1)]
        bank = full_bank(dve, b, t2(e, 3))
        dve.e.scalar_tensor_tensor(TMP[:, par:par + 1, :], HF[:, step_at(e, k), :], d, bank[:].rearrange("p (a n) -> p a n", a=1),
                                   ALU.mult, ALU.add).then_inc(bank_free[b % 4], 1)

    def dve_s5_rest(dve, e, k):
        par = k % 2
        dve.wait(hi_ready)
        dve.e.tensor_tensor(HL[:, step_at(e, k), :], SQ[:, par:par + 1, :], HH[:, step_at(e, k), :].bitcast(F32), ALU.subtract)\
             .then_inc(h_ready, 1)
        dve.passed(h_ready, 1)

    def dve_s5(dve):
        w = s5_sems
        dve_s5_start(dve)

        def step(e, k):
            if e is not None or k < KD - 1:
                dve_s5_prepare(dve, e, k + 1)
            if e is not None or k:
                dve_s5_skip(dve, e, k - 1)
            dve_s5_states(dve, e, k)
            if e is not None or k:
                dve_s5_rest(dve, e, k - 1)

        def last():
            dve_s5_skip(dve, None, KD - 1)
            dve_s5_rest(dve, None, KD - 1)

        s5_loop(dve, lambda: dve_s5_prepare(dve, None, 0), step, last,
                {w["bu"]: 2, w["turning"]: 2, w["state"]: 2, w["ca"]: 2, hi_ready: 2, h_ready: 2, dve.chain: 12})

    out_saved = sem("out_saved")

    def sp_store(sp):
        for b in range(plan.b["store"] + KD - 4, plan.b["store"] + KD):
            sp.wait_ge(bank_free[b % 4], b // 4 + 1)
        sp.dma_start(out[0].rearrange("(t p) d -> p t d", p=P), OTOK[:]).then_inc(out_saved, 16)
        sp.wait_ge(out_saved, 16)

    def pe_store(pe):
        b = plan.b["store"]
        pe_after_h(pe, plan.p["store"])
        for k in range(KD):
            bank = take_bank(pe, b + k)
            for tt in range(NT):
                ins = nc.tensor.transpose(bank[:, tt * P:tt * P + P], X[:, k, tt * P:tt * P + P], IDENT[:])
            ins.then_inc(bank_ready, 1)

    def act_store(act):
        b = plan.b["store"]
        for k in range(KD):
            bank = full_bank(act, b + k)
            act.e.activation(OTOK[:, :, k * P:k * P + P], bank[:].rearrange("p (t c) -> p t c", c=P), ACT.Copy)\
                 .then_inc(bank_free[(b + k) % 4], 1)

    def act_program(act):
        act_loads(act.e)
        act_norm(act, 0)
        act_mixin(act)
        act_pool(act)
        act_attention(act, 0, S0, PT0)
        act_norm(act, 1)
        act_router(act, 0)
        act_moe(act, 0)
        act_norm(act, 2)
        act_dt(act)
        act_ssm(act)
        act_ssm_out(act)
        act_norm(act, 3)
        act_router(act, 1)
        act_moe(act, 1)
        act_norm(act, FINAL)
        act_norm(act, 5)
        act_s5_rows(act)
        act_evin(act)
        act_gmlp(act)
        act_qknorm(act)
        act_attention(act, 1, S1, PT1)
        act_s5_vectors(act)
        act_norm(act, 6)
        act_ffn(act, 0)
        act_ple_load(act, 0)
        act_s5_load(act)
        act_norm(act, 7)
        act_ple(act, 0)
        act_norm(act, PLAIN)
        act_s5(act)
        act_glu(act)
        act_norm(act, 9)
        act_ffn(act, 1)
        act_ple_load(act, 1)
        act_norm(act, 10)
        act_ple(act, 1)

    def pe_program(pe):
        pe_start(pe)
        pe_norm(pe, 0)
        pe_mixin(pe)
        pe_pool(pe)
        pe_attention(pe, 0, Q0, K0, V0, S0, PT0, False)
        pe_banks_read(pe, plan.b["att0"])
        pe_after_h(pe, plan.p["mixout"])
        pe_matrix(pe, "mixout", 4)
        pe_norm(pe, 1)
        pe_router(pe, 0)
        pe_moe(pe, 0)
        pe_norm(pe, 2)
        pe_dt(pe)
        pe_ssm(pe)
        pe_ssm_out(pe)
        pe_norm(pe, 3)
        pe_router(pe, 1)
        pe_moe(pe, 1)
        pe_norm(pe, FINAL)
        pe_norm(pe, 5)
        pe_evin(pe)
        pe_gmlp(pe)
        pe_qknorm(pe)
        pe_attention(pe, 1, Q1, K1, V1, S1, PT1, True)
        pe_s5_vectors(pe)
        pe.wait(half_ready, 4)
        pe_after_h(pe, plan.p["evout"])
        pe_matrix(pe, "evout", 4)
        pe_norm(pe, 6)
        pe_ffn(pe, 0)
        pe_norm(pe, 7)
        pe_ple(pe, 0)
        pe_norm(pe, PLAIN)
        pe_s5(pe)
        pe_glu(pe)
        pe_norm(pe, 9)
        pe_ffn(pe, 1)
        pe_norm(pe, 10)
        pe_ple(pe, 1)

    def dve_program(dve):
        dve_start(dve)
        dve_norm(dve, 0)
        dve_pool(dve)
        dve.wait(strip_ready)
        dve_attention(dve, 0, S0, lambda h: STRIP[:, h, :])
        dve_residual(dve, "mixout", 4, 1, (0, 2))
        dve_router_weights(dve, 0)
        dve_norm(dve, 1)
        dve_router(dve, 0)
        dve_moe(dve, 0)
        dve_cut_narrow(dve, DT_WH[:], DT_WL[:], DT_W[:])
        dve_norm(dve, 2)
        dve_dt(dve)
        dve_ssm(dve)
        dve_ssm_out(dve)
        dve_router_weights(dve, 1)
        dve_norm(dve, 3)
        dve_router(dve, 1)
        dve_moe(dve, 1)
        dve_norm(dve, FINAL)
        dve_norm(dve, 5)
        dve_evin(dve)
        dve_gmlp(dve)
        dve_qknorm(dve)
        dve_attention(dve, 1, S1, lambda h: CAUSAL[:])
        dve_s5_vectors(dve)
        dve_residual(dve, "evout", 4, 1, None)
        dve_norm(dve, 6)
        dve_ffn(dve, 0)
        dve_norm(dve, 7)
        dve_ple(dve, 0)
        dve_ple_gates(dve, 0)
        dve_norm(dve, PLAIN)
        dve_s5(dve)
        dve_glu(dve)
        dve_norm(dve, 9)
        dve_ffn(dve, 1)
        dve_norm(dve, 10)
        dve_ple(dve, 1)
        dve_ple_gates(dve, 1)

    def pool_program(pool):
        pool_constants(pool)
        split_units(pool.e, 0, 2)
        pool_norm(pool)
        split_units(pool.e, 2, plan.u["moe0"])
        pool_norm(pool)
        pool_moe(pool, 0)
        split_units(pool.e, plan.u["norm2"], plan.u["norm2"] + 2)
        pool_norm(pool)
        split_units(pool.e, plan.u["norm2"] + 2, plan.u["moe1"])
        pool_norm(pool)
        pool_moe(pool, 1)
        split_units(pool.e, plan.u["norm5"], plan.u["norm5"] + 2)
        pool_norm(pool)
        split_units(pool.e, plan.u["norm5"] + 2, plan.u["norm6"] + 2)
        pool_norm(pool)
        split_units(pool.e, plan.u["norm6"] + 2, plan.u["norm7"] + 2)
        pool_norm(pool)
        split_units(pool.e, plan.u["norm7"] + 2, plan.u["glu"] + 2)
        pool_s5(pool)
        split_units(pool.e, plan.u["glu"] + 2, plan.u["norm9"] + 2)
        pool_norm(pool)
        split_units(pool.e, plan.u["norm9"] + 2, plan.u["norm10"] + 2)
        pool_norm(pool)
        split_units(pool.e, plan.u["norm10"] + 2, plan.unit)

    def pe_banks_read(pe, b):
        for k in range(b - 4, b):
            pe.e.wait_ge(bank_free[k % 4], k // 4 + 1)

    sp_chain, pe_chain = sem("sp_chain"), sem("pe_chain")

    with ctx:
        block = ctx.enter_context(nc.Block())

        @block.scalar
        def _(eng):
            act = Engine(eng, act_chain)
            act_program(act)
            act_store(act)

        @block.sync
        def _(eng):
            sp = Engine(eng, sp_chain)
            sp_load_all(sp)
            sp_store(eng)

        @block.gpsimd
        def _(eng):
            pool_program(Engine(eng, pool_chain))

        @block.tensor
        def _(eng):
            pe = Engine(eng, pe_chain)
            pe_program(pe)
            pe_store(pe)

        @block.vector
        def _(eng):
            dve_program(Engine(eng, dve_chain))


def kernel(**inputs):
    import numpy as np
    import concourse.bacc as bacc
    from concourse.bass_utils import run_bass_kernel_spmd

    nc = bacc.Bacc("TRN2", target_bir_lowering=False, num_devices=1)
    arrays = {f"in_{name}": np.ascontiguousarray(value) for name, value in inputs.items()}
    arrays["in_rel_flip"] = np.ascontiguousarray(np.asarray(inputs["rel_bias"])[..., ::-1])
    t = {name[3:]: nc.dram_tensor(name, a.shape, F32, kind="ExternalInput").ap() for name, a in arrays.items()}
    out = nc.dram_tensor("out_0_dram", (1, SEQ, D), F32, kind="ExternalOutput").ap()
    build(nc, t, out)
    return run_bass_kernel_spmd(nc, [arrays], core_ids=[0]).results[0]["out_0_dram"]
```

```python
from contextlib import ExitStack

import concourse.bass as bass
from concourse import mybir

F32 = mybir.dt.float32
F32R = mybir.dt.float32r
I32 = mybir.dt.int32
ACT = mybir.ActivationFunctionType
ALU = mybir.AluOpType
AX = mybir.AxisListType

P = 128
SEQ = 512
D = 1024
KD = D // P
NT = SEQ // P
EPS = 1e-6
NEG = -1e30
UNIT = 2048
HALF = D // 2
HEADS = 8
HD = 64
REL_CLIP = 256
SSM_G = 8
SSM_H = 32
SSM_INNER = 2048
EXPERTS = 32
GROUPS = 4
EPG = 8
NO_ROW = 8192.0
SLOTS = -(-(EXPERTS + (2 * SEQ - EXPERTS) // P) // 4) * 4
FF = 2816
FB = FF // P
S5_P = 64
S5_C = 16
S5_TILES = 32
S5_L = 4
S5_N = SEQ // S5_L
S5_LOW, S5_HIGH = 16, 8
S5_IDX = S5_LOW + S5_HIGH
TRI = sum(SEQ - P * i for i in range(NT))
TRI_AT = [0, 512, 896, 1152]
TWO_PI = 6.283185307179586
ROUND = 12582912.0
TWO_PI_PARTS = (6.28125, 0.00193500518798828125, 3.0199159819e-07)
EXP_SERIES = [1 / f for f in (362880, 40320, 5040, 720, 120, 24, 6, 2, 1)]


class Plan:

    def __init__(self):
        self.unit, self.pair, self.bank = 0, 0, 0
        self.u, self.p, self.b = {}, {}, {}

    def step(self, name, units=0, pairs=0, banks=0):
        self.u[name], self.p[name], self.b[name] = self.unit, self.pair, self.bank
        self.unit += units
        self.pair += pairs
        self.bank += banks


def make_plan():
    plan = Plan()
    plan.step("columns", banks=1)
    plan.step("load", banks=8)

    def norm(n):
        plan.step(f"norm{n}", banks=1)

    def moe(layer):
        plan.step(f"moe{layer}", units=SLOTS, pairs=NT + 2 * SLOTS + 4, banks=4 + 2 * SLOTS)

    def ffn(layer):
        plan.step(f"ffn{layer}", units=34, pairs=26)

    def ple(layer):
        plan.step(f"ple{layer}", units=6, pairs=8)

    norm(0)
    plan.step("ada", banks=2)
    plan.step("columns_rest", banks=5)
    plan.step("mixin", units=8, pairs=8)
    plan.step("ada_mixin", banks=4)
    plan.step("pool", banks=4)
    plan.step("att0", pairs=2 * HEADS, banks=4 * HEADS)
    plan.step("mixout", units=4, pairs=4)
    norm(1)
    plan.step("ada_norm1", banks=3)
    moe(0)
    norm(2)
    plan.step("dt", banks=4)
    plan.step("ssm", units=24, pairs=24, banks=8 * SSM_G)
    plan.step("ssmout", units=8, pairs=8)
    norm(3)
    moe(1)
    norm(4)
    norm(5)
    plan.step("evin", units=10, pairs=10)
    plan.step("gate", banks=4)
    plan.step("qknorm", banks=8)
    plan.step("gmlp", banks=4)
    plan.step("att1", pairs=2 * HEADS, banks=4 * HEADS)
    plan.step("s5a", banks=1)
    plan.step("evout", units=4, pairs=4)
    norm(6)
    ffn(0)
    plan.step("ple_rows0", banks=2)
    norm(7)
    ple(0)
    norm(8)
    plan.step("s5c", banks=4)
    plan.step("s5", pairs=8, banks=6 * KD)
    plan.step("glu", units=8, pairs=8)
    norm(9)
    ffn(1)
    plan.step("ple_rows1", banks=2)
    norm(10)
    ple(1)
    plan.step("store", banks=8)
    return plan


class Engine:

    def __init__(self, eng, chain):
        self.e, self.chain = eng, chain
        self.count = {}

    def _entry(self, sem):
        return self.count.setdefault(sem.name, [0, 0, sem])

    def wait(self, sem, events=1):
        entry = self._entry(sem)
        entry[0] += events
        self.e.wait_ge(sem, entry[1] + entry[0])

    def seen(self, sem):
        entry = self._entry(sem)
        return entry[1] + entry[0]

    def passed(self, sem, events):
        self._entry(sem)[0] += events

    def link(self, ins):
        ins.then_inc(self.chain, 1)
        self.wait(self.chain)

    def loop(self, times, per):
        return Loop(self, times, per)


class Loop:

    def __init__(self, engine, times, per):
        self.engine, self.times, self.per = engine, times, per

    def __enter__(self):
        self.fori = self.engine.e.Fori(0, self.times)
        i = self.fori.__enter__()
        self.saved = {}
        for sem, n in self.per.items():
            entry = self.engine._entry(sem)
            self.saved[sem.name] = (entry[0], entry[1])
            entry[1] = i * n + (entry[1] + entry[0])
            entry[0] = 0
        return i

    def __exit__(self, *exc):
        if exc[0] is None:
            for sem, n in self.per.items():
                entry = self.engine._entry(sem)
                assert entry[0] == n, (sem.name, entry[0], n)
                done, before = self.saved[sem.name]
                entry[0], entry[1] = done + self.times * n, before
        return self.fori.__exit__(*exc)


def column_vectors(t):
    rows = [
        ("c", t["c"].rearrange("b (k p) -> (b k) p", p=P)),
        ("ada_b", t["ada_b"].rearrange("l (k p) -> (l k) p", p=P)),
        ("norm1", t["norm1_w"].rearrange("l (k p) -> (l k) p", p=P)),
        ("norm2", t["norm2_w"].rearrange("l (k p) -> (l k) p", p=P)),
        ("pool_scale", t["pool_scale"].rearrange("l (k p) -> (l k) p", p=P)),
        ("conv_w", t["ssm_conv_w"].rearrange("l j (k p) -> (l j k) p", p=P)),
        ("conv_b", t["ssm_conv_b"].rearrange("l (k p) -> (l k) p", p=P)),
        ("ssm_norm", t["ssm_norm_w"].rearrange("l (k p) -> (l k) p", p=P)),
        ("final", t["final_norm_w"].rearrange("(k p) -> k p", p=P)),
        ("norm_mix", t["norm_mix_2"].rearrange("l (k p) -> (l k) p", p=P)),
        ("norm_ffn", t["norm_ffn_2"].rearrange("l (k p) -> (l k) p", p=P)),
        ("od_d", t["od_d_2"].rearrange("l (k p) -> (l k) p", p=P)),
        ("fconv_w", t["ffn_conv_w_2"].rearrange("l j (k p) -> (l j k) p", p=P)),
        ("fconv_b", t["ffn_conv_b_2"].rearrange("l (k p) -> (l k) p", p=P)),
    ]
    at, n = {}, 0
    for name, ap in rows:
        at[name] = n
        n += ap.shape[0]
    return rows, at, n


def bcast(ap, dim, n):
    shape = list(ap.shape)
    return ap.unsqueeze(dim).broadcast_to(shape[:dim] + [n] + shape[dim:])


def build(nc, t, out):
    plan = make_plan()
    ctx = ExitStack()

    def sem(name):
        return ctx.enter_context(nc.semaphore(name))

    def sb(name, shape, dt=F32, where=None):
        return (where or ctx).enter_context(nc.sbuf_tensor(name, shape, dt))

    X = sb("X", [P, KD, SEQ])
    HH = sb("HH", [P, KD, SEQ], F32R)
    r = ExitStack()
    HL = sb("HL", [P, KD, SEQ], F32R, r)
    r.close()
    HF = sb("HF", [P, KD, SEQ])
    RAW = sb("RAW", [P, 2, UNIT])
    WH = sb("WH", [P, 2, UNIT], F32R)
    WL = sb("WL", [P, 2, UNIT], F32R)
    rows, col_at, n_cols = column_vectors(t)
    n_row_tiles = -(-n_cols // P)
    COLS = sb("COLS", [P, n_row_tiles * P])
    IDENT = sb("IDENT", [P, P])
    ONES = sb("ONES", [P, P])
    HEAD_ONES = sb("HEAD_ONES", [P, P])
    r = ExitStack()
    LATER = sb("LATER", [P, SEQ], F32, r)
    CAUSAL = sb("CAUSAL", [P, SEQ], F32, r)
    r.close()
    FUP = sb("FUP", [P, 2, SEQ])
    MOD = sb("MOD", [P, 2 * 6 * KD])
    GAIN = sb("GAIN", [P, 4, KD])
    SQ = sb("SQ", [P, 2, SEQ])
    RSTD = sb("RSTD", [P, SEQ])
    TMP = sb("TMP", [P, 2, SEQ])
    r = ExitStack()
    ROUTER_W = sb("ROUTER_W", [P, 2, KD, GROUPS + EXPERTS], F32, r)
    ROUTER_B = sb("ROUTER_B", [P, 2, GROUPS + EXPERTS], F32, r)
    DT_W = sb("DT_W", [P, KD, SSM_H], F32, r)
    DT_ROW = sb("DT_ROW", [P, 2, SSM_H], F32, r)
    D_ROW = sb("D_ROW", [P, SSM_H], F32, r)
    D_COL = sb("D_COL", [P, 2 * SSM_G], F32, r)
    r.close()
    S5K = sb("S5K", [P, 5, S5_TILES])
    A_POW = sb("A_POW", [P, 2, S5_L + 1, S5_TILES])
    A_REV = sb("A_REV", [P, 2, S5_L, S5_TILES])
    SPARE = sb("SPARE", [P, (4064 - 23 * 4 * S5_TILES) // 4])
    FG_W = sb("FG_W", [P, KD, HEADS])
    FG_B = sb("FG_B", [P, HEADS])
    QK_GAIN = sb("QK_GAIN", [P, 2])
    INV_COUNT = sb("INV_COUNT", [P, 16])
    FALLING = sb("FALLING", [P, EPG])
    C_ACT = sb("C_ACT", [P, KD])
    MX = sb("MX", [P, 2, 2, NT])
    TURN = sb("TURN", [P, 2])
    SUMS = sb("SUMS", [P, 2, NT])

    def region():
        return ExitStack()

    r = region()
    STRIP = sb("STRIP", [P, HEADS, SEQ], F32, r)
    XTOK = sb("XTOK", [P, NT, D], F32, r)
    ROWS = sb("ROWS", [P, n_row_tiles, P], F32, r)
    REL = sb("REL", [P, 640], F32, r)
    GAP0 = sb("GAP0", [P, 40 * 256 - HEADS * SEQ - NT * D - n_row_tiles * P - 640], F32, r)
    ADA_A = sb("ADA_A", [P, 2, 2, D], F32, r)
    ADA_SUM0 = sb("ADA_SUM0", [P, D], F32, r)
    ADA_B = sb("ADA_B", [P, 2, 2, D], F32, r)
    ADA_SUM2 = sb("ADA_SUM2", [P, D], F32, r)
    GAP1 = sb("GAP1", [P, 4 * P], F32, r)
    ADA_SUM1 = sb("ADA_SUM1", [P, D], F32, r)
    r.close()
    r = region()
    STRIP_ = sb("STRIP_", [P, HEADS, SEQ], F32, r)
    Q0 = sb("Q0", [P, 4, SEQ], F32, r)
    K0 = sb("K0", [P, 4, SEQ], F32, r)
    V0 = sb("V0", [P, NT, HALF], F32, r)
    S0 = sb("S0", [P, 2, TRI], F32, r)
    PT0 = sb("PT0", [P, 2, TRI], F32, r)
    U = sb("U", [P, 4, SEQ], F32, r)
    POOLED = sb("POOLED", [P, 4, SEQ], F32, r)
    PSCR = sb("PSCR", [P, 2, SEQ], F32, r)
    POOL_W = sb("POOL_W", [P, 4, P], F32, r)
    r.close()
    r = region()
    r2 = region()
    HTOK = sb("HTOK", [P, NT, D], F32, r2)
    r2.close()
    W2H = sb("W2H", [P, 2, D], F32R, r)
    W2L = sb("W2L", [P, 2, D], F32R, r)
    W2RAW = sb("W2RAW", [P, 2, D], F32, r)
    XG = sb("XG", [P, 2, D], F32, r)
    OG = sb("OG", [P, 2, D], F32, r)
    GH = sb("GH", [P, 2, KD, P], F32R, r)
    GL = sb("GL", [P, 2, KD, P], F32R, r)
    HS = sb("HS", [P, 2, P], F32, r)
    HID = sb("HID", [P, 2, P], F32, r)
    HTH = sb("HTH", [P, 2, P], F32R, r)
    HTL = sb("HTL", [P, 2, P], F32R, r)
    IDENT_R = sb("IDENT_R", [P, P], F32R, r)
    STRICT = sb("STRICT", [P, P], F32, r)
    ROUTER_WH = sb("ROUTER_WH", [P, KD, GROUPS + EXPERTS], F32R, r)
    ROUTER_WL = sb("ROUTER_WL", [P, KD, GROUPS + EXPERTS], F32R, r)
    LOGIT = sb("LOGIT", [P, NT, GROUPS + EXPERTS], F32, r)
    GATE = sb("GATE", [P, 12, NT, EPG], F32, r)
    ESEL = sb("ESEL", [P, NT, GROUPS, EPG], F32, r)
    MASK = sb("MASK", [P, 2, NT, EXPERTS], F32, r)
    BOTH = sb("BOTH", [P, NT, EXPERTS], F32, r)
    SHARE = sb("SHARE", [P, 2, NT], F32, r)
    PLACE = sb("PLACE", [P, 3, EXPERTS], F32, r)
    POS = sb("POS", [P, 2, NT], F32, r)
    ROW_AT = sb("ROW_AT", [P, 2, NT], F32, r)
    SLOT_AT = sb("SLOT_AT", [P, SLOTS], F32, r)
    SLOT_E = sb("SLOT_E", [P, SLOTS], F32, r)
    SLOT_I = sb("SLOT_I", [P, SLOTS], I32, r)
    GATHER_I = sb("GATHER_I", [P, SLOTS], I32, r)
    SCATTER_I = sb("SCATTER_I", [P, SLOTS], I32, r)
    OWNER = sb("OWNER", [P, SLOTS, EXPERTS], F32, r)
    PLACE_AT = sb("PLACE_AT", [P, P], F32, r)
    SLOT_ROW = sb("SLOT_ROW", [P, SLOTS], F32, r)
    ROW_SLOT = sb("ROW_SLOT", [P, 2 * NT], F32, r)
    ROW_PLACE = sb("ROW_PLACE", [P, 2 * NT], F32, r)
    r.close()
    r = region()
    G = sb("G", [P, 2 * SSM_G, SEQ], F32, r)
    ZS = sb("ZS", [P, 2, 2, SEQ], F32, r)
    CONV = sb("CONV", [P, 2, 4, SEQ], F32, r)
    r2 = region()
    DT_WH = sb("DT_WH", [P, KD, SSM_H], F32R, r2)
    DT_WL = sb("DT_WL", [P, KD, SSM_H], F32R, r2)
    r2.close()
    XDT = sb("XDT", [P, NT, 256], F32, r)
    CBM = sb("CBM", [P, TRI], F32, r)
    DECAY = sb("DECAY", [P, 2, TRI], F32, r)
    ACS_ROW = sb("ACS_ROW", [P, 2, SEQ], F32, r)
    DT = sb("DT", [P, NT, SSM_H], F32, r)
    DTS = sb("DTS", [P, 6, NT, SSM_H], F32, r)
    ACS = sb("ACS", [SSM_H, 2, SEQ], F32, r)
    ACS_COL = sb("ACS_COL", [P, NT, SSM_H], F32, r)
    r.close()
    r = region()
    UA = sb("UA", [P, 4, SEQ], F32, r)
    VA = sb("VA", [P, NT, HALF], F32, r)
    VSQ = sb("VSQ", [P, NT, HALF], F32, r)
    Q1 = sb("Q1", [P, 4, SEQ], F32, r)
    K1 = sb("K1", [P, 4, SEQ], F32, r)
    V1 = sb("V1", [P, NT, HALF], F32, r)
    S1 = sb("S1", [P, 2, TRI], F32, r)
    PT1 = sb("PT1", [P, 2, TRI], F32, r)
    SPAT = sb("SPAT", [P, 4, P], F32, r)
    SPAT_T = sb("SPAT_T", [P, 4, P], F32, r)
    SPAT_B = sb("SPAT_B", [P, 4, P], F32, r)
    V_GAIN = sb("V_GAIN", [P, HALF], F32, r)
    FG_WH = sb("FG_WH", [P, KD, HEADS], F32R, r)
    FG_WL = sb("FG_WL", [P, KD, HEADS], F32R, r)
    FGL = sb("FGL", [P, 6, NT, HEADS], F32, r)
    FCUM = sb("FCUM", [HEADS, 2, SEQ], F32, r)
    MINUS_HEAD = sb("MINUS_HEAD", [HEADS, HEADS, P], F32, r)
    VR = sb("VR", [P, 16], F32, r)
    AROW = sb("AROW", [S5_TILES, 2, P], F32, r)
    LDT_ROW = sb("LDT_ROW", [P, 2 * S5_TILES], F32, r)
    r.close()
    r = region()
    FHH = sb("FHH", [P, FB, SEQ], F32R, r)
    FHL = sb("FHL", [P, FB, SEQ], F32R, r)
    r.close()
    r = region()
    PTOK = sb("PTOK", [P, NT, 256], F32, r)
    PH = sb("PH", [P, 2, SEQ], F32R, r)
    PL = sb("PL", [P, 2, SEQ], F32R, r)
    PROJ = sb("PROJ", [P, 4, SEQ], F32, r)
    OTOK = sb("OTOK", [P, NT, D], F32, r)
    r.close()
    r = region()
    BB = sb("BB", [P, 2, S5_TILES, S5_C], F32, r)
    CK = sb("CK", [P, 2, S5_TILES, S5_C], F32, r)
    TAB = sb("TAB", [P, 2, S5_TILES, S5_IDX], F32, r)
    W1X = sb("W1X", [P, 2, 2, 4, S5_L, 2, S5_C], F32, r)
    r2 = region()
    CRAW = sb("CRAW", [P, 2, KD, 2, S5_P], F32, r2)
    BRAW = sb("BRAW", [P, 2, S5_TILES, S5_C], F32, r2)
    ANGLE = sb("ANGLE", [P, 2, S5_TILES, S5_IDX], F32, r2)
    r2.close()
    TURNING = sb("TURNING", [P, 2, 3, 4, S5_N], F32, r)
    PRP = sb("PRP", [P, 2, 4, S5_N], F32, r)
    PAD = sb("PAD", [P, S5_N * 4], F32, r)
    CAX = sb("CAX", [P, 2, 2, 4, S5_L + 1, 2, S5_C], F32, r)
    W1_T = sb("W1_T", [P, 2, 2, 4, P], F32, r)
    W3 = sb("W3", [P, 2, 4, P], F32, r)
    U4 = sb("U4", [P, 2, 4, S5_N], F32, r)
    XS = sb("XS", [P, 2, 4, S5_N], F32, r)
    PR = sb("PR", [P, 4, 4, S5_N], F32, r)
    S5_AT = sb("S5_AT", [P, S5_IDX], F32, r)
    FIRST = sb("FIRST", [P, S5_N], F32, r)
    Y4 = sb("Y4", [P, 4, S5_N], F32, r)
    r.close()

    PAIR = [ctx.enter_context(nc.psum_tensor(f"PAIR{i}", [P, 2, SEQ], F32)) for i in range(2)]
    BANK = [ctx.enter_context(nc.psum_tensor(f"BANK{i}", [P, SEQ], F32)) for i in range(4)]

    strip_dram = nc.dram_tensor("strip_scratch", (P, HEADS, 640), F32, kind="Internal").ap()
    rel_dram = nc.dram_tensor("rel_scratch", (HEADS, 640), F32, kind="Internal").ap()
    htok_dram = nc.dram_tensor("htok_scratch", (SEQ, D), F32, kind="Internal").ap()
    y_dram = nc.dram_tensor("y_scratch", (2 * SEQ, D), F32, kind="Internal").ap()
    acs_dram = nc.dram_tensor("acs_scratch", (SSM_H, SEQ), F32, kind="Internal").ap()

    landed = [sem("unit_landed0"), sem("unit_landed1")]
    split_hi = sem("split_hi")
    split_ready = sem("split_ready")
    unit_done = sem("unit_done")
    evac = [sem("pair_evacuated0"), sem("pair_evacuated1")]
    bank_ready = sem("bank_ready")
    bank_free = [sem(f"bank_free{i}") for i in range(4)]
    consts_ready = sem("consts_ready")
    dve_chain, act_chain, pool_chain = sem("dve_chain"), sem("act_chain"), sem("pool_chain")
    x_landed, small_landed = sem("x_landed"), sem("small_landed")
    rows_landed = [sem("rows_landed"), sem("more_rows_landed")]
    ada_landed = [sem(f"ada_landed{i}") for i in range(4)]
    ada_used, ada_added = sem("ada_used"), sem("ada_added")
    c_ready, x_ready = sem("c_ready"), sem("x_ready")
    sq_ready, sq_used, var_ready, root_ready = sem("sq_ready"), sem("sq_used"), sem("var_ready"), sem("root_ready")
    pre_ready, hi_ready, h_ready = sem("pre_ready"), sem("hi_ready"), sem("h_ready")
    norm_pre, norm_hi = sem("norm_pre"), sem("norm_hi")

    def take_bank(pe, b, turns=0):
        if b // 4 + (0 if isinstance(turns, int) else 1) > 0:
            pe.e.wait_ge(bank_free[b % 4], turns + b // 4)
        return BANK[b % 4]

    def full_bank(eng, b, turns=0):
        eng.e.wait_ge(bank_ready, turns * 4 + (b + 1))
        return BANK[b % 4]

    def take_pair(pe, p, turns=0):
        if p // 2 + (0 if isinstance(turns, int) else 1) > 0:
            pe.e.wait_ge(evac[p % 2], turns + p // 2)
        return PAIR[p % 2]

    def mm3(o, wh, wl, xh, xl, start, stop):
        nc.tensor.matmul(o, wh, xh, start=start, stop=False)
        nc.tensor.matmul(o, wh, xl, start=False, stop=False)
        return nc.tensor.matmul(o, wl, xh, start=False, stop=stop)

    def unit_channels(pe, u, pair, xh, xl, tiles, first=True, last=True, off=0):
        s = u % 2
        pe.e.wait_ge(split_ready, off + (u + 1))
        for m in range(2):
            for k in range(tiles):
                c = (k * 2 + m) * P
                ins = mm3(pair[:, m, :], WH[:, s, c:c + P], WL[:, s, c:c + P], xh(k), xl(k),
                          first and k == 0, last and k == tiles - 1)
        ins.then_inc(unit_done, 1)

    def first_unit(pe, u, pair, h, off=0):
        s = u % 2
        pe.e.wait_ge(split_ready, off + (u + 1))
        for k in range(KD):
            pe.e.wait_ge(h_ready, h + k + 1)
            for m in range(2):
                c = (k * 2 + m) * P
                ins = mm3(pair[:, m, :], WH[:, s, c:c + P], WL[:, s, c:c + P], HH[:, k, :], HL[:, k, :], k == 0, k == KD - 1)
        ins.then_inc(unit_done, 1)

    def unit_tokens(pe, u, pair):
        s = u % 2
        pe.e.wait_ge(split_ready, u + 1)
        for tt in range(NT):
            o = pair[:, tt // 2, (tt % 2) * 256:(tt % 2) * 256 + 256]
            for k in range(KD):
                c, a = slice(k * 256, k * 256 + 256), slice(tt * P, tt * P + P)
                ins = mm3(o, HH[:, k, a], HL[:, k, a], WH[:, s, c], WL[:, s, c], k == 0, k == KD - 1)
        ins.then_inc(unit_done, 1)

    def full_pair(eng, u, p, off=0):
        eng.e.wait_ge(unit_done, off + (u + 1))
        return PAIR[p % 2]

    hh = lambda k: HH[:, k, :]
    hl = lambda k: HL[:, k, :]

    def mod(layer, c, k):
        at = (layer * 6 + c) * KD + k
        return MOD[:, at:at + 1]

    def col(name, i):
        at = col_at[name] + i
        return COLS[:, at:at + 1]

    dram = lambda name, offset, ap: bass.AP(t[name].tensor, t[name].offset + offset, ap)

    def ada_slot(n):
        return n % 4 if n < 12 else n % 2 if n < 24 else 2 + n % 2

    def ada_place(n):
        others = [i for i in range(n) if ada_slot(i) == ada_slot(n)]
        return ada_slot(n), len(others), others[-1] if others else None

    def ada_piece(slot):
        return (ADA_A, ADA_B)[slot // 2][:, slot % 2]

    def ada_sum(q):
        return ADA_SUM0 if q == 11 else ADA_SUM1 if q % 2 else ADA_SUM0 if q < 6 else ADA_SUM2

    def ada_bank(q):
        for name, first, n in (("ada", 0, 2), ("ada_mixin", 2, 4), ("ada_norm1", 9, 3)):
            if first <= q < first + n:
                return plan.b[name] + q - first

    def dve_ada(dve, first, last):
        for n in range(first, last):
            q, j = n // 4, n % 4
            slot, uses, _ = ada_place(n)
            acc = ada_sum(q)
            dve.e.wait_ge(ada_landed[slot], 16 * (uses + 1))
            if n:
                dve.e.wait_ge(ada_used, n)
            if j == 0:
                dve.link(dve.e.tensor_scalar(acc[:], ada_piece(slot)[:, 0, :], C_ACT[:, 0:1], None, ALU.mult))
            else:
                dve.link(dve.e.scalar_tensor_tensor(acc[:], ada_piece(slot)[:, 0, :], C_ACT[:, 2 * j:2 * j + 1], acc[:],
                                                    ALU.mult, ALU.add))
            dve.e.scalar_tensor_tensor(acc[:], ada_piece(slot)[:, 1, :], C_ACT[:, 2 * j + 1:2 * j + 2], acc[:],
                                       ALU.mult, ALU.add).then_inc(ada_used, 1)

    def pe_ada(pe, q, o=None):
        pe.e.wait_ge(ada_used, 4 * (q + 1))
        own = o is None
        if own:
            o = take_bank(pe, ada_bank(q))
        for m in range(KD):
            ins = nc.tensor.matmul(o[:, m:m + 1], ada_sum(q)[:, m * P:m * P + P], ONES[:, 0:1], start=True, stop=True)
        if own:
            ins.then_inc(bank_ready, 1)
        return ins

    def dve_ada_end(dve, q, o=None):
        done, value = ada_added, q - 5
        if o is None:
            b = ada_bank(q)
            o, done, value = full_bank(dve, b), bank_free[b % 4], b // 4 + 1
        at = col_at["ada_b"] + q * KD
        dve.e.tensor_tensor(MOD[:, q * KD:q * KD + KD], o[:, 0:KD], COLS[:, at:at + KD], ALU.add).then_inc(done, 1)
        dve.e.wait_ge(done, value)
        if q % 3 == 1:
            n = q // 3
            w = col_at[("norm1", "norm2")[n % 2]] + n // 2 * KD
            dve.link(dve.e.scalar_tensor_tensor(GAIN[:, n, :], MOD[:, q * KD:q * KD + KD], 1.0, COLS[:, w:w + KD],
                                                ALU.add, ALU.mult))

    sp_unit = [0]

    def load_unit(sp, first, second, off=0, u=None):
        if u is None:
            u = sp_unit[0]
            sp_unit[0] += 1
        s = u % 2
        if u >= 2 or not isinstance(off, int):
            sp.wait_ge(split_ready, off + (u - 1))
        for src, dst in (first, second):
            sp.dma_start(dst(RAW[:, s, :]), src).then_inc(landed[s], 16)

    def block_unit(w, c0, rows=KD, row0=0):
        h = rows // 2
        view = w.rearrange("(k p) n -> p k n", p=P)
        part = lambda a, b: (view[:, row0 + a:row0 + b, bass.ds(c0, 256)] if not isinstance(c0, int)
                             else view[:, row0 + a:row0 + b, c0:c0 + 256],
                             lambda raw: raw[:, a * 256:b * 256].rearrange("p (k n) -> p k n", n=256))
        return part(0, h), part(h, rows)

    def paired_unit(w1, c1, w2, c2):
        def part(w, c, m):
            cols = slice(c, c + P) if isinstance(c, int) else bass.ds(c, P)
            return (w.rearrange("(k p) n -> p k n", p=P)[:, :, cols],
                    lambda raw: raw.rearrange("p (k m n) -> p k m n", m=2, n=P)[:, :, m, :])
        return part(w1, c1, 0), part(w2, c2, 1)

    def sp_load_all(engine):
        sp = engine.e
        mix_in, mix_out = t["mix_w_in"][0], t["mix_w_out"][0]
        def ada(first, last):
            for n in range(first, last):
                slot, uses, before = ada_place(n)
                if before is not None:
                    sp.wait_ge(ada_used, before + 1)
                q, j = n // 4, n % 4
                src = t["ada_w"][q // 6].rearrange("(k p) n -> p k n", p=P)[:, 2 * j:2 * j + 2, (q % 6) * D:(q % 6) * D + D]
                sp.dma_start(ada_piece(slot), src).then_inc(ada_landed[slot], 16)

        def plain(w, n):
            for i in range(n):
                load_unit(sp, *block_unit(w, i * 256))

        def ffn(layer):
            u0 = plan.u[f"ffn{layer}"]
            w = t["ffn_w_up_2"][layer]
            with sp.Fori(0, FB // 2) as i:
                for b in range(2):
                    load_unit(sp, *paired_unit(w, i * 256 + b * P, w, i * 256 + (b * P + FF)), off=i * 2, u=u0 + b)
            w = t["ffn_w_down_2"][layer]
            with sp.Fori(0, 2) as i:
                for c in range(2):
                    for j, (k0, n) in enumerate(((0, 8), (8, 8), (16, 6))):
                        load_unit(sp, *block_unit(w, i * 512 + c * 256, n, k0), off=i * 6, u=u0 + FB + 3 * c + j)
            sp_unit[0] += 34

        def ple(layer):
            wp, wg = t["ple_w_proj_2"][layer], t["ple_w_gate_2"][layer]
            for half in range(2):
                view = wp.rearrange("(k p) n -> p k n", p=P)
                part = lambda k: (view[:, k, half * 512:half * 512 + 512], lambda raw: raw[:, k * 512:k * 512 + 512])
                load_unit(sp, part(0), part(1))
                for i in range(2):
                    load_unit(sp, *block_unit(wg, half * 512 + i * 256))

        sp.wait_ge(rows_landed[0], 16 * row_dmas[0])
        ada(0, 2)
        sp.dma_start(XTOK[:], t["x"][0].rearrange("(t p) d -> p t d", p=P)).then_inc(x_landed, 16)
        ada(2, 8)
        for i in range(8):
            load_unit(sp, *block_unit(mix_in, i * 256))
            if i == 1:
                ada(8, 12)
            if 3 <= i <= 7:
                ada(*((12, 14), (14, 16), (16, 18), (18, 20), (20, 24))[i - 3])
        plain(mix_out, 4)
        sp.wait_ge(bank_ready, plan.b["pool"] + 4)
        ada(24, 48)
        sp_moe(engine, 0)
        w = t["ssm_w_in"][0]
        gates = w[:, 0:SSM_INNER].rearrange("(k p) (g n) -> p k g n", p=P, n=256)

        def gate_unit(g):
            half = lambda a: (gates[:, a:a + 4, bass.ds(g, 1), :].rearrange("p k g n -> p k (g n)"),
                              lambda raw: raw[:, a * 256:a * 256 + 1024].rearrange("p (k n) -> p k n", n=256))
            return half(0), half(4)

        with sp.Fori(0, SSM_G // 2) as i:
            for b in range(2):
                u = plan.u["ssm"] + 3 * b
                c = i * 256 + (2 * SSM_INNER + b * P)
                load_unit(sp, *paired_unit(w, c, w, c + SSM_G * P), off=i * 6, u=u)
                load_unit(sp, *block_unit(w, i * 512 + (SSM_INNER + b * 256)), off=i * 6, u=u + 1)
                load_unit(sp, *gate_unit(i * 2 + b), off=i * 6, u=u + 2)
        sp_unit[0] += 24
        for half in range(2):
            for i in range(4):
                load_unit(sp, *block_unit(t["ssm_w_out"][0], i * 256, KD, half * KD))
        sp_moe(engine, 1)
        plain(t["ev_w_in_2"][0], 10)
        plain(t["ev_w_out_2"][0], 4)
        ffn(0)
        ple(0)
        w = t["od_w_glu_2"][0]
        for i in range(KD):
            load_unit(sp, *paired_unit(w, i * P, w, D + i * P))
        ffn(1)
        ple(1)
        assert sp_unit[0] == plan.unit

    def pool_constants(engine):
        pool, link = engine.e, engine.link
        pool.memset(IDENT[:], 0.0)
        pool.memset(ONES[:], 1.0)
        pool.memset(HEAD_ONES[:], 0.0)
        pool.memset(LATER[:], 1.0)
        for n in range(16):
            pool.memset(INV_COUNT[:, n:n + 1], 1.0 / (n + 1))
        for n in range(EPG):
            pool.memset(FALLING[:, n:n + 1], float(EPG - n))
        link(pool.memset(CAUSAL[:], 0.0))
        for h in range(2):
            link(pool.memset(HEAD_ONES[h * HD:h * HD + HD, h * HD:h * HD + HD], 1.0))
        pool.affine_select(out=IDENT[:], in_=IDENT[:], compare_op=ALU.not_equal, fill=1.0, base=0,
                           pattern=[[-1, P]], channel_multiplier=1)
        pool.affine_select(out=LATER[:], in_=LATER[:], compare_op=ALU.is_ge, fill=0.0, base=0,
                           pattern=[[1, SEQ]], channel_multiplier=-1)
        pool.affine_select(out=CAUSAL[:], in_=CAUSAL[:], compare_op=ALU.is_ge, fill=NEG, base=SEQ - P,
                           pattern=[[-1, SEQ]], channel_multiplier=1).then_inc(consts_ready, 1)

    def split_unit(pool, u, off=0):
        s = u % 2
        pool.wait_ge(landed[s], off * 16 + 32 * (u // 2 + 1))
        if u >= 2 or not isinstance(off, int):
            pool.wait_ge(unit_done, off + (u - 1))
        pool.tensor_tensor(TURN[:, s:s + 1], ONES[:, 0:1], ONES[:, 0:1], ALU.mult)
        pool.tensor_scalar(WH[:, s], RAW[:, s], 1.0, 1.0, ALU.mult, ALU.mult).then_inc(split_hi, 1)
        pool.wait_ge(split_hi, off + (u + 1))
        pool.tensor_tensor(WL[:, s], RAW[:, s], WH[:, s].bitcast(F32), ALU.subtract).then_inc(split_ready, 1)

    def split_units(pool, first, last):
        last = min(last, plan.unit)
        if last - first >= 4:
            with pool.Fori(0, (last - first) // 2) as i:
                for b in range(2):
                    split_unit(pool, first + b, off=i * 2)
        else:
            for u in range(first, last):
                split_unit(pool, u)

    def act_loads(act):
        def load(dst, src, s):
            act.dma_start(dst, src).then_inc(s, 16)

        def load_rows(rest):
            for name, ap in rows:
                at, left, done = col_at[name], ap.shape[0], 0
                while left:
                    k = min(left, P - at % P)
                    if (at >= P) == rest:
                        load(ROWS[at % P:at % P + k, at // P, :], ap[done:done + k], rows_landed[rest])
                        row_dmas[rest] += 1
                    at, left, done = at + k, left - k, done + k

        load_rows(False)
        load(REL[0:HEADS, CLIPPED:640], t["rel_flip"][0, :, 0:640 - CLIPPED], rel_step)
        b = plan.b["columns"]
        act.wait_ge(bank_free[b % 4], b // 4 + 1)
        act.activation(C_ACT[:], COLS[:, col_at["c"]:col_at["c"] + KD], ACT.Silu).then_inc(c_ready, 1)
        act.wait_ge(rel_step, 16)
        act.activation(REL[0:HEADS, 0:CLIPPED], REL[0:HEADS, CLIPPED:CLIPPED + 1].broadcast_to([HEADS, CLIPPED]), ACT.Copy)\
           .then_inc(rel_step, 1)
        load_rows(True)

    def act_small_loads(act):
        def load(dst, src, s):
            act.e.dma_start(dst, src).then_inc(s, 16)
            n_small[0] += 1

        for layer in range(2):
            load(ROUTER_W[:, layer, :, 0:GROUPS], t["moe_w_group"][layer].rearrange("(k p) g -> p k g", p=P), small_landed)
            load(ROUTER_W[:, layer, :, GROUPS:], t["moe_w_expert"][layer].rearrange("(k p) g e -> p k (g e)", p=P), small_landed)
            load(ROUTER_B[:, layer, 0:GROUPS], t["moe_b_group"][layer].partition_broadcast(P), small_landed)
            load(ROUTER_B[:, layer, GROUPS:], t["moe_b_expert"][layer].rearrange("g e -> (g e)").partition_broadcast(P), small_landed)
        load(DT_W[:], t["ssm_w_in"][0][:, 3 * SSM_INNER:].rearrange("(k p) n -> p k n", p=P), small_landed)
        load(DT_ROW[:, 0, :], t["ssm_dt_bias"][0].partition_broadcast(P), small_landed)
        load(DT_ROW[:, 1, :], t["ssm_A_log"][0].partition_broadcast(P), small_landed)
        load(D_ROW[:], t["ssm_D"][0].partition_broadcast(P), small_landed)
        load(FG_W[:], t["ev_w_in_2"][0][:, 5 * HALF:].rearrange("(k p) n -> p k n", p=P), small_landed)
        load(FG_B[:], t["ev_b_fgate_2"][0].partition_broadcast(P), small_landed)
        for i, name in enumerate(("ev_q_norm_2", "ev_k_norm_2")):
            for h in range(2):
                load(QK_GAIN[h * HD:h * HD + HD, i:i + 1], dram(name, 0, [[1, HD], [1, 1]]), small_landed)

    def act_x(act):
        b = plan.b["load"]
        for k in range(KD):
            act.e.activation(X[:, k, :], full_bank(act, b + k)[:], ACT.Copy).then_inc(bank_free[(b + k) % 4], 1)

    def pool_loads(pool):
        pool.wait_ge(consts_ready, 1)
        pool.wait_ge(rel_step, 17)
        pool.dma_start(rel_dram, REL[0:HEADS, :]).then_inc(rel_saved, 16)

    def pool_strip_dram(pool):
        pool.wait_ge(rel_saved, 16)
        pool.dma_start(strip_dram, rel_dram.partition_broadcast(P)).then_inc(strip_saved, 16)

    def pool_strip(pool):
        pool.wait_ge(strip_saved, 16)
        pool.dma_start(STRIP[:], bass.AP(strip_dram.tensor, P - 1, [[HEADS * 640 - 1, P], [640, HEADS], [1, SEQ]]))\
            .then_inc(strip_landed, 16)

    CLIPPED = SEQ - 1 - REL_CLIP
    row_dmas, n_small = [0, 0], [0]
    rel_saved, strip_saved = sem("rel_saved"), sem("strip_saved")
    rel_step, strip_landed, strip_ready = sem("rel_step"), sem("strip_landed"), sem("strip_ready")

    def pe_start(pe):
        b = plan.b["columns"]
        pe.e.wait_ge(consts_ready, 1)
        pe.e.wait_ge(rows_landed[0], 16 * row_dmas[0])
        nc.tensor.transpose(take_bank(pe, b)[:, 0:P], ROWS[:, 0, :], IDENT[:]).then_inc(bank_ready, 1)
        b = plan.b["load"]
        pe.e.wait_ge(x_landed, 16)
        for k in range(KD):
            bank = take_bank(pe, b + k)
            for tt in range(NT):
                ins = nc.tensor.transpose(bank[:, tt * P:tt * P + P], XTOK[:, tt, k * P:k * P + P], IDENT[:])
            ins.then_inc(bank_ready, 1)
    def pe_columns_rest(pe):
        pe.e.wait_ge(rows_landed[1], 16 * row_dmas[1])
        for r in range(1, n_row_tiles):
            n = min(P, n_cols - r * P)
            bank = take_bank(pe, plan.b["columns_rest"] + r - 1)
            nc.tensor.transpose(bank[:, 0:n], ROWS[0:n, r, :], IDENT[0:n, 0:n]).then_inc(bank_ready, 1)

    def dve_columns_rest(dve):
        for r in range(1, n_row_tiles):
            n, b = min(P, n_cols - r * P), plan.b["columns_rest"] + r - 1
            dve.e.tensor_copy(COLS[:, r * P:r * P + n], full_bank(dve, b)[:, 0:n]).then_inc(bank_free[b % 4], 1)

    def dve_start(dve):
        b = plan.b["columns"]
        dve.e.tensor_copy(COLS[:, 0:P], full_bank(dve, b)[:, 0:P]).then_inc(bank_free[b % 4], 1)
        dve.wait(c_ready)
        dve_ada(dve, 0, 6)
        dve_root(dve, 0)
        dve_ada(dve, 6, 8)
        dve_ada_end(dve, 0)
        dve_ada_end(dve, 1)

    def dve_strip(dve):
        dve.wait(strip_landed, 16)
        dve.e.memset(STRIP[0:HD, :, SEQ - HD:SEQ], NEG).then_inc(strip_ready, 1)

    norm_gain = {0: lambda k: GAIN[:, 0, k:k + 1], 1: lambda k: GAIN[:, 1, k:k + 1], 2: lambda k: GAIN[:, 2, k:k + 1],
                 3: lambda k: GAIN[:, 3, k:k + 1], 4: lambda k: col("final", k), 5: lambda k: col("norm_mix", k),
                 6: lambda k: col("norm_ffn", k), 7: lambda k: 1.0, 8: lambda k: col("norm_mix", KD + k),
                 9: lambda k: col("norm_ffn", KD + k), 10: lambda k: 1.0}
    norm_shift = {0: (0, 0), 1: (0, 3), 2: (1, 0), 3: (1, 3)}
    FINAL, PLAIN = 4, 8

    def pe_norm(pe, n):
        bank = take_bank(pe, plan.b[f"norm{n}"])
        for k in range(KD):
            pe.wait(sq_ready)
            ins = nc.tensor.matmul(bank[:], ONES[:], SQ[:, k % 2, :], start=k == 0, stop=k == KD - 1)
            if k < KD - 1:
                ins.then_inc(sq_used, 1)
        ins.then_inc(bank_ready, 1)

    def act_root(act, tile, ready):
        act.wait(ready)
        act.e.activation(tile, tile, ACT.Sqrt).then_inc(root_ready, 1)

    def residual_pairs(n):
        last = plan.p[f"norm{n}"]
        if n in (1, 2, 3, 4, 6, 7, 10):
            return [last - 4 + k // 2 for k in range(KD)]
        return [last - 1] * KD

    def norm_buffer(k):
        return (TMP, SQ)[k // 2 % 2][:, k % 2, :]

    def act_norm(act, n):
        pairs = residual_pairs(n)
        if n == 0:
            b = plan.b["load"] + KD - 1
            act.e.wait_ge(bank_free[b % 4], b // 4 + 1)
        if n == FINAL + 1:
            act.wait(x_ready)
        for k in range(KD):
            if k == 0 or pairs[k] != pairs[k - 1]:
                for p in (pairs[k] - 1, pairs[k]):
                    act.e.wait_ge(evac[p % 2], p // 2 + 1)
            if k >= 2:
                act.wait(sq_used)
            act.e.activation(SQ[:, k % 2, :], X[:, k, :], ACT.Square).then_inc(sq_ready, 1)
            if k == 3 and n in (7, 10):
                act_ple_rows(act, (n - 7) // 3)
        act.e.activation(MX[:, 0, 0, 0:1], ONES[:, 0:1], ACT.Sqrt)
        act.wait(sq_used)
        act_root(act, RSTD[:], var_ready)
        if n in (FINAL, PLAIN):
            return
        for k in range(KD):
            act.wait(norm_pre)
            act.e.activation(HH[:, k, :], norm_buffer(k), ACT.Copy).then_inc(norm_hi, 1)

    def pool_norm(pool):
        for k in range(KD):
            pool.wait(norm_hi)
            pool.e.tensor_tensor(HL[:, k, :], norm_buffer(k), HH[:, k, :].bitcast(F32), ALU.subtract).then_inc(h_ready, 1)

    def dve_rstd(dve, total, tile, count):
        ins = dve.e.tensor_scalar(tile, total, 1.0 / count, EPS, ALU.mult, ALU.add)
        ins.then_inc(var_ready, 1)
        dve.wait(root_ready)
        dve.link(dve.e.reciprocal(tile, tile))

    def dve_root(dve, n):
        b = plan.b[f"norm{n}"]
        bank = full_bank(dve, b)
        dve.e.tensor_scalar(RSTD[:], bank[:], 1.0 / D, EPS, ALU.mult, ALU.add).then_inc(var_ready, 1)
        dve.wait(root_ready)
        dve.e.reciprocal(RSTD[:], RSTD[:]).then_inc(bank_free[b % 4], 1)
        dve.e.wait_ge(bank_free[b % 4], b // 4 + 1)

    def dve_norm(dve, n):
        if n:
            dve_root(dve, n)
        gain = norm_gain[n]
        if n in (FINAL, PLAIN):
            to = X if n == FINAL else HF
            for k in range(KD):
                ins = dve.e.scalar_tensor_tensor(to[:, k, :], X[:, k, :], gain(k), RSTD[:], ALU.mult, ALU.mult)
            ins.then_inc(x_ready if n == FINAL else h_ready, 1)
            dve.passed(x_ready if n == FINAL else h_ready, 1)
            return

        def scale(k):
            if k >= 4:
                dve.wait(h_ready)
            if n in norm_shift:
                dve.e.tensor_tensor(norm_buffer(k), X[:, k, :], RSTD[:], ALU.mult).then_inc(dve.chain, 1)
            else:
                dve.e.scalar_tensor_tensor(norm_buffer(k), X[:, k, :], gain(k), RSTD[:], ALU.mult, ALU.mult).then_inc(norm_pre, 1)

        scale(0)
        for k in range(KD):
            if k + 1 < KD:
                scale(k + 1)
            if n in norm_shift:
                dve.wait(dve.chain)
                dve.e.tensor_scalar(norm_buffer(k), norm_buffer(k), gain(k), mod(*norm_shift[n], k), ALU.mult, ALU.add)\
                     .then_inc(norm_pre, 1)
        dve.passed(h_ready, 4)

    def dve_residual(dve, name, n, units_per_pair, gate, first=0):
        for i in range(first, n):
            p = plan.p[name] + i
            pair = full_pair(dve, plan.u[name] + (i + 1) * units_per_pair - 1, p)
            c = 2 * (i % 4)
            if gate is None:
                dve.e.tensor_tensor(X[:, c:c + 2, :], pair[:], X[:, c:c + 2, :], ALU.add).then_inc(evac[p % 2], 1)
            else:
                for m in range(2):
                    ins = dve.e.scalar_tensor_tensor(X[:, c + m, :], pair[:, m, :], mod(*gate, c + m), X[:, c + m, :],
                                                     ALU.mult, ALU.add)
                ins.then_inc(evac[p % 2], 1)

    def pe_matrix(pe, name, n, first=0):
        for i in range(first, n):
            unit_channels(pe, plan.u[name] + i, take_pair(pe, plan.p[name] + i), hh, hl, KD)

    def pe_mixin(pe):
        first_unit(pe, plan.u["mixin"], take_pair(pe, plan.p["mixin"]), pe.seen(h_ready))
        pe.passed(h_ready, KD)
        for i in range(1, 6):
            unit_channels(pe, plan.u["mixin"] + i, take_pair(pe, plan.p["mixin"] + i), hh, hl, KD)
            if i >= 2:
                pe_ada(pe, i)
        for i in range(6, 8):
            unit_tokens(pe, plan.u["mixin"] + i, take_pair(pe, plan.p["mixin"] + i))

    def act_copy_pairs(act, name, first, n, to, tokens, func=ACT.Copy):
        for i in range(n):
            u, p = plan.u[name] + first + i, plan.p[name] + first + i
            pair = full_pair(act, u, p)
            if tokens:
                ins = act.e.activation(to[:, :, i * 256:i * 256 + 256],
                                       pair[:].rearrange("p b (j n) -> p (b j) n", n=256), func)
            else:
                ins = act.e.activation(to[:, 2 * i:2 * i + 2, :], pair[:], func)
            ins.then_inc(evac[p % 2], 1)

    def act_mixin(act):
        act.e.dma_start(POOL_W[:], t["pool_w"][0].rearrange("g c d -> c g d")).then_inc(pool_w_landed, 16)
        act.e.wait_ge(ada_used, 12)
        act_copy_pairs(act, "mixin", 0, 2, U, False)
        act_copy_pairs(act, "mixin", 2, 2, Q0, False)
        act_copy_pairs(act, "mixin", 4, 2, K0, False)
        act_copy_pairs(act, "mixin", 6, 2, V0, True)

    pool_w_landed = sem("pool_w_landed")
    pooled_ready = sem("pooled_ready")

    def dve_pool_window(dve, g):
        u, w = U[:, g, :], 2 << g
        if g % 2 == 0:
            p = plan.p["mixin"] + g // 2
            dve.e.wait_ge(evac[p % 2], p // 2 + 1)
        cur = u
        for level in range(g + 1):
            sh, new = 1 << level, PSCR[:, level % 2, :]
            dve.e.tensor_tensor(new[:, sh:], cur[:, sh:], cur[:, :SEQ - sh], ALU.add)
            dve.link(dve.e.tensor_copy(new[:, :sh], cur[:, :sh]))
            cur = new
        dve.e.scalar_tensor_tensor(POOLED[:, g, w:], cur[:, w:], 1.0 / w, u[:, w:], ALU.mult, ALU.subtract)
        dve.link(dve.e.tensor_tensor(POOLED[:, g, :w], cur[:, :w], INV_COUNT[:, :w], ALU.mult))
        dve.e.tensor_tensor(POOLED[:, g, :w], POOLED[:, g, :w], u[:, :w], ALU.subtract).then_inc(pooled_ready, 1)

    def pe_pool(pe):
        pe.e.wait_ge(pool_w_landed, 16)
        for g in range(4):
            pe.wait(pooled_ready)
            bank = take_bank(pe, plan.b["pool"] + g)
            nc.tensor.matmul(bank[:], POOL_W[:, g, :], POOLED[:, g, :], start=True, stop=True).then_inc(bank_ready, 1)

    def dve_ada_mixin(dve):
        dve_ada(dve, 8, 16)
        for q in range(4, 6):
            full_bank(dve, ada_bank(q - 2))
            dve_ada(dve, 4 * q, 4 * q + 4)
        for q in range(2, 6):
            dve_ada_end(dve, q)

    def dve_mixout(dve):
        att_full(dve, 0, HEADS - 2, 3)
        dve_ada(dve, 40, 48)
        dve_residual(dve, "mixout", 4, 1, (0, 2))

    def dve_pool(dve):
        for g in range(4):
            dve_pool_window(dve, g)
        dve.e.wait_ge(unit_done, plan.u["mixin"] + 8)
        for g in range(4):
            b = plan.b["pool"] + g
            if g >= 2:
                dve.e.wait_ge(bank_free[(b - 2) % 4], (b - 2) // 4 + 1)
            dve.e.tensor_scalar(TMP[:, g % 2, :], full_bank(dve, b)[:], col("pool_scale", g), None, ALU.mult)\
                 .then_inc(pre_ready, 1)
            dve.wait(pre_ready)
            dve.wait(hi_ready)
            dve.e.tensor_tensor(HL[:, g, :], TMP[:, g % 2, :], HH[:, g, :].bitcast(F32), ALU.subtract)\
                 .then_inc(bank_free[b % 4], 1)

    def act_pool(act):
        for g in range(4):
            act.wait(pre_ready)
            act.e.activation(HH[:, g, :], TMP[:, g % 2, :], ACT.Copy).then_inc(hi_ready, 1)

    SEG = [0, P, 3 * P, 6 * P]
    HOME = {3: (0, 0), 2: (1, 0), 0: (1, 3 * P), 1: (2, 0)}
    PT_HOME = {0: (0, 0), 1: (1, 0), 3: (1, 3 * P), 2: (2, 0)}
    att_sems = [{s: sem(f"att{n}_{s}") for s in ("scaled", "exp", "probs", "turned", "out")} for n in range(2)]

    def att_bank(n, h, i):
        return plan.b[f"att{n}"] + 4 * h + i

    def att_full(eng, n, h, i):
        if i == 3:
            at = min(6 + 4 * h, 4 * HEADS - 1)
        else:
            at = 3 * h + i + max(0, h - 1)
        eng.e.wait_ge(bank_ready, plan.b[f"att{n}"] + at + 1)
        return BANK[att_bank(n, h, i) % 4]

    def out_half(n, i):
        return PAIR[(plan.p[f"att{n}"] + 1) % 2][:, i % 2, :]

    def pe_attention(pe, n, q, k, v, s, pt, fox):
        w = att_sems[n]
        p0 = plan.p[f"att{n}"]

        def scores(h):
            a, tile = (h % 2) * HD, h // 2
            for i in range(3):
                bank = take_bank(pe, att_bank(n, h, i))
                mine = [j for j in HOME if HOME[j][0] == i]
                for j in mine:
                    at, wide = HOME[j][1], P * (j + 1)
                    ins = nc.tensor.matmul(bank[:, at:at + wide], q[a:a + HD, tile, j * P:j * P + P],
                                           k[a:a + HD, tile, 0:wide], start=True, stop=not fox)
                    if fox:
                        ins = nc.tensor.matmul(bank[:, at:at + wide], MINUS_HEAD[:, h, :], FCUM[:, 1, 0:wide],
                                               start=False, stop=True)
                ins.then_inc(bank_ready, 1)

        def turned(h):
            bank = take_bank(pe, att_bank(n, h, 3))
            if n == 0 and h % 2 == 0 and h:
                pe_ada(pe, 5 + h // 2, bank[:, 2 * P:])
            pe.wait(w["probs"])
            pair = take_pair(pe, p0 + 2 * h)
            for i in range(3):
                o = bank if i == 2 else pair[:, i, :]
                for kt in [x for x in PT_HOME if PT_HOME[x][0] == i]:
                    for j in range(kt, NT):
                        at = PT_HOME[kt][1] + (j - kt) * P
                        ins = nc.tensor.transpose(o[:, at:at + P], s[:, h % 2, SEG[j] + kt * P:SEG[j] + kt * P + P], IDENT[:])
                ins.then_inc(w["turned"] if i < 2 else bank_ready, 1)

        def outputs(h):
            p, a = p0 + 1, (h % 2) * HD
            if h % 2 == 0:
                pe.e.wait_ge(evac[p % 2], p // 2 + max(0, h - 2))
            b = att_bank(n, h, 3)
            pe.e.wait_ge(bank_free[b % 4], b // 4 + 1)
            o = out_half(n, h // 2)
            for kt in range(NT):
                ins = nc.tensor.matmul(o[a:a + HD, kt * P:SEQ], v[:, kt, h * HD:h * HD + HD],
                                       pt[:, h % 2, TRI_AT[kt]:TRI_AT[kt] + SEQ - kt * P],
                                       start=kt == 0, stop=kt == NT - 1)
            ins.then_inc(w["out"], 1)

        scores(0)
        scores(1)
        for h in range(HEADS):
            turned(h)
            if h + 2 < HEADS:
                scores(h + 2)
            outputs(h)

    def dve_attention(dve, n, s, bias):
        w = att_sems[n]

        def scale(h):
            for i in range(3):
                b = att_bank(n, h, i)
                bank = att_full(dve, n, h, i)
                for j in [x for x in HOME if HOME[x][0] == i]:
                    at, wide = HOME[j][1], P * (j + 1)
                    ins = dve.e.scalar_tensor_tensor(s[:, h % 2, SEG[j]:SEG[j] + wide], bank[:, at:at + wide],
                                                     HD ** -0.5, bias(h)[:, SEQ - wide:SEQ], ALU.mult, ALU.add)
                ins.then_inc(bank_free[b % 4], 1)
            dve.e.wait_ge(bank_free[b % 4], b // 4 + 1)
            for j in range(NT):
                ins = dve.e.tensor_reduce(MX[:, h % 2, 0, j:j + 1], s[:, h % 2, SEG[j]:SEG[j] + P * (j + 1)], AX.X, ALU.max)
            dve.link(ins)
            dve.e.tensor_scalar(MX[:, h % 2, 1, :], MX[:, h % 2, 0, :], -1.0, None, ALU.mult).then_inc(w["scaled"], 1)

        def normalise(h):
            dve.wait(w["exp"])
            dve.link(dve.e.reciprocal(SUMS[:, h % 2, :], SUMS[:, h % 2, :]))
            for j in range(NT):
                seg = s[:, h % 2, SEG[j]:SEG[j] + P * (j + 1)]
                ins = dve.e.tensor_scalar(seg, seg, SUMS[:, h % 2, j:j + 1], None, ALU.mult)
            ins.then_inc(w["probs"], 1)

        def rest(i):
            dve.wait(hi_ready)
            dve.e.tensor_tensor(HL[:, 4 + i, :], out_half(n, i), HH[:, 4 + i, :].bitcast(F32),
                                ALU.subtract).then_inc(evac[(plan.p[f"att{n}"] + 1) % 2], 2)

        def ada_pieces(h):
            if h in (4, 6):
                att_full(dve, n, h - 2, 3)
            dve_ada(dve, 24 + 2 * h, 26 + 2 * h)

        scale(0)
        scale(1)
        for h in range(HEADS):
            normalise(h)
            if n == 0:
                ada_pieces(h)
            if h % 2 and h > 1:
                rest(h // 2 - 1)
            if h + 2 < HEADS:
                scale(h + 2)
            if n == 0 and h % 2 == 0 and h:
                b = att_bank(n, h, 3)
                dve.e.wait_ge(bank_free[b % 4], b // 4 + 1)
                dve_ada_end(dve, 5 + h // 2, att_full(dve, n, h, 3)[:, 2 * P:])
        rest(HEADS // 2 - 1)

    def act_attention(act, n, s, pt):
        w = att_sems[n]

        def exponential(h):
            act.wait(w["scaled"])
            for j in range(NT):
                seg = s[:, h % 2, SEG[j]:SEG[j] + P * (j + 1)]
                ins = act.e.activation(seg, seg, ACT.Exp, bias=MX[:, h % 2, 1, j:j + 1], accum_out=SUMS[:, h % 2, j:j + 1])
            ins.then_inc(w["exp"], 1)

        def high(i):
            act.wait(w["out"], 2)
            act.e.activation(HH[:, 4 + i, :], out_half(n, i), ACT.Copy).then_inc(hi_ready, 1)

        def copy(h):
            p = plan.p[f"att{n}"] + 2 * h
            for i in range(3):
                if i < 2:
                    act.wait(w["turned"])
                    o, done = PAIR[p % 2][:, i, :], evac[p % 2]
                else:
                    o, done = att_full(act, n, h, 3), bank_free[att_bank(n, h, 3) % 4]
                for kt in [x for x in PT_HOME if PT_HOME[x][0] == i]:
                    at, wide = PT_HOME[kt][1], SEQ - kt * P
                    ins = act.e.activation(pt[:, h % 2, TRI_AT[kt]:TRI_AT[kt] + wide], o[:, at:at + wide], ACT.Copy)
                if i:
                    ins.then_inc(done, 1)

        exponential(0)
        exponential(1)
        for h in range(HEADS):
            copy(h)
            if h + 2 < HEADS:
                exponential(h + 2)
            if h % 2 == 0 and h:
                high(h // 2 - 1)
        high(HEADS // 2 - 1)

    def pe_after_h(pe, pairs):
        for s in range(2):
            pe.e.wait_ge(evac[s], pairs // 2)

    moe_sems = {s: sem(f"moe_{s}") for s in ("exp_in", "exp_out", "consts", "mask", "experts", "mapped", "index", "saved", "rows_hi", "silu", "hidden_hi", "w2_hi",
                                             "w2_ready", "summed", "rows", "down", "combined",
                                             "y_turned")}
    gathered = [sem("gathered0"), sem("gathered1")]
    scattered = [sem("scattered0"), sem("scattered1")]
    y_landed = [sem("y_landed0"), sem("y_landed1")]
    w2_landed = [sem("w2_landed0"), sem("w2_landed1")]

    narrow_ready = sem("narrow_ready")
    IN_PLACE = OG[:, 0, :].rearrange("p (r n) -> p r n", n=P)
    IN_SLOT = OG[:, 1, 0:2 * NT * SLOTS].rearrange("p (r n) -> p r n", n=SLOTS)

    def dve_cut_narrow(dve, wh, wl, w):
        dve.link(dve.e.tensor_copy(wh, w))
        dve.e.tensor_tensor(wl, w, wh.bitcast(F32), ALU.subtract).then_inc(narrow_ready, 1)

    def pe_logits(pe, b, wh, wl, n, fresh):
        pe.wait(narrow_ready)
        bank = take_bank(pe, b)
        for k in range(KD):
            if fresh:
                pe.wait(h_ready)
            ins = mm3(bank[0:n, :], wh[:, k, :], wl[:, k, :], HH[:, k, :], HL[:, k, :], k == 0, k == KD - 1)
        ins.then_inc(bank_ready, 1)
        pe.e.wait_ge(bank_free[b % 4], b // 4 + 1)
        bank = take_bank(pe, b + 1)
        for tt in range(NT):
            ins = nc.tensor.transpose(bank[:, tt * n:tt * n + n], RSTD[0:n, tt * P:tt * P + P], IDENT[0:n, 0:n])
        ins.then_inc(bank_ready, 1)

    def dve_logits(dve, b, n):
        bank = full_bank(dve, b)
        dve.e.tensor_copy(RSTD[0:n, :], bank[0:n, :]).then_inc(bank_free[b % 4], 1)
        return full_bank(dve, b + 1)[:, 0:NT * n].rearrange("p (t n) -> p t n", n=n)

    def dve_first_max(dve, values, best, mark, scratch, n):
        dve.link(dve.e.tensor_reduce(best, values, AX.X, ALU.max))
        dve.link(dve.e.tensor_tensor(scratch, values, bcast(best, 2, n), ALU.is_equal))
        dve.link(dve.e.tensor_tensor(scratch, scratch, bcast(FALLING[:, EPG - n:EPG], 1, NT), ALU.mult))
        first = GATE[:, 11, :, 0]
        dve.link(dve.e.tensor_reduce(first, scratch, AX.X, ALU.max))
        dve.link(dve.e.tensor_tensor(mark, scratch, bcast(first, 2, n), ALU.is_equal))

    def dve_router(dve, layer):
        w = moe_sems
        b = plan.b[f"moe{layer}"]
        logits = dve_logits(dve, b, GROUPS + EXPERTS)
        b += 1
        dve.e.tensor_tensor(LOGIT[:], logits, bcast(ROUTER_B[:, layer, :], 1, NT), ALU.add).then_inc(bank_free[b % 4], 1)
        dve.e.wait_ge(bank_free[b % 4], b // 4 + 1)
        gl = LOGIT[:, :, 0:GROUPS]
        group, e1, e2, scratch = GATE[:, 0, :, 0:GROUPS], GATE[:, 1], GATE[:, 2], GATE[:, 3]
        gmax, top1, top2 = GATE[:, 4, :, 0], GATE[:, 4, :, 1], GATE[:, 4, :, 2]
        gprob = GATE[:, 4, :, 3]
        es, es2 = GATE[:, 5], GATE[:, 6]
        expo = GATE[:, 7]
        dve_first_max(dve, gl, gmax, group, scratch[:, :, 0:GROUPS], GROUPS)
        dve.e.tensor_tensor(expo[:, :, 0:GROUPS], gl, bcast(gmax, 2, GROUPS), ALU.subtract)
        dve.link(dve.e.tensor_tensor(ESEL[:], LOGIT[:, :, GROUPS:].rearrange("p t (g e) -> p t g e", e=EPG),
                                     bcast(group, 3, EPG), ALU.mult))
        dve.link(dve.e.tensor_reduce(es, ESEL[:].rearrange("p t g e -> p t e g"), AX.X, ALU.add))
        dve_first_max(dve, es, top1, e1, scratch, EPG)
        dve.link(dve.e.scalar_tensor_tensor(es2, e1, 2 * NEG, es, ALU.mult, ALU.add))
        dve_first_max(dve, es2, top2, e2, scratch, EPG)
        dve.e.tensor_tensor(expo[:, :, GROUPS], top2, top1, ALU.subtract).then_inc(w["exp_in"], 1)
        for r, e in enumerate((e1, e2)):
            ins = dve.e.tensor_tensor(MASK[:, r].rearrange("p t (g e) -> p t g e", e=EPG), bcast(e, 2, GROUPS),
                                      bcast(group, 3, EPG), ALU.mult)
        dve.link(ins)
        dve.e.tensor_tensor(BOTH[:], MASK[:, 0], MASK[:, 1], ALU.add).then_inc(w["mask"], 1)
        dve.wait(w["exp_out"])
        dve.e.tensor_reduce(gprob, expo[:, :, 0:GROUPS], AX.X, ALU.add)
        dve.link(dve.e.tensor_scalar(SHARE[:, 0, :], expo[:, :, GROUPS], 1.0, None, ALU.add))
        dve.link(dve.e.tensor_tensor(SHARE[:, 0, :], SHARE[:, 0, :], gprob, ALU.mult))
        dve.link(dve.e.reciprocal(SHARE[:, 0, :], SHARE[:, 0, :]))
        dve.link(dve.e.tensor_tensor(SHARE[:, 1, :], SHARE[:, 0, :], expo[:, :, GROUPS], ALU.mult))
        b += 1
        bank = full_bank(dve, b)
        place, rows = (bank[:, i * NT * EXPERTS:(i + 1) * NT * EXPERTS].rearrange("p (t e) -> p t e", e=EXPERTS) for i in range(2))
        n, end, total = PLACE[:, 0, :], PLACE[:, 1, :], PLACE[:, 2, :]
        base = ESEL[:].rearrange("p t g e -> p t (g e)")
        dve.link(dve.e.tensor_reduce(total, rows.rearrange("p t e -> p e t"), AX.X, ALU.add))
        dve.link(dve.e.tensor_scalar(n, total, 0.5, None, ALU.is_gt))
        for i in range(1, NT):
            dve.link(dve.e.scalar_tensor_tensor(n, total, i * P + 0.5, n, ALU.is_gt, ALU.add))
        dve.link(dve.e.tensor_tensor_scan(end, ONES[:, 0:1].broadcast_to([P, EXPERTS]), n, 0.0, ALU.mult, ALU.add))
        dve.link(dve.e.tensor_tensor(base[:, 0, :], end, n, ALU.subtract))
        dve.link(dve.e.tensor_scalar(base[:, 0, :], base[:, 0, :], float(P), None, ALU.mult))
        for tt in range(1, NT):
            dve.link(dve.e.tensor_tensor(base[:, tt, :], rows[:, tt - 1, :], base[:, tt - 1, :], ALU.add))
        dve.e.tensor_tensor(BOTH[:], place, base, ALU.add).then_inc(bank_free[b % 4], 1)
        dve.e.wait_ge(bank_free[b % 4], b // 4 + 1)
        dve.link(dve.e.tensor_tensor(MASK[:], MASK[:], bcast(BOTH[:], 1, 2), ALU.mult))
        dve.link(dve.e.tensor_reduce(POS[:], MASK[:], AX.X, ALU.add))
        pos = POS[:].rearrange("p r t -> p (r t)")
        dve.wait(w["consts"])
        dve.link(dve.e.tensor_tensor(IN_SLOT, bcast(SLOT_ROW[:], 1, 2 * NT), bcast(pos, 2, SLOTS), ALU.is_le))
        dve.link(dve.e.tensor_reduce(ROW_SLOT[:], IN_SLOT, AX.X, ALU.add))
        dve.link(dve.e.tensor_scalar(ROW_SLOT[:], ROW_SLOT[:], 1.0, None, ALU.subtract))
        dve.link(dve.e.scalar_tensor_tensor(ROW_PLACE[:], ROW_SLOT[:], -float(P), pos, ALU.mult, ALU.add))
        dve.e.tensor_tensor(IN_PLACE, bcast(PLACE_AT[:], 1, 2 * NT), bcast(ROW_PLACE[:], 2, P), ALU.is_equal)
        dve.link(dve.e.tensor_tensor(IN_SLOT, bcast(SLOT_AT[:], 1, 2 * NT), bcast(ROW_SLOT[:], 2, SLOTS), ALU.is_equal))
        dve.e.tensor_tensor(IN_SLOT, IN_SLOT, bcast(ROW_AT[:].rearrange("p r t -> p (r t)"), 2, SLOTS), ALU.mult)\
             .then_inc(w["mapped"], 1)
        dve.link(dve.e.tensor_tensor(OWNER[:], bcast(end, 1, SLOTS), bcast(SLOT_AT[:], 2, EXPERTS), ALU.is_le))
        dve.link(dve.e.tensor_reduce(SLOT_E[:], OWNER[:], AX.X, ALU.add))
        dve.e.tensor_scalar(SLOT_I[:], SLOT_E[:], float(EXPERTS - 1), None, ALU.min).then_inc(w["experts"], 1)
        b += 1
        v = SLOT_ROW[:]
        dve.wait(w["experts"])
        dve.e.tensor_scalar(v, full_bank(dve, b)[:, 0:SLOTS], NO_ROW, None, ALU.add).then_inc(bank_free[b % 4], 1)
        dve.e.wait_ge(bank_free[b % 4], b // 4 + 1)
        dve.link(dve.e.tensor_scalar(SLOT_E[:], v, SEQ - 0.5, float(SEQ), ALU.is_gt, ALU.mult))
        dve.link(dve.e.tensor_tensor(GATHER_I[:], v, SLOT_E[:], ALU.subtract))
        dve.e.tensor_copy(SCATTER_I[:], v).then_inc(w["index"], 1)

    def pe_router(pe, layer):
        w, b, p0 = moe_sems, plan.b[f"moe{layer}"], plan.p[f"moe{layer}"]
        pe_logits(pe, b, ROUTER_WH, ROUTER_WL, GROUPS + EXPERTS, True)
        def by_token(tt):
            pair = take_pair(pe, p0 + tt)
            for k in range(KD):
                o = pair[:, k // 4, (k % 4) * P:(k % 4) * P + P]
                nc.tensor.matmul(o, HH[:, k, tt * P:tt * P + P], IDENT_R[:], start=True, stop=False)
                ins = nc.tensor.matmul(o, HL[:, k, tt * P:tt * P + P], IDENT_R[:], start=False, stop=True)
            ins.then_inc(w["summed"], 1)

        by_token(0)
        by_token(1)
        pe.wait(w["mask"])
        bank = take_bank(pe, b + 2)
        both = BOTH[:].rearrange("p t e -> p (t e)")
        nc.tensor.matmul(bank[:, 0:NT * EXPERTS], STRICT[:], both, start=True, stop=True)
        nc.tensor.matmul(bank[:, NT * EXPERTS:2 * NT * EXPERTS], ONES[:], both, start=True, stop=True).then_inc(bank_ready, 1)
        by_token(2)
        by_token(3)
        pe.wait(w["mapped"])
        bank = take_bank(pe, b + 3)
        for i in range(2 * NT):
            ins = nc.tensor.matmul(bank[:, 0:SLOTS], IN_PLACE[:, i, :], IN_SLOT[:, i, :], start=i == 0, stop=i == 2 * NT - 1)
        ins.then_inc(bank_ready, 1)

    def dve_router_weights(dve, layer):
        if layer == 0:
            dve.e.wait_ge(small_landed, 16 * n_small[0])
        dve.e.tensor_copy(IDENT_R[:], IDENT[:])
        dve.e.tensor_tensor(STRICT[:], LATER[:, 0:P], IDENT[:], ALU.subtract)
        dve_cut_narrow(dve, ROUTER_WH[:], ROUTER_WL[:], ROUTER_W[:, layer])

    def act_router(act, layer):
        w, p0 = moe_sems, plan.p[f"moe{layer}"]
        act.wait(w["exp_in"])
        expo = GATE[:, 7, :, 0:GROUPS + 1]
        act.e.activation(expo, expo, ACT.Exp).then_inc(w["exp_out"], 1)
        for tt in range(NT):
            act.wait(w["summed"])
            p = p0 + tt
            act.e.activation(HTOK[:, tt, :].rearrange("p (b n) -> p b n", b=2), PAIR[p % 2][:], ACT.Copy).then_inc(evac[p % 2], 1)
            act.e.wait_ge(evac[p % 2], p // 2 + 1)
            act.e.dma_start(htok_dram[tt * P:tt * P + P, :], HTOK[:, tt, :]).then_inc(w["saved"], 16)

    def rows_pair(layer, s):
        return plan.p[f"moe{layer}"] + NT + 2 * s

    def slot_bank(layer, s, turned):
        return plan.b[f"moe{layer}"] + 4 + 2 * s + turned

    def slot_loop(eng, first, step, per):
        first()
        step(None, 0)
        with eng.loop(SLOTS // 2 - 1, per) as e:
            for s in (1, 2):
                step(e, s)
        step(None, SLOTS - 1)
        step(None, SLOTS)

    def stage(e, s, behind=0):
        return e is not None or 0 <= s - behind < SLOTS

    def pe_moe(pe, layer):
        w, u0 = moe_sems, plan.u[f"moe{layer}"]

        rows_of = lambda s: XG[:, s % 2, :].rearrange("p (c k) -> p c k", k=KD)

        def rows(e, s):
            pe.wait(gathered[s % 2], 16)
            pair = take_pair(pe, rows_pair(layer, s), turns(e, 2))
            for k in range(KD):
                ins = nc.tensor.transpose(pair[:, k // 4, (k % 4) * P:(k % 4) * P + P], rows_of(s)[:, :, k], IDENT[:])
            ins.then_inc(w["rows"], 1)

        def up(e, s):
            p, u, bank = rows_pair(layer, s), u0 + s, take_bank(pe, slot_bank(layer, s, 0), turns(e, 1))
            pe.e.wait_ge(evac[p % 2], turns(e, 2) + (p // 2 + 1))
            pe.e.wait_ge(split_ready, turns(e, 2) + (u + 1))
            for k in range(KD):
                wh, wl = (a[:, u % 2].rearrange("p (m k n) -> p k m n", m=2, k=KD)[:, k] for a in (WH, WL))
                ins = mm3(bank[:, 0:256].rearrange("p (m n) -> p m n", m=2), GH[:, s % 2, k, :], GL[:, s % 2, k, :], wh, wl,
                          k == 0, k == KD - 1)
            ins.then_inc(unit_done, 1)

        def turn(e, s):
            b = slot_bank(layer, s, 0)
            pe.e.wait_ge(bank_free[b % 4], turns(e, 1) + (b // 4 + 1))
            bank = take_bank(pe, b + 1, turns(e, 1))
            nc.tensor.transpose(bank[:, 0:P], HID[:, s % 2, :], IDENT[:]).then_inc(bank_ready, 2)

        def down(e, s):
            b, p = slot_bank(layer, s, 1), rows_pair(layer, s) + 1
            pair = take_pair(pe, p, turns(e, 2))
            pe.e.wait_ge(bank_free[b % 4], turns(e, 1) + (b // 4 + 1))
            pe.wait(w["w2_ready"])
            for m in range(2):
                c = slice(m * SEQ, m * SEQ + SEQ)
                ins = mm3(pair[:, m, :], HTH[:, s % 2, :], HTL[:, s % 2, :], W2H[:, s % 2, c], W2L[:, s % 2, c], True, True)
            ins.then_inc(w["down"], 1)

        def step(e, s):
            if stage(e, s, -1):
                rows(e, s + 1)
            if stage(e, s, 1):
                turn(e, s - 1)
            if stage(e, s):
                up(e, s)
            if stage(e, s, 1):
                down(e, s - 1)

        slot_loop(pe, lambda: rows(None, 0), step, {gathered[0]: 16, gathered[1]: 16, w["w2_ready"]: 2})
        for tt in range(NT):
            pe.wait(w["combined"])
        for i in range(4):
            pair = take_pair(pe, rows_pair(layer, SLOTS) + i)
            for m in range(2):
                for tt in range(NT):
                    c = (2 * i + m) * P
                    ins = nc.tensor.transpose(pair[:, m, tt * P:tt * P + P], HTOK[:, tt, c:c + P], IDENT[:])
            ins.then_inc(w["y_turned"], 1)

    def act_moe(act, layer):
        w, u0 = moe_sems, plan.u[f"moe{layer}"]

        def rows(e, s):
            act.wait(w["rows"])
            act.e.activation(GH[:, s % 2].rearrange("p (b k) n -> p b (k n)", b=2), PAIR[rows_pair(layer, s) % 2][:], ACT.Copy)\
                 .then_inc(w["rows_hi"], 1)

        def turned(e, s):
            bank = full_bank(act, slot_bank(layer, s, 1), turns(e, 1))
            act.e.activation(HTH[:, s % 2, :], bank[:, 0:P], ACT.Copy).then_inc(w["hidden_hi"], 1)

        def weights(e, s):
            u = u0 + s
            act.e.wait_ge(landed[u % 2], turns(e, 32) + 32 * (u // 2 + 1))
            act.e.wait_ge(unit_done, turns(e, 2) + (u - 1))
            act.e.activation(WH[:, u % 2], RAW[:, u % 2], ACT.Copy).then_inc(split_hi, 1)

        def hidden(e, s):
            bank = BANK[slot_bank(layer, s, 0) % 4]
            act.e.wait_ge(unit_done, turns(e, 2) + (u0 + s + 1))
            act.e.activation(HS[:, s % 2, :], bank[:, 0:P], ACT.Silu).then_inc(w["silu"], 1)

        def first():
            weights(None, 0)
            rows(None, 0)

        def step(e, s):
            if stage(e, s, -1):
                rows(e, s + 1)
            if stage(e, s, 1):
                turned(e, s - 1)
            if stage(e, s, -1):
                weights(e, s + 1)
            if stage(e, s):
                hidden(e, s)

        slot_loop(act, first, step, {w["rows"]: 2})
        for c in range(2):
            act.e.wait_ge(scattered[c], 16 * (SLOTS // 2) * (layer + 1))
        for tt in range(NT):
            to = (XG, OG)[tt % 2]
            if tt >= 2:
                act.e.wait_ge(w["combined"], 4 * layer + tt - 1)
            for r in range(2):
                row = r * SEQ + tt * P
                act.e.dma_start(to[:, r, :], y_dram[row:row + P, :]).then_inc(y_landed[tt % 2], 16)

    def dve_moe(dve, layer):
        w, u0 = moe_sems, plan.u[f"moe{layer}"]

        def rows(e, s):
            p = rows_pair(layer, s)
            dve.wait(w["rows_hi"])
            dve.e.tensor_tensor(GL[:, s % 2].rearrange("p (b k) n -> p b (k n)", b=2), PAIR[p % 2][:],
                                GH[:, s % 2].rearrange("p (b k) n -> p b (k n)", b=2).bitcast(F32), ALU.subtract).then_inc(evac[p % 2], 1)

        def turned(e, s):
            b = slot_bank(layer, s, 1)
            dve.wait(w["hidden_hi"])
            dve.e.tensor_tensor(HTL[:, s % 2, :], BANK[b % 4][:, 0:P], HTH[:, s % 2, :].bitcast(F32), ALU.subtract)\
                 .then_inc(bank_free[b % 4], 1)

        def weights(e, s):
            u = u0 + s
            dve.e.wait_ge(split_hi, turns(e, 2) + (u + 1))
            dve.e.tensor_tensor(WL[:, u % 2], RAW[:, u % 2], WH[:, u % 2].bitcast(F32), ALU.subtract).then_inc(split_ready, 1)

        def hidden(e, s):
            b = slot_bank(layer, s, 0)
            dve.wait(w["silu"])
            dve.e.tensor_tensor(HID[:, s % 2, :], HS[:, s % 2, :], BANK[b % 4][:, P:2 * P], ALU.mult).then_inc(bank_free[b % 4], 1)

        def output(e, s):
            p = rows_pair(layer, s) + 1
            dve.wait(w["down"])
            if e is not None or s >= 2:
                dve.e.wait_ge(scattered[s % 2], turns(e, 16) + 16 * (SLOTS // 2 * layer + s // 2))
            dve.e.tensor_copy(OG[:, s % 2, :].rearrange("p (b n) -> p b n", b=2), PAIR[p % 2][:]).then_inc(evac[p % 2], 1)

        def first():
            weights(None, 0)
            rows(None, 0)

        def step(e, s):
            if stage(e, s, -1):
                rows(e, s + 1)
            if stage(e, s, 1):
                turned(e, s - 1)
            if stage(e, s, -1):
                weights(e, s + 1)
            if stage(e, s):
                hidden(e, s)
            if stage(e, s, 1):
                output(e, s - 1)

        slot_loop(dve, first, step, {w["rows_hi"]: 2, w["hidden_hi"]: 2, w["silu"]: 2, w["down"]: 2})
        for tt in range(NT):
            src = (XG, OG)[tt % 2]
            dve.wait(y_landed[tt % 2], 32)
            dve.link(dve.e.tensor_scalar(HTOK[:, tt, :], src[:, 0, :], SHARE[:, 0, tt:tt + 1], None, ALU.mult))
            dve.e.scalar_tensor_tensor(HTOK[:, tt, :], src[:, 1, :], SHARE[:, 1, tt:tt + 1], HTOK[:, tt, :], ALU.mult, ALU.add)\
                 .then_inc(w["combined"], 1)
        for i in range(4):
            p = rows_pair(layer, SLOTS) + i
            dve.wait(w["y_turned"])
            for m in range(2):
                c = 2 * i + m
                ins = dve.e.scalar_tensor_tensor(X[:, c, :], PAIR[p % 2][:, m, :], mod(layer, 5, c), X[:, c, :], ALU.mult, ALU.add)
            ins.then_inc(evac[p % 2], 1)

    def pool_moe(pool, layer):
        w = moe_sems
        pool.e.memset(XG[:], 0.0)
        pool.e.iota(SLOT_AT[:], [[1, SLOTS]], base=0, channel_multiplier=0, allow_small_or_imprecise_dtypes=True)
        pool.e.iota(ROW_AT[:], [[SEQ, 2], [P, NT]], base=-int(NO_ROW), channel_multiplier=1, allow_small_or_imprecise_dtypes=True)
        pool.e.iota(PLACE_AT[:], [[1, P]], base=0, channel_multiplier=0, allow_small_or_imprecise_dtypes=True)
        pool.e.iota(SLOT_ROW[:], [[P, SLOTS]], base=0, channel_multiplier=0, allow_small_or_imprecise_dtypes=True)\
            .then_inc(w["consts"], 1)
        pool.wait(w["consts"])
        pool.wait(w["index"])
        pool.wait(w["saved"], 16 * NT)

        def gather(s):
            if s >= 2:
                p = rows_pair(layer, s - 2)
                pool.e.wait_ge(evac[p % 2], p // 2 + 1)
            pool.e.indirect_dma_start(XG[:, s % 2, :], None, htok_dram, bass.IndirectOffsetOnAxis(ap=GATHER_I[:, s:s + 1], axis=0),
                                      bounds_check=SEQ - 1, oob_is_err=False).then_inc(gathered[s % 2], 16)

        def scatter(s):
            p = rows_pair(layer, s) + 1
            pool.e.wait_ge(evac[p % 2], p // 2 + 1)
            pool.e.indirect_dma_start(y_dram, bass.IndirectOffsetOnAxis(ap=SCATTER_I[:, s:s + 1], axis=0), OG[:, s % 2, :], None,
                                      bounds_check=2 * SEQ - 1, oob_is_err=False).then_inc(scattered[s % 2], 16)

        def weights(s):
            if s >= 2:
                p = rows_pair(layer, s - 2) + 1
                pool.e.wait_ge(evac[p % 2], p // 2 + 1)
            pool.e.wait_ge(w2_landed[s % 2], 16 * (SLOTS // 2 * layer + s // 2 + 1))
            pool.e.tensor_scalar(W2H[:, s % 2], W2RAW[:, s % 2], 1.0, 1.0, ALU.mult, ALU.mult).then_inc(w["w2_hi"], 1)
            pool.wait(w["w2_hi"])
            pool.e.tensor_tensor(W2L[:, s % 2], W2RAW[:, s % 2], W2H[:, s % 2].bitcast(F32), ALU.subtract).then_inc(w["w2_ready"], 1)

        gather(0)
        gather(1)
        for s in range(SLOTS):
            if s + 2 < SLOTS:
                gather(s + 2)
            if s >= 2:
                scatter(s - 2)
            weights(s)
        scatter(SLOTS - 2)
        scatter(SLOTS - 1)

    def sp_moe(engine, layer):
        w, sp, u0 = moe_sems, engine.e, plan.u[f"moe{layer}"]
        engine.wait(w["experts"])

        def two_slots(i, first):
            for c in range(2):
                expert = sp.value_load(SLOT_I[0:1, at(i, first + c)], min_val=0, max_val=EXPERTS - 1)
                w1, w3, w2 = (t[n][layer][bass.ds(expert, 1)].rearrange("e d f -> (e d) f") for n in ("moe_w1", "moe_w3", "moe_w2"))
                part = lambda m, wm: (wm.rearrange("(p k) n -> p (k n)", k=KD), lambda raw: raw[:, m * D:m * D + D])
                load_unit(sp, part(0, w1), part(1, w3), off=i, u=u0 + first + c)
                if layer or first:
                    sp.wait_ge(w["w2_ready"], i + (SLOTS * layer + first + c - 1))
                sp.dma_start(W2RAW[:, c, :], w2).then_inc(w2_landed[c], 16)

        two_slots(0, 0)
        with sp.Fori(0, SLOTS // 2 - 1) as i:
            two_slots(i * 2, 2)
        sp_unit[0] += SLOTS
        for c in range(2):
            engine.wait(y_landed[c], 2 * 32)


    ssm_sems = {s: sem(f"ssm_{s}") for s in ("exp_in", "exp_out", "log_ready", "cum_ready", "cum_saved", "conv_in", "conv_ready",
                                             "decay_in", "decay_out", "masked", "first_head", "gated")}
    row_landed = [sem("decay_row_landed0"), sem("decay_row_landed1")]
    SERIES = [1 / 13, 1 / 11, 1 / 9, 1 / 7, 1 / 5, 1 / 3]

    def at(expr, n, size=1):
        return slice(n, n + size) if isinstance(expr, int) else bass.ds(expr + n, size)

    def settle(act):
        act.e.wait_ge(consts_ready, 1)

    def dve_softplus(dve, x, o, s, exp_in, exp_out, sign):
        dve.link(dve.e.tensor_scalar(s[0], x, -1.0, None, ALU.mult))
        dve.e.tensor_tensor(s[0], s[0], x, ALU.max).then_inc(exp_in, 1)
        dve.wait(exp_out)
        dve.link(dve.e.tensor_scalar(s[1], s[0], 2.0, None, ALU.add))
        dve.link(dve.e.reciprocal(s[1], s[1]))
        dve.link(dve.e.tensor_tensor(s[1], s[0], s[1], ALU.mult))
        dve.link(dve.e.tensor_tensor(s[2], s[1], s[1], ALU.mult))
        dve.link(dve.e.tensor_scalar(s[3], s[2], SERIES[0], None, ALU.mult))
        for c in SERIES[1:]:
            dve.link(dve.e.scalar_tensor_tensor(s[3], s[3], c, s[2], ALU.add, ALU.mult))
        dve.link(dve.e.scalar_tensor_tensor(s[3], s[3], 1.0, s[1], ALU.add, ALU.mult))
        dve.link(dve.e.tensor_scalar(s[0], x, 0.0, None, ALU.max if sign > 0 else ALU.min))
        dve.link(dve.e.scalar_tensor_tensor(o, s[3], 2.0 * sign, s[0], ALU.mult, ALU.add))

    def act_softplus(act, y, exp_in, exp_out):
        act.wait(exp_in)
        act.e.activation(y, y, ACT.Exp, scale=-1.0).then_inc(exp_out, 1)

    def pe_dt(pe):
        b = plan.b["dt"]
        pe_logits(pe, b, DT_WH, DT_WL, SSM_H, True)
        b += 1
        pe.wait(ssm_sems["log_ready"])
        bank = take_bank(pe, b + 1)
        for tt in range(NT):
            ins = nc.tensor.transpose(bank[0:SSM_H, tt * P:tt * P + P], DTS[:, 4, tt, :], IDENT[:])
        ins.then_inc(bank_ready, 1)
        pe.wait(ssm_sems["cum_ready"])
        bank = take_bank(pe, b + 2)
        for tt in range(NT):
            ins = nc.tensor.transpose(bank[:, tt * SSM_H:tt * SSM_H + SSM_H], ACS[:, 1, tt * P:tt * P + P],
                                      IDENT[0:SSM_H, 0:SSM_H])
        ins.then_inc(bank_ready, 1)

    def act_dt(act):
        w = ssm_sems
        act.wait(w["exp_in"])
        act.e.activation(DTS[:, 0], DTS[:, 0], ACT.Exp, scale=-1.0)
        act.e.activation(DT_ROW[:, 1, :], DT_ROW[:, 1, :], ACT.Exp).then_inc(w["exp_out"], 1)
        act.wait(w["cum_ready"])
        act.e.dma_start(acs_dram, ACS[:, 1, :]).then_inc(w["cum_saved"], 16)
        act.wait(w["cum_saved"], 16)
        for hh in range(2):
            act_decay_row(act, 0, hh)

    def act_decay_row(act, e, head):
        act.e.dma_start(ACS_ROW[:, head % 2, :], acs_dram[at(e, head), :].rearrange("a n -> (a n)").partition_broadcast(P))\
             .then_inc(row_landed[head % 2], 16)

    def dve_dt(dve):
        w, b = ssm_sems, plan.b["dt"]
        for h in range(2):
            dve.e.tensor_copy(D_COL[h * HD:h * HD + HD, :], D_ROW[h * HD:h * HD + HD, :].rearrange("p (m h) -> p h m", h=2)[:, h, :])
        logits = dve_logits(dve, b, SSM_H)
        b += 1
        dve.e.tensor_tensor(DTS[:, 5], logits, bcast(DT_ROW[:, 0, :], 1, NT), ALU.add).then_inc(bank_free[b % 4], 1)
        dve.e.wait_ge(bank_free[b % 4], b // 4 + 1)
        dve_softplus(dve, DTS[:, 5], DT[:], [DTS[:, i] for i in range(4)], w["exp_in"], w["exp_out"], 1)
        dve.e.scalar_tensor_tensor(DTS[:, 4], DT[:], -1.0, bcast(DT_ROW[:, 1, :], 1, NT), ALU.mult, ALU.mult)\
             .then_inc(w["log_ready"], 1)
        b += 1
        dve.e.tensor_copy(ACS[:, 0, :], full_bank(dve, b)[0:SSM_H, :]).then_inc(bank_free[b % 4], 1)
        dve.e.wait_ge(bank_free[b % 4], b // 4 + 1)
        dve.e.tensor_tensor_scan(ACS[:, 1, :], ONES[0:SSM_H, 0:1].broadcast_to([SSM_H, SEQ]), ACS[:, 0, :], 0.0,
                                 ALU.mult, ALU.add).then_inc(w["cum_ready"], 1)
        b += 1
        dve.link(dve.e.tensor_copy(ACS_COL[:].rearrange("p t h -> p (t h)"), full_bank(dve, b)[:, 0:NT * SSM_H]))
        dve.e.tensor_copy(RSTD[0:1, 0:1], ONES[0:1, 0:1]).then_inc(bank_free[b % 4], 1)

    def pe_ssm_unit(pe, e, c, j):
        pair = take_pair(pe, plan.p["ssm"] + 3 * c + j, turns(e, 3))
        unit_channels(pe, plan.u["ssm"] + 3 * c + j, pair, hh, hl, KD, off=times(e, 6))

    def turns(e, n):
        return 0 if e is None else e * n

    times = turns

    def conv_tiles(c, j):
        return (2, (16 + c, 24 + c), 2) if j == 0 else (0, (2 * c, 2 * c + 1), 4)

    def act_ssm_conv(act, e, c, j):
        w, par = ssm_sems, c % 2
        first, tiles, step = conv_tiles(c, j)
        p = plan.p["ssm"] + 3 * c + j
        pair = full_pair(act, plan.u["ssm"] + 3 * c + j, p, times(e, 6))
        settle(act)
        for m, ct in enumerate(tiles):
            wc = COLS[:, at(times(e, step), col_at["conv_w"] + 3 * 32 + ct)]
            bc = COLS[:, at(times(e, step), col_at["conv_b"] + ct)]
            act.e.activation(CONV[:, par, first + m, :], pair[:, m, :], ACT.Identity, bias=bc, scale=wc).then_inc(w["conv_in"], 1)
        act.e.wait_ge(evac[p % 2], turns(e, 3) + (p // 2 + 1))
        both = CONV[:, par, first:first + 2, :]
        act.e.activation(both, both, ACT.Silu).then_inc(w["conv_ready"], 1)

    def act_ssm_gate(act, e, c):
        u, p = plan.u["ssm"] + 3 * c + 2, plan.p["ssm"] + 3 * c + 2
        pair = full_pair(act, u, p, times(e, 6))
        act.e.activation(ZS[:, c % 2], pair[:], ACT.Silu).then_inc(evac[p % 2], 1)

    def dve_ssm_conv(dve, e, c, j):
        w, par = ssm_sems, c % 2
        first, tiles, step = conv_tiles(c, j)
        p = plan.p["ssm"] + 3 * c + j
        pair = PAIR[p % 2]
        for m, ct in enumerate(tiles):
            acc = CONV[:, par, first + m, :]
            dve.wait(w["conv_in"])
            for sh in range(1, 4):
                wc = COLS[:, at(times(e, step), col_at["conv_w"] + (3 - sh) * 32 + ct)]
                ins = dve.e.scalar_tensor_tensor(acc[:, sh:], pair[:, m, :SEQ - sh], wc, acc[:, sh:], ALU.mult, ALU.add)
                if m == 0 or sh < 3:
                    dve.link(ins)
        ins.then_inc(evac[p % 2], 1)

    def ssm_scores_bank(c, j):
        return plan.b["ssm"] + (8 * c - 1 if c else 0) + j

    def ssm_norm_bank(c):
        return plan.b["ssm"] + (8 * c + 12 if c + 1 < SSM_G else 8 * SSM_G - 1)

    def ssm_heads_bank(c, m):
        return plan.b["ssm"] + 8 * c + 5 + m

    CB_HOME = {0: (2, 0), 1: (3, 0), 3: (3, 384), 2: (4, 0)}

    def pe_ssm_scores(pe, e, c):
        par = c % 2
        pe.wait(ssm_sems["conv_ready"], 2)
        for m in range(2):
            bank = take_bank(pe, ssm_scores_bank(c, m), turns(e, 4))
            for tt in range(NT):
                ins = nc.tensor.transpose(bank[:, tt * P:tt * P + P], CONV[:, par, m, tt * P:tt * P + P], IDENT[:])
            ins.then_inc(bank_ready, 1)
        for j in (2, 3, 4):
            bank = take_bank(pe, ssm_scores_bank(c, j), turns(e, 4))
            for i in [x for x in CB_HOME if CB_HOME[x][0] == j]:
                a, wide = CB_HOME[i][1], SEQ - i * P
                ins = nc.tensor.matmul(bank[:, a:a + wide], CONV[:, par, 2, i * P:i * P + P], CONV[:, par, 3, i * P:SEQ],
                                       start=True, stop=True)
            ins.then_inc(bank_ready, 1)

    def pe_ssm_heads(pe, e, c, m):
        w = ssm_sems
        bank = take_bank(pe, ssm_heads_bank(c, m), turns(e, 4))
        for hd in (2 * m, 2 * m + 1):
            a = (hd % 2) * HD
            pe.wait(w["masked"])
            for i in range(NT):
                ins = nc.tensor.matmul(bank[a:a + HD, i * P:SEQ], XDT[:, i, hd * HD:hd * HD + HD],
                                       DECAY[:, hd % 2, TRI_AT[i]:TRI_AT[i] + SEQ - i * P], start=i == 0, stop=i == NT - 1)
            if hd == 0:
                ins.then_inc(w["first_head"], 1)
            elif hd % 2:
                ins.then_inc(bank_ready, 1)

    def pe_ssm_norm(pe, e, c):
        pe.wait(sq_ready)
        bank = take_bank(pe, ssm_norm_bank(c), turns(e, 4))
        for m in range(2):
            ins = nc.tensor.matmul(bank[:], ONES[:], SQ[:, m, :], start=m == 0, stop=m == 1)
        ins.then_inc(bank_ready, 1)

    def act_ssm_decay(act, e, c, heads, more):
        w = ssm_sems
        for hd in heads:
            act.wait(w["decay_in"])
            act.e.activation(DECAY[:, hd % 2, :], DECAY[:, hd % 2, :], ACT.Exp).then_inc(w["decay_out"], 1)
            if more or hd < 2:
                act_decay_row(act, 0 if e is None else e * 8, 4 * c + hd + 2)

    def act_ssm_square(act, e, c):
        w = ssm_sems
        act.wait(w["gated"])
        settle(act)
        act.e.activation(SQ[:], G[:, at(times(e, 4), 2 * c, 2), :], ACT.Square).then_inc(sq_ready, 1)

    def dve_ssm_scores(dve, e, c):
        for m in range(2):
            b = ssm_scores_bank(c, m)
            bank = full_bank(dve, b, turns(e, 4))
            dt = DT[:, :, at(times(e, 8), 4 * c + 2 * m, 2)]
            dve.e.tensor_tensor(XDT[:, :, m * P:m * P + P].rearrange("p t (h q) -> p t h q", q=HD),
                                bank[:].rearrange("p (t h q) -> p t h q", t=NT, q=HD), bcast(dt, 3, HD), ALU.mult)\
                 .then_inc(bank_free[b % 4], 1)
        for j in (2, 3, 4):
            b = ssm_scores_bank(c, j)
            bank = full_bank(dve, b, turns(e, 4))
            for i in [x for x in CB_HOME if CB_HOME[x][0] == j]:
                a, wide = CB_HOME[i][1], SEQ - i * P
                ins = dve.e.tensor_tensor(CBM[:, TRI_AT[i]:TRI_AT[i] + wide], bank[:, a:a + wide], LATER[:, 0:wide], ALU.mult)
            ins.then_inc(bank_free[b % 4], 1)

    def dve_ssm_decay(dve, e, c, heads):
        w = ssm_sems
        for hd in heads:
            if hd == 2:
                dve.wait(w["first_head"])
            if hd == 3:
                full_bank(dve, ssm_heads_bank(c, 0), turns(e, 4))
            dve.wait(row_landed[hd % 2], 16)
            for i in range(NT):
                cum = ACS_COL[:, i, at(times(e, 8), 4 * c + hd)]
                ins = dve.e.tensor_scalar(DECAY[:, hd % 2, TRI_AT[i]:TRI_AT[i] + SEQ - i * P], ACS_ROW[:, hd % 2, i * P:SEQ],
                                          cum, 0.0, ALU.subtract, ALU.min)
            ins.then_inc(w["decay_in"], 1)

    def dve_ssm_mask(dve, heads):
        w = ssm_sems
        for hd in heads:
            dve.wait(w["decay_out"])
            dve.e.tensor_tensor(DECAY[:, hd % 2, :], DECAY[:, hd % 2, :], CBM[:], ALU.mult).then_inc(w["masked"], 1)

    def dve_ssm_output(dve, e, c):
        w, par = ssm_sems, c % 2
        for m in range(2):
            b = ssm_heads_bank(c, m)
            bank = full_bank(dve, b, turns(e, 4))
            dve.e.scalar_tensor_tensor(TMP[:, m, :], CONV[:, par, m, :], D_COL[:, at(times(e, 4), 2 * c + m)], bank[:],
                                       ALU.mult, ALU.add).then_inc(bank_free[b % 4], 1)
        dve.e.wait_ge(bank_free[b % 4], turns(e, 4) + (b // 4 + 1))
        dve.e.tensor_tensor(G[:, at(times(e, 4), 2 * c, 2), :], TMP[:], ZS[:, par], ALU.mult).then_inc(w["gated"], 1)

    def dve_ssm_variance(dve, e, c):
        bank = full_bank(dve, ssm_norm_bank(c), turns(e, 4))
        dve.e.tensor_scalar(RSTD[:], bank[:], 1.0 / 256, EPS, ALU.mult, ALU.add).then_inc(var_ready, 1)

    def dve_ssm_norm(dve, e, c):
        b = ssm_norm_bank(c)
        dve.wait(root_ready)
        dve.e.reciprocal(RSTD[:], RSTD[:]).then_inc(bank_free[b % 4], 1)
        dve.e.wait_ge(bank_free[b % 4], turns(e, 4) + (b // 4 + 1))
        for m in range(2):
            gm = G[:, at(times(e, 4), 2 * c + m), :]
            ins = dve.e.scalar_tensor_tensor(gm, gm, COLS[:, at(times(e, 4), col_at["ssm_norm"] + 2 * c + m)],
                                             bcast(RSTD[:], 1, 1), ALU.mult, ALU.mult)
        dve.link(ins)

    def ssm_program(eng, group, per):
        group(None, 0)
        with eng.loop((SSM_G - 2) // 2, per) as i:
            for c in (1, 2):
                group(i, c)
        group(None, SSM_G - 1)

    def pe_ssm(pe):
        w = ssm_sems

        def unit(e, c, j):
            if c < SSM_G:
                pe_ssm_unit(pe, e, c, j)

        def group(e, c):
            pe_ssm_scores(pe, e, c)
            if c:
                pe_ssm_norm(pe, e, c - 1)
            unit(e, c + 1, 0)
            pe_ssm_heads(pe, e, c, 0)
            unit(e, c + 1, 1)
            pe_ssm_heads(pe, e, c, 1)
            unit(e, c + 1, 2)

        for j in range(3):
            unit(None, 0, j)
        ssm_program(pe, group, {w["conv_ready"]: 4, w["masked"]: 8, sq_ready: 2})
        pe_ssm_norm(pe, None, SSM_G - 1)

    def act_ssm(act):
        w = ssm_sems

        def conv(e, c, j):
            if c < SSM_G:
                act_ssm_conv(act, e, c, j)

        def group(e, c):
            act_ssm_decay(act, e, c, (0, 1), True)
            if c:
                act_root(act, RSTD[:], var_ready)
            conv(e, c + 1, 0)
            act_ssm_decay(act, e, c, (2, 3), c + 1 < SSM_G)
            conv(e, c + 1, 1)
            act_ssm_square(act, e, c)
            if c + 1 < SSM_G:
                act_ssm_gate(act, e, c + 1)

        conv(None, 0, 0)
        conv(None, 0, 1)
        act_ssm_gate(act, None, 0)
        ssm_program(act, group, {w["decay_in"]: 8, w["gated"]: 2, var_ready: 2})
        act_root(act, RSTD[:], var_ready)

    def dve_ssm(dve):
        w = ssm_sems

        def conv(e, c, j):
            if c < SSM_G:
                dve_ssm_conv(dve, e, c, j)

        def group(e, c):
            dve_ssm_scores(dve, e, c)
            dve_ssm_decay(dve, e, c, (0, 1))
            if c:
                dve_ssm_variance(dve, e, c - 1)
            dve_ssm_mask(dve, (0, 1))
            if c:
                dve_ssm_norm(dve, e, c - 1)
            conv(e, c + 1, 0)
            dve_ssm_decay(dve, e, c, (2, 3))
            dve_ssm_mask(dve, (2, 3))
            conv(e, c + 1, 1)
            dve_ssm_output(dve, e, c)

        conv(None, 0, 0)
        conv(None, 0, 1)
        ssm_program(dve, group, {w["conv_in"]: 8, w["first_head"]: 2, w["decay_out"]: 8, row_landed[0]: 64, row_landed[1]: 64,
                                 root_ready: 2, dve.chain: 22})
        dve_ssm_variance(dve, None, SSM_G - 1)
        dve_ssm_norm(dve, None, SSM_G - 1)

    def act_ssm_out(act):
        for half in range(2):
            act.e.wait_ge(unit_done, plan.u["ssmout"] + 4 * half)
            if half == 0:
                act.wait(g_ready)
            for k in range(KD):
                act.e.activation(HH[:, k, :], G[:, half * KD + k, :], ACT.Copy).then_inc(hi_ready, 1)

    g_ready = sem("g_ready")

    def dve_ssm_out(dve):
        dve.e.tensor_copy(RSTD[:, 0:1], ONES[:, 0:1]).then_inc(g_ready, 1)
        for half in range(2):
            for k in range(KD):
                dve.wait(hi_ready)
                dve.e.tensor_tensor(HL[:, k, :], G[:, half * KD + k, :], HH[:, k, :].bitcast(F32), ALU.subtract)\
                     .then_inc(h_ready, 1)
            dve.passed(h_ready, KD)
            for i in range(4):
                p = plan.p["ssmout"] + 4 * half + i
                pair = full_pair(dve, plan.u["ssmout"] + 4 * half + i, p)
                for m in range(2):
                    c = 2 * i + m
                    ins = dve.e.scalar_tensor_tensor(X[:, c, :], pair[:, m, :], mod(1, 2, c), X[:, c, :], ALU.mult, ALU.add)
                ins.then_inc(evac[p % 2], 1)

    def pe_ssm_out(pe):
        for half in range(2):
            pe.wait(h_ready, KD)
            for i in range(4):
                pair = take_pair(pe, plan.p["ssmout"] + 4 * half + i)
                unit_channels(pe, plan.u["ssmout"] + 4 * half + i, pair, hh, hl, KD)

    gate_sems = {s: sem(f"gate_{s}") for s in ("exp_in", "exp_out", "log_ready", "cum_ready")}
    gmlp_landed, half_ready, qk_ready, spatial_ready = (sem(s) for s in ("gmlp_landed", "half_ready", "qk_ready", "spatial_ready"))

    def evin_copied(eng, first):
        for p in (plan.p["evin"] + first, plan.p["evin"] + first + 1):
            eng.e.wait_ge(evac[p % 2], p // 2 + 1)

    def pe_evin(pe):
        b = plan.b["gate"]
        for i in range(10):
            u, pair = plan.u["evin"] + i, take_pair(pe, plan.p["evin"] + i)
            if i == 0:
                first_unit(pe, u, pair, pe.seen(h_ready))
                pe.passed(h_ready, KD)
            elif i in (2, 3, 8, 9):
                unit_tokens(pe, u, pair)
            else:
                unit_channels(pe, u, pair, hh, hl, KD)
            if i == 0:
                pe_logits(pe, b, FG_WH, FG_WL, HEADS, False)
            if i == 1:
                pe.e.wait_ge(gmlp_landed, 48)
                bank = take_bank(pe, b + 2)
                for g in range(4):
                    ins = nc.tensor.transpose(bank[:, g * P:g * P + P], SPAT[:, g, :], IDENT[:])
                ins.then_inc(bank_ready, 1)
            if i == 3:
                pe.wait(gate_sems["log_ready"])
                bank = take_bank(pe, b + 3)
                for tt in range(NT):
                    ins = nc.tensor.transpose(bank[0:HEADS, tt * P:tt * P + P], FGL[:, 5, tt, :], IDENT[:])
                ins.then_inc(bank_ready, 1)
            if i in (6, 8):
                for m in range(4):
                    pe.wait(sq_ready)
                    bank = take_bank(pe, plan.b["qknorm"] + 4 * (i // 8) + m)
                    nc.tensor.matmul(bank[:], HEAD_ONES[:], norm_buffer(m), start=True, stop=True).then_inc(bank_ready, 1)

    def act_evin(act):
        act.e.dma_start(SPAT[:], t["ev_w_spatial_2"][0].rearrange("g t s -> t g s")).then_inc(gmlp_landed, 16)
        act.e.dma_start(SPAT_B[:], t["ev_b_spatial_2"][0].partition_broadcast(P)).then_inc(gmlp_landed, 16)
        act.e.dma_start(V_GAIN[:], t["ev_v_norm_2"][0].partition_broadcast(P)).then_inc(gmlp_landed, 16)
        act_copy_pairs(act, "evin", 0, 2, UA, False, ACT.Gelu_apprx_tanh)
        act_softplus(act, FGL[:, 0], gate_sems["exp_in"], gate_sems["exp_out"])
        act_copy_pairs(act, "evin", 2, 2, VA, True, ACT.Gelu_apprx_tanh)
        act_root(act, VR[:], var_ready)
        act_copy_pairs(act, "evin", 4, 2, Q1, False)
        act.e.wait_ge(unit_done, plan.u["evin"] + 1)
        evin_copied(act, 4)
        act_squares(act, 0)
        act_copy_pairs(act, "evin", 6, 1, K1, False)
        act_qk_root(act, 0)
        act_copy_pairs(act, "evin", 7, 1, K1[:, 2:4], False)
        act.e.wait_ge(bank_ready, plan.b["qknorm"] + 4)
        evin_copied(act, 6)
        act_squares(act, 1)
        act_copy_pairs(act, "evin", 8, 1, V1, True)
        act_qk_root(act, 1)
        act_copy_pairs(act, "evin", 9, 1, V1[:, :, 256:], True)

    def dve_evin(dve):
        w, b = gate_sems, plan.b["gate"]
        dve.e.tensor_scalar(MINUS_HEAD[:], bcast(IDENT[0:HEADS, 0:HEADS], 2, P), -HD ** 0.5, None, ALU.mult)
        dve_cut_narrow(dve, FG_WH[:], FG_WL[:], FG_W[:])
        logits = dve_logits(dve, b, HEADS)
        b += 1
        dve.e.tensor_tensor(FGL[:, 5], logits, bcast(FG_B[:], 1, NT), ALU.add).then_inc(bank_free[b % 4], 1)
        dve.e.wait_ge(bank_free[b % 4], b // 4 + 1)
        dve_softplus(dve, FGL[:, 5], FGL[:, 4], [FGL[:, i] for i in range(4)], w["exp_in"], w["exp_out"], -1)
        dve.e.tensor_copy(FGL[:, 5], FGL[:, 4]).then_inc(w["log_ready"], 1)
        b += 1
        dve.e.wait_ge(gmlp_landed, 48)
        dve.e.tensor_tensor(SPAT_T[:], full_bank(dve, b)[:].rearrange("p (g t) -> p g t", t=P), bcast(LATER[:, 0:P], 1, 4),
                            ALU.mult).then_inc(bank_free[b % 4], 1)
        b += 1
        dve.e.tensor_copy(FCUM[:, 0, :], full_bank(dve, b)[0:HEADS, :]).then_inc(bank_free[b % 4], 1)
        dve.e.wait_ge(bank_free[b % 4], b // 4 + 1)
        dve.e.tensor_tensor_scan(FCUM[:, 1, :], ONES[0:HEADS, 0:1].broadcast_to([HEADS, SEQ]), FCUM[:, 0, :], 0.0,
                                 ALU.mult, ALU.add).then_inc(w["cum_ready"], 1)
        dve_gmlp_norm(dve)
        for i in range(2):
            dve_qknorm(dve, i)

    def pe_gmlp(pe):
        b = plan.b["gmlp"]
        pe.wait(spatial_ready)
        for g in range(4):
            bank = take_bank(pe, b + g)
            for n in range(NT):
                ins = nc.tensor.matmul(bank[:, n * P:n * P + P], VA[:, n, g * P:g * P + P], SPAT_T[:, g, :], start=True, stop=True)
            ins.then_inc(bank_ready, 1)
        pe.wait(qk_ready, 2)
        pe.wait(gate_sems["cum_ready"])
        evin_copied(pe, 8)

    def act_gmlp(act):
        for g in range(4):
            act.wait(pre_ready)
            act.e.activation(HH[:, g, :], VSQ[:, g, :], ACT.Copy).then_inc(hi_ready, 1)

    def dve_gmlp_norm(dve):
        evin_copied(dve, 2)
        groups = VA[:].rearrange("p n (g c) -> p (n g) c", c=P)
        dve.link(dve.e.tensor_tensor(VSQ[:], VA[:], VA[:], ALU.mult))
        dve.link(dve.e.tensor_reduce(VR[:], VSQ[:].rearrange("p n (g c) -> p (n g) c", c=P), AX.X, ALU.add))
        dve_rstd(dve, VR[:], VR[:], P)
        dve.link(dve.e.tensor_tensor(groups, groups, bcast(VR[:], 2, P), ALU.mult))
        dve.e.tensor_tensor(VA[:], VA[:], bcast(V_GAIN[:], 1, NT), ALU.mult).then_inc(spatial_ready, 1)

    def dve_gmlp(dve):
        b = plan.b["gmlp"]
        dve.wait(qk_ready)
        evin_copied(dve, 0)
        for g in range(4):
            bank = full_bank(dve, b + g)
            dve.e.tensor_tensor(VSQ[:, g, :].rearrange("p (n t) -> p n t", t=P), bank[:].rearrange("p (n t) -> p n t", t=P),
                                bcast(SPAT_B[:, g, :], 1, NT), ALU.add).then_inc(bank_free[(b + g) % 4], 1)
        for g in range(4):
            dve.e.wait_ge(bank_free[(b + g) % 4], (b + g) // 4 + 1)
            dve.e.tensor_tensor(VSQ[:, g, :], VSQ[:, g, :], UA[:, g, :], ALU.mult).then_inc(pre_ready, 1)
        dve.wait(pre_ready, 4)
        for g in range(4):
            dve.wait(hi_ready)
            dve.e.tensor_tensor(HL[:, g, :], VSQ[:, g, :], HH[:, g, :].bitcast(F32), ALU.subtract).then_inc(half_ready, 1)

    def act_squares(act, i):
        for m in range(4):
            act.e.activation(norm_buffer(m), (Q1, K1)[i][:, m, :], ACT.Square).then_inc(sq_ready, 1)

    def act_qk_root(act, i):
        last = plan.b["qknorm"] + 4 * i + 3
        act.e.wait_ge(bank_free[last % 4], last // 4 + 1)
        act.e.activation(VSQ[:], VSQ[:], ACT.Sqrt).then_inc(root_ready, 1)

    def dve_qknorm(dve, i):
        b, arr = plan.b["qknorm"] + 4 * i, (Q1, K1)[i]
        if i:
            dve.wait(qk_ready)
        else:
            dve.wait(spatial_ready)
        for m in range(4):
            dve.e.tensor_scalar(VSQ[:, m, :], full_bank(dve, b + m)[:], 1.0 / HD, EPS, ALU.mult, ALU.add)\
                 .then_inc(bank_free[(b + m) % 4], 1)
        dve.wait(root_ready)
        dve.link(dve.e.reciprocal(VSQ[:], VSQ[:]))
        for m in range(4):
            ins = dve.e.scalar_tensor_tensor(arr[:, m, :], arr[:, m, :], QK_GAIN[:, i:i + 1], VSQ[:, m, :], ALU.mult, ALU.mult)
        ins.then_inc(qk_ready, 1)

    ffn_sems = {s: sem(f"ffn_{s}") for s in ("conv_in", "gate", "hidden", "hidden_hi", "hidden_ready")}
    FFN_PARTS = ((0, 8), (8, 8), (16, 6))

    def pe_ffn(pe, layer):
        w, u0, p0 = ffn_sems, plan.u[f"ffn{layer}"], plan.p[f"ffn{layer}"]
        with pe.e.Fori(0, FB // 2) as i:
            first_unit(pe, u0, take_pair(pe, p0, i), pe.seen(h_ready), off=i * 2)
            unit_channels(pe, u0 + 1, take_pair(pe, p0 + 1, i), hh, hl, KD, off=i * 2)
        pe.passed(h_ready, KD)
        with pe.e.Fori(0, 2) as i:
            for c in range(2):
                pair = take_pair(pe, p0 + FB + c, i)
                if c == 0:
                    pe.e.wait_ge(w["hidden_ready"], FB * (layer + 1))
                for j, (k0, n) in enumerate(FFN_PARTS):
                    unit_channels(pe, u0 + FB + 3 * c + j, pair, lambda k: FHH[:, k0 + k, :], lambda k: FHL[:, k0 + k, :], n,
                                  first=j == 0, last=j == 2, off=i * 6)

    def act_ffn(act, layer):
        w, u0, p0 = ffn_sems, plan.u[f"ffn{layer}"], plan.p[f"ffn{layer}"]
        with act.loop(FB // 2, {w["hidden"]: 2}) as i:
            for b in range(2):
                pair = full_pair(act, u0 + b, p0 + b, i * 2)
                settle(act)
                for m in range(2):
                    wc = COLS[:, bass.ds(i * 2 + (col_at["fconv_w"] + layer * 6 * FB + 4 * FB + m * FB + b), 1)]
                    bc = COLS[:, bass.ds(i * 2 + (col_at["fconv_b"] + layer * 2 * FB + m * FB + b), 1)]
                    act.e.activation((SQ, FUP)[m][:, b, :], pair[:, m, :], ACT.Identity, bias=bc, scale=wc).then_inc(w["conv_in"], 1)
                act.e.wait_ge(evac[b], i + ((p0 + b) // 2 + 1))
                act.e.activation(SQ[:, b, :], SQ[:, b, :], ACT.Silu).then_inc(w["gate"], 1)
                act.wait(w["hidden"])
                settle(act)
                act.e.activation(FHH[:, bass.ds(i * 2 + b, 1), :], TMP[:, b:b + 1, :], ACT.Copy).then_inc(w["hidden_hi"], 1)

    def dve_ffn(dve, layer):
        w, u0, p0 = ffn_sems, plan.u[f"ffn{layer}"], plan.p[f"ffn{layer}"]
        with dve.loop(FB // 2, {w["conv_in"]: 4, w["gate"]: 2, w["hidden"]: 2, w["hidden_hi"]: 2, dve.chain: 2}) as i:
            for b in range(2):
                pair = PAIR[b]
                dve.wait(w["conv_in"], 2)
                for sh in (1, 2):
                    for m in range(2):
                        wc = COLS[:, bass.ds(i * 2 + (col_at["fconv_w"] + layer * 6 * FB + (2 - sh) * 2 * FB + m * FB + b), 1)]
                        acc = (SQ, FUP)[m][:, b, sh:]
                        ins = dve.e.scalar_tensor_tensor(acc, pair[:, m, :SEQ - sh], wc, acc, ALU.mult, ALU.add)
                    if sh == 1:
                        dve.link(ins)
                ins.then_inc(evac[b], 1)
                dve.wait(w["gate"])
                dve.e.tensor_tensor(TMP[:, b, :], SQ[:, b, :], FUP[:, b, :], ALU.mult).then_inc(w["hidden"], 1)
                dve.wait(w["hidden"])
                dve.wait(w["hidden_hi"])
                f = bass.ds(i * 2 + b, 1)
                dve.e.tensor_tensor(FHL[:, f, :], TMP[:, b:b + 1, :], FHH[:, f, :].bitcast(F32), ALU.subtract)\
                     .then_inc(w["hidden_ready"], 1)
        with dve.e.Fori(0, 2) as i:
            for c in range(2):
                pair = full_pair(dve, u0 + FB + 3 * c + 2, p0 + FB + c, i * 6)
                x = X[:, bass.ds(i * 4 + 2 * c, 2), :]
                dve.e.tensor_tensor(x, pair[:], x, ALU.add).then_inc(evac[c], 1)

    ple_landed, ple_hi, ple_gate = sem("ple_landed"), sem("ple_hi"), sem("ple_gate")

    def act_ple_load(act, layer):
        for s in range(2):
            act.e.wait_ge(evac[s], plan.p[f"ple{layer}"] // 2)
        act.e.dma_start(PTOK[:], t["p_2"][layer, 0].rearrange("(t p) d -> p t d", p=P)).then_inc(ple_landed, 16)

    def pe_ple_rows(pe, layer):
        b = plan.b[f"ple_rows{layer}"]
        pe.wait(ple_landed, 16)
        for k in range(2):
            bank = take_bank(pe, b + k)
            for tt in range(NT):
                ins = nc.tensor.transpose(bank[:, tt * P:tt * P + P], PTOK[:, tt, k * P:k * P + P], IDENT[:])
            ins.then_inc(bank_ready, 1)

    def pe_ple(pe, layer):
        b, u0, p0 = plan.b[f"ple_rows{layer}"], plan.u[f"ple{layer}"], plan.p[f"ple{layer}"]
        for k in range(2):
            pe.e.wait_ge(bank_free[(b + k) % 4], (b + k) // 4 + 1)
        for half in range(2):
            u, p = u0 + 3 * half, p0 + 4 * half
            pe.e.wait_ge(split_ready, u + 1)
            for q in range(2):
                pair = take_pair(pe, p + q)
                for m in range(2):
                    for k in range(2):
                        c = (k * 4 + 2 * q + m) * P
                        ins = mm3(pair[:, m, :], WH[:, u % 2, c:c + P], WL[:, u % 2, c:c + P], PH[:, k, :], PL[:, k, :], k == 0, k == 1)
            ins.then_inc(unit_done, 1)
            for i in range(2):
                pair = take_pair(pe, p + 2 + i)
                if half == 0 and i == 0:
                    first_unit(pe, u + 1, pair, pe.seen(h_ready))
                    pe.passed(h_ready, KD)
                else:
                    unit_channels(pe, u + 1 + i, pair, hh, hl, KD)

    def act_ple_rows(act, layer):
        for k in range(2):
            act.e.activation(PH[:, k, :], full_bank(act, plan.b[f"ple_rows{layer}"] + k)[:], ACT.Copy).then_inc(ple_hi, 1)

    def act_ple(act, layer):
        u0, p0 = plan.u[f"ple{layer}"], plan.p[f"ple{layer}"]
        for half in range(2):
            u, p = u0 + 3 * half, p0 + 4 * half
            for i in range(4):
                pair = full_pair(act, u + max(i - 1, 0), p + i)
                if half and i == 0 or i == 3:
                    act.e.wait_ge(evac[(p + i - 1) % 2], (p + i - 1) // 2 + 1)
                if i < 2:
                    act.e.activation(PROJ[:, 2 * i:2 * i + 2, :], pair[:], ACT.Copy).then_inc(evac[(p + i) % 2], 1)
                else:
                    act.e.activation(SQ[:], pair[:], ACT.Sigmoid).then_inc(ple_gate, 1)

    def dve_ple(dve, layer):
        b = plan.b[f"ple_rows{layer}"]
        for k in range(2):
            dve.wait(ple_hi)
            dve.e.tensor_tensor(PL[:, k, :], full_bank(dve, b + k)[:], PH[:, k, :].bitcast(F32), ALU.subtract)\
                 .then_inc(bank_free[(b + k) % 4], 1)

    def dve_ple_gates(dve, layer):
        p0 = plan.p[f"ple{layer}"]
        for half in range(2):
            for i in range(2):
                p, c = p0 + 4 * half + 2 + i, 4 * half + 2 * i
                dve.wait(ple_gate)
                dve.link(dve.e.tensor_tensor(TMP[:], SQ[:], PROJ[:, 2 * i:2 * i + 2, :], ALU.mult))
                dve.e.tensor_tensor(X[:, c:c + 2, :], TMP[:], X[:, c:c + 2, :], ALU.add).then_inc(evac[p % 2], 1)

    glu_gate = sem("glu_gate")

    def pe_glu(pe):
        pe.wait(h_ready, KD)
        pe_matrix(pe, "glu", KD)

    def act_glu(act):
        for i in range(KD):
            pair = full_pair(act, plan.u["glu"] + i, plan.p["glu"] + i)
            act.e.activation(SQ[:, i % 2, :], pair[:, 1, :], ACT.Sigmoid).then_inc(glu_gate, 1)

    def dve_glu(dve):
        for i in range(KD):
            p = plan.p["glu"] + i
            dve.wait(glu_gate)
            dve.link(dve.e.tensor_tensor(TMP[:, i % 2, :], PAIR[p % 2][:, 0, :], SQ[:, i % 2, :], ALU.mult))
            dve.e.tensor_tensor(X[:, i, :], TMP[:, i % 2, :], X[:, i, :], ALU.add).then_inc(evac[p % 2], 1)

    s5_sems = {s: sem(f"s5_{s}") for s in ("a_landed", "landed", "vec_in", "vec_out", "consts", "bb", "angles", "tab", "w1x",
                                           "ca", "turning", "bu", "state", "gelu")}
    CR, CI, STEP_HI, STEP_LO, MAG4 = range(5)
    BELOW_TWO_PI = 6.283185
    GRID = 16384.0

    def act_s5_rows(act):
        for i, name in enumerate(("od_a_re_2", "od_a_im_2")):
            act.e.dma_start(AROW[:, i, :], t[name][0].rearrange("(t h) p -> t (h p)", h=2)).then_inc(s5_sems["a_landed"], 16)
        act.e.dma_start(LDT_ROW[:], t["od_log_dt_2"][0].partition_broadcast(P)).then_inc(s5_sems["a_landed"], 16)

    def pe_s5_vectors(pe):
        b = plan.b["s5a"]
        pe.e.wait_ge(s5_sems["a_landed"], 48)
        bank = take_bank(pe, b)
        for i in range(2):
            ins = nc.tensor.transpose(bank[:, i * S5_TILES:i * S5_TILES + S5_TILES], AROW[:, i, :], IDENT[0:S5_TILES, 0:S5_TILES])
        ins.then_inc(bank_ready, 1)

    S5_NAMES = ("lr", "li", "ldt", "dt", "e", "th", "n", "turn", "red", "cos", "sin", "half", "big", "ec", "poly", "small",
                "em1", "mag", "nr", "den", "p", "q", "turn4")
    vec = {name: S1[:, 0, i * S5_TILES:(i + 1) * S5_TILES] for i, name in enumerate(S5_NAMES)}

    def act_s5_vectors(act):
        w = s5_sems
        act.wait(w["vec_in"])
        act.e.activation(vec["dt"], vec["ldt"], ACT.Exp).then_inc(w["vec_out"], 1)
        act.wait(w["vec_in"])
        act.e.activation(vec["big"], vec["e"], ACT.Exp)
        act.e.activation(vec["sin"], vec["red"], ACT.Sin)
        act.e.activation(vec["half"], vec["red"], ACT.Sin, scale=0.5)
        act.e.activation(vec["cos"], vec["q"], ACT.Sin, scale=BELOW_TWO_PI).then_inc(w["vec_out"], 1)

    def dve_s5_vectors(dve):
        w, v = s5_sems, vec

        def tt(o, a, b, op):
            dve.link(dve.e.tensor_tensor(o, a, b, op))

        def ts(o, a, s1, s2, *ops):
            dve.link(dve.e.tensor_scalar(o, a, s1, s2, *ops))

        def stt(o, a, s, b, op1, op2):
            dve.link(dve.e.scalar_tensor_tensor(o, a, s, b, op1, op2))

        def nearest(o, a):
            ts(o, a, ROUND, ROUND, ALU.add, ALU.subtract)

        b = plan.b["s5a"]
        bank = full_bank(dve, b)
        dve.e.tensor_copy(v["lr"], bank[:, 0:S5_TILES])
        dve.e.tensor_copy(v["li"], bank[:, S5_TILES:2 * S5_TILES]).then_inc(bank_free[b % 4], 1)
        dve.e.wait_ge(s5_sems["a_landed"], 48)
        for h in range(2):
            ins = dve.e.tensor_copy(v["ldt"][h * HD:h * HD + HD, :], LDT_ROW[h * HD:h * HD + HD, :].rearrange("p (t h) -> p h t", h=2)[:, h, :])
        ins.then_inc(w["vec_in"], 1)
        dve.wait(w["vec_out"])
        tt(v["e"], v["lr"], v["dt"], ALU.mult)
        tt(v["th"], v["li"], v["dt"], ALU.mult)
        ts(v["n"], v["th"], 1 / TWO_PI, None, ALU.mult)
        nearest(v["n"], v["n"])
        stt(v["red"], v["n"], -TWO_PI_PARTS[0], v["th"], ALU.mult, ALU.add)
        stt(v["red"], v["n"], -TWO_PI_PARTS[1], v["red"], ALU.mult, ALU.add)
        stt(v["red"], v["n"], -TWO_PI_PARTS[2], v["red"], ALU.mult, ALU.add)
        ts(v["turn"], v["red"], 1 / TWO_PI, 0.5, ALU.mult, ALU.min)
        ts(v["turn"], v["turn"], -0.5, None, ALU.max)
        ts(v["red"], v["red"], BELOW_TWO_PI / 2, -BELOW_TWO_PI / 2, ALU.min, ALU.max)
        ts(v["q"], v["turn"], 0.25, None, ALU.add)
        nearest(v["p"], v["q"])
        dve.e.tensor_tensor(v["q"], v["q"], v["p"], ALU.subtract).then_inc(w["vec_in"], 1)
        ts(v["ec"], v["e"], 0.5, -0.5, ALU.min, ALU.max)
        ts(v["poly"], v["ec"], EXP_SERIES[0], None, ALU.mult)
        for c in EXP_SERIES[1:]:
            stt(v["poly"], v["poly"], c, v["ec"], ALU.add, ALU.mult)
        tt(v["p"], v["e"], v["e"], ALU.mult)
        ts(v["small"], v["p"], 0.25, None, ALU.is_lt)
        dve.wait(w["vec_out"])
        ts(v["big"], v["big"], 1.0, None, ALU.subtract)
        tt(v["poly"], v["poly"], v["big"], ALU.subtract)
        tt(v["poly"], v["poly"], v["small"], ALU.mult)
        tt(v["em1"], v["poly"], v["big"], ALU.add)
        ts(v["mag"], v["em1"], 1.0, None, ALU.add)
        tt(v["half"], v["half"], v["half"], ALU.mult)
        tt(v["nr"], v["em1"], v["cos"], ALU.mult)
        stt(v["nr"], v["half"], -2.0, v["nr"], ALU.mult, ALU.add)
        power = lambda part, n: A_POW[:, part, n, :]
        tt(power(0, 1), v["mag"], v["cos"], ALU.mult)
        tt(power(1, 1), v["mag"], v["sin"], ALU.mult)
        tt(v["den"], v["lr"], v["lr"], ALU.mult)
        tt(v["p"], v["li"], v["li"], ALU.mult)
        tt(v["den"], v["den"], v["p"], ALU.add)
        dve.link(dve.e.reciprocal(v["den"], v["den"]))
        for o, a, b, op in ((CR, ("nr", "lr"), "li", ALU.add), (CI, ("nr", "li"), "lr", ALU.subtract)):
            tt(v["p"], v[a[0]], v[a[1]], ALU.mult)
            tt(v["q"], power(1, 1), v[b], ALU.mult)
            tt(v["q"], v["q"], v["p"], op)
            tt(S5K[:, o, :], v["q"], v["den"], ALU.mult)
        dve.e.memset(power(0, 0), 1.0)
        dve.link(dve.e.memset(power(1, 0), 0.0))
        for n in range(2, S5_L + 1):
            tt(v["p"], power(0, n - 1), power(0, 1), ALU.mult)
            tt(v["q"], power(1, n - 1), power(1, 1), ALU.mult)
            tt(power(0, n), v["p"], v["q"], ALU.subtract)
            tt(v["p"], power(0, n - 1), power(1, 1), ALU.mult)
            tt(v["q"], power(1, n - 1), power(0, 1), ALU.mult)
            tt(power(1, n), v["p"], v["q"], ALU.add)
        for n in range(S5_L):
            ins = dve.e.tensor_copy(A_REV[:, :, n, :], A_POW[:, :, S5_L - 1 - n, :])
        tt(v["p"], v["mag"], v["mag"], ALU.mult)
        tt(S5K[:, MAG4, :], v["p"], v["p"], ALU.mult)
        ts(v["turn4"], v["turn"], float(S5_L), None, ALU.mult)
        nearest(v["p"], v["turn4"])
        tt(v["turn4"], v["turn4"], v["p"], ALU.subtract)
        ts(v["p"], v["turn4"], GRID, None, ALU.mult)
        nearest(v["p"], v["p"])
        ts(S5K[:, STEP_HI, :], v["p"], 1 / GRID, None, ALU.mult)
        tt(S5K[:, STEP_LO, :], v["turn4"], S5K[:, STEP_HI, :], ALU.subtract)

    def act_s5_load(act):
        w = s5_sems
        for i, (bn, cn) in enumerate((("od_b_re_2", "od_c_re_2"), ("od_b_im_2", "od_c_im_2"))):
            act.e.dma_start(BRAW[:, i], t[bn][0].rearrange("(t h) p c -> (h p) t c", h=2)).then_inc(w["landed"], 16)
            for twice in range(2):
                act.e.dma_start(CRAW[:, i, :, twice, :], t[cn][0].rearrange("(k g) c p -> (g c) k p", g=8)).then_inc(w["landed"], 16)

    def at4(e, k, size=4):
        return slice(4 * k, 4 * k + 4) if e is None else bass.ds(e * 8 + 4 * k, 4)

    def step_at(e, k):
        return slice(k, k + 1) if e is None else bass.ds(e * 2 + k, 1)

    def s5_a(k, i):
        return plan.b["s5"] + (4 + 6 * (k - 1) + i if k else i)

    def s5_y(k):
        return plan.b["s5"] + (4 + 6 * k + 4 if k < KD - 1 else 6 * KD - 2)

    def s5_out(k):
        return s5_y(k) + 1

    def s5_loop(eng, first, step, last, per):
        first()
        step(None, 0)
        with eng.loop((KD - 2) // 2, per) as e:
            for k in (1, 2):
                step(e, k)
        step(None, KD - 1)
        last()

    def t2(e, n):
        return 0 if e is None else e * n

    def pool_s5_consts(pool):
        w = s5_sems
        pool.e.wait_ge(s5_sems["landed"], 96)
        for s in range(2):
            pool.e.wait_ge(evac[s], plan.p["s5"] // 2)
        for n in range(S5_LOW):
            pool.e.memset(S5_AT[:, n:n + 1], float(n))
        for n in range(S5_HIGH):
            pool.e.memset(S5_AT[:, S5_LOW + n:S5_LOW + n + 1], float(n * S5_LOW))
        pool.link(pool.e.memset(FIRST[:], 1.0))
        pool.e.memset(FIRST[:, 0:1], 0.0)
        pool.e.memset(W3[:], 0.0)
        pool.e.memset(W1X[:], 0.0)
        pool.e.memset(CAX[:], 0.0).then_inc(w["consts"], 1)
        pool.wait(w["consts"])
        pool.wait(w["bb"])
        pool.wait(w["tab"])
        pool.e.wait_ge(bank_ready, plan.b["s5c"] + 4)

    def pool_tt(pool, o, a, b, op):
        pool.link(pool.e.tensor_tensor(o, a, b, op))

    def pool_s5_step(pool, k):
        w, par, tiles = s5_sems, k % 2, slice(4 * k, 4 * k + 4)
        if k >= 2:
            pool.e.wait_ge(bank_ready, s5_a(k - 2, 2) + 1)
        q = PRP[:].rearrange("p a t n -> p (a t n)").rearrange("p (q t j c) -> p q t j c", q=4, t=4, j=S5_L)
        shape = lambda a: bcast(a, 2, S5_L)
        br, bi = (shape(BB[:, i, tiles, :]) for i in range(2))
        ar, ai = (bcast(A_REV[:, i, :, tiles].rearrange("p j t -> p t j"), 3, S5_C) for i in range(2))
        for i, (a, b) in enumerate(((br, ar), (bi, ai), (br, ai), (bi, ar))):
            pool_tt(pool, q[:, i], a, b, ALU.mult)
        for part, op in ((0, ALU.subtract), (1, ALU.add)):
            for h in range(2):
                rows = slice(h * HD, h * HD + HD)
                ins = pool.e.tensor_tensor(W1X[rows, par, part, :, :, h, :], q[rows, 2 * part], q[rows, 2 * part + 1], op)
                if part + h < 2:
                    pool.link(ins)
        ins.then_inc(w["w1x"], 1)
        pool.wait(w["w1x"])
        if k >= 2:
            pool.e.wait_ge(w["state"], k - 1)
        low = lambda i: bcast(TAB[:, i, tiles, 0:S5_LOW], 2, S5_HIGH)
        high = lambda i: bcast(TAB[:, i, tiles, S5_LOW:], 3, S5_LOW)
        table = lambda i: TURNING[:, par, i].rearrange("p t (h l) -> p t h l", l=S5_LOW)
        tmp = [PRP[:, i].rearrange("p t (h l) -> p t h l", l=S5_LOW) for i in range(2)]
        for i, (a, b, c, d, op) in enumerate(((1, 1, 0, 0, ALU.subtract), (0, 1, 1, 0, ALU.add))):
            pool_tt(pool, tmp[0], high(a), low(b), ALU.mult)
            pool_tt(pool, tmp[1], high(c), low(d), ALU.mult)
            pool_tt(pool, table(i), tmp[0], tmp[1], op)
        pool.e.tensor_tensor(TURNING[:, par, 2], bcast(FIRST[:], 1, 4), bcast(S5K[:, MAG4, tiles], 2, S5_N), ALU.mult)\
            .then_inc(w["turning"], 1)
        pool.wait(w["turning"])

    def pool_s5(pool):
        pool_s5_consts(pool)
        for k in range(KD):
            pool_s5_step(pool, k)

    def pe_s5_prepare(pe, e, k):
        w, par = s5_sems, k % 2
        pe.wait(w["w1x"])
        for part in range(2):
            bank = take_bank(pe, s5_a(k, part), t2(e, 3))
            for i in range(4):
                ins = nc.tensor.transpose(bank[:, i * P:i * P + P], W1X[:, par, part, i].rearrange("p j h c -> p (j h c)"), IDENT[:])
            ins.then_inc(bank_ready, 1)
        pe.wait(w["ca"])
        bank = take_bank(pe, s5_a(k, 2), t2(e, 3))
        for i in range(4):
            for part in range(2):
                ins = nc.tensor.matmul(bank[0:32, i * P:i * P + P], W1X[:, par, part, i, S5_L - 1].rearrange("p h c -> p (h c)"),
                                       CAX[:, par, part, i, 0:S5_L].rearrange("p j h c -> p (j h c)"), start=part == 0, stop=part == 1)
        ins.then_inc(bank_ready, 1)
        bank = take_bank(pe, s5_a(k, 3), t2(e, 3))
        for i in range(4):
            for j in range(S5_L):
                src = HF[:, step_at(e, k), :].rearrange("p k (n l) -> p (k n) l", l=S5_L)[:, :, j]
                ins = nc.tensor.matmul(bank[32 * j:32 * j + 32, i * P:i * P + P], IDENT[:, 32 * i:32 * i + 32], src, start=True, stop=True)
        ins.then_inc(bank_ready, 1)
        pair = take_pair(pe, plan.p["s5"] + k, t2(e, 1))
        b = s5_a(k, 3)
        pe.e.wait_ge(bank_free[b % 4], t2(e, 3) + (b // 4 + 1))
        for part in range(2):
            for i in range(4):
                ins = nc.tensor.matmul(pair[:, part, i * P:i * P + P], W1_T[:, par, part, i, :], U4[:, par, i, :], start=True, stop=True)
        ins.then_inc(w["bu"], 1)

    def pe_s5_output(pe, e, k):
        w, par = s5_sems, k % 2
        pe.wait(w["state"])
        bank = take_bank(pe, s5_y(k), t2(e, 3))
        for i in range(4):
            nc.tensor.matmul(bank[:, i * P:i * P + P], W3[:, par, i, :], U4[:, par, i, :], start=True, stop=False)
            for part in range(2):
                ins = nc.tensor.matmul(bank[:, i * P + 1:i * P + P], CAX[:, par, part, i, 1:].rearrange("p j h c -> p (j h c)"),
                                       XS[:, part, i, 0:S5_N - 1], start=False, stop=part == 1)
        ins.then_inc(bank_ready, 1)
        bank = take_bank(pe, s5_out(k), t2(e, 3))
        b = s5_y(k)
        pe.e.wait_ge(bank_free[b % 4], t2(e, 3) + (b // 4 + 1))
        for i in range(4):
            for j in range(S5_L):
                ins = nc.tensor.matmul(bank[32 * i:32 * i + 32, :].rearrange("p (n l) -> p n l", l=S5_L)[:, :, j],
                                       IDENT[:, 32 * j:32 * j + 32], Y4[:, i, :], start=True, stop=True)
        ins.then_inc(bank_ready, 1)

    def pe_s5(pe):
        w = s5_sems
        b = plan.b["s5c"]
        pe.e.wait_ge(w["landed"], 96)
        for m in range(4):
            bank = take_bank(pe, b + m)
            for n in range(4):
                part, k = m // 2, 4 * (m % 2) + n
                ins = nc.tensor.transpose(bank[:, n * P:n * P + P], CRAW[:, part, k].rearrange("p d q -> p (d q)"), IDENT[:])
            ins.then_inc(bank_ready, 1)
        pe.wait(h_ready)

        def step(e, k):
            if e is not None or k < KD - 1:
                pe_s5_prepare(pe, e, k + 1)
            pe_s5_output(pe, e, k)

        pe_s5_prepare(pe, None, 0)
        for k in range(KD):
            step(None, k)

    def act_s5_prepare(act, e, k):
        par = k % 2
        if k >= 2:
            act.e.wait_ge(bank_ready, t2(e, 12) + (s5_y(k - 2) + 1))
        for part in range(2):
            b = s5_a(k, part)
            bank = full_bank(act, b, t2(e, 3))
            act.e.activation(W1_T[:, par, part].rearrange("p t n -> p (t n)"), bank[:], ACT.Copy).then_inc(bank_free[b % 4], 1)
        b = s5_a(k, 2)
        kernel = full_bank(act, b, t2(e, 3))[0:32, :].rearrange("p (t n) -> p t n", n=P)
        for j in range(S5_L):
            ins = act.e.activation(W3[32 * j:32 * j + 32, par, :, 32 * j:], kernel[:, :, 0:P - 32 * j], ACT.Copy)
        ins.then_inc(bank_free[b % 4], 1)
        b = s5_a(k, 3)
        act.e.activation(U4[:, par].rearrange("p t n -> p (t n)"), full_bank(act, b, t2(e, 3))[:], ACT.Copy).then_inc(bank_free[b % 4], 1)

    def act_s5_output(act, e, k):
        b = s5_y(k)
        if e is not None or k:
            act.e.wait_ge(bank_ready, t2(e, 12) + (s5_out(k - 1) + 1))
        act.e.activation(Y4[:].rearrange("p t n -> p (t n)"), full_bank(act, b, t2(e, 3))[:], ACT.Copy).then_inc(bank_free[b % 4], 1)

    def act_s5_gelu(act, e, k):
        w, par, b = s5_sems, k % 2, s5_out(k)
        act.e.wait_ge(bank_free[b % 4], t2(e, 3) + (b // 4 + 1))
        act.e.activation(SQ[:, par, :], TMP[:, par, :], ACT.Gelu_apprx_tanh).then_inc(w["gelu"], 1)
        act.wait(w["gelu"])
        settle(act)
        act.e.activation(HH[:, step_at(e, k), :], SQ[:, par:par + 1, :], ACT.Copy).then_inc(hi_ready, 1)

    def act_s5(act):
        w, b = s5_sems, plan.b["s5c"]
        for m in range(4):
            bank = full_bank(act, b + m)[:].rearrange("p (t h c) -> p t h c", h=2, c=S5_C)
            for h in range(2):
                rows = slice(h * HD, h * HD + HD)
                ins = act.e.activation(CK[rows, m // 2, 16 * (m % 2):16 * (m % 2) + 16, :], bank[rows, :, h, :], ACT.Copy)
            ins.then_inc(bank_free[(b + m) % 4], 1)
        act.wait(w["angles"])
        act.e.activation(TAB[:], TAB[:], ACT.Sin, scale=BELOW_TWO_PI).then_inc(w["tab"], 1)
        act.wait(w["consts"])

        def step(e, k):
            if e is not None or k < KD - 1:
                act_s5_prepare(act, e, k + 1)
            if e is not None or k:
                act_s5_gelu(act, e, k - 1)
            act_s5_output(act, e, k)

        s5_loop(act, lambda: act_s5_prepare(act, None, 0), step, lambda: act_s5_gelu(act, None, KD - 1), {w["gelu"]: 2})

    def dve_s5_start(dve):
        w = s5_sems
        dve.e.wait_ge(w["landed"], 96)
        dve.wait(w["consts"])
        q = [PR[:, i].rearrange("p t n -> p (t n)").rearrange("p (t c) -> p t c", c=S5_C) for i in range(4)]
        cr, ci = (bcast(S5K[:, i, :], 2, S5_C) for i in (CR, CI))
        for i, (a, b) in enumerate(((0, cr), (1, ci), (1, cr), (0, ci))):
            ins = dve.e.tensor_tensor(q[i], BRAW[:, a], b, ALU.mult)
        dve.link(ins)
        dve.e.tensor_tensor(BB[:, 0], q[0], q[1], ALU.subtract)
        dve.e.tensor_tensor(BB[:, 1], q[2], q[3], ALU.add).then_inc(w["bb"], 1)
        x, n = ANGLE[:, 0], ANGLE[:, 1]
        index = bcast(S5_AT[:], 1, S5_TILES)
        nearest = lambda: dve.link(dve.e.tensor_scalar(n, x, ROUND, ROUND, ALU.add, ALU.subtract))
        dve.link(dve.e.tensor_tensor(x, bcast(S5K[:, STEP_HI, :], 2, S5_IDX), index, ALU.mult))
        nearest()
        dve.link(dve.e.tensor_tensor(x, x, n, ALU.subtract))
        dve.link(dve.e.tensor_tensor(n, bcast(S5K[:, STEP_LO, :], 2, S5_IDX), index, ALU.mult))
        dve.link(dve.e.tensor_tensor(x, x, n, ALU.add))
        nearest()
        dve.link(dve.e.tensor_tensor(TAB[:, 0], x, n, ALU.subtract))
        dve.link(dve.e.tensor_scalar(x, x, 0.25, None, ALU.add))
        nearest()
        dve.e.tensor_tensor(TAB[:, 1], x, n, ALU.subtract).then_inc(w["angles"], 1)
        b = plan.b["s5c"] + 3
        dve.e.wait_ge(bank_free[b % 4], b // 4 + 1)

    def dve_s5_prepare(dve, e, k):
        w, par, tiles = s5_sems, k % 2, at4(e, k)
        n = 4 * (S5_L + 1) * S5_C
        q = [PR[:, i].rearrange("p t n -> p (t n)")[:, 0:n].rearrange("p (t j c) -> p t j c", t=4, c=S5_C) for i in range(4)]
        cr, ci = (bcast(CK[:, i, tiles, :], 2, S5_L + 1) for i in range(2))
        ar, ai = (bcast(A_POW[:, i, :, tiles].rearrange("p j t -> p t j"), 3, S5_C) for i in range(2))
        for i, (a, b) in enumerate(((cr, ar), (ci, ai), (cr, ai), (ci, ar))):
            ins = dve.e.tensor_tensor(q[i], a, b, ALU.mult)
        dve.link(ins)
        if k >= 2:
            dve.e.wait_ge(bank_ready, t2(e, 12) + (s5_y(k - 2) + 1))
        for h in range(2):
            rows = slice(h * HD, h * HD + HD)
            dve.e.tensor_tensor(CAX[rows, par, 0, :, :, h, :], q[0][rows], q[1][rows], ALU.subtract)
            ins = dve.e.scalar_tensor_tensor(CAX[rows, par, 1, :, :, h, :], q[2][rows], -1.0, q[3][rows], ALU.mult, ALU.subtract)
        ins.then_inc(w["ca"], 1)
        dve.wait(w["ca"])

    def dve_s5_states(dve, e, k):
        w, par, p = s5_sems, k % 2, plan.p["s5"] + k
        pair = PAIR[p % 2]
        dve.wait(w["bu"])
        dve.wait(w["turning"])
        flat = lambda a: a.rearrange("p t n -> p (t n)")
        cos, sin, decay = (flat(TURNING[:, par, i]) for i in range(3))
        q = [flat(PR[:, i]) for i in range(4)]
        for i, (part, tab) in enumerate(((0, cos), (1, sin), (1, cos), (0, sin))):
            ins = dve.e.tensor_tensor(q[i], pair[:, part, :], tab, ALU.mult)
        ins.then_inc(evac[p % 2], 1)
        dve.e.wait_ge(evac[p % 2], t2(e, 1) + (p // 2 + 1))
        dve.e.tensor_tensor(q[0], q[0], q[1], ALU.add)
        dve.link(dve.e.tensor_tensor(q[2], q[2], q[3], ALU.subtract))
        for i in (0, 2):
            ins = dve.e.tensor_tensor_scan(q[i + 1], decay, q[i], 0.0, ALU.mult, ALU.add)
        dve.link(ins)
        if e is not None or k:
            dve.e.wait_ge(bank_ready, t2(e, 12) + (s5_y(k - 1) + 1))
        for part, (a, b, op) in enumerate(((cos, sin, ALU.subtract), (sin, cos, ALU.add))):
            dve.e.tensor_tensor(q[0], q[1], a, ALU.mult)
            dve.link(dve.e.tensor_tensor(q[2], q[3], b, ALU.mult))
            ins = dve.e.tensor_tensor(flat(XS[:, part]), q[0], q[2], op)
            if part == 0:
                dve.link(ins)
        ins.then_inc(w["state"], 1)
        dve.wait(w["state"])

    def dve_s5_skip(dve, e, k):
        par, b = k % 2, s5_out(k)
        d = COLS[:, col_at["od_d"] + k:col_at["od_d"] + k + 1] if e is None else COLS[:, bass.ds(e * 2 + (col_at["od_d"] + k), 1)]
        bank = full_bank(dve, b, t2(e, 3))
        dve.e.scalar_tensor_tensor(TMP[:, par:par + 1, :], HF[:, step_at(e, k), :], d, bank[:].rearrange("p (a n) -> p a n", a=1),
                                   ALU.mult, ALU.add).then_inc(bank_free[b % 4], 1)

    def dve_s5_rest(dve, e, k):
        par = k % 2
        dve.wait(hi_ready)
        dve.e.tensor_tensor(HL[:, step_at(e, k), :], SQ[:, par:par + 1, :], HH[:, step_at(e, k), :].bitcast(F32), ALU.subtract)\
             .then_inc(h_ready, 1)
        dve.passed(h_ready, 1)

    def dve_s5(dve):
        w = s5_sems
        dve_s5_start(dve)

        def step(e, k):
            if e is not None or k < KD - 1:
                dve_s5_prepare(dve, e, k + 1)
            if e is not None or k:
                dve_s5_skip(dve, e, k - 1)
            dve_s5_states(dve, e, k)
            if e is not None or k:
                dve_s5_rest(dve, e, k - 1)

        def last():
            dve_s5_skip(dve, None, KD - 1)
            dve_s5_rest(dve, None, KD - 1)

        s5_loop(dve, lambda: dve_s5_prepare(dve, None, 0), step, last,
                {w["bu"]: 2, w["turning"]: 2, w["state"]: 2, w["ca"]: 2, hi_ready: 2, h_ready: 2, dve.chain: 12})

    out_saved = sem("out_saved")

    def sp_store(sp):
        for b in range(plan.b["store"] + KD - 4, plan.b["store"] + KD):
            sp.wait_ge(bank_free[b % 4], b // 4 + 1)
        sp.dma_start(out[0].rearrange("(t p) d -> p t d", p=P), OTOK[:]).then_inc(out_saved, 16)
        sp.wait_ge(out_saved, 16)

    def pe_store(pe):
        b = plan.b["store"]
        pe_after_h(pe, plan.p["store"])
        for k in range(KD):
            bank = take_bank(pe, b + k)
            for tt in range(NT):
                ins = nc.tensor.transpose(bank[:, tt * P:tt * P + P], X[:, k, tt * P:tt * P + P], IDENT[:])
            ins.then_inc(bank_ready, 1)

    def act_store(act):
        b = plan.b["store"]
        for k in range(KD):
            bank = full_bank(act, b + k)
            act.e.activation(OTOK[:, :, k * P:k * P + P], bank[:].rearrange("p (t c) -> p t c", c=P), ACT.Copy)\
                 .then_inc(bank_free[(b + k) % 4], 1)

    def act_program(act):
        act_loads(act.e)
        act_x(act)
        act_norm(act, 0)
        act_small_loads(act)
        act_mixin(act)
        act_pool(act)
        act_attention(act, 0, S0, PT0)
        act_norm(act, 1)
        act_router(act, 0)
        act_moe(act, 0)
        act_norm(act, 2)
        act_dt(act)
        act_ssm(act)
        act_ssm_out(act)
        act_norm(act, 3)
        act_router(act, 1)
        act_moe(act, 1)
        act_norm(act, FINAL)
        act_norm(act, 5)
        act_s5_rows(act)
        act_evin(act)
        act_gmlp(act)
        act_attention(act, 1, S1, PT1)
        act_s5_vectors(act)
        act_norm(act, 6)
        act_ffn(act, 0)
        act_ple_load(act, 0)
        act_s5_load(act)
        act_norm(act, 7)
        act_ple(act, 0)
        act_norm(act, PLAIN)
        act_s5(act)
        act_glu(act)
        act_norm(act, 9)
        act_ffn(act, 1)
        act_ple_load(act, 1)
        act_norm(act, 10)
        act_ple(act, 1)

    def pe_program(pe):
        pe_start(pe)
        pe_norm(pe, 0)
        pe_ada(pe, 0)
        pe_ada(pe, 1)
        pe_columns_rest(pe)
        pe_mixin(pe)
        pe_pool(pe)
        pe_attention(pe, 0, Q0, K0, V0, S0, PT0, False)
        pe_banks_read(pe, plan.b["att0"])
        pe_after_h(pe, plan.p["mixout"])
        pe_matrix(pe, "mixout", 4)
        pe_norm(pe, 1)
        for q in range(9, 12):
            pe_ada(pe, q)
        pe_router(pe, 0)
        pe_moe(pe, 0)
        pe_norm(pe, 2)
        pe_dt(pe)
        pe_ssm(pe)
        pe_ssm_out(pe)
        pe_norm(pe, 3)
        pe_router(pe, 1)
        pe_moe(pe, 1)
        pe_norm(pe, FINAL)
        pe_norm(pe, 5)
        pe_evin(pe)
        pe_gmlp(pe)
        pe_attention(pe, 1, Q1, K1, V1, S1, PT1, True)
        pe_s5_vectors(pe)
        pe.wait(half_ready, 4)
        pe_after_h(pe, plan.p["evout"])
        pe_matrix(pe, "evout", 4)
        pe_norm(pe, 6)
        pe_ffn(pe, 0)
        pe_ple_rows(pe, 0)
        pe_norm(pe, 7)
        pe_ple(pe, 0)
        pe_norm(pe, PLAIN)
        pe_s5(pe)
        pe_glu(pe)
        pe_norm(pe, 9)
        pe_ffn(pe, 1)
        pe_ple_rows(pe, 1)
        pe_norm(pe, 10)
        pe_ple(pe, 1)

    def dve_program(dve):
        dve_start(dve)
        dve_columns_rest(dve)
        dve_norm(dve, 0)
        dve_ada_mixin(dve)
        dve_pool(dve)
        dve_strip(dve)
        dve.wait(strip_ready)
        dve_attention(dve, 0, S0, lambda h: STRIP[:, h, :])
        dve_mixout(dve)
        dve_router_weights(dve, 0)
        dve_norm(dve, 1)
        for q in range(9, 12):
            dve_ada_end(dve, q)
        dve_router(dve, 0)
        dve_moe(dve, 0)
        dve_cut_narrow(dve, DT_WH[:], DT_WL[:], DT_W[:])
        dve_norm(dve, 2)
        dve_dt(dve)
        dve_ssm(dve)
        dve_ssm_out(dve)
        dve_router_weights(dve, 1)
        dve_norm(dve, 3)
        dve_router(dve, 1)
        dve_moe(dve, 1)
        dve_norm(dve, FINAL)
        dve_norm(dve, 5)
        dve_evin(dve)
        dve_gmlp(dve)
        dve_attention(dve, 1, S1, lambda h: CAUSAL[:])
        dve_s5_vectors(dve)
        dve_residual(dve, "evout", 4, 1, None)
        dve_norm(dve, 6)
        dve_ffn(dve, 0)
        dve_ple(dve, 0)
        dve_norm(dve, 7)
        dve_ple_gates(dve, 0)
        dve_norm(dve, PLAIN)
        dve_s5(dve)
        dve_glu(dve)
        dve_norm(dve, 9)
        dve_ffn(dve, 1)
        dve_ple(dve, 1)
        dve_norm(dve, 10)
        dve_ple_gates(dve, 1)

    def pool_program(pool):
        pool_constants(pool)
        pool_loads(pool.e)
        split_units(pool.e, 0, 2)
        pool_strip_dram(pool.e)
        pool_norm(pool)
        split_units(pool.e, 2, 4)
        split_units(pool.e, 4, 6)
        pool_strip(pool.e)
        split_units(pool.e, 6, plan.u["moe0"])
        pool_norm(pool)
        pool_moe(pool, 0)
        split_units(pool.e, plan.u["norm2"], plan.u["norm2"] + 2)
        pool_norm(pool)
        split_units(pool.e, plan.u["norm2"] + 2, plan.u["moe1"])
        pool_norm(pool)
        pool_moe(pool, 1)
        split_units(pool.e, plan.u["norm5"], plan.u["norm5"] + 2)
        pool_norm(pool)
        split_units(pool.e, plan.u["norm5"] + 2, plan.u["norm6"] + 2)
        pool_norm(pool)
        split_units(pool.e, plan.u["norm6"] + 2, plan.u["norm7"] + 2)
        pool_norm(pool)
        split_units(pool.e, plan.u["norm7"] + 2, plan.u["glu"] + 2)
        pool_s5(pool)
        split_units(pool.e, plan.u["glu"] + 2, plan.u["norm9"] + 2)
        pool_norm(pool)
        split_units(pool.e, plan.u["norm9"] + 2, plan.u["norm10"] + 2)
        pool_norm(pool)
        split_units(pool.e, plan.u["norm10"] + 2, plan.unit)

    def pe_banks_read(pe, b):
        for k in range(b - 4, b):
            pe.e.wait_ge(bank_free[k % 4], k // 4 + 1)

    sp_chain, pe_chain = sem("sp_chain"), sem("pe_chain")

    with ctx:
        block = ctx.enter_context(nc.Block())

        @block.scalar
        def _(eng):
            act = Engine(eng, act_chain)
            act_program(act)
            act_store(act)

        @block.sync
        def _(eng):
            sp = Engine(eng, sp_chain)
            sp_load_all(sp)
            sp_store(eng)

        @block.gpsimd
        def _(eng):
            pool_program(Engine(eng, pool_chain))

        @block.tensor
        def _(eng):
            pe = Engine(eng, pe_chain)
            pe_program(pe)
            pe_store(pe)

        @block.vector
        def _(eng):
            dve_program(Engine(eng, dve_chain))


def kernel(**inputs):
    import numpy as np
    import concourse.bacc as bacc
    from concourse.bass_utils import run_bass_kernel_spmd

    nc = bacc.Bacc("TRN2", target_bir_lowering=False, num_devices=1)
    arrays = {f"in_{name}": np.ascontiguousarray(value) for name, value in inputs.items()}
    arrays["in_rel_flip"] = np.ascontiguousarray(np.asarray(inputs["rel_bias"])[..., ::-1])
    t = {name[3:]: nc.dram_tensor(name, a.shape, F32, kind="ExternalInput").ap() for name, a in arrays.items()}
    out = nc.dram_tensor("out_0_dram", (1, SEQ, D), F32, kind="ExternalOutput").ap()
    build(nc, t, out)
    return run_bass_kernel_spmd(nc, [arrays], core_ids=[0]).results[0]["out_0_dram"]
```
